# Optimizing a Trainium2 kernel written in Bass

```python
import jax
import jax.numpy as jnp
from jax import lax
import numpy as np
import math

D_MODEL = 1024
BATCH = 1
SEQ = 256
DEPTH = 2

CTX_LEN = 256
GRID_W = 64
N_MOD = 6
RMS_EPS = 1e-6
NEG_INF = -1e30
D_POOL = D_MODEL // 2
POOL_WINDOWS = (2, 4, 8, 16)
D_POOL_GROUP = D_POOL // len(POOL_WINDOWS)
NA_HEAD_DIM = 64
D_NA = D_MODEL - D_POOL
NA_HEADS = D_NA // NA_HEAD_DIM
WIN_R = 8
WIN_C = 16
D_IN_EVEN = D_POOL + 3 * D_NA
RW_HEAD = 64
RW_HEADS = D_MODEL // RW_HEAD
DECAY_LORA = 64
AAA_LORA = 64
GATE_LORA = 128
GN_EPS = 64e-5
D_FF = 4 * D_MODEL


def rms_norm(x, g):
    xf = x.astype(jnp.float32)
    y = xf * lax.rsqrt(jnp.mean(xf * xf, axis=-1, keepdims=True) + RMS_EPS)
    return (y * g.astype(jnp.float32)).astype(x.dtype)

def modulate(h, shift, scale):
    return h * (1 + scale) + shift

def squared_relu_mlp(h, w1, w2):
    return jnp.square(jax.nn.relu(h @ w1)) @ w2

def split_heads(t, n_heads, head_dim):
    return t.reshape(t.shape[0], t.shape[1], n_heads, head_dim)

def pool_mixer(u, pool_w, pool_scale):
    L = u.shape[1]
    uf = u.astype(jnp.float32)
    cs = jnp.concatenate([jnp.zeros_like(uf[:, :1]), jnp.cumsum(uf, axis=1)], axis=1)
    t = jnp.arange(L)
    outs = []
    for gi, w in enumerate(POOL_WINDOWS):
        lo = jnp.clip(t - w // 2, 0, L)
        hi = jnp.clip(t + w // 2, 0, L)
        sl = slice(gi * D_POOL_GROUP, (gi + 1) * D_POOL_GROUP)
        csg = cs[..., sl]
        mean = (jnp.take(csg, hi, axis=1) - jnp.take(csg, lo, axis=1)) / (hi - lo).astype(jnp.float32)[None, :, None]
        outs.append((mean - uf[..., sl]).astype(u.dtype) @ pool_w[gi])
    return jnp.concatenate(outs, axis=-1) * pool_scale

def context_attention(q, k, v):
    B, L = q.shape[:2]
    s = jnp.einsum('bqhd,bkhd->bhqk', q, k).astype(jnp.float32) * (NA_HEAD_DIM ** -0.5)
    p = jax.nn.softmax(s, axis=-1).astype(v.dtype)
    return jnp.einsum('bhqk,bkhd->bqhd', p, v).reshape(B, L, D_NA)

def neighbourhood_attention(q, k, v, k_ctx, v_ctx, rpb):
    B, L = q.shape[:2]
    rows = L // GRID_W
    kr = min(WIN_R, rows)
    scale = NA_HEAD_DIM ** -0.5
    grid = lambda t: t.reshape(B, rows, GRID_W, NA_HEADS, NA_HEAD_DIM)
    qg, kg, vg = grid(q), grid(k), grid(v)
    col = jnp.arange(GRID_W)
    c_start = jnp.clip(col - WIN_C // 2, 0, GRID_W - WIN_C)
    col_ok = (col[None, :] >= c_start[:, None]) & (col[None, :] < c_start[:, None] + WIN_C)
    dc_idx = jnp.clip(col[None, :] - col[:, None], -(WIN_C - 1), WIN_C - 1) + WIN_C - 1
    rpb_c = rpb.astype(jnp.float32)[:, :, dc_idx]

    def row_block(args):
        q_row, r = args
        start = jnp.clip(r - kr // 2, 0, rows - kr)
        k_band = lax.dynamic_slice_in_dim(kg, start, kr, axis=1)
        v_band = lax.dynamic_slice_in_dim(vg, start, kr, axis=1)
        s_lat = jnp.einsum('bqhd,brkhd->bhqrk', q_row, k_band).astype(jnp.float32) * scale
        dr_idx = start + jnp.arange(kr) - r + WIN_R - 1
        bias = jnp.take(rpb_c, dr_idx, axis=1).transpose(0, 2, 1, 3)
        s_lat = jnp.where(col_ok[:, None, :], s_lat + bias, NEG_INF)
        s_ctx = jnp.einsum('bqhd,bchd->bhqc', q_row, k_ctx).astype(jnp.float32) * scale
        s = jnp.concatenate([s_lat.reshape(B, NA_HEADS, GRID_W, kr * GRID_W), s_ctx], axis=-1)
        p = jax.nn.softmax(s, axis=-1).astype(v.dtype)
        p_lat = p[..., :kr * GRID_W].reshape(B, NA_HEADS, GRID_W, kr, GRID_W)
        p_ctx = p[..., kr * GRID_W:]
        return (jnp.einsum('bhqrk,brkhd->bqhd', p_lat, v_band)
                + jnp.einsum('bhqc,bchd->bqhd', p_ctx, v_ctx))

    out = lax.map(row_block, (jnp.moveaxis(qg, 1, 0), jnp.arange(rows)))
    return jnp.moveaxis(out, 0, 1).reshape(B, L, D_NA)

def even_mixer(h, hc, w_in, w_out, pool_w, pool_scale, rpb, with_ctx):
    heads = lambda t: split_heads(t, NA_HEADS, NA_HEAD_DIM)
    u = h @ w_in
    q = heads(u[..., D_POOL:D_POOL + D_NA])
    k = heads(u[..., D_POOL + D_NA:D_POOL + 2 * D_NA])
    v = heads(u[..., D_POOL + 2 * D_NA:])
    if with_ctx:
        uc = hc @ w_in
        kv_c = uc[..., D_POOL + D_NA:]
    else:
        kv_c = hc @ w_in[:, D_POOL + D_NA:]
    k_c, v_c = heads(kv_c[..., :D_NA]), heads(kv_c[..., D_NA:])
    y = jnp.concatenate([pool_mixer(u[..., :D_POOL], pool_w, pool_scale),
                         neighbourhood_attention(q, k, v, k_c, v_c, rpb)], axis=-1) @ w_out
    if with_ctx:
        yc = jnp.concatenate([pool_mixer(uc[..., :D_POOL], pool_w, pool_scale),
                              context_attention(heads(uc[..., D_POOL:D_POOL + D_NA]), k_c, v_c)], axis=-1) @ w_out
    else:
        yc = None
    return y, yc

def centred_shift(x):
    prev = jnp.pad(x[:, :-1], ((0, 0), (1, 0), (0, 0)))
    nxt = jnp.pad(x[:, 1:], ((0, 0), (0, 1), (0, 0)))
    return 0.5 * (prev + nxt) - x

def rwkv_features(h, mu, wr, wk, wv, w0, w1, w2, a0, a1, a2, g1, g2, k_k, k_a, with_rg):
    B, L, _ = h.shape
    heads = lambda t: split_heads(t, RW_HEADS, RW_HEAD).astype(jnp.float32)
    xx = centred_shift(h)
    mix = lambda j: h + xx * mu[j]
    xw, xk, xv, xa = mix(1), mix(2), mix(3), mix(4)
    k = xk @ wk
    v = heads(xv @ wv)
    kk = heads(k * k_k)
    kk = kk * lax.rsqrt(jnp.maximum(jnp.sum(kk * kk, axis=-1, keepdims=True), 1e-24))
    kh = heads(k)
    k_a_h = k_a.reshape(RW_HEADS, RW_HEAD).astype(jnp.float32)
    dirs = []
    for d in range(2):
        w_raw = heads(w0[d] + jnp.tanh(xw @ w1[d]) @ w2[d])
        decay = jnp.exp(-jnp.exp(-jax.nn.softplus(-w_raw) - 0.5))
        a = jax.nn.sigmoid(heads(a0[d] + (xa @ a1[d]) @ a2[d]))
        k_d = kh * (1 + (a - 1) * k_a_h)
        dirs.append((decay, k_d, a))
    if with_rg:
        r = heads(mix(0) @ wr)
        g = jax.nn.sigmoid(mix(5) @ g1) @ g2
    else:
        r, g = None, None
    return v, kk, dirs, r, g

def wkv_scan(s0, decay, k, v, kk, a, r, reverse):
    tm = lambda t: jnp.moveaxis(t.astype(jnp.float32), 1, 0)
    emit = r is not None
    xs = (tm(decay), tm(k), tm(v), tm(kk), tm(kk * a)) + ((tm(r),) if emit else ())

    def step(S, inp):
        w_t, k_t, v_t, kk_t, kka_t = inp[:5]
        S = (S * w_t[:, :, None, :]
             - jnp.einsum('bhij,bhj->bhi', S, kk_t)[..., None] * kka_t[:, :, None, :]
             + v_t[..., None] * k_t[:, :, None, :])
        y = jnp.einsum('bhij,bhj->bhi', S, inp[5]) if emit else None
        return S, y

    S, ys = lax.scan(step, s0, xs, reverse=reverse)
    return S, (jnp.moveaxis(ys, 0, 1) if emit else None)

def rwkv_readout(y, r, k_sum, v, g, r_k, ln_g, ln_b, wo, dtype):
    B, L = y.shape[:2]
    mean = jnp.mean(y, axis=-1, keepdims=True)
    var = jnp.mean(jnp.square(y - mean), axis=-1, keepdims=True)
    yn = ((y - mean) * lax.rsqrt(var + GN_EPS)).reshape(B, L, D_MODEL) * ln_g + ln_b
    bonus = (jnp.sum(r * k_sum * r_k.astype(jnp.float32), axis=-1, keepdims=True) * v).reshape(B, L, D_MODEL)
    return ((yn + bonus) * g).astype(dtype) @ wo

def odd_mixer(h, hc, mu, wr, wk, wv, wo, w0, w1, w2, a0, a1, a2, g1, g2, k_k, k_a, r_k, ln_g, ln_b, with_ctx):
    feat = lambda t, rg: rwkv_features(t, mu, wr, wk, wv, w0, w1, w2, a0, a1, a2, g1, g2, k_k, k_a, rg)
    v, kk, dirs, r, g = feat(h, True)
    v_c, kk_c, dirs_c, r_c, g_c = feat(hc, with_ctx)
    s0 = jnp.zeros((h.shape[0], RW_HEADS, RW_HEAD, RW_HEAD), jnp.float32)
    ys, ys_c = [], []
    for d, reverse in enumerate((False, True)):
        decay_c, k_dc, a_c = dirs_c[d]
        s_ctx, y_c = wkv_scan(s0, decay_c, k_dc, v_c, kk_c, a_c, r_c, reverse)
        decay, k_d, a = dirs[d]
        _, y_d = wkv_scan(s_ctx, decay, k_d, v, kk, a, r, reverse)
        ys.append(y_d)
        ys_c.append(y_c)
    y = rwkv_readout(ys[0] + ys[1], r, dirs[0][1] + dirs[1][1], v, g, r_k, ln_g, ln_b, wo, h.dtype)
    if with_ctx:
        yc = rwkv_readout(ys_c[0] + ys_c[1], r_c, dirs_c[0][1] + dirs_c[1][1], v_c, g_c, r_k, ln_g, ln_b, wo, hc.dtype)
    else:
        yc = None
    return y, yc

def first_inputs(seed: int = 0) -> dict:
    key = jax.random.key(seed)
    ks = iter(jax.random.split(key, 40))
    n_even = (DEPTH + 1) // 2
    n_odd = DEPTH // 2
    D = D_MODEL
    nrm = lambda shape, s: jax.random.normal(next(ks), shape, jnp.float32) * s
    return {
        "x": nrm((BATCH, SEQ, D), 1.0),
        "c": nrm((BATCH, D), 1.0),
        "ctx": nrm((BATCH, CTX_LEN, D), 1.0),
        "c_ctx": nrm((D,), 1.0),
        "ada_w": nrm((DEPTH, D, N_MOD * D), 0.5 * D ** -0.5),
        "ada_b": nrm((DEPTH, N_MOD * D), 0.02),
        "norm_g": 1.0 + nrm((DEPTH, 4, D), 0.1),
        "mlp_w1": nrm((DEPTH, D, D_FF), D ** -0.5),
        "mlp_w2": nrm((DEPTH, D_FF, D), D_FF ** -0.5),
        "ev_w_in": nrm((n_even, D, D_IN_EVEN), D ** -0.5),
        "ev_w_out": nrm((n_even, D, D), D ** -0.5),
        "ev_pool_w": nrm((n_even, len(POOL_WINDOWS), D_POOL_GROUP, D_POOL_GROUP), D_POOL_GROUP ** -0.5),
        "ev_pool_scale": 1.0 + nrm((n_even, D_POOL), 0.1),
        "ev_rpb": nrm((n_even, NA_HEADS, 2 * WIN_R - 1, 2 * WIN_C - 1), 0.1),
        "rw_mu": jax.random.uniform(next(ks), (n_odd, 6, D), jnp.float32),
        "rw_wr": nrm((n_odd, D, D), D ** -0.5),
        "rw_wk": nrm((n_odd, D, D), D ** -0.5),
        "rw_wv": nrm((n_odd, D, D), D ** -0.5),
        "rw_wo": nrm((n_odd, D, D), D ** -0.5),
        "rw_w0": -2.0 + nrm((n_odd, 2, D), 0.5),
        "rw_w1": nrm((n_odd, 2, D, DECAY_LORA), D ** -0.5),
        "rw_w2": nrm((n_odd, 2, DECAY_LORA, D), 0.1 * DECAY_LORA ** -0.5),
        "rw_a0": nrm((n_odd, 2, D), 0.1),
        "rw_a1": nrm((n_odd, 2, D, AAA_LORA), D ** -0.5),
        "rw_a2": nrm((n_odd, 2, AAA_LORA, D), 0.1 * AAA_LORA ** -0.5),
        "rw_g1": nrm((n_odd, D, GATE_LORA), D ** -0.5),
        "rw_g2": nrm((n_odd, GATE_LORA, D), GATE_LORA ** -0.5),
        "rw_kk": 0.85 + nrm((n_odd, D), 0.05),
        "rw_ka": 1.0 + nrm((n_odd, D), 0.05),
        "rw_rk": nrm((n_odd, RW_HEADS, RW_HEAD), 0.1),
        "rw_lng": 1.0 + nrm((n_odd, D), 0.1),
        "rw_lnb": nrm((n_odd, D), 0.01),
    }

def first_block(x, c, ctx, c_ctx, ada_w, ada_b, norm_g, mlp_w1, mlp_w2,
              ev_w_in, ev_w_out, ev_pool_w, ev_pool_scale, ev_rpb,
              rw_mu, rw_wr, rw_wk, rw_wv, rw_wo, rw_w0, rw_w1, rw_w2,
              rw_a0, rw_a1, rw_a2, rw_g1, rw_g2, rw_kk, rw_ka, rw_rk, rw_lng, rw_lnb):
    silu_c = jax.nn.silu(c)
    silu_cc = jax.nn.silu(c_ctx)
    for i in range(DEPTH):
        j = i // 2
        with_ctx = i < DEPTH - 1
        mod = (silu_c @ ada_w[i] + ada_b[i])[:, None, :]
        mod_c = silu_cc @ ada_w[i] + ada_b[i]
        sh1, sc1, gt1, sh2, sc2, gt2 = jnp.split(mod, N_MOD, axis=-1)
        sh1c, sc1c, gt1c, sh2c, sc2c, gt2c = jnp.split(mod_c, N_MOD, axis=-1)
        h = modulate(rms_norm(x, norm_g[i, 0]), sh1, sc1)
        hc = modulate(rms_norm(ctx, norm_g[i, 0]), sh1c, sc1c)
        if i % 2 == 0:
            y, yc = even_mixer(h, hc, ev_w_in[j], ev_w_out[j], ev_pool_w[j], ev_pool_scale[j], ev_rpb[j], with_ctx)
        else:
            y, yc = odd_mixer(h, hc, rw_mu[j], rw_wr[j], rw_wk[j], rw_wv[j], rw_wo[j],
                              rw_w0[j], rw_w1[j], rw_w2[j], rw_a0[j], rw_a1[j], rw_a2[j],
                              rw_g1[j], rw_g2[j], rw_kk[j], rw_ka[j], rw_rk[j], rw_lng[j], rw_lnb[j], with_ctx)
        x = x + gt1 * rms_norm(y, norm_g[i, 1])
        h = modulate(rms_norm(x, norm_g[i, 2]), sh2, sc2)
        x = x + gt2 * rms_norm(squared_relu_mlp(h, mlp_w1[i], mlp_w2[i]), norm_g[i, 3])
        if with_ctx:
            ctx = ctx + gt1c * rms_norm(yc, norm_g[i, 1])
            hc = modulate(rms_norm(ctx, norm_g[i, 2]), sh2c, sc2c)
            ctx = ctx + gt2c * rms_norm(squared_relu_mlp(hc, mlp_w1[i], mlp_w2[i]), norm_g[i, 3])
    return x


HEAD_DIM = 64
ROPE_DIM = HEAD_DIM // 4
ROPE_THETA = 500000.0
NORM_EPS = 1e-6
NEG_INF_2 = -1e30
FORCE_SCORE = 1e6

MOBA_HEADS = D_MODEL // (2 * HEAD_DIM)
MOBA_BLOCK = 256
MOBA_TOPK = 3
MOBA_QCHUNK = 32
DIFF_HEADS = D_MODEL // (4 * HEAD_DIM)
DIFF_VDIM = 2 * HEAD_DIM
DIFF_QCHUNK = 128
MOBA_W = MOBA_HEADS * HEAD_DIM
DIFF_QK_W = DIFF_HEADS * 2 * HEAD_DIM
DIFF_V_W = DIFF_HEADS * DIFF_VDIM
EVEN_IN = 3 * MOBA_W + 2 * DIFF_QK_W + DIFF_V_W
EVEN_MIX = MOBA_W + DIFF_V_W

NSA_HEADS = D_MODEL // HEAD_DIM
NSA_GROUP = 4
NSA_KV_HEADS = NSA_HEADS // NSA_GROUP
CMP_BLOCK = 32
CMP_STRIDE = 16
CMP_HIDDEN = 256
SLC_BLOCK = 64
SLC_TOPN = 16
WINDOW = 512
NSA_QCHUNK = 16
NSA_Q_W = NSA_HEADS * HEAD_DIM
NSA_KV_W = NSA_KV_HEADS * HEAD_DIM
ODD_IN = NSA_Q_W + 6 * NSA_KV_W + 3 * NSA_HEADS
ODD_MIX = NSA_Q_W

MOE_GROUPS = 4
MOE_PER_GROUP = 4
MOE_EXPERTS = MOE_GROUPS * MOE_PER_GROUP
MOE_TOPK = 2
MOE_FF = 256

N_EVEN = (DEPTH + 1) // 2
N_ODD = DEPTH // 2


def rms_norm_2(x, g):
    xf = x.astype(jnp.float32)
    y = xf * lax.rsqrt(jnp.mean(xf * xf, axis=-1, keepdims=True) + NORM_EPS)
    return (y * g.astype(jnp.float32)).astype(x.dtype)

def rope_tables(seq):
    pos = jnp.arange(seq, dtype=jnp.float32)
    inv = ROPE_THETA ** (-jnp.arange(0, ROPE_DIM, 2, dtype=jnp.float32) / ROPE_DIM)
    ang = pos[:, None] * inv[None, :]
    return jnp.cos(ang), jnp.sin(ang)

def apply_rope(t, cos, sin):
    half = ROPE_DIM // 2
    c = cos.astype(t.dtype)
    s = sin.astype(t.dtype)
    t1 = t[..., :half]
    t2 = t[..., half:ROPE_DIM]
    return jnp.concatenate([t1 * c - t2 * s, t2 * c + t1 * s, t[..., ROPE_DIM:]], axis=-1)

def split_heads_2(t, n):
    b, s, _ = t.shape
    return t.reshape(b, s, n, -1).transpose(0, 2, 1, 3)

def merge_heads(t):
    b, h, s, d = t.shape
    return t.transpose(0, 2, 1, 3).reshape(b, s, h * d)

def gather_blocks(blocks, idx):
    return jax.vmap(jax.vmap(lambda bl, ix: bl[ix]))(blocks, idx)

def moba_attention(q, k, v):
    b, h, s, d = q.shape
    nb = -(-s // MOBA_BLOCK)
    pad = nb * MOBA_BLOCK - s
    kp = jnp.pad(k, ((0, 0), (0, 0), (0, pad), (0, 0)))
    vp = jnp.pad(v, ((0, 0), (0, 0), (0, pad), (0, 0)))
    kb = kp.reshape(b, h, nb, MOBA_BLOCK, d)
    vb = vp.reshape(b, h, nb, MOBA_BLOCK, d)
    kmean = jnp.mean(kb.astype(jnp.float32), axis=3)
    ksel = max(1, min(MOBA_TOPK, nb - 1))
    scale = d ** -0.5
    nq = s // MOBA_QCHUNK
    qc = jnp.moveaxis(q.reshape(b, h, nq, MOBA_QCHUNK, d), 2, 0)

    def chunk(args):
        qi, ci = args
        q0 = ci * MOBA_QCHUNK
        qpos = q0 + jnp.arange(MOBA_QCHUNK)
        own = q0 // MOBA_BLOCK
        gs = jnp.einsum('bhqd,bhnd->bhqn', qi.astype(jnp.float32), kmean)
        gs = jnp.where(jnp.arange(nb) < own, gs, NEG_INF_2)
        _, idx = lax.top_k(gs, ksel)
        valid = idx < own
        k_sel = gather_blocks(kb, idx)
        v_sel = gather_blocks(vb, idx)
        s_sel = jnp.einsum('bhqd,bhqnld->bhqnl', qi, k_sel).astype(jnp.float32) * scale
        s_sel = jnp.where(valid[..., None], s_sel, NEG_INF_2).reshape(b, h, MOBA_QCHUNK, ksel * MOBA_BLOCK)
        k_own = lax.dynamic_slice_in_dim(kp, own * MOBA_BLOCK, MOBA_BLOCK, axis=2)
        v_own = lax.dynamic_slice_in_dim(vp, own * MOBA_BLOCK, MOBA_BLOCK, axis=2)
        kpos = own * MOBA_BLOCK + jnp.arange(MOBA_BLOCK)
        s_own = jnp.einsum('bhqd,bhld->bhql', qi, k_own).astype(jnp.float32) * scale
        s_own = jnp.where(kpos[None, :] <= qpos[:, None], s_own, NEG_INF_2)
        p = jax.nn.softmax(jnp.concatenate([s_sel, s_own], axis=-1), axis=-1).astype(v.dtype)
        p_sel = p[..., :ksel * MOBA_BLOCK].reshape(b, h, MOBA_QCHUNK, ksel, MOBA_BLOCK)
        p_own = p[..., ksel * MOBA_BLOCK:]
        return (jnp.einsum('bhqnl,bhqnld->bhqd', p_sel, v_sel)
                + jnp.einsum('bhql,bhld->bhqd', p_own, v_own))

    o = lax.map(chunk, (qc, jnp.arange(nq)))
    return jnp.moveaxis(o, 0, 2).reshape(b, h, s, d)

def diff_attention(q, k, v, lam):
    b, h, _, s, d = q.shape
    nq = s // DIFF_QCHUNK
    scale = d ** -0.5
    kpos = jnp.arange(s)
    qc = jnp.moveaxis(q.reshape(b, h, 2, nq, DIFF_QCHUNK, d), 3, 0)

    def chunk(args):
        qi, ci = args
        qpos = ci * DIFF_QCHUNK + jnp.arange(DIFF_QCHUNK)
        sc = jnp.einsum('bhmqd,bhmkd->bhmqk', qi, k).astype(jnp.float32) * scale
        sc = jnp.where(kpos[None, :] <= qpos[:, None], sc, NEG_INF_2)
        p = jax.nn.softmax(sc, axis=-1)
        w = p[:, :, 0] - lam * p[:, :, 1]
        return jnp.einsum('bhqk,bhke->bhqe', w.astype(v.dtype), v)

    o = lax.map(chunk, (qc, jnp.arange(nq)))
    return jnp.moveaxis(o, 0, 2).reshape(b, h, s, -1)

def compress_blocks(t, pos_emb, w1, b1, w2, b2):
    b, g, s, d = t.shape
    nc = (s - CMP_BLOCK) // CMP_STRIDE + 1
    idx = jnp.arange(nc)[:, None] * CMP_STRIDE + jnp.arange(CMP_BLOCK)[None, :]
    blocks = t[:, :, idx, :] + pos_emb.astype(t.dtype)
    hid = jax.nn.gelu(jnp.einsum('bgnld,ldf->bgnf', blocks, w1.reshape(CMP_BLOCK, d, -1)) + b1)
    return jnp.einsum('bgnf,fe->bgne', hid, w2) + b2

def nsa_attention(q, kc, vc, ks, vs, kw, vw, gates):
    b, hq, s, d = q.shape
    g = NSA_KV_HEADS
    r = NSA_GROUP
    nc = kc.shape[2]
    ns = s // SLC_BLOCK
    nsel = min(SLC_TOPN, ns)
    scale = d ** -0.5
    cmp_start = jnp.arange(nc) * CMP_STRIDE
    cmp_end = cmp_start + CMP_BLOCK - 1
    slc_start = jnp.arange(ns) * SLC_BLOCK
    overlap = ((cmp_start[:, None] <= slc_start[None, :] + SLC_BLOCK - 1)
               & (cmp_end[:, None] >= slc_start[None, :])).astype(jnp.float32)
    ksb = ks.reshape(b, g, ns, SLC_BLOCK, d)
    vsb = vs.reshape(b, g, ns, SLC_BLOCK, d)
    kwp = jnp.pad(kw, ((0, 0), (0, 0), (WINDOW, 0), (0, 0)))
    vwp = jnp.pad(vw, ((0, 0), (0, 0), (WINDOW, 0), (0, 0)))
    nq = s // NSA_QCHUNK
    qc = jnp.moveaxis(q.reshape(b, hq, nq, NSA_QCHUNK, d), 2, 0)
    gc = jnp.moveaxis(gates.reshape(b, hq, nq, NSA_QCHUNK, 3), 2, 0)
    blk = jnp.arange(ns)

    def chunk(args):
        qi, gi, ci = args
        q0 = ci * NSA_QCHUNK
        qpos = q0 + jnp.arange(NSA_QCHUNK)
        qg = qi.reshape(b, g, r, NSA_QCHUNK, d)
        s_c = jnp.einsum('bgrqd,bgnd->bgrqn', qg, kc).astype(jnp.float32) * scale
        s_c = jnp.where(cmp_end[None, :] <= qpos[:, None], s_c, NEG_INF_2)
        p_c = jax.nn.softmax(s_c, axis=-1)
        p_c = jnp.where((qpos >= CMP_BLOCK - 1)[:, None], p_c, 0.0)
        o_c = jnp.einsum('bgrqn,bgnd->bgrqd', p_c.astype(vc.dtype), vc)
        imp = jnp.einsum('bgrqn,nj->bgqj', p_c, overlap)
        own = qpos // SLC_BLOCK
        started = slc_start[None, :] <= qpos[:, None]
        forced = (blk[None, :] == 0) | (blk[None, :] == own[:, None]) | (blk[None, :] == own[:, None] - 1)
        imp = jnp.where(started, jnp.where(forced, FORCE_SCORE, imp), NEG_INF_2)
        _, sidx = lax.top_k(imp, nsel)
        k_sel = gather_blocks(ksb, sidx)
        v_sel = gather_blocks(vsb, sidx)
        s_s = jnp.einsum('bgrqd,bgqnld->bgrqnl', qg, k_sel).astype(jnp.float32) * scale
        tok = sidx[..., None] * SLC_BLOCK + jnp.arange(SLC_BLOCK)
        s_s = jnp.where((tok <= qpos[:, None, None])[:, :, None], s_s, NEG_INF_2)
        p_s = jax.nn.softmax(s_s.reshape(b, g, r, NSA_QCHUNK, -1), axis=-1).reshape(s_s.shape)
        o_s = jnp.einsum('bgrqnl,bgqnld->bgrqd', p_s.astype(v_sel.dtype), v_sel)
        k_w = lax.dynamic_slice_in_dim(kwp, q0, WINDOW + NSA_QCHUNK, axis=2)
        v_w = lax.dynamic_slice_in_dim(vwp, q0, WINDOW + NSA_QCHUNK, axis=2)
        kpos = q0 - WINDOW + jnp.arange(WINDOW + NSA_QCHUNK)
        band = ((kpos[None, :] <= qpos[:, None]) & (kpos[None, :] > qpos[:, None] - WINDOW)
                & (kpos[None, :] >= 0))
        s_w = jnp.einsum('bgrqd,bgkd->bgrqk', qg, k_w).astype(jnp.float32) * scale
        p_w = jax.nn.softmax(jnp.where(band, s_w, NEG_INF_2), axis=-1)
        o_w = jnp.einsum('bgrqk,bgkd->bgrqd', p_w.astype(v_w.dtype), v_w)
        gt = gi.reshape(b, g, r, NSA_QCHUNK, 3).astype(o_c.dtype)
        o = gt[..., 0:1] * o_c + gt[..., 1:2] * o_s + gt[..., 2:3] * o_w
        return o.reshape(b, hq, NSA_QCHUNK, d)

    o = lax.map(chunk, (qc, gc, jnp.arange(nq)))
    return jnp.moveaxis(o, 0, 2).reshape(b, hq, s, d)

def even_mixer_2(h, w_in, w_out, lam_p, subln_g, lambda_init, cos, sin):
    b, s, _ = h.shape
    p = h @ w_in
    c1 = MOBA_W
    c2 = 2 * MOBA_W
    c3 = 3 * MOBA_W
    c4 = c3 + DIFF_QK_W
    c5 = c4 + DIFF_QK_W
    qa, ka, va, qb, kb, vb = jnp.split(p, [c1, c2, c3, c4, c5], axis=-1)
    qa = apply_rope(split_heads_2(qa, MOBA_HEADS), cos, sin)
    ka = apply_rope(split_heads_2(ka, MOBA_HEADS), cos, sin)
    oa = moba_attention(qa, ka, split_heads_2(va, MOBA_HEADS))
    qb = apply_rope(qb.reshape(b, s, DIFF_HEADS, 2, HEAD_DIM).transpose(0, 2, 3, 1, 4), cos, sin)
    kb = apply_rope(kb.reshape(b, s, DIFF_HEADS, 2, HEAD_DIM).transpose(0, 2, 3, 1, 4), cos, sin)
    lp = lam_p.astype(jnp.float32)
    lam = jnp.exp(jnp.sum(lp[0] * lp[1])) - jnp.exp(jnp.sum(lp[2] * lp[3])) + lambda_init
    ob = diff_attention(qb, kb, split_heads_2(vb, DIFF_HEADS), lam)
    ob = rms_norm_2(ob, subln_g) * (1.0 - lambda_init)
    o = jnp.concatenate([merge_heads(oa), merge_heads(ob)], axis=-1)
    return o @ w_out

def odd_mixer_2(h, w_in, w_out, cmp_pos, cmp_w1, cmp_b1, cmp_w2, cmp_b2, cos, sin):
    b, s, _ = h.shape
    p = h @ w_in
    cuts = [NSA_Q_W + i * NSA_KV_W for i in range(7)]
    q, kc, vc, ks, vs, kw, vw, gl = jnp.split(p, cuts, axis=-1)
    q = apply_rope(split_heads_2(q, NSA_HEADS), cos, sin)
    kc = apply_rope(split_heads_2(kc, NSA_KV_HEADS), cos, sin)
    ks = apply_rope(split_heads_2(ks, NSA_KV_HEADS), cos, sin)
    kw = apply_rope(split_heads_2(kw, NSA_KV_HEADS), cos, sin)
    vc = split_heads_2(vc, NSA_KV_HEADS)
    vs = split_heads_2(vs, NSA_KV_HEADS)
    vw = split_heads_2(vw, NSA_KV_HEADS)
    gates = jax.nn.sigmoid(gl.astype(jnp.float32)).reshape(b, s, NSA_HEADS, 3).transpose(0, 2, 1, 3)
    k_cmp = compress_blocks(kc, cmp_pos[0], cmp_w1[0], cmp_b1[0], cmp_w2[0], cmp_b2[0])
    v_cmp = compress_blocks(vc, cmp_pos[1], cmp_w1[1], cmp_b1[1], cmp_w2[1], cmp_b2[1])
    o = nsa_attention(q, k_cmp, v_cmp, ks, vs, kw, vw, gates)
    return merge_heads(o) @ w_out

def hier_moe(h, wg, bg, we, be, w_gate, w_up, w_down):
    b, s, d = h.shape
    t = h.reshape(-1, d)
    n = t.shape[0]
    gl = (t @ wg + bg).astype(jnp.float32)
    gp = jax.nn.softmax(gl, axis=-1)
    _, gsel = lax.top_k(gl, 1)
    g_oh = jax.nn.one_hot(gsel[:, 0], MOE_GROUPS, dtype=jnp.float32)
    gw = jnp.sum(gp * g_oh, axis=-1, keepdims=True)
    el = (t @ we + be).astype(jnp.float32).reshape(n, MOE_GROUPS, MOE_PER_GROUP)
    el_g = jnp.sum(el * g_oh[:, :, None], axis=1)
    tv, ti = lax.top_k(el_g, MOE_TOPK)
    tw = jax.nn.softmax(tv, axis=-1)
    w_grp = jnp.sum(jax.nn.one_hot(ti, MOE_PER_GROUP, dtype=jnp.float32) * tw[..., None], axis=1)
    comb = ((g_oh * gw)[:, :, None] * w_grp[:, None, :]).reshape(n, MOE_EXPERTS)
    a = jax.nn.silu(jnp.einsum('td,edf->tef', t, w_gate)) * jnp.einsum('td,edf->tef', t, w_up)
    y = jnp.einsum('tef,efd->td', a * comb[:, :, None].astype(a.dtype), w_down)
    return y.reshape(b, s, d)

def second_inputs(seed: int = 0) -> dict:
    key = jax.random.key(seed)
    ks = jax.random.split(key, 28)
    D = D_MODEL

    def nrm(k, shape, std):
        return jax.random.normal(k, shape, jnp.float32) * std

    return {
        'x': nrm(ks[0], (BATCH, SEQ, D), 1.0),
        'c': nrm(ks[1], (BATCH, D), 1.0),
        'norm1_g': 1.0 + nrm(ks[2], (DEPTH, D), 0.02),
        'norm2_g': 1.0 + nrm(ks[3], (DEPTH, D), 0.02),
        'final_g': 1.0 + nrm(ks[4], (D,), 0.02),
        'ada_w': nrm(ks[5], (DEPTH, D, 6 * D), 0.5 * D ** -0.5),
        'ada_b': nrm(ks[6], (DEPTH, 6 * D), 0.02),
        'ev_w_in': nrm(ks[7], (N_EVEN, D, EVEN_IN), D ** -0.5),
        'ev_w_out': nrm(ks[8], (N_EVEN, EVEN_MIX, D), EVEN_MIX ** -0.5),
        'ev_lambda': nrm(ks[9], (N_EVEN, 4, HEAD_DIM), 0.1),
        'ev_subln_g': 1.0 + nrm(ks[10], (N_EVEN, DIFF_VDIM), 0.02),
        'od_w_in': nrm(ks[11], (N_ODD, D, ODD_IN), D ** -0.5),
        'od_w_out': nrm(ks[12], (N_ODD, ODD_MIX, D), ODD_MIX ** -0.5),
        'od_cmp_pos': nrm(ks[13], (N_ODD, 2, CMP_BLOCK, HEAD_DIM), 0.1),
        'od_cmp_w1': nrm(ks[14], (N_ODD, 2, CMP_BLOCK * HEAD_DIM, CMP_HIDDEN), (CMP_BLOCK * HEAD_DIM) ** -0.5),
        'od_cmp_b1': nrm(ks[15], (N_ODD, 2, CMP_HIDDEN), 0.01),
        'od_cmp_w2': nrm(ks[16], (N_ODD, 2, CMP_HIDDEN, HEAD_DIM), CMP_HIDDEN ** -0.5),
        'od_cmp_b2': nrm(ks[17], (N_ODD, 2, HEAD_DIM), 0.01),
        'moe_wg': nrm(ks[18], (DEPTH, D, MOE_GROUPS), D ** -0.5),
        'moe_bg': nrm(ks[19], (DEPTH, MOE_GROUPS), 0.01),
        'moe_we': nrm(ks[20], (DEPTH, D, MOE_EXPERTS), D ** -0.5),
        'moe_be': nrm(ks[21], (DEPTH, MOE_EXPERTS), 0.01),
        'moe_w_gate': nrm(ks[22], (DEPTH, MOE_EXPERTS, D, MOE_FF), D ** -0.5),
        'moe_w_up': nrm(ks[23], (DEPTH, MOE_EXPERTS, D, MOE_FF), D ** -0.5),
        'moe_w_down': nrm(ks[24], (DEPTH, MOE_EXPERTS, MOE_FF, D), MOE_FF ** -0.5),
    }

def second_block(x, c, norm1_g, norm2_g, final_g, ada_w, ada_b, ev_w_in, ev_w_out, ev_lambda,
              ev_subln_g, od_w_in, od_w_out, od_cmp_pos, od_cmp_w1, od_cmp_b1, od_cmp_w2,
              od_cmp_b2, moe_wg, moe_bg, moe_we, moe_be, moe_w_gate, moe_w_up, moe_w_down):
    s = x.shape[1]
    cos, sin = rope_tables(s)
    cs = jax.nn.silu(c)
    for l in range(DEPTH):
        mod = (cs @ ada_w[l] + ada_b[l])[:, None, :]
        sh1, sc1, g1, sh2, sc2, g2 = jnp.split(mod, 6, axis=-1)
        h = rms_norm_2(x, norm1_g[l]) * (1.0 + sc1) + sh1
        if l % 2 == 0:
            i = l // 2
            lambda_init = 0.8 - 0.6 * math.exp(-0.3 * l)
            y = even_mixer_2(h, ev_w_in[i], ev_w_out[i], ev_lambda[i], ev_subln_g[i], lambda_init, cos, sin)
        else:
            i = l // 2
            y = odd_mixer_2(h, od_w_in[i], od_w_out[i], od_cmp_pos[i], od_cmp_w1[i], od_cmp_b1[i],
                          od_cmp_w2[i], od_cmp_b2[i], cos, sin)
        x = x + g1 * y
        h = rms_norm_2(x, norm2_g[l]) * (1.0 + sc2) + sh2
        x = x + g2 * hier_moe(h, moe_wg[l], moe_bg[l], moe_we[l], moe_be[l],
                              moe_w_gate[l], moe_w_up[l], moe_w_down[l])
    return rms_norm_2(x, final_g)


def setup_inputs(seed=0):
    out = dict(first_inputs(seed))
    for name, value in second_inputs(seed + 1).items():
        if name != "x":
            out[name + "_2"] = value
    return out


def reference(
    x, c, ctx, c_ctx, ada_w, ada_b, norm_g, mlp_w1, mlp_w2, ev_w_in, ev_w_out, ev_pool_w,
    ev_pool_scale, ev_rpb, rw_mu, rw_wr, rw_wk, rw_wv, rw_wo, rw_w0, rw_w1, rw_w2, rw_a0, rw_a1,
    rw_a2, rw_g1, rw_g2, rw_kk, rw_ka, rw_rk, rw_lng, rw_lnb, c_2, norm1_g_2, norm2_g_2,
    final_g_2, ada_w_2, ada_b_2, ev_w_in_2, ev_w_out_2, ev_lambda_2, ev_subln_g_2, od_w_in_2,
    od_w_out_2, od_cmp_pos_2, od_cmp_w1_2, od_cmp_b1_2, od_cmp_w2_2, od_cmp_b2_2, moe_wg_2,
    moe_bg_2, moe_we_2, moe_be_2, moe_w_gate_2, moe_w_up_2, moe_w_down_2,
):
    x = first_block(
        x, c, ctx, c_ctx, ada_w, ada_b, norm_g, mlp_w1, mlp_w2, ev_w_in, ev_w_out, ev_pool_w,
        ev_pool_scale, ev_rpb, rw_mu, rw_wr, rw_wk, rw_wv, rw_wo, rw_w0, rw_w1, rw_w2, rw_a0,
        rw_a1, rw_a2, rw_g1, rw_g2, rw_kk, rw_ka, rw_rk, rw_lng, rw_lnb,
    )
    return second_block(
        x, c_2, norm1_g_2, norm2_g_2, final_g_2, ada_w_2, ada_b_2, ev_w_in_2, ev_w_out_2,
        ev_lambda_2, ev_subln_g_2, od_w_in_2, od_w_out_2, od_cmp_pos_2, od_cmp_w1_2,
        od_cmp_b1_2, od_cmp_w2_2, od_cmp_b2_2, moe_wg_2, moe_bg_2, moe_we_2, moe_be_2,
        moe_w_gate_2, moe_w_up_2, moe_w_down_2,
    )


_drawn_inputs = setup_inputs


def setup_inputs(seed=0):
    import zlib

    import numpy as np

    out = dict(_drawn_inputs(seed))
    spreads = {}
    factors = {'ev_rpb': 8.0,
     'rw_w1': 8.0,
     'rw_w2': 8.0,
     'rw_a0': 3.521,
     'rw_a1': 4.479,
     'rw_a2': 4.112,
     'rw_kk': 3.099,
     'rw_lnb': 8.0,
     'norm1_g_2': 8.0,
     'norm2_g_2': 4.039,
     'final_g_2': 2.894,
     'ev_lambda_2': 8.0,
     'ev_subln_g_2': 8.0,
     'od_cmp_pos_2': 6.59,
     'od_cmp_b1_2': 8.0,
     'od_cmp_b2_2': 8.0,
     'moe_bg_2': 8.0,
     'moe_be_2': 8.0}
    for name, (base, spread) in spreads.items():
        noise = np.random.default_rng([zlib.crc32(name.encode()), seed]).standard_normal(out[name].shape)
        drawn = base * np.exp(spread * noise) if base else spread * noise
        out[name] = jnp.asarray(drawn.astype(out[name].dtype))
    for name, factor in factors.items():
        out[name] = (out[name] * factor).astype(out[name].dtype)
    return out
```

```python
import numpy as np
import concourse.bass as bass
from concourse import mybir
from contextlib import ExitStack

FP32 = mybir.dt.float32
ALU = mybir.AluOpType
ACT = mybir.ActivationFunctionType
AX = mybir.AxisListType

P = 128
D = 1024
KT = D // P
SEQ = 256
CTX, X = 0, 1
HD = 64
SLOT = 2048
N_SLOTS = 4
NEG = -1e30
GRID_W, WIN_C, WIN_R = 64, 16, 8
CHUNK = 64
N_CHUNK = SEQ // CHUNK
PAIRS = KT
LEVELS = 6
N_CMP = (SEQ - 32) // 16 + 1
N_EXPERTS = 16
MOD_TILES = 6 * KT
RMS_EPS = 1e-6
GN_EPS = 64e-5

CONST_COLS = {}


def _const(name, width, _at=[0]):
    CONST_COLS[name] = (_at[0], width)
    _at[0] += width


for _n, _w in (("ident", 128), ("ones", 128), ("block_ones", 128), ("swap", 128), ("cos", 256), ("sin", 256),
               ("causal", 128), ("cmp_mask", 2 * N_CMP), ("cmp_live", 2), 
               ("order", 2 * 128), ("first_level", 2 * 64), ("later_levels", 2 * 5 * 64), ("ident64", 64),
               ("scan_keep", 512), ("tie", 4), ("eps", 2)):
    _const(_n, _w)
N_CONST = sum(w for _, w in CONST_COLS.values())


def constants():
    c = {}
    i = np.arange(P)
    c["ident"] = np.eye(P)
    c["ones"] = np.ones((P, P))
    c["block_ones"] = (i[:, None] // HD == i[None, :] // HD).astype(np.float64)
    swap = np.zeros((P, P))
    cos, sin = np.ones((P, SEQ), np.float32), np.zeros((P, SEQ), np.float32)
    inv = np.float32(500000.0) ** (-np.arange(0, 16, 2, dtype=np.float32) / np.float32(16))
    ang = np.arange(SEQ, dtype=np.float32)[:, None] * inv[None, :]
    for p in range(P):
        d = p % HD
        if d < 16:
            swap[p, p + 8 if d < 8 else p - 8] = 1.0
            cos[p] = np.cos(ang[:, d % 8])
            sin[p] = np.sin(ang[:, d % 8]) * (-1 if d < 8 else 1)
    c["swap"], c["cos"], c["sin"] = swap, cos, sin
    c["causal"] = np.where(i[None, :] <= i[:, None], 0.0, NEG)
    q = np.arange(SEQ).reshape(2, P).T
    end = np.arange(N_CMP) * 16 + 31
    c["cmp_mask"] = np.where(end[None, None, :] <= q[:, :, None], 0.0, NEG).reshape(P, -1)
    c["cmp_live"] = (q >= 31).astype(np.float64)
    r, s = (i % 64)[:, None], np.arange(64)[None, :]
    c["order"] = np.concatenate([r < s, r <= s, r > s, r >= s], 1)
    first = lambda a, b: (a // 2 == b // 2) & (a % 2 == 1) & (b % 2 == 0)
    c["first_level"] = np.concatenate([first(r, s), first(s, r)], 1)
    later = []
    for direction in range(2):
        for lv in range(1, LEVELS):
            a, b = (r >> lv, s >> lv) if direction == 0 else (s >> lv, r >> lv)
            later.append((a // 2 == b // 2) & (a % 2 == 1) & (b % 2 == 0))
    c["later_levels"] = np.concatenate(later, 1)
    c["ident64"] = (r == s)
    c["scan_keep"] = np.broadcast_to(np.arange(512) % CHUNK != 0, (P, 512))
    c["tie"] = np.broadcast_to(np.array([4.0, 3.0, 2.0, 1.0]), (P, 4))
    c["eps"] = np.broadcast_to(np.array([RMS_EPS, GN_EPS]), (P, 2))
    out = np.concatenate([np.asarray(c[n], np.float64).reshape(P, w) for n, (_, w) in CONST_COLS.items()], 1)
    return np.ascontiguousarray(out.astype(np.float32))


def pool_inverses():
    t = np.arange(SEQ)
    inverse = [1.0 / (np.clip(t + w // 2, 0, SEQ) - np.clip(t - w // 2, 0, SEQ)) for w in (2, 4, 8, 16)]
    return np.ascontiguousarray(np.broadcast_to(np.concatenate(inverse).astype(np.float32), (P, 4 * SEQ)))


PARAM_COLS = {}


def _param(name, width, _at=[0]):
    PARAM_COLS[name] = (_at[0], width)
    _at[0] += width


for _n, _w in (("c", 16), ("c2", 8), ("ada_b", 4 * MOD_TILES), ("norm_g", 2 * 4 * KT), ("pool_scale", 4),
               ("mu", 6 * KT), ("w0", 2 * KT), ("a0", 2 * KT), ("kk", KT), ("ka", KT), ("rk", KT), ("lng", KT),
               ("lnb", KT), ("norm1_g2", 2 * KT), ("norm2_g2", 2 * KT), ("final_g2", KT), ("lam", 4), ("subln", 1),
               ("cmp_pos", 2 * 16), ("cmp_b1", 4), ("cmp_b2k", 1), ("cmp_b2v", 64), ("cmp_w2", 2 * 2 * 64),
               ("router_b", 2 * 20), ("router_w", 2 * KT * 20), ("gate_w", KT * 48)):
    _param(_n, _w)
N_PARAM = sum(w for _, w in PARAM_COLS.values())


def columns(v):
    v = np.asarray(v)
    return v.reshape(-1, P).T


def parameters(a):
    p = {}
    p["c"] = np.stack([columns(a["c_ctx"]), columns(a["c"])], 2).reshape(P, 16)
    p["c2"] = columns(a["c_2"])
    p["ada_b"] = np.concatenate([columns(a["ada_b"]), columns(a["ada_b_2"])], 1)
    p["norm_g"] = columns(a["norm_g"])
    p["pool_scale"] = columns(a["ev_pool_scale"])
    for n, k in (("mu", "rw_mu"), ("w0", "rw_w0"), ("a0", "rw_a0"), ("kk", "rw_kk"), ("ka", "rw_ka"), ("rk", "rw_rk"),
                 ("lng", "rw_lng"), ("lnb", "rw_lnb"), ("norm1_g2", "norm1_g_2"), ("norm2_g2", "norm2_g_2"),
                 ("final_g2", "final_g_2"), ("subln", "ev_subln_g_2"), ("cmp_b1", "od_cmp_b1_2")):
        p[n] = columns(a[k])
    lam = np.asarray(a["ev_lambda_2"])[0].T
    p["lam"] = np.concatenate([lam, np.zeros_like(lam)], 0)
    p["cmp_pos"] = np.concatenate([columns(np.asarray(a["od_cmp_pos_2"])[0, i].reshape(-1)) for i in range(2)], 1)
    b2 = np.asarray(a["od_cmp_b2_2"])[0]
    p["cmp_b2k"] = np.concatenate([b2[0], b2[0]])[:, None]
    p["cmp_b2v"] = np.broadcast_to(b2[1], (P, 64))
    w2 = np.asarray(a["od_cmp_w2_2"])[0]
    p["cmp_w2"] = w2.reshape(2, 2, P, 64).transpose(2, 0, 1, 3).reshape(P, -1)
    rb = np.concatenate([np.asarray(a["moe_bg_2"]), np.asarray(a["moe_be_2"])], 1)
    p["router_b"] = np.broadcast_to(rb.reshape(1, -1), (P, 40))
    rw = np.concatenate([np.asarray(a["moe_wg_2"]), np.asarray(a["moe_we_2"])], 2)
    p["router_w"] = rw.reshape(2, KT, P, 20).transpose(2, 0, 1, 3).reshape(P, -1)
    gw = np.asarray(a["od_w_in_2"])[0][:, 2560:2608]
    p["gate_w"] = gw.reshape(KT, P, 48).transpose(1, 0, 2).reshape(P, -1)
    return np.ascontiguousarray(np.concatenate([p[n].reshape(P, w) for n, (_, w) in PARAM_COLS.items()], 1))


def weight_blocks(a):
    def cols(w):
        w = np.asarray(w)
        n = w.shape[1] // 256
        return list(w.reshape(KT, P, n, 256).transpose(2, 1, 0, 3).reshape(n, P, SLOT))

    def deep(w):
        w = np.asarray(w)
        return list(w.reshape(2, 16, P, 8, P).transpose(3, 0, 2, 1, 4).reshape(16, P, SLOT))

    def halves(w):
        return list(np.asarray(w).reshape(2, KT, P, 256).transpose(0, 2, 1, 3).reshape(2, P, SLOT))

    def wide(w):
        return [np.asarray(w).reshape(2, P, D).transpose(1, 0, 2).reshape(P, SLOT)]

    mods = [cols(a["ada_w"][0]), cols(a["ada_w"][1]), cols(a["ada_w_2"][0]), cols(a["ada_w_2"][1])]
    g = {
        "mod0": mods[0], "mod1": mods[1], "mod2": mods[2], "mod3": mods[3],
        "ev_in": cols(a["ev_w_in"][0]), "ev_out": cols(a["ev_w_out"][0]),
        "mlp1_0": cols(a["mlp_w1"][0]), "mlp2_0": deep(a["mlp_w2"][0]),
        "mlp1_1": cols(a["mlp_w1"][1]), "mlp2_1": deep(a["mlp_w2"][1]),
        "wr": cols(a["rw_wr"][0]), "wk": cols(a["rw_wk"][0]), "wv": cols(a["rw_wv"][0]), "wo": cols(a["rw_wo"][0]),
        "ev2_in": cols(a["ev_w_in_2"][0]), "ev2_out": cols(a["ev_w_out_2"][0]),
        "od_in": cols(np.asarray(a["od_w_in_2"])[0][:, :2560]), "od_out": cols(a["od_w_out_2"][0]),
        "cmp_k": halves(np.asarray(a["od_cmp_w1_2"])[0, 0]), "cmp_v": halves(np.asarray(a["od_cmp_w1_2"])[0, 1]),
    }
    for layer in range(2):
        up = [cols(a["moe_w_gate_2"][layer, e]) + cols(a["moe_w_up_2"][layer, e]) for e in range(N_EXPERTS)]
        down = [wide(a["moe_w_down_2"][layer, e]) for e in range(N_EXPERTS)]
        g[f"moe{layer}"] = up[0] + [b for e in range(1, N_EXPERTS) for b in up[e] + down[e - 1]] + down[-1]
    taken = dict.fromkeys(g, 0)
    out = []
    for name in block_order():
        out.append(g[name][taken[name]])
        taken[name] += 1
    assert all(taken[n] == len(g[n]) for n in g), taken
    return np.ascontiguousarray(np.stack(out))


def mixed(*runs):
    name, count = runs[0]
    out = []
    done = [0] * len(runs)
    for i in range(count):
        out.append(name)
        for r, (other, n) in list(enumerate(runs))[1:]:
            while done[r] < n * (i + 1) // count:
                out.append(other)
                done[r] += 1
    return out


def block_order():
    order = ["mod0"] * 24 + ["ev_in"] * 8 + ["ev_out"] * 4
    order += mixed(("mlp1_0", 16), ("mod1", 24)) + mixed(("mlp2_0", 16), ("mod2", 24))
    order += ["wr"] * 4 + ["wk"] * 4 + ["wv"] * 4 + ["wo"] * 4
    order += ["mlp1_1"] * 16 + mixed(("mlp2_1", 16), ("mod3", 24))
    order += ["ev2_in"] * 12 + ["ev2_out"] * 4 + ["moe0"] * 48
    order += ["od_in"] * 10 + ["cmp_k"] * 2 + ["cmp_v"] * 2 + ["od_out"] * 4 + ["moe1"] * 48
    return order


def small_weights(a):
    tall = lambda w: np.asarray(w).reshape(KT, P, P).transpose(1, 0, 2).reshape(P, D)
    pair = lambda w: tall(np.concatenate([np.asarray(w)[0, 0], np.asarray(w)[0, 1]], 1))
    stack = lambda w: np.asarray(w)[0].reshape(P, D)
    pool = np.asarray(a["ev_pool_w"])[0].transpose(1, 0, 2).reshape(P, 512)
    return np.ascontiguousarray(np.concatenate(
        [pair(a["rw_w1"]), pair(a["rw_a1"]), tall(a["rw_g1"]), stack(a["rw_w2"]), stack(a["rw_a2"]),
         np.asarray(a["rw_g2"])[0], pool], 1))


def position_bias(rpb):
    rpb = np.asarray(rpb)[0]
    t = np.arange(SEQ)
    row, col = t // GRID_W, t % GRID_W
    start = np.clip(col - WIN_C // 2, 0, GRID_W - WIN_C)
    ok = (col[None, :] >= start[:, None]) & (col[None, :] < start[:, None] + WIN_C)
    dc = np.clip(col[None, :] - col[:, None], -(WIN_C - 1), WIN_C - 1) + WIN_C - 1
    dr = row[None, :] - row[:, None] + WIN_R - 1
    full = np.where(ok[None], rpb[:, dr, dc], np.float32(NEG))
    return np.ascontiguousarray(full.reshape(8, 2, P, SEQ).transpose(2, 0, 1, 3).reshape(P, -1))


class Events:

    def __init__(self, known=None):
        self.known = known.at if known else {}
        self.where_known = known.where if known else {}
        self.at = {}
        self.where = {}


class Steps:

    def __init__(self, eng, semaphore, events, name):
        self.eng, self.semaphore, self.events, self.name = eng, semaphore, events, name
        self.reached = {}
        self.count = {}
        self.own = (None, 0)
        self.counter = None
        self.at_block = 0
        self.taken = {}

    def stage(self, name):
        self.counter = f"{name}_{self.name}"

    def step(self, *event, by=1, sem=None):
        s = sem or self.counter
        self.count[s] = self.count.get(s, 0) + by
        self.own = (s, self.count[s])
        if event:
            self.mark(*event)
        return self.semaphore(s), by

    def mark(self, *event):
        assert event not in self.events.at, event
        self.events.at[event] = self.own

    def wait_ge(self, name, value):
        if name is not None and self.reached.get(name, 0) < value:
            self.reached[name] = value
            self.eng.wait_ge(self.semaphore(name), value)


def bass_two_blocks(nc, weights, consts, params, small, bias, pool_inv, x_t, out_t, events):
    ctx = ExitStack()
    with ctx:
        sems = {}

        def semaphore(name):
            if name not in sems:
                sems[name] = ctx.enter_context(nc.semaphore(name))
            return sems[name]

        def after(*event):
            if not events.known:
                return None, 0
            return events.known[event]

        sb = lambda name, width: ctx.enter_context(nc.sbuf_tensor(name, [P, width], FP32))
        ring = sb("weight_slots", N_SLOTS * SLOT)
        CN = sb("constants", N_CONST)
        PR = sb("parameters", N_PARAM)
        MD = sb("modulations", 4 * 96)
        ARENA = 40100
        arena = sb("arena", ARENA)
        ps = ctx.enter_context(nc.psum_tensor("banks", [P, 8, 512], FP32))

        def cn(name, a=0, w=None, rows=slice(0, P)):
            at, width = CONST_COLS[name]
            return CN[rows, at + a:at + (a + w if w else width)]

        def pr(name, a=0, w=None, rows=slice(0, P)):
            at, width = PARAM_COLS[name]
            return PR[rows, at + a:at + (a + w if w else width)]

        def area(at, *dims):
            n = int(np.prod(dims))
            assert at + n <= ARENA, (at, dims)
            v = arena[:, at:at + n]
            if len(dims) == 1:
                return v
            names = "abcd"[:len(dims)]
            return v.rearrange(f"p ({' '.join(names)}) -> p {' '.join(names)}", **dict(zip(names, dims)))

        def psum(bank, a=0, w=512, rows=slice(0, P)):
            return ps[rows, bank, a:a + w]

        XT = area(0, 2, KT, SEQ)
        HT = area(4096, 2, KT, SEQ)
        YT = area(8192, 2, KT, SEQ)
        SQ = area(12288, 2, KT, SEQ)
        RS = area(16384, 2, SEQ)
        FREE = 16896
        SMALL = ARENA - 6144

        order = block_order()
        N_BLOCKS = len(order)
        block_of = {}
        for j, n in enumerate(order):
            block_of.setdefault(n, []).append(j)


        def load_blocks(sp):
            sp.stage("weights")
            for j in range(N_BLOCKS):
                if j >= N_SLOTS:
                    sp.wait_ge(*after("used", j - N_SLOTS))
                s = j % N_SLOTS
                sp.eng.dma_start(ring[:, s * SLOT:(s + 1) * SLOT], weights[j]).then_inc(*sp.step("block", j, by=16, sem=f"weight_slot{s}"))

        def slot(j, k, width, a=0, w=None, rows=slice(0, P)):
            at = (j % N_SLOTS) * SLOT + k * width + a
            return ring[rows, at:at + (w or width)]

        bank_state = {"next": 0, "holder": [None] * 8, "open": list(range(7))}

        def take_bank(pe, key, banks=None):
            pool = banks or bank_state["open"]
            b = pool[bank_state["next"] % len(pool)]
            bank_state["next"] += 1
            if bank_state["holder"][b] is not None:
                pe.wait_ge(*after("taken", *bank_state["holder"][b]))
            bank_state["holder"][b] = key
            events.where[key] = b
            return b

        def bank_of(key):
            return events.where_known.get(key, 0)

        def side_blocks(pe, j_next):
            while pe.at_block < j_next:
                j = pe.at_block
                name = order[j]
                assert name.startswith("mod"), (name, j, j_next)
                mod_block(pe, int(name[3]), j)

        def next_block(pe, name):
            j = block_of[name][pe.taken.get(name, 0)]
            pe.taken[name] = pe.taken.get(name, 0) + 1
            side_blocks(pe, j)
            pe.wait_ge(*after("block", j))
            assert pe.at_block == j
            pe.at_block += 1
            return j

        MOD = [MD[:, 96 * m:96 * m + 96].rearrange("p (t s) -> p t s", s=2) for m in range(4)]
        SC = ctx.enter_context(nc.sbuf_tensor("silu_c", [P, 24], FP32))

        def mod_block(pe, m, j):
            n = block_of[f"mod{m}"].index(j)
            wide = 2 if m < 2 else 1
            if n == 0:
                pe.wait_ge(*after("silu_c"))
                if bank_state["holder"][7] is not None:
                    pe.wait_ge(*after("taken", *bank_state["holder"][7]))
                bank_state["holder"][7] = ("mod", m)
                events.where[("mod", m)] = 7
            pe.wait_ge(*after("block", j))
            pe.at_block += 1
            for i in range(2):
                t = 2 * n + i
                for k in range(KT):
                    rhs = SC[:, 2 * k:2 * k + 2] if m < 2 else SC[:, 16 + k:17 + k]
                    ins = nc.tensor.matmul(psum(7, t * wide, wide), slot(j, k, 256, i * P, P), rhs,
                                           start=(k == 0), stop=(k == KT - 1))
            ins.then_inc(*pe.step("mod_tiles", m, n))
            pe.mark("used", j)

        def silu_c(act):
            act.stage("mod")
            act.wait_ge(*after("params"))
            nc.scalar.activation(SC[:, 0:16], pr("c"), ACT.Silu).then_inc(*act.step())
            nc.scalar.activation(SC[:, 16:24], pr("c2"), ACT.Silu).then_inc(*act.step("silu_c"))

        def mod_vectors(v, m):
            v.stage("mod")
            wide = 2 if m < 2 else 1
            v.wait_ge(*after("mod_tiles", m, 23))
            v.wait_ge(*after("params"))
            M = MOD[m]
            src = psum(7, 0, MOD_TILES * wide).rearrange("p (t s) -> p t s", s=wide)
            b = pr("ada_b", m * MOD_TILES, MOD_TILES).unsqueeze(2).to_broadcast([P, MOD_TILES, wide])
            nc.vector.tensor_tensor(M[:, :, 0:wide], src, b, ALU.add).then_inc(*v.step("taken", "mod", m))
            v.wait_ge(*v.own)

            def times(chunk, gains, plus):
                g = gains.unsqueeze(2).to_broadcast([P, KT, wide])
                part = M[:, chunk * KT:(chunk + 1) * KT, 0:wide]
                nc.vector.scalar_tensor_tensor(part, part, plus, g, ALU.add, ALU.mult).then_inc(*v.step())
            if m < 2:
                for chunk, n, plus in ((1, 0, 1.0), (2, 1, 0.0), (4, 2, 1.0), (5, 3, 0.0)):
                    times(chunk, pr("norm_g", (m * 4 + n) * KT, KT), plus)
            else:
                times(1, pr("norm1_g2", (m - 2) * KT, KT), 1.0)
                times(4, pr("norm2_g2", (m - 2) * KT, KT), 1.0)
            v.mark("mod_ready", m)

        def mod_col(m, chunk, tile, seg):
            s = seg if m < 2 else 0
            return MOD[m][:, chunk * KT + tile, s:s + 1]

        def rms_scalar(act, key, src, segs, inputs):
            act.stage("norm")
            for e in inputs:
                act.wait_ge(*after(*e))
            for seg in segs:
                nc.scalar.activation(SQ[:, seg, 0:4, :], src[:, seg, 0:4, :], ACT.Square).then_inc(*act.step("squares_low", key, seg))
            a, w = segs[0] * SEQ, len(segs) * SEQ
            act.wait_ge(*after("sums", key))
            nc.scalar.activation(RS[:, segs[0]:segs[-1] + 1, :],
                                 psum(bank_of(("sums", key)), 0, w).rearrange("p (s t) -> p s t", t=SEQ),
                                 ACT.Sqrt, bias=cn("eps", 0, 1), scale=1.0 / D).then_inc(*act.step("taken", "sums", key))

        def rms_vector(v, key, src, segs, inputs):
            v.stage("norm")
            for e in inputs:
                v.wait_ge(*after(*e))
            for seg in segs:
                nc.vector.tensor_tensor(SQ[:, seg, 4:8, :], src[:, seg, 4:8, :], src[:, seg, 4:8, :], ALU.mult).then_inc(*v.step("squares_high", key, seg))
            v.wait_ge(*after("taken", "sums", key))
            part = RS[:, segs[0]:segs[-1] + 1, :]
            nc.vector.reciprocal(part, part).then_inc(*v.step("rms", key))

        def rms_tensor(pe, key, segs):
            pe.stage("norm")
            b = take_bank(pe, ("sums", key))
            for seg in segs:
                pe.wait_ge(*after("squares_low", key, seg))
                pe.wait_ge(*after("squares_high", key, seg))
            pe.wait_ge(*after("consts"))
            for k in range(KT):
                ins = nc.tensor.matmul(psum(b, 0, len(segs) * SEQ), cn("ones"), SQ[:, segs[0]:segs[-1] + 1, k, :],
                                       start=(k == 0), stop=(k == KT - 1))
            ins.then_inc(*pe.step("sums", key))

        def modulate_vector(v, key, m, half, segs, freed):
            v.wait_ge(*after("mod_ready", m))
            for e in freed:
                v.wait_ge(*after(*e))
            v.wait_ge(*v.own)
            for k in range(KT):
                for seg in segs:
                    nc.vector.scalar_tensor_tensor(HT[:, seg, k, :], XT[:, seg, k, :],
                                                   mod_col(m, 3 * half + 1, k, seg), RS[:, seg, :],
                                                   ALU.mult, ALU.mult).then_inc(*v.step("scaled", key, k, seg))
            v.mark("scaled_all", key)

        def modulate_scalar(act, key, m, half, segs):
            act.wait_ge(*after("mod_ready", m))
            for k in range(KT):
                for seg in segs:
                    act.wait_ge(*after("scaled", key, k, seg))
                    nc.scalar.activation(HT[:, seg, k, :], HT[:, seg, k, :], ACT.Identity,
                                         bias=mod_col(m, 3 * half, k, seg)).then_inc(*act.step("h", key, k, seg))
            act.mark("h_all", key)

        def residual_vector(v, key, m, half, segs, normed):
            v.stage("residual")
            v.wait_ge(*after("mod_ready", m))
            if normed:
                v.wait_ge(*after("rms", "y_" + key))
                for seg in segs:
                    r = RS[:, seg, :].unsqueeze(1).to_broadcast([P, KT, SEQ])
                    nc.vector.tensor_tensor(YT[:, seg, :, :], YT[:, seg, :, :], r, ALU.mult).then_inc(*v.step())
            else:
                v.wait_ge(*after("y_all", key))
                v.wait_ge(*after("y_all2", key))
            v.wait_ge(*v.own)
            for seg in segs:
                for k in range(KT):
                    nc.vector.scalar_tensor_tensor(XT[:, seg, k, :], YT[:, seg, k, :],
                                                   mod_col(m, 3 * half + 2, k, seg), XT[:, seg, k, :],
                                                   ALU.mult, ALU.add).then_inc(*v.step())
            v.mark("x", key)

        def project_tensor(pe, key, name, moving, ready, segs, stage="project"):
            pe.stage(stage)
            w = len(segs) * SEQ
            n_tiles = 2 * len(block_of[name])
            for g in range(0, n_tiles, 2):
                j = next_block(pe, name)
                for i in range(2):
                    b = take_bank(pe, (key, g + i))
                    for k in range(KT):
                        if ready is not None and g == 0 and i == 0:
                            for e in ready(k):
                                pe.wait_ge(*after(*e))
                        ins = nc.tensor.matmul(psum(b, 0, w), slot(j, k, 256, i * P, P), moving(k),
                                               start=(k == 0), stop=(k == KT - 1))
                    ins.then_inc(*pe.step(key, g + i))
                pe.mark("used", j)

        def take_out(q, key, tiles, place, segs, done, fn=None):
            for g in tiles:
                q.wait_ge(*after(key, g))
                b = bank_of((key, g))
                src = psum(b, 0, len(segs) * SEQ)
                if len(segs) == 2:
                    src = src.rearrange("p (s t) -> p s t", t=SEQ)
                if fn is not None:
                    ins = fn(g, place(g), src)
                elif q.name == "scalar":
                    ins = nc.scalar.activation(place(g), src, ACT.Copy)
                else:
                    ins = nc.vector.tensor_copy(place(g), src)
                ins.then_inc(*q.step("taken", key, g))
            q.mark(done, key)

        def seg_of(segs):
            return slice(segs[0], segs[-1] + 1)

        def h_moving(segs):
            if len(segs) == 2:
                return lambda k: HT[:, :, k, :]
            return lambda k: HT[:, segs[0], k, :]

        def h_ready(key, segs):
            return lambda k: [("h", key, k, seg) for seg in segs]

        def y_place(segs):
            if len(segs) == 2:
                return lambda g: YT[:, :, g, :]
            return lambda g: YT[:, segs[0], g, :]


        S_W, T_W = 528, 640

        def att_places(base):
            return (area(base, 3, S_W), area(base + 3 * S_W, 2, T_W), area(base + 3 * S_W + 2 * T_W, 3, 12))

        def att_tensor(pe, A):
            pe.stage(A.name)

            def scores(u):
                for n, mms in enumerate(A.scores(u)):
                    b = take_bank(pe, (A.name, "scores", u, n))
                    for e in A.ready(u):
                        pe.wait_ge(*after(*e))
                    for (col, w, lhs, rhs) in mms:
                        ins = nc.tensor.matmul(psum(b, col, w), lhs, rhs, start=True, stop=True)
                    ins.then_inc(*pe.step(A.name, "scores", u, n))

            def transposes(u):
                S = att_places(A.base)[0]
                pe.wait_ge(*after(A.name, "weights", u))
                blocks = A.blocks(u)
                for n in range(0, len(blocks), 4):
                    b = take_bank(pe, (A.name, "turned", u, n // 4))
                    for i, (col, w) in enumerate(blocks[n:n + 4]):
                        ins = nc.tensor.transpose(psum(b, i * P, P, slice(0, w)), S[:, u % 3, col:col + w], cn("ident"))
                    ins.then_inc(*pe.step(A.name, "turned", u, n // 4))

            def values(u):
                T = att_places(A.base)[1]
                rows, vs = A.values(u)
                b = take_bank(pe, (A.name, "out", u))
                pe.wait_ge(*after(A.name, "T", u))
                for e in A.values_ready(u):
                    pe.wait_ge(*after(*e))
                for i, (v, (col, w)) in enumerate(zip(vs, A.blocks(u))):
                    ins = nc.tensor.matmul(psum(b, 0, P, rows), v, T[0:w, u % 2, i * P:(i + 1) * P],
                                           start=(i == 0), stop=(i == len(vs) - 1))
                ins.then_inc(*pe.step(A.name, "out", u))

            for i in range(A.n + 2):
                if i < A.n:
                    scores(i)
                if 0 <= i - 1 < A.n:
                    transposes(i - 1)
                if 0 <= i - 2 < A.n:
                    values(i - 2)

        def att_vector(v, A):
            v.stage(A.name)
            S, T, M = att_places(A.base)
            v.wait_ge(*after(*A.place_free))

            def maxima(u):
                s = S[:, u % 3, :]
                if u >= 3:
                    v.wait_ge(*after(A.name, "turned", u - 3, (len(A.blocks(u - 3)) - 1) // 4))
                for i, (n, col, dst, w, mask) in enumerate(A.pieces(u)):
                    v.wait_ge(*after(A.name, "scores", u, n))
                    b = bank_of((A.name, "scores", u, n))
                    if mask is None:
                        ins = nc.vector.tensor_scalar(s[:, dst:dst + w], psum(b, col, w), A.pre, None, ALU.mult)
                    else:
                        ins = nc.vector.scalar_tensor_tensor(s[:, dst:dst + w], psum(b, col, w), A.pre, mask,
                                                             ALU.mult, ALU.add)
                    ins.then_inc(*v.step())
                    if i == A.last_piece(u, n):
                        v.mark("taken", A.name, "scores", u, n)
                v.wait_ge(*v.own)
                maps = A.maps(u)
                for j, (c, w) in enumerate(maps):
                    nc.vector.tensor_reduce(M[:, u % 3, j:j + 1], s[:, c:c + w], AX.X, ALU.max).then_inc(*v.step())
                v.wait_ge(*v.own)
                k = len(maps)
                nc.vector.tensor_scalar(M[:, u % 3, 3:3 + k], M[:, u % 3, 0:k], -A.post, None, ALU.mult).then_inc(*v.step(A.name, "max", u))

            def weights(u):
                s = S[:, u % 3, :]
                maps = A.maps(u)
                k = len(maps)
                v.wait_ge(*after(A.name, "exp", u))
                nc.vector.reciprocal(M[:, u % 3, 9:9 + k], M[:, u % 3, 6:6 + k]).then_inc(*v.step())
                v.wait_ge(*v.own)
                if A.factor is not None:
                    f = A.factor(u)
                    nc.vector.tensor_tensor(M[:, u % 3, 9:9 + k], M[:, u % 3, 9:9 + k], f, ALU.mult).then_inc(*v.step())
                    v.wait_ge(*v.own)
                if A.subtract:
                    (c0, w), (c1, _) = maps
                    nc.vector.tensor_scalar(s[:, c0:c0 + w], s[:, c0:c0 + w], M[:, u % 3, 9:10], None, ALU.mult).then_inc(*v.step())
                    v.wait_ge(*v.own)
                    nc.vector.scalar_tensor_tensor(s[:, c0:c0 + w], s[:, c1:c1 + w], M[:, u % 3, 10:11],
                                                   s[:, c0:c0 + w], ALU.mult, ALU.add).then_inc(*v.step())
                else:
                    for j, (c, w) in enumerate(maps):
                        nc.vector.tensor_scalar(s[:, c:c + w], s[:, c:c + w], M[:, u % 3, 9 + j:10 + j], None,
                                                ALU.mult).then_inc(*v.step())
                v.mark(A.name, "weights", u)

            for i in range(A.n + 1):
                if i < A.n:
                    maxima(i)
                if i >= 1:
                    weights(i - 1)

        def att_scalar(act, A):
            act.stage(A.name)
            S, T, M = att_places(A.base)

            def exps(u):
                act.wait_ge(*after(A.name, "max", u))
                for j, (c, w) in enumerate(A.maps(u)):
                    nc.scalar.activation(S[:, u % 3, c:c + w], S[:, u % 3, c:c + w], ACT.Exp,
                                         bias=M[:, u % 3, 3 + j:4 + j], scale=A.post,
                                         accum_out=M[:, u % 3, 6 + j:7 + j]).then_inc(*act.step())
                act.mark(A.name, "exp", u)

            def turned(u):
                blocks = A.blocks(u)
                if u >= 2:
                    act.wait_ge(*after(A.name, "out", u - 2))
                for n in range(0, len(blocks), 4):
                    act.wait_ge(*after(A.name, "turned", u, n // 4))
                    b = bank_of((A.name, "turned", u, n // 4))
                    part = blocks[n:n + 4]
                    full = [x for x in part if x[1] == P]
                    runs = [(i, 1, w) for i, (_, w) in enumerate(part) if w != P]
                    if full:
                        runs.append((part.index(full[0]), len(full), P))
                    for i, m, w in runs:
                        nc.scalar.activation(T[0:w, u % 2, (n + i) * P:(n + i + m) * P],
                                             psum(b, i * P, m * P, slice(0, w)), ACT.Copy).then_inc(*act.step())
                    act.mark("taken", A.name, "turned", u, n // 4)
                act.mark(A.name, "T", u)

            def out(u):
                act.wait_ge(*after(A.name, "out", u))
                rows, _ = A.values(u)
                nc.scalar.activation(A.place(u), psum(bank_of((A.name, "out", u)), 0, P, rows), ACT.Copy).then_inc(*act.step("taken", A.name, "out", u))

            for i in range(A.n + 3):
                if i < A.n:
                    exps(i)
                if 0 <= i - 1 < A.n:
                    turned(i - 1)
                if 0 <= i - 2 < A.n:
                    out(i - 2)
            act.mark(A.name, "done")

        class Attention:
            factor = None
            subtract = False
            pre, post = 1.0, HD ** -0.5
            place_free = ("consts",)

            def last_piece(self, u, n):
                return max(i for i, p in enumerate(self.pieces(u)) if p[0] == n)

            def ready(self, u):
                return ()

            def values_ready(self, u):
                return ()

        def half(h):
            return slice(HD * (h % 2), HD * (h % 2) + HD)

        QA = area(FREE, 4, 512)
        KA = area(FREE + 2048, 4, 512)
        VA = area(FREE + 4096, 4, 512)
        UP = area(FREE + 6144, 4, 2, 288)
        PW = area(FREE + 8448, 4, P)
        PINV = area(FREE + 8960, 4, SEQ)
        PD = area(FREE + 9984, 4, 2, SEQ)
        PT3 = area(FREE + 12032, 3, 2, 288)
        ATT_A = FREE + 13760
        CAT = SQ
        BIAS = area(8192, 8, 2, SEQ)
        assert ATT_A + 3 * S_W + 2 * T_W + 36 <= SMALL

        def loads_pool(g):
            g.stage("load")
            g.eng.dma_start(PR[:, :], params).then_inc(*g.step("params", by=16, sem="params_loaded"))
            g.eng.dma_start(XT[:, :, :, :].rearrange("p a b c -> p (a b c)"), x_t).then_inc(*g.step("x0", by=16, sem="x_loaded"))
            g.eng.dma_start(CN[:, :], consts).then_inc(*g.step("consts", by=16, sem="consts_loaded"))
            g.eng.dma_start(area(8192, 4096), bias).then_inc(*g.step("bias", by=16, sem="bias_loaded"))
            g.eng.dma_start(PW.rearrange("p a b -> p (a b)"), small[:, 6144:6656]).then_inc(*g.step("pool_w", by=16, sem="pool_w_loaded"))
            g.eng.dma_start(PINV.rearrange("p a b -> p (a b)"), pool_inv).then_inc(*g.step("pool_inv", by=16, sem="pool_inverse_loaded"))
            g.eng.dma_start(area(SMALL, 6144), small[:, 0:6144]).then_inc(*g.step("small", by=16, sem="small_loaded"))

        def pool_pool(g):
            g.stage("pooling")
            nc.gpsimd.memset(UP, 0.0).then_inc(*g.step("pads"))
            g.wait_ge(*after("taken_all", "ev_in"))
            g.wait_ge(*after("taken_all2", "ev_in"))
            g.wait_ge(*after("pool_inv"))
            for gi in range(4):
                u = UP[:, gi]
                src, shifts = u, []
                for lv in range(gi + 1):
                    dst = PT3[:, lv % 2]
                    up, down = (0, 1) if lv == 0 else (1 << (lv - 1), 1 << (lv - 1))
                    lo, hi = 1 << lv, 288 - (1 << lv)
                    g.wait_ge(*g.own)
                    nc.gpsimd.tensor_tensor(dst[:, :, lo:hi], src[:, :, lo + up:hi + up],
                                            src[:, :, lo - down:hi - down], ALU.add).then_inc(*g.step())
                    src = dst
                g.wait_ge(*g.own)
                inv = PINV[:, gi].unsqueeze(1).to_broadcast([P, 2, SEQ])
                nc.gpsimd.tensor_tensor(PD[:, gi], src[:, :, 16:272], inv, ALU.mult).then_inc(*g.step())
                g.wait_ge(*g.own)
                nc.gpsimd.tensor_tensor(PD[:, gi], PD[:, gi], u[:, :, 16:272], ALU.subtract).then_inc(*g.step("pooled", gi))

        def pool_tensor(pe):
            pe.stage("pooling")
            pe.wait_ge(*after("pool_w"))
            for gi in range(4):
                b = take_bank(pe, ("pool", gi))
                pe.wait_ge(*after("pooled", gi))
                ins = nc.tensor.matmul(psum(b), PW[:, gi], PD[:, gi], start=True, stop=True)
                ins.then_inc(*pe.step("pool", gi))

        def pool_scalar(act):
            act.stage("pooling")
            for gi in range(4):
                act.wait_ge(*after("pool", gi))
                b = bank_of(("pool", gi))
                nc.scalar.activation(CAT[:, :, gi, :], psum(b).rearrange("p (s t) -> p s t", t=SEQ), ACT.Copy,
                                     scale=pr("pool_scale", gi, 1)).then_inc(*act.step("taken", "pool", gi))
            act.mark("pool_done")

        def ev_in_tensor(pe):
            project_tensor_n(pe, "ev_in", "ev_in", 6, h_moving([0, 1]), h_ready("n1_0", [0, 1]), [0, 1])
            values_natural(pe, "ev_in", "ev_v", 2, 4, 256)

        def project_tensor_n(pe, key, name, blocks, moving, ready, segs):
            pe.stage("project_" + key)
            w = len(segs) * SEQ
            for g in range(0, 2 * blocks, 2):
                j = next_block(pe, name)
                for i in range(2):
                    b = take_bank(pe, (key, g + i))
                    for k in range(KT):
                        if g == 0 and i == 0 and ready:
                            for e in ready(k):
                                pe.wait_ge(*after(*e))
                        ins = nc.tensor.matmul(psum(b, 0, w), slot(j, k, 256, i * P, P), moving(k),
                                               start=(k == 0), stop=(k == KT - 1))
                    ins.then_inc(*pe.step(key, g + i))
                pe.mark("used", j)

        def values_natural(pe, name, key, blocks, n_tok, width, segs=(0, 1)):
            for jj in range(blocks):
                j = next_block(pe, name)
                for seg in range(n_tok // 2):
                    b = take_bank(pe, (key, jj, seg))
                    for half_ in range(2):
                        for k in range(KT):
                            s = segs[seg]
                            ins = nc.tensor.matmul(psum(b, half_ * 256, 256), HT[:, s, k, half_ * P:(half_ + 1) * P],
                                                   slot(j, k, 256), start=(k == 0), stop=(k == KT - 1))
                    ins.then_inc(*pe.step(key, jj, seg))
                pe.mark("used", j)

        def take_values(q, key, blocks, n_tok, place, shares, copy):
            for jj in range(blocks):
                for seg in range(n_tok // 2):
                    if (jj * (n_tok // 2) + seg) % 2 != shares:
                        continue
                    q.wait_ge(*after(key, jj, seg))
                    b = bank_of((key, jj, seg))
                    copy(place(jj, seg), psum(b).rearrange("p (t c) -> p t c", c=256)).then_inc(*q.step("taken", key, jj, seg))
            q.mark(key + "_out", shares)

        act_copy = lambda o, i: nc.scalar.activation(o, i, ACT.Copy)
        dve_copy = lambda o, i: nc.vector.tensor_copy(o, i)

        def ev_place(g):
            if g < 4:
                return UP[:, g, :, 16:272]
            dst = QA[:, g - 4] if g < 8 else KA[:, g - 8]
            return dst.rearrange("p (s t) -> p s t", t=SEQ)

        def ev_out_of(q, share, copy):
            q.stage("project_ev_in")
            q.wait_ge(*after("pads"))
            for g in range(share, 12, 2):
                q.wait_ge(*after("ev_in", g))
                copy(ev_place(g), psum(bank_of(("ev_in", g))).rearrange("p (s t) -> p s t", t=SEQ)).then_inc(*q.step("taken", "ev_in", g))
                if g == 2 + share:
                    q.mark("taken_all" if share == 0 else "taken_all2", "ev_in")
            q.mark("qk_out", share)
            take_values(q, "ev_v", 2, 4, lambda jj, seg: VA[:, 2 * seg:2 * seg + 2, jj * 256:(jj + 1) * 256], share, copy)

        class LatentAttention(Attention):
            name, n, base = "latent_attention", 16, ATT_A
            pre, post = HD ** -0.5, 1.0
            place_free = ("bias",)

            def ready(self, u):
                return (("qk_out", 0), ("qk_out", 1))

            def values_ready(self, u):
                return (("ev_v_out", 0), ("ev_v_out", 1))

            def scores(self, u):
                h, qt = divmod(u, 2)
                r = half(h)
                return [[(0, 512, QA[r, h // 2, 256 + qt * P:256 + (qt + 1) * P], KA[r, h // 2, :])]]

            def pieces(self, u):
                h, qt = divmod(u, 2)
                return [(0, 0, 0, 256, None), (0, 256, 256, 256, BIAS[:, h, qt, :])]

            def maps(self, u):
                return [(0, 512)]

            def blocks(self, u):
                return [(i * P, P) for i in range(4)]

            def values(self, u):
                h = u // 2
                return half(h), [VA[:, i, h * HD:(h + 1) * HD] for i in range(4)]

            def place(self, u):
                h, qt = divmod(u, 2)
                return CAT[half(h), X, 4 + h // 2, qt * P:(qt + 1) * P]

        class ContextAttention(LatentAttention):
            name = "context_attention"

            def scores(self, u):
                h, qt = divmod(u, 2)
                r = half(h)
                return [[(0, 256, QA[r, h // 2, qt * P:(qt + 1) * P], KA[r, h // 2, 0:256])]]

            def pieces(self, u):
                return [(0, 0, 0, 256, None)]

            def maps(self, u):
                return [(0, 256)]

            def blocks(self, u):
                return [(i * P, P) for i in range(2)]

            def values(self, u):
                h = u // 2
                return half(h), [VA[:, i, h * HD:(h + 1) * HD] for i in range(2)]

            def place(self, u):
                h, qt = divmod(u, 2)
                return CAT[half(h), CTX, 4 + h // 2, qt * P:(qt + 1) * P]
            place_free = ("latent_attention", "done")

        LAT, CON = LatentAttention(), ContextAttention()

        HID = area(FREE, 2, 32, SEQ)

        def mlp_tensor(pe, key, layer, segs, hkey):
            project_tensor(pe, key + "_up", f"mlp1_{layer}", h_moving(segs), h_ready(hkey, segs), segs, "mlp_up")
            pe.stage("mlp_down")
            w = len(segs) * SEQ
            for g in range(KT):
                b = take_bank(pe, (key + "_down", g))
                for part in range(2):
                    j = next_block(pe, f"mlp2_{layer}")
                    for k in range(16):
                        t = part * 16 + k
                        if g == 0 and t % 8 == 0:
                            for f in range(t, t + 8):
                                pe.wait_ge(*after("hidden", key, f))
                        ins = nc.tensor.matmul(psum(b, 0, w), slot(j, k, P), HID[:, seg_of(segs), t, :],
                                               start=(t == 0), stop=(t == 31))
                    ins.then_inc(*pe.step())
                    pe.mark("used", j)
                pe.mark(key + "_down", g)

        def mlp_scalar(act, key, segs):
            act.stage("mlp_up")
            for f in range(32):
                act.wait_ge(*after(key + "_up", f))
                b = bank_of((key + "_up", f))
                nc.scalar.activation(HID[:, seg_of(segs), f, :],
                                     psum(b, 0, len(segs) * SEQ).rearrange("p (s t) -> p s t", t=SEQ),
                                     ACT.Relu).then_inc(*act.step("taken", key + "_up", f))
            act.stage("mlp_down")
            take_out(act, key + "_down", range(0, KT, 2), y_place(segs), segs, "y_all")

        def mlp_vector(v, key, segs, mods=None):
            v.stage("mlp_up")
            for f in range(32):
                v.wait_ge(*after("taken", key + "_up", f))
                part = HID[:, seg_of(segs), f, :]
                nc.vector.tensor_tensor(part, part, part, ALU.mult).then_inc(*v.step("hidden", key, f))
            if mods is not None:
                mod_vectors(v, mods)
            v.stage("mlp_down")
            take_out(v, key + "_down", range(1, KT, 2), y_place(segs), segs, "y_all2")

        RR = area(0, KT, SEQ)
        XX = area(8192, 2, KT, SEQ)
        MIX = [area(12288, 2, KT, SEQ), area(16896, 2, KT, SEQ)]
        KK = area(16896, KT, 512)
        KR = area(20992, KT, 512)
        VP = area(25088, 8, PAIRS, HD)
        HW, HA = area(29184, 512), area(29696, 512)
        GH = area(16384, SEQ)
        LOW = {n: area(SMALL + 1024 * i, D) for i, n in enumerate(("w1", "a1", "g1", "w2", "a2", "g2"))}
        MIX_ORDER = [("r", 0, [X]), ("k", 2, [CTX, X]), ("v", 3, [CTX, X]), ("w", 1, [CTX, X]), ("a", 4, [CTX, X]),
                     ("g", 5, [X])]
        MIX_END = {"r": ("wr", 7), "k": ("wk", 7), "v": ("wv", 3, 1), "w": ("low_w",), "a": ("low_a",)}

        def mixes_vector(v):
            v.stage("mixes")
            v.wait_ge(*after("h_all", "n1_1"))
            H = HT.rearrange("p a b c -> p (a b) c")
            S = XX.rearrange("p a b c -> p (a b) c")
            nc.vector.tensor_tensor(S[:, :, 1:255], H[:, :, 0:254], H[:, :, 2:256], ALU.add).then_inc(*v.step())
            nc.vector.tensor_copy(S[:, :, 0:1], H[:, :, 1:2]).then_inc(*v.step())
            nc.vector.tensor_copy(S[:, :, 255:256], H[:, :, 254:255]).then_inc(*v.step())
            v.wait_ge(*v.own)
            nc.vector.scalar_tensor_tensor(S, S, 0.5, H, ALU.mult, ALU.subtract).then_inc(*v.step())
            v.wait_ge(*v.own)
            for i, (n, mu, segs) in enumerate(MIX_ORDER):
                if i >= 2:
                    v.wait_ge(*after(*MIX_END[MIX_ORDER[i - 2][0]]))
                sg = seg_of(segs)
                for k in range(KT):
                    nc.vector.scalar_tensor_tensor(MIX[i % 2][:, sg, k, :], XX[:, sg, k, :],
                                                   pr("mu", mu * KT + k, 1), HT[:, sg, k, :], ALU.mult, ALU.add).then_inc(*v.step("mix", n, k))
                if n == "k":
                    rw_out(v, "wr", 1, dve_copy)
                if n == "v":
                    rw_out(v, "wk", 1, dve_copy)
                if n == "a":
                    rwv_out(v, 1, dve_copy)

        def rw_out(q, name, share, copy):
            q.stage("project_" + name)
            for g in range(share, KT, 2):
                q.wait_ge(*after(name, g))
                w = SEQ if name == "wr" else 512
                dst = RR[:, g] if name == "wr" else KR[:, g]
                copy(dst, psum(bank_of((name, g)), 0, w)).then_inc(*q.step("taken", name, g))
                q.mark(name + "_out", g)
            q.mark(name + "_out_all", share)

        def rwv_out(q, share, copy):
            q.stage("project_wv")
            for jj in range(4):
                seg = share
                q.wait_ge(*after("wv", jj, seg))
                b = bank_of(("wv", jj, seg))
                copy(VP[:, 4 * seg:4 * seg + 4, 2 * jj:2 * jj + 2, :].rearrange("p c a i -> p c (a i)"),
                     psum(b).rearrange("p (c n) -> p c n", n=P)).then_inc(*q.step("taken", "wv", jj, seg))
            q.mark("wv_out", share)

        def features_tensor(pe):
            mv = lambda i, segs: (lambda k: MIX[i % 2][:, seg_of(segs), k, :])
            project_tensor(pe, "wr", "wr", lambda k: MIX[0][:, X, k, :], lambda k: [("mix", "r", k)], [X], "project_wr")
            project_tensor(pe, "wk", "wk", mv(1, [0, 1]), lambda k: [("mix", "k", k)], [CTX, X], "project_wk")
            pe.stage("project_wv")
            pe.wait_ge(*after("mix", "v", KT - 1))
            for jj in range(4):
                j = next_block(pe, "wv")
                for seg in range(2):
                    b = take_bank(pe, ("wv", jj, seg))
                    for c in range(N_CHUNK):
                        for odd in range(2):
                            for k in range(KT):
                                rhs = slot(j, k, 256).rearrange("p (a o i) -> p a o i", o=2, i=HD)[:, :, odd, :]
                                ins = nc.tensor.matmul(psum(b, c * P, P, half(odd)),
                                                       MIX[0][:, seg, k, c * CHUNK:(c + 1) * CHUNK], rhs,
                                                       start=(k == 0), stop=(k == KT - 1))
                    ins.then_inc(*pe.step("wv", jj, seg))
                pe.mark("used", j)
            pe.stage("low_rank")
            pe.wait_ge(*after("small"))
            for i, (n, w, segs) in enumerate((("w", "w1", [0, 1]), ("a", "a1", [0, 1]), ("g", "g1", [X]))):
                b = take_bank(pe, ("low_" + n,))
                for k in range(KT):
                    pe.wait_ge(*after("mix", n, k))
                    ins = nc.tensor.matmul(psum(b, 0, len(segs) * SEQ), LOW[w][:, k * P:(k + 1) * P],
                                           MIX[(i + 1) % 2][:, seg_of(segs), k, :], start=(k == 0), stop=(k == KT - 1))
                ins.then_inc(*pe.step("low_" + n))
            pe.stage("removal_key")
            for t in range(KT):
                b = take_bank(pe, ("kk_sum", t))
                pe.wait_ge(*after("kk_squares", t))
                nc.tensor.matmul(psum(b), cn("block_ones"), XX_SQ[:, t], start=True, stop=True).then_inc(*pe.step("kk_sum", t))

        XX_SQ = area(8192, KT, 512)

        def features_scalar(act):
            rw_out(act, "wr", 0, act_copy)
            rw_out(act, "wk", 0, act_copy)
            rwv_out(act, 0, act_copy)
            act.stage("low_rank")
            for n, fn, dst, w in (("w", ACT.Tanh, HW, 512), ("a", ACT.Copy, HA, 512), ("g", ACT.Sigmoid, GH, SEQ)):
                act.wait_ge(*after("low_" + n))
                nc.scalar.activation(dst, psum(bank_of(("low_" + n,)), 0, w), fn).then_inc(*act.step("taken", "low_" + n))
            act.stage("removal_key")
            act.wait_ge(*after("mix", "g", KT - 1))
            act.wait_ge(*after("wk_out", KT - 1))
            for t in range(KT):
                nc.scalar.activation(XX_SQ[:, t], KR[:, t], ACT.Square, scale=pr("kk", t, 1)).then_inc(*act.step("kk_squares", t))
            for t in range(KT):
                act.wait_ge(*after("kk_floor", t))
                nc.scalar.activation(XX_SQ[:, t], XX_SQ[:, t], ACT.Sqrt).then_inc(*act.step("kk_root", t))

        def removal_key_vector(v):
            v.stage("removal_key")
            v.wait_ge(*after("wk_out", KT - 2))
            v.wait_ge(*after("low_g"))
            for t in range(KT):
                nc.vector.tensor_scalar(KK[:, t], KR[:, t], pr("kk", t, 1), None, ALU.mult).then_inc(*v.step())
                v.wait_ge(*after("kk_sum", t))
                nc.vector.tensor_scalar(XX_SQ[:, t], psum(bank_of(("kk_sum", t))), 1e-24, None, ALU.max).then_inc(*v.step("taken", "kk_sum", t))
                v.mark("kk_floor", t)
            for t in range(KT):
                v.wait_ge(*after("kk_root", t))
                nc.vector.reciprocal(XX_SQ[:, t], XX_SQ[:, t]).then_inc(*v.step())
                v.wait_ge(*v.own)
                nc.vector.tensor_tensor(KK[:, t], KK[:, t], XX_SQ[:, t], ALU.mult).then_inc(*v.step())
            v.mark("features")

        DECAY = float(np.exp(-0.5))
        at = 4096
        WK = {}
        for n, dims in (("Y", (PAIRS, SEQ)), ("KS", (PAIRS, SEQ)), ("AR", (2, PAIRS, 128)), ("BM", (2, PAIRS, 128)),
                        ("GM", (2, PAIRS, 128)), ("B", (2, PAIRS, 64)), ("G", (2, PAIRS, 64))):
            WK[n] = area(at, *dims)
            at += int(np.prod(dims))
        assert at <= 16384, at
        at = 30208
        for n in ("E", "A", "L", "BN", "C", "S"):
            WK[n] = area(at, 2, PAIRS, 64)
            at += 1024
        assert at <= SMALL + 3072, at
        DEND = ctx.enter_context(nc.sbuf_tensor("decay_end", [P, 16], FP32))[:, :].rearrange("p (d a) -> p d a", d=2)
        WK["X"], WK["XI"], WK["Z"], WK["U"], WK["GN"] = WK["E"], WK["A"], WK["L"], WK["B"], WK["C"]

        def place_of(c, d):
            if d == 0:
                return c
            return 3 - c if c < 4 else 11 - c

        def flat(v):
            return v.rearrange("p a b -> p (a b)")

        def bank3(key, w=64):
            return psum(bank_of(key)).rearrange("p (a b) -> p a b", b=w)

        def pairs_matmul(pe, key, terms, width=64, pairs=range(PAIRS), ready=()):
            b = take_bank(pe, key)
            for e in ready:
                pe.wait_ge(*after(*e))
            for n, p in enumerate(pairs):
                for h in range(2):
                    r = half(h)
                    ts = terms(p, r)
                    for i, (lhs, rhs) in enumerate(ts):
                        ins = nc.tensor.matmul(psum(b, n * width, width, r), lhs, rhs, start=(i == 0),
                                               stop=(i == len(ts) - 1))
            ins.then_inc(*pe.step(*key))

        def wkv_tensor(pe):
            pe.stage("recurrence")
            pe.wait_ge(*after("taken", "low_a"))
            pe.wait_ge(*after("taken", "low_w"))
            for c in range(8):
                main = c >= 4
                for d in range(2):
                    tok = place_of(c, d) * CHUNK
                    rows = half(d)
                    for n, low, hid in (("w_raw", "w2", HW), ("a_raw", "a2", HA)):
                        key = (n, c, d)
                        b = take_bank(pe, key)
                        for p in range(PAIRS):
                            ins = nc.tensor.matmul(psum(b, p * 64, 64), LOW[low][rows, p * P:(p + 1) * P],
                                                   hid[rows, tok:tok + CHUNK], start=True, stop=True)
                        ins.then_inc(*pe.step(*key))
                for d in range(2):
                    B, G, AR = WK["B"][:, d], WK["G"][:, d], WK["AR"][:, d]
                    w = 128 if main else 64
                    for part in range(2):
                        ps_ = range(4 * part, 4 * part + 4)
                        pairs_matmul(pe, ("bm", c, d, part), lambda p, r: [(B[r, p, :], AR[r, p, 0:w])], w if main else 64,
                                     ps_, [("beta", c, d), ("rho", c, d)])
                    pairs_matmul(pe, ("l", c, d), lambda p, r: [(AR[r, p, 0:64], B[r, p, :])])
                    for part in range(2):
                        ps_ = range(4 * part, 4 * part + 4)
                        pairs_matmul(pe, ("gm", c, d, part), lambda p, r: [(G[r, p, :], AR[r, p, 0:w])], w if main else 64,
                                     ps_, [("gamma", c, d)])
                    I = cn("ident64")
                    pairs_matmul(pe, ("bn", c, d), lambda p, r: [(B[r, p, :], I[r, :])])
                    pairs_matmul(pe, ("gn", c, d), lambda p, r: [(G[r, p, :], I[r, :])])
                for lv in range(1, LEVELS):
                    for d in range(2):
                        Xm, XI, BM = WK["X"][:, d], WK["XI"][:, d], WK["BM"][:, d]
                        pairs_matmul(pe, ("z", c, d, lv), lambda p, r: [(BM[r, p, 0:64], Xm[r, p, :])],
                                     ready=[("inverse", c, d, lv - 1), ("bm_out", c, d)])
                    for d in range(2):
                        XI, Z = WK["XI"][:, d], WK["Z"][:, d]
                        pairs_matmul(pe, ("dxi", c, d, lv), lambda p, r: [(Z[r, p, :], XI[r, p, :])],
                                     ready=[("z_out", c, d, lv), ("inverse_t", c, d, lv - 1)])
                        if lv < LEVELS - 1:
                            pairs_matmul(pe, ("dx", c, d, lv), lambda p, r: [(XI[r, p, :], Z[r, p, :])])
                for d in range(2):
                    AR, GM, S, cc = WK["AR"][:, d], WK["GM"][:, d], WK["S"][:, d], place_of(c, d)
                    pairs_matmul(pe, ("w", c, d),
                                 lambda p, r: ([(AR[r, p, 0:64], S[r, p, :])] if c else [])
                                 + [(GM[r, p, 0:64], VP[r, cc, p, :])],
                                 ready=[("gm_out", c, d), ("wv_out", 0), ("wv_out", 1)] + ([("state", c - 1, d)] if c else []))
                for d in range(2):
                    XI, W = WK["XI"][:, d], WK["Z"][:, d]
                    pairs_matmul(pe, ("u", c, d), lambda p, r: [(XI[r, p, :], W[r, p, :])],
                                 ready=[("w_out", c, d), ("inverse_t", c, d, LEVELS - 1)])
                for d in range(2):
                    AR, BM, GM, S, U = (WK[n][:, d] for n in ("AR", "BM", "GM", "S", "U"))
                    BN, GN, cc = WK["BN"][:, d], WK["GN"][:, d], place_of(c, d)
                    pairs_matmul(pe, ("s", c, d), lambda p, r: [(BN[r, p, :], U[r, p, :]), (GN[r, p, :], VP[r, cc, p, :])],
                                 ready=[("u_out", c, d), ("bn_out", c, d), ("gn_out", c, d)])
                    if main:
                        pairs_matmul(pe, ("y", c, d), lambda p, r: [(S[r, p, :], AR[r, p, 64:128]),
                                                                    (U[r, p, :], BM[r, p, 64:128]),
                                                                    (VP[r, cc, p, :], GM[r, p, 64:128])])

        def wkv_scalar(act):
            act.stage("recurrence")
            for c in range(8):
                main = c >= 4
                for d in range(2):
                    E, A, L, C = (WK[n][:, d] for n in ("E", "A", "L", "C"))
                    for n, buf in (("w_in", L), ("a_in", A)):
                        act.wait_ge(*after(n, c, d))
                        nc.scalar.activation(flat(buf), flat(buf), ACT.Sigmoid).then_inc(*act.step(n + "_sig", c, d))
                for d in range(2):
                    E, A, L, C = (WK[n][:, d] for n in ("E", "A", "L", "C"))
                    act.wait_ge(*after("running", c, d))
                    nc.scalar.activation(DEND[:, d], C[:, :, 63] if d == 0 else C[:, :, 0], ACT.Exp,
                                         scale=-DECAY).then_inc(*act.step("decay_end", c, d))
                    nc.scalar.activation(flat(E), flat(E), ACT.Exp, scale=-DECAY).then_inc(*act.step("before", c, d))
                    nc.scalar.activation(flat(L), flat(C), ACT.Exp, scale=DECAY).then_inc(*act.step("inverse_decay", c, d))
                    if main:
                        act.wait_ge(*act.own)
                        nc.scalar.activation(flat(C), flat(C), ACT.Exp, scale=-DECAY).then_inc(*act.step("decay", c, d))
                for d in range(2):
                    for n, dst in (("bn", "BN"), ("gn", "GN")):
                        act.wait_ge(*after(n, c, d))
                        nc.scalar.activation(WK[dst][:, d], bank3((n, c, d)), ACT.Copy).then_inc(*act.step("taken", n, c, d))
                        act.mark(n + "_out", c, d)
                for n, dst in (("w", "Z"), ("u", "U")):
                    for d in range(2):
                        act.wait_ge(*after(n, c, d))
                        nc.scalar.activation(WK[dst][:, d], bank3((n, c, d)), ACT.Copy).then_inc(*act.step("taken", n, c, d))
                        act.mark(n + "_out", c, d)

        def wkv_vector(v):
            v.stage("recurrence")
            mul, add, sub = ALU.mult, ALU.add, ALU.subtract
            tt, stt = nc.vector.tensor_tensor, nc.vector.scalar_tensor_tensor

            def over_steps(name, d=0):
                return pr(name, d * KT, KT).unsqueeze(2).to_broadcast([P, PAIRS, 64])
            for c in range(8):
                main = c >= 4
                toks = [slice(place_of(c, d) * CHUNK, place_of(c, d) * CHUNK + CHUNK) for d in range(2)]
                xtoks = [slice(t.start - SEQ, t.stop - SEQ) for t in toks]
                for d in range(2):
                    A, L = WK["A"][:, d], WK["L"][:, d]
                    for n, buf, bias_name in (("w", L, "w0"), ("a", A, "a0")):
                        if c:
                            v.wait_ge(*after("u", c - 1, d))
                        v.wait_ge(*after(n + "_raw", c, d))
                        tt(buf, bank3((n + "_raw", c, d)), over_steps(bias_name, d), add).then_inc(*v.step("taken", n + "_raw", c, d))
                        v.mark(n + "_in", c, d)
                for d in range(2):
                    E, A, L, C = (WK[n][:, d] for n in ("E", "A", "L", "C"))
                    if c:
                        v.wait_ge(*after("s", c - 1, d))
                    v.wait_ge(*after("w_in_sig", c, d))
                    nc.vector.tensor_tensor_scan(flat(C), cn("scan_keep"), flat(L), 0.0, mul, add).then_inc(*v.step())
                    v.wait_ge(*v.own)
                    if d == 0:
                        tt(E, C, L, sub).then_inc(*v.step())
                    else:
                        tt(E, C[:, :, 63:64].to_broadcast([P, PAIRS, 64]), C, sub).then_inc(*v.step())
                        v.wait_ge(*v.own)
                        tt(C, E, L, add).then_inc(*v.step())
                    v.mark("running", c, d)
                for d in range(2):
                    E, A, L, C, B, G = (WK[n][:, d] for n in ("E", "A", "L", "C", "B", "G"))
                    AR = WK["AR"][:, d]
                    kk, k = KK[:, :, toks[d]], KR[:, :, toks[d]]
                    if c > 4:
                        v.wait_ge(*after("y", c - 1, d))
                    v.wait_ge(*after("before", c, d))
                    tt(AR[:, :, 0:64], kk, E, mul).then_inc(*v.step("alpha", c, d))
                    v.wait_ge(*after("inverse_decay", c, d))
                    v.wait_ge(*after("a_in_sig", c, d))
                    v.wait_ge(*v.own)
                    tt(E, kk, L, mul).then_inc(*v.step())
                    v.wait_ge(*v.own)
                    stt(flat(B), flat(E), -1.0, flat(A), mul, mul).then_inc(*v.step("beta", c, d))
                    if main:
                        v.wait_ge(*after("decay", c, d))
                        tt(AR[:, :, 64:128], RR[:, :, xtoks[d]], C, mul).then_inc(*v.step())
                    v.mark("rho", c, d)
                    v.wait_ge(*v.own)
                    stt(E, A, 1.0, over_steps("ka"), sub, mul).then_inc(*v.step())
                    v.wait_ge(*v.own)
                    stt(E, E, 1.0, k, add, mul).then_inc(*v.step())
                    v.wait_ge(*v.own)
                    if main:
                        ks = WK["KS"][:, :, xtoks[d]]
                        if c < 6:
                            nc.vector.tensor_copy(ks, E).then_inc(*v.step())
                        else:
                            tt(ks, ks, E, add).then_inc(*v.step())
                    tt(G, E, L, mul).then_inc(*v.step("gamma", c, d))
                for d in range(2):
                    X_, XI = WK["X"][:, d], WK["XI"][:, d]
                    I = cn("ident64").unsqueeze(1).to_broadcast([P, PAIRS, 64])
                    w = 128 if main else 64
                    bm, gm = WK["BM"][:, d], WK["GM"][:, d]
                    mask = cn("order", d * 128, w).unsqueeze(1).to_broadcast([P, 4, w])

                    def masked(name, dst):
                        for part in range(2):
                            v.wait_ge(*after(name, c, d, part))
                            src = psum(bank_of((name, c, d, part)), 0, 4 * w).rearrange("p (a b) -> p a b", b=w)
                            tt(dst[:, 4 * part:4 * part + 4, 0:w], src, mask, mul).then_inc(*v.step("taken", name, c, d, part))
                        v.mark(name + "_out", c, d)
                    masked("bm", bm)
                    first = [cn("first_level", 64 * (n ^ d), 64).unsqueeze(1).to_broadcast([P, PAIRS, 64]) for n in (0, 1)]
                    v.wait_ge(*after("l", c, d))
                    tt(X_, bank3(("l", c, d)), first[0], mul).then_inc(*v.step("taken", "l", c, d))
                    v.wait_ge(*v.own)
                    tt(XI, bm[:, :, 0:64], first[1], mul).then_inc(*v.step())
                    tt(X_, X_, I, add).then_inc(*v.step("inverse", c, d, 0))
                    v.wait_ge(*v.own)
                    tt(XI, XI, I, add).then_inc(*v.step("inverse_t", c, d, 0))
                    masked("gm", gm)
                for lv in range(1, LEVELS):
                    for d in range(2):
                        mask = cn("later_levels", (d * 5 + lv - 1) * 64, 64).unsqueeze(1).to_broadcast([P, PAIRS, 64])
                        v.wait_ge(*after("z", c, d, lv))
                        tt(WK["Z"][:, d], bank3(("z", c, d, lv)), mask, mul).then_inc(*v.step("taken", "z", c, d, lv))
                        v.mark("z_out", c, d, lv)
                    for d in range(2):
                        X_, XI = WK["X"][:, d], WK["XI"][:, d]
                        for key, buf, ev in (("dxi", XI, "inverse_t"), ("dx", X_, "inverse")):
                            if key == "dx" and lv == LEVELS - 1:
                                continue
                            v.wait_ge(*after(key, c, d, lv))
                            if key == "dxi" and lv < LEVELS - 1:
                                v.wait_ge(*after("dx", c, d, lv))
                            tt(buf, buf, bank3((key, c, d, lv)), add).then_inc(*v.step("taken", key, c, d, lv))
                            v.mark(ev, c, d, lv)
                for d in range(2):
                    S = WK["S"][:, d]
                    end = DEND[:, d].unsqueeze(2).to_broadcast([P, PAIRS, 64])
                    if main:
                        v.wait_ge(*after("y", c, d))
                        ys = WK["Y"][:, :, xtoks[d]]
                        src = bank3(("y", c, d))
                        if c < 6:
                            nc.vector.tensor_copy(ys, src).then_inc(*v.step("taken", "y", c, d))
                        else:
                            tt(ys, ys, src, add).then_inc(*v.step("taken", "y", c, d))
                    v.wait_ge(*after("s", c, d))
                    v.wait_ge(*after("decay_end", c, d))
                    if c:
                        tt(S, S, bank3(("s", c, d)), add).then_inc(*v.step("taken", "s", c, d))
                        v.wait_ge(*v.own)
                        tt(S, S, end, mul).then_inc(*v.step("state", c, d))
                    else:
                        tt(S, bank3(("s", c, d)), end, mul).then_inc(*v.step("taken", "s", c, d))
                        v.mark("state", c, d)
            v.mark("recurrence_done")

        VT = area(16896, KT, SEQ)
        YC = area(18944, KT, SEQ)
        Q1 = area(8192, KT, SEQ)
        Q2 = area(10240, KT, SEQ)
        RD = area(12288, KT, SEQ)

        def readout_tensor(pe):
            pe.stage("readout")
            I = cn("ident64")
            for part in range(4):
                b = take_bank(pe, ("vt", part))
                pe.wait_ge(*after("recurrence_done"))
                for n in range(2):
                    p = 2 * part + n
                    for c in range(4):
                        for h in range(2):
                            ins = nc.tensor.matmul(psum(b, n * SEQ + c * 64, 64, half(h)), VP[half(h), 4 + c, p, :],
                                                   I[half(h), :], start=True, stop=True)
                ins.then_inc(*pe.step("vt", part))
            for t in range(KT):
                b = take_bank(pe, ("y_mean", t))
                nc.tensor.matmul(psum(b, 0, SEQ), cn("block_ones"), WK["Y"][:, t], start=True, stop=True).then_inc(*pe.step("y_mean", t))
            for t in range(KT):
                b = take_bank(pe, ("bonus", t))
                pe.wait_ge(*after("rks", t))
                nc.tensor.matmul(psum(b, 0, SEQ), cn("block_ones"), Q2[:, t], start=True, stop=True).then_inc(*pe.step("bonus", t))
                b = take_bank(pe, ("y_var", t))
                pe.wait_ge(*after("yc_square", t))
                nc.tensor.matmul(psum(b, 0, SEQ), cn("block_ones"), Q1[:, t], start=True, stop=True).then_inc(*pe.step("y_var", t))
                b = take_bank(pe, ("gate", t))
                pe.wait_ge(*after("taken", "low_g"))
                nc.tensor.matmul(psum(b, 0, SEQ), LOW["g2"][:, t * P:(t + 1) * P], GH, start=True, stop=True).then_inc(*pe.step("gate", t))

        def readout_scalar(act):
            act.stage("readout")
            for part in range(4):
                act.wait_ge(*after("vt", part))
                nc.scalar.activation(VT[:, 2 * part:2 * part + 2], psum(bank_of(("vt", part))).rearrange(
            "p (a b) -> p a b", b=SEQ), ACT.Copy).then_inc(*act.step("taken", "vt", part))
            for t in range(KT):
                act.wait_ge(*after("yc", t))
                nc.scalar.activation(Q1[:, t], YC[:, t], ACT.Square).then_inc(*act.step("yc_square", t))
            for t in range(KT):
                act.wait_ge(*after("y_var", t))
                nc.scalar.activation(RD[:, t], psum(bank_of(("y_var", t)), 0, SEQ), ACT.Sqrt,
                                     bias=cn("eps", 1, 1), scale=1.0 / HD).then_inc(*act.step("taken", "y_var", t))

        def readout_vector(v):
            v.stage("readout")
            stt, tt = nc.vector.scalar_tensor_tensor, nc.vector.tensor_tensor
            v.wait_ge(*v.own)
            for t in range(KT):
                v.wait_ge(*after("y_mean", t))
                stt(YC[:, t], psum(bank_of(("y_mean", t)), 0, SEQ), -1.0 / HD, WK["Y"][:, t], ALU.mult, ALU.add).then_inc(*v.step("taken", "y_mean", t))
                v.mark("yc", t)
            v.wait_ge(*after("y_mean", KT - 1))
            for t in range(KT):
                stt(Q2[:, t], RR[:, t], pr("rk", t, 1), WK["KS"][:, t], ALU.mult, ALU.mult).then_inc(*v.step("rks", t))
            v.wait_ge(*after("taken", "vt", 3))
            for t in range(KT):
                v.wait_ge(*after("bonus", t))
                tt(VT[:, t], psum(bank_of(("bonus", t)), 0, SEQ), VT[:, t], ALU.mult).then_inc(*v.step("taken", "bonus", t))
                v.wait_ge(*after("taken", "y_var", t))
                nc.vector.reciprocal(RD[:, t], RD[:, t]).then_inc(*v.step())
                v.wait_ge(*v.own)
                stt(YC[:, t], YC[:, t], pr("lng", t, 1), RD[:, t], ALU.mult, ALU.mult).then_inc(*v.step())
                v.wait_ge(*v.own)
                stt(YC[:, t], YC[:, t], pr("lnb", t, 1), VT[:, t], ALU.add, ALU.add).then_inc(*v.step())
                v.wait_ge(*v.own)
                v.wait_ge(*after("gate", t))
                tt(MIX[0][:, X, t, :], YC[:, t], psum(bank_of(("gate", t)), 0, SEQ), ALU.mult).then_inc(*v.step("taken", "gate", t))
                v.mark("read", t)

        CAT2 = area(12288, KT, SEQ)
        B2 = 31100

        def rope_tensor(pe, key, raw, g, ready):
            b = take_bank(pe, (key + "_rot", g))
            pe.wait_ge(*after(*ready))
            nc.tensor.matmul(psum(b, 0, SEQ), cn("swap"), raw, start=True, stop=True).then_inc(*pe.step(key + "_rot", g))

        def rope_pool(g_, key, g, raw, dst, ready):
            g_.wait_ge(*after(*ready))
            nc.gpsimd.tensor_tensor(dst, raw, cn("cos"), ALU.mult).then_inc(*g_.step(key + "_cos", g))

        def rope_vector(v, key, g, raw, dst):
            v.wait_ge(*after(key + "_rot", g))
            v.wait_ge(*after(key + "_cos", g))
            nc.vector.tensor_tensor(raw, psum(bank_of((key + "_rot", g)), 0, SEQ), cn("sin"), ALU.mult).then_inc(*v.step("taken", key + "_rot", g))
            v.wait_ge(*v.own)
            nc.vector.tensor_tensor(dst, dst, raw, ALU.add).then_inc(*v.step(key + "_roped", g))

        RAW = area(FREE, 16, SEQ)
        QK = area(FREE + 4096, 16, SEQ)
        VV = area(FREE + 8192, 2, D)
        OB = area(FREE + 10240, 4, SEQ)
        ATT_B = FREE + 11264
        LF = area(B2, 16)
        E2_BLOCKS = [("t", 0), ("t", 1), ("t", 2), ("t", 3), ("v", 0), ("v", 1), ("t", 4), ("t", 5), ("t", 6), ("t", 7),
                     ("v", 2), ("v", 3)]
        LAMBDA_INIT = 0.8 - 0.6

        def ev2_tensor(pe):
            pe.stage("project_ev2")
            for k in range(KT):
                pe.wait_ge(*after("h", "n1_2", k, X))
            prev = []
            for kind, n in E2_BLOCKS:
                if kind == "t":
                    j = next_block(pe, "ev2_in")
                    for i in range(2):
                        b = take_bank(pe, ("e2", 2 * n + i))
                        for k in range(KT):
                            ins = nc.tensor.matmul(psum(b, 0, SEQ), slot(j, k, 256, i * P, P), HT[:, X, k, :],
                                                   start=(k == 0), stop=(k == KT - 1))
                        ins.then_inc(*pe.step("e2", 2 * n + i))
                    pe.mark("used", j)
                else:
                    natural_block(pe, "ev2_in", ("e2v", n))
                for g in prev:
                    rope_tensor(pe, "e2", RAW[:, g], g, ("taken", "e2", g))
                prev = [2 * n, 2 * n + 1] if kind == "t" else []
            assert not prev

        def natural_block(pe, name, key):
            j = next_block(pe, name)
            b = take_bank(pe, key)
            for tt_ in range(2):
                for k in range(KT):
                    ins = nc.tensor.matmul(psum(b, tt_ * 256, 256), HT[:, X, k, tt_ * P:(tt_ + 1) * P],
                                           slot(j, k, 256), start=(k == 0), stop=(k == KT - 1))
            ins.then_inc(*pe.step(*key))
            pe.mark("used", j)

        def ev2_scalar(act):
            act.stage("project_ev2")
            for kind, n in E2_BLOCKS:
                if kind == "t":
                    for g in (2 * n, 2 * n + 1):
                        act.wait_ge(*after("e2", g))
                        nc.scalar.activation(RAW[:, g], psum(bank_of(("e2", g)), 0, SEQ), ACT.Copy).then_inc(*act.step("taken", "e2", g))
                else:
                    act.wait_ge(*after("e2v", n))
                    nc.scalar.activation(VV[:, :, n * 256:(n + 1) * 256], psum(bank_of(("e2v", n))).rearrange(
                "p (a b) -> p a b", b=256), ACT.Copy).then_inc(*act.step("taken", "e2v", n))
            act.wait_ge(*after("lambda_sums"))
            nc.scalar.activation(LF[:, 4:6], psum(bank_of(("lambda_sums",)), 0, 2), ACT.Exp).then_inc(*act.step("taken", "lambda_sums"))

        def ev2_pool(g_):
            g_.stage("project_ev2")
            for g in range(16):
                rope_pool(g_, "e2", g, RAW[:, g], QK[:, g], ("taken", "e2", g))

        def lambda_tensor(pe):
            b = take_bank(pe, ("lambda_sums",))
            pe.wait_ge(*after("lambda_products"))
            nc.tensor.matmul(psum(b, 0, 2), cn("ones"), LF[:, 0:2], start=True, stop=True).then_inc(*pe.step("lambda_sums"))

        def ev2_vector(v):
            v.stage("project_ev2")
            lp = pr("lam")
            nc.vector.tensor_tensor(LF[:, 0:1], lp[:, 0:1], lp[:, 1:2], ALU.mult).then_inc(*v.step())
            nc.vector.tensor_tensor(LF[:, 1:2], lp[:, 2:3], lp[:, 3:4], ALU.mult).then_inc(*v.step("lambda_products"))
            for g in range(16):
                rope_vector(v, "e2", g, RAW[:, g], QK[:, g])
            v.wait_ge(*after("taken", "lambda_sums"))
            nc.vector.memset(LF[:, 8:9], 1.0).then_inc(*v.step())
            nc.vector.tensor_tensor(LF[:, 6:7], LF[:, 5:6], LF[:, 4:5], ALU.subtract).then_inc(*v.step())
            v.wait_ge(*v.own)
            nc.vector.tensor_scalar(LF[:, 9:10], LF[:, 6:7], -LAMBDA_INIT, None, ALU.add).then_inc(*v.step("lambda"))

        def causal_pieces(n, col, dst, qt):
            full = [(n, col, dst, P, None)] if qt else []
            return full + [(n, col + qt * P, dst + qt * P, P, cn("causal"))]

        class CausalAttention(Attention):
            name, n, base = "causal_attention", 16, ATT_B
            place_free = ("e2_roped", 15)

            def ready(self, u):
                return (("e2_roped", 15),)

            def values_ready(self, u):
                return (("taken", "e2v", 3),)

            def scores(self, u):
                h, qt = divmod(u, 2)
                r = half(h)
                return [[(0, P * (qt + 1), QK[r, h // 2, qt * P:(qt + 1) * P], QK[r, 4 + h // 2, 0:P * (qt + 1)])]]

            def pieces(self, u):
                return causal_pieces(0, 0, 0, u % 2)

            def maps(self, u):
                return [(0, P * (u % 2 + 1))]

            def blocks(self, u):
                return [(i * P, P) for i in range(u % 2 + 1)]

            def values(self, u):
                h, qt = divmod(u, 2)
                return half(h), [VV[:, i, h * HD:(h + 1) * HD] for i in range(qt + 1)]

            def place(self, u):
                h, qt = divmod(u, 2)
                return CAT2[half(h), h // 2, qt * P:(qt + 1) * P]

        class DifferentialAttention(CausalAttention):
            name, n = "differential_attention", 8
            subtract = True
            place_free = ("causal_attention", "done")

            def factor(self, u):
                return LF[:, 8:10]

            def scores(self, u):
                h, qt = divmod(u, 2)
                w = P * (qt + 1)
                return [[(0, w, QK[half(m), 8 + h, qt * P:(qt + 1) * P], QK[half(m), 12 + h, 0:w])]
                        for m in range(2)]

            def pieces(self, u):
                return causal_pieces(0, 0, 0, u % 2) + causal_pieces(1, 0, 256, u % 2)

            def maps(self, u):
                w = P * (u % 2 + 1)
                return [(0, w), (256, w)]

            def values(self, u):
                h, qt = divmod(u, 2)
                return slice(0, P), [VV[:, i, 512 + h * P:512 + (h + 1) * P] for i in range(qt + 1)]

            def place(self, u):
                h, qt = divmod(u, 2)
                return OB[:, h, qt * P:(qt + 1) * P]

        CAU, DIF = CausalAttention(), DifferentialAttention()

        def subln_tensor(pe):
            pe.stage("head_norm")
            for h in range(4):
                b = take_bank(pe, ("head_sum", h))
                pe.wait_ge(*after("head_square", h))
                nc.tensor.matmul(psum(b, 0, SEQ), cn("ones"), RAW[:, h], start=True, stop=True).then_inc(*pe.step("head_sum", h))

        def subln_scalar(act):
            act.stage("head_norm")
            act.wait_ge(*act.own)
            for h in range(4):
                nc.scalar.activation(RAW[:, h], OB[:, h], ACT.Square).then_inc(*act.step("head_square", h))
            for h in range(4):
                act.wait_ge(*after("head_sum", h))
                nc.scalar.activation(RAW[:, 4 + h], psum(bank_of(("head_sum", h)), 0, SEQ), ACT.Sqrt,
                                     bias=cn("eps", 0, 1), scale=1.0 / P).then_inc(*act.step("taken", "head_sum", h))

        def subln_vector(v):
            v.stage("head_norm")
            nc.vector.tensor_scalar(LF[:, 10:11], pr("subln"), 1.0 - LAMBDA_INIT, None, ALU.mult).then_inc(*v.step())
            for h in range(4):
                v.wait_ge(*after("taken", "head_sum", h))
                nc.vector.reciprocal(RAW[:, 4 + h], RAW[:, 4 + h]).then_inc(*v.step())
                v.wait_ge(*v.own)
                nc.vector.scalar_tensor_tensor(CAT2[:, 4 + h], OB[:, h], LF[:, 10:11], RAW[:, 4 + h],
                                               ALU.mult, ALU.mult).then_inc(*v.step("head_normed", h))

        CB = area(FREE, N_EXPERTS, SEQ)
        SG = area(FREE + 4096, 3, 512)
        AE = area(FREE + 5632, 3, 512)
        CT = area(FREE + 7168, SEQ)
        RT = FREE + 7424
        LG = area(RT, 2, 20)
        ROUTE_BANKS = [0, 1, 2, 7]
        SUM_BANKS = [3, 4, 5, 6]

        def moe_tensor(pe, l):
            pe.stage(f"router{l}")
            b = take_bank(pe, ("route", l), ROUTE_BANKS)
            for tt_ in range(2):
                for k in range(KT):
                    if tt_ == 0:
                        pe.wait_ge(*after("h", f"n2_{l + 2}", k, X))
                    ins = nc.tensor.matmul(psum(b, tt_ * 20, 20), HT[:, X, k, tt_ * P:(tt_ + 1) * P],
                                           pr("router_w", (l * KT + k) * 20, 20), start=(k == 0), stop=(k == KT - 1))
            ins.then_inc(*pe.step("route", l))

            def gate_up(e):
                for which in ("gate", "up"):
                    j = next_block(pe, f"moe{l}")
                    b = take_bank(pe, (which, l, e), ROUTE_BANKS)
                    for i in range(2):
                        for k in range(KT):
                            ins = nc.tensor.matmul(psum(b, i * SEQ, SEQ), slot(j, k, 256, i * P, P), HT[:, X, k, :],
                                                   start=(k == 0), stop=(k == KT - 1))
                    ins.then_inc(*pe.step(which, l, e))
                    pe.mark("used", j)

            def down(e):
                j = next_block(pe, f"moe{l}")
                pe.wait_ge(*after("expert", l, e))
                if e == 0:
                    for bk in SUM_BANKS:
                        if bank_state["holder"][bk] is not None:
                            pe.wait_ge(*after("taken", *bank_state["holder"][bk]))
                        bank_state["holder"][bk] = ("moe_y", l, bk)
                        events.where[("moe_y", l, bk)] = bk
                for t in range(KT):
                    for k in range(2):
                        first = e == 0 and k == 0 and t % 2 == 0
                        ins = nc.tensor.matmul(psum(3 + t // 2, (t % 2) * SEQ, SEQ), slot(j, k, D, t * P, P),
                                               AE[:, e % 3, k * SEQ:(k + 1) * SEQ], start=first,
                                               stop=(e == N_EXPERTS - 1 and k == 1), skip_group_check=True)
                ins.then_inc(*pe.step("down", l, e))
                pe.mark("used", j)

            gate_up(0)
            b = take_bank(pe, ("comb_t", l), SUM_BANKS)
            pe.wait_ge(*after("comb", l))
            for tt_ in range(2):
                ins = nc.tensor.transpose(psum(b, tt_ * P, P, slice(0, 16)), COMB[:, tt_, :], cn("ident"))
            ins.then_inc(*pe.step("comb_t", l))
            for n in range(8):
                b = take_bank(pe, ("comb_rows", l, n), SUM_BANKS)
                pe.wait_ge(*after("taken", "comb_t", l))
                for i in range(2):
                    e = 2 * n + i
                    pick = cn("ident", e, 1, slice(0, 16)).to_broadcast([16, P])
                    ins = nc.tensor.matmul(psum(b, i * SEQ, SEQ), pick, CT[0:16, :], start=True, stop=True)
                ins.then_inc(*pe.step("comb_rows", l, n))
            for e in range(1, N_EXPERTS):
                gate_up(e)
                down(e - 1)
            down(N_EXPERTS - 1)

        COMB = area(RT + 200, 2, 16)

        def moe_vector(v, l):
            v.stage(f"router{l}")
            tt, ts = nc.vector.tensor_tensor, nc.vector.tensor_scalar
            at_ = [RT + 400]

            def tmp(*dims):
                r = area(at_[0], *dims)
                at_[0] += int(np.prod(dims))
                return r

            def step(ins):
                ins.then_inc(*v.step())
                v.wait_ge(*v.own)
            v.wait_ge(*after("route", l))
            bias_ = pr("router_b", l * 20, 20).unsqueeze(1).to_broadcast([P, 2, 20])
            tt(LG, psum(bank_of(("route", l)), 0, 40).rearrange("p (a b) -> p a b", b=20), bias_, ALU.add).then_inc(*v.step("taken", "route", l))
            v.wait_ge(*v.own)
            GL = LG[:, :, 0:4]

            def four(x):
                return x.unsqueeze(2).to_broadcast([P, 2, 4])

            def first_max(x):
                m, o, t = tmp(2), tmp(2, 4), tmp(2)
                step(nc.vector.tensor_reduce(m, x, AX.X, ALU.max))
                step(tt(o, x, four(m), ALU.is_equal))
                step(tt(o, o, cn("tie").unsqueeze(1).to_broadcast([P, 2, 4]), ALU.mult))
                step(nc.vector.tensor_reduce(t, o, AX.X, ALU.max))
                step(tt(o, o, four(t), ALU.is_equal))
                return m, o
            gm, goh = first_max(GL)
            z, zs, gw = tmp(2, 4), tmp(2), tmp(2)
            tt(z, GL, four(gm), ALU.subtract).then_inc(*v.step("group_less", l))
            big, elg = tmp(2, 4, 4), tmp(2, 4)
            v.wait_ge(*v.own)
            step(tt(big, LG[:, :, 4:20].rearrange("p t (g e) -> p t g e", e=4),
                    goh.unsqueeze(3).to_broadcast([P, 2, 4, 4]), ALU.mult))
            step(nc.vector.tensor_reduce(elg, big.rearrange("p t g e -> p t e g"), AX.X, ALU.add))
            m1, oh1 = first_max(elg)
            el2 = tmp(2, 4)
            step(nc.vector.scalar_tensor_tensor(el2, oh1, NEG, elg, ALU.mult, ALU.add))
            m2, oh2 = first_max(el2)
            d, w1, w2 = tmp(2), tmp(2), tmp(2)
            tt(d, m2, m1, ALU.subtract).then_inc(*v.step("top_less", l))
            v.wait_ge(*after("route_exp", l))
            step(nc.vector.tensor_reduce(zs, z, AX.X, ALU.add))
            step(nc.vector.reciprocal(gw, zs))
            step(ts(w1, d, 1.0, None, ALU.add))
            step(nc.vector.reciprocal(w1, w1))
            step(tt(w1, w1, gw, ALU.mult))
            step(tt(w2, d, w1, ALU.mult))
            step(tt(oh1, oh1, four(w1), ALU.mult))
            step(tt(oh2, oh2, four(w2), ALU.mult))
            step(tt(oh1, oh1, oh2, ALU.add))
            tt(COMB.rearrange("p t (g e) -> p t g e", e=4), goh.unsqueeze(3).to_broadcast([P, 2, 4, 4]),
               oh1.unsqueeze(2).to_broadcast([P, 2, 4, 4]), ALU.mult).then_inc(*v.step("comb", l))
            v.stage(f"experts{l}")
            for n in range(1, 8, 2):
                v.wait_ge(*after("comb_rows", l, n))
                nc.vector.tensor_copy(CB[:, 2 * n:2 * n + 2], psum(bank_of(("comb_rows", l, n))).rearrange(
              "p (a b) -> p a b", b=SEQ)).then_inc(*v.step("taken", "comb_rows", l, n))
                v.mark("comb_rows_out", l, n)
            for e in range(N_EXPERTS):
                a_ = AE[:, e % 3]
                v.wait_ge(*after("silu", l, e))
                v.wait_ge(*after("up", l, e))
                if e >= 3:
                    v.wait_ge(*after("down", l, e - 3))
                tt(a_, SG[:, e % 3], psum(bank_of(("up", l, e))), ALU.mult).then_inc(*v.step("taken", "up", l, e))
                v.wait_ge(*after("comb_rows_out", l, (e // 2) & ~1))
                v.wait_ge(*v.own)
                a2 = a_.rearrange("p (a b) -> p a b", b=SEQ)
                tt(a2, a2, CB[:, e].unsqueeze(1).to_broadcast([P, 2, SEQ]), ALU.mult).then_inc(*v.step("expert", l, e))
            v.wait_ge(*after("down", l, N_EXPERTS - 1))
            for b in (4, 6):
                t = 2 * (b - 3)
                nc.vector.tensor_copy(YT[:, X, t:t + 2, :], psum(b).rearrange("p (a b) -> p a b", b=SEQ)).then_inc(*v.step("taken", "moe_y", l, b))
            v.mark("y_all2", f"moe{l}")

        Z_AT = RT + 400 + 2 + 8 + 2
        D_AT = Z_AT + 8 + 2 + 2 + 32 + 8 + 12 + 8 + 12

        def moe_scalar(act, l):
            act.stage(f"router{l}")
            z, d = area(Z_AT, 8), area(D_AT, 2)
            act.wait_ge(*after("group_less", l))
            nc.scalar.activation(z, z, ACT.Exp).then_inc(*act.step())
            act.wait_ge(*after("top_less", l))
            nc.scalar.activation(d, d, ACT.Exp).then_inc(*act.step("route_exp", l))
            act.wait_ge(*after("comb_t", l))
            nc.scalar.activation(CT[0:16, :], psum(bank_of(("comb_t", l)), 0, SEQ, slice(0, 16)), ACT.Copy).then_inc(*act.step("taken", "comb_t", l))
            act.stage(f"experts{l}")
            for n in range(0, 8, 2):
                act.wait_ge(*after("comb_rows", l, n))
                nc.scalar.activation(CB[:, 2 * n:2 * n + 2], psum(bank_of(("comb_rows", l, n))).rearrange(
            "p (a b) -> p a b", b=SEQ), ACT.Copy).then_inc(*act.step("taken", "comb_rows", l, n))
                act.mark("comb_rows_out", l, n)
            for e in range(N_EXPERTS):
                act.wait_ge(*after("gate", l, e))
                if e >= 3:
                    act.wait_ge(*after("taken", "up", l, e - 3))
                nc.scalar.activation(SG[:, e % 3], psum(bank_of(("gate", l, e))), ACT.Silu).then_inc(*act.step("taken", "gate", l, e))
                act.mark("silu", l, e)
            act.wait_ge(*after("down", l, N_EXPERTS - 1))
            for b in (3, 5):
                t = 2 * (b - 3)
                nc.scalar.activation(YT[:, X, t:t + 2, :], psum(b).rearrange("p (a b) -> p a b", b=SEQ),
                                     ACT.Copy).then_inc(*act.step("taken", "moe_y", l, b))
            act.mark("y_all", f"moe{l}")

        RQ = area(FREE, KT, SEQ)
        RK = area(FREE + 2048, 4, 4, SEQ)
        QR = area(FREE + 6144, KT, SEQ)
        KRT = area(FREE + 8192, 3, 4, SEQ)
        ATT_C = FREE + 11264
        VS = area(B2, 2, 256)
        VW = area(B2 + 512, 2, 256)
        BK = area(B2 + 1024, 2, 16, 4, N_CMP)
        HC = area(B2 + 2944, 2, 2, 4 * N_CMP)
        KC = area(B2 + 3184, 4 * N_CMP)
        VC = area(B2 + 3244, 4, HD)
        GT = area(B2 + 3500, 2, 48)
        ROPED = {0: 0, 2: 1, 3: 2}
        OD_BLOCKS = [("q", 0), ("q", 1), ("q", 2), ("q", 3), ("k", 0), ("k", 1), ("k", 2), ("v", 0), ("k", 3), ("v", 1)]

        def od_tensor(pe):
            pe.stage("project_od")
            for k in range(KT):
                pe.wait_ge(*after("h", "n1_3", k, X))
            prev = []
            for kind, n in OD_BLOCKS:
                if kind == "v":
                    natural_block(pe, "od_in", ("odv", n))
                elif kind == "q":
                    j = next_block(pe, "od_in")
                    for i in range(2):
                        b = take_bank(pe, ("odq", 2 * n + i))
                        for k in range(KT):
                            ins = nc.tensor.matmul(psum(b, 0, SEQ), slot(j, k, 256, i * P, P), HT[:, X, k, :],
                                                   start=(k == 0), stop=(k == KT - 1))
                        ins.then_inc(*pe.step("odq", 2 * n + i))
                    pe.mark("used", j)
                else:
                    j = next_block(pe, "od_in")
                    for i in range(2):
                        b = take_bank(pe, ("odk", 2 * n + i))
                        for g in range(2):
                            for h in range(2):
                                for k in range(KT):
                                    ins = nc.tensor.matmul(psum(b, g * SEQ, SEQ, half(h)),
                                                           slot(j, k, 256, (2 * i + g) * HD, HD), HT[:, X, k, :],
                                                           start=(k == 0), stop=(k == KT - 1))
                        ins.then_inc(*pe.step("odk", 2 * n + i))
                    pe.mark("used", j)
                for e in prev:
                    rope_tensor(pe, "od", *e)
                prev = od_ropes(kind, n)
            b = take_bank(pe, ("od_gates",))
            for tt_ in range(2):
                for k in range(KT):
                    ins = nc.tensor.matmul(psum(b, tt_ * 48, 48), HT[:, X, k, tt_ * P:(tt_ + 1) * P],
                                           pr("gate_w", k * 48, 48), start=(k == 0), stop=(k == KT - 1))
            ins.then_inc(*pe.step("od_gates"))

        def od_ropes(kind, n):
            if kind == "q":
                return [(RQ[:, g], g, ("taken", "odq", g)) for g in (2 * n, 2 * n + 1)]
            if kind == "k" and n in ROPED:
                return [(RK[:, n, g], 8 + 4 * ROPED[n] + g, ("taken", "odk", 2 * n + g // 2)) for g in range(4)]
            return []

        def od_dst(g):
            return QR[:, g] if g < 8 else KRT[:, (g - 8) // 4, (g - 8) % 4]

        def od_scalar(act):
            act.stage("project_od")
            for kind, n in OD_BLOCKS:
                if kind == "q":
                    for g in (2 * n, 2 * n + 1):
                        act.wait_ge(*after("odq", g))
                        nc.scalar.activation(RQ[:, g], psum(bank_of(("odq", g)), 0, SEQ), ACT.Copy).then_inc(*act.step("taken", "odq", g))
                elif kind == "k":
                    for i in range(2):
                        act.wait_ge(*after("odk", 2 * n + i))
                        nc.scalar.activation(RK[:, n, 2 * i:2 * i + 2], psum(bank_of(("odk", 2 * n + i))).rearrange(
                    "p (a b) -> p a b", b=SEQ), ACT.Copy).then_inc(*act.step("taken", "odk", 2 * n + i))
                else:
                    act.wait_ge(*after("odv", n))
                    nc.scalar.activation(VS if n == 0 else VW, psum(bank_of(("odv", n))).rearrange(
                "p (a b) -> p a b", b=256), ACT.Copy).then_inc(*act.step("taken", "odv", n))
            act.wait_ge(*after("od_gates"))
            nc.scalar.activation(GT, psum(bank_of(("od_gates",)), 0, 96).rearrange("p (a b) -> p a b", b=48),
                                 ACT.Sigmoid).then_inc(*act.step("taken", "od_gates"))

        def od_pool(g_):
            g_.stage("project_od")
            for kind, n in OD_BLOCKS:
                for raw, g, ready in od_ropes(kind, n):
                    rope_pool(g_, "od", g, raw, od_dst(g), ready)

        def od_vector(v):
            v.stage("project_od")
            for kind, n in OD_BLOCKS:
                for raw, g, _ in od_ropes(kind, n):
                    rope_vector(v, "od", g, raw, od_dst(g))
                if (kind, n) == ("k", 1):
                    windows_vector(v)
            v.wait_ge(*after("taken", "od_gates"))
            for qt in range(2):
                c = GT[:, qt, :].rearrange("p (h b) -> p h b", b=3)[:, :, 0:1]
                nc.vector.tensor_scalar(c, c, cn("cmp_live", qt, 1), None, ALU.mult).then_inc(*v.step())
            v.mark("gates")

        def windows_vector(v):
            v.wait_ge(*after("taken", "odk", 3))
            v.wait_ge(*v.own)
            for which, src in ((0, KRT[:, 0]), (1, RK[:, 1])):
                for h in range(2):
                    for g in range(4):
                        rows = half(h)
                        base = src[rows, g, :]
                        lo = base[:, 0:240].rearrange("p (n l o) -> p l n o", l=8, o=2)[:, :, :, h]
                        hi = base[:, 16:256].rearrange("p (n l o) -> p l n o", l=8, o=2)[:, :, :, h]
                        pos = pr("cmp_pos", which * 16, 16, rows)
                        for part, s in ((0, lo), (1, hi)):
                            nc.vector.tensor_tensor(
                          BK[rows, which, 8 * part:8 * part + 8, g, :], s,
                          pos[:, 8 * part:8 * part + 8].unsqueeze(2).to_broadcast([HD, 8, N_CMP]), ALU.add).then_inc(*v.step())
            v.mark("windows")

        def compress_tensor(pe):
            pe.stage("compress")
            pe.wait_ge(*after("windows"))
            for which, name in ((0, "cmp_k"), (1, "cmp_v")):
                banks = [take_bank(pe, ("cmp", which, ft)) for ft in range(2)]
                for part in range(2):
                    j = next_block(pe, name)
                    for ft in range(2):
                        for k in range(KT):
                            t = part * 8 + k
                            ins = nc.tensor.matmul(psum(banks[ft], 0, 4 * N_CMP), slot(j, k, 256, ft * P, P),
                                                   BK[:, which, t].rearrange("p g n -> p (g n)"), start=(t == 0),
                                                   stop=(t == 15))
                        ins.then_inc(*pe.step("cmp", which, ft, part))
                    pe.mark("used", j)
            w2 = lambda which, ft: pr("cmp_w2", (which * 2 + ft) * 64, 64)
            b = take_bank(pe, ("cmp_k2",))
            pe.wait_ge(*after("cmp_hidden", 0, 1))
            for h in range(2):
                for ft in range(2):
                    ins = nc.tensor.matmul(psum(b, 0, 4 * N_CMP, half(h)), w2(0, ft), HC[:, 0, ft], start=(ft == 0),
                                           stop=(ft == 1))
            ins.then_inc(*pe.step("cmp_k2"))
            b = take_bank(pe, ("cmp_v2",))
            pe.wait_ge(*after("cmp_hidden", 1, 1))
            for g in range(4):
                for ft in range(2):
                    ins = nc.tensor.matmul(psum(b, g * HD, HD, slice(0, N_CMP)), HC[:, 1, ft, g * N_CMP:(g + 1) * N_CMP],
                                           w2(1, ft), start=(ft == 0), stop=(ft == 1))
            ins.then_inc(*pe.step("cmp_v2"))

        def compress_scalar(act):
            act.stage("compress")
            for which in range(2):
                for ft in range(2):
                    act.wait_ge(*after("cmp", which, ft, 1))
                    nc.scalar.activation(HC[:, which, ft], psum(bank_of(("cmp", which, ft)), 0, 4 * N_CMP),
                                         ACT.Gelu_apprx_tanh, bias=pr("cmp_b1", which * 2 + ft, 1)).then_inc(*act.step("taken", "cmp", which, ft))
                    act.mark("cmp_hidden", which, ft)
            act.wait_ge(*after("cmp_k2"))
            nc.scalar.activation(KC, psum(bank_of(("cmp_k2",)), 0, 4 * N_CMP), ACT.Identity,
                                 bias=pr("cmp_b2k")).then_inc(*act.step("taken", "cmp_k2"))

        def compress_vector(v):
            v.stage("compress")
            v.wait_ge(*after("cmp_v2"))
            r = slice(0, N_CMP)
            nc.vector.tensor_tensor(VC[r], psum(bank_of(("cmp_v2",)), 0, 256, r).rearrange("p (a b) -> p a b", b=HD),
                                    pr("cmp_b2v", rows=r).unsqueeze(1).to_broadcast([N_CMP, 4, HD]), ALU.add).then_inc(*v.step("taken", "cmp_v2"))

        class SparseAttention(Attention):
            name, n, base = "sparse_attention", 32, ATT_C
            place_free = ("gates",)

            def factor(self, u):
                h, qt = divmod(u, 2)
                return GT[:, qt, 3 * h:3 * h + 3]

            def ready(self, u):
                return (("od_roped", 19), ("taken", "cmp_k2"))

            def values_ready(self, u):
                return (("taken", "cmp_v2"), ("taken", "odv", 1))

            def scores(self, u):
                h, qt = divmod(u, 2)
                g, r, w = h // 4, half(h), P * (qt + 1)
                q = QR[r, h // 2, qt * P:(qt + 1) * P]
                first = [(0, N_CMP, q, KC[r, g * N_CMP:(g + 1) * N_CMP]), (16, w, q, KRT[r, 1, g, 0:w])]
                last = (144 if qt == 0 else 0, w, q, KRT[r, 2, g, 0:w])
                return [first + [last]] if qt == 0 else [first, [last]]

            def pieces(self, u):
                qt = u % 2
                last = (0, 144) if qt == 0 else (1, 0)
                return ([(0, 0, 0, N_CMP, cn("cmp_mask", qt * N_CMP, N_CMP))] + causal_pieces(0, 16, 16, qt)
                        + causal_pieces(*last, 272, qt))

            def maps(self, u):
                w = P * (u % 2 + 1)
                return [(0, N_CMP), (16, w), (272, w)]

            def blocks(self, u):
                n = u % 2 + 1
                return [(0, N_CMP)] + [(16 + i * P, P) for i in range(n)] + [(272 + i * P, P) for i in range(n)]

            def values(self, u):
                h, qt = divmod(u, 2)
                g, n = h // 4, qt + 1
                return half(h), ([VC[0:N_CMP, g]] + [VS[:, i, g * HD:(g + 1) * HD] for i in range(n)]
                                 + [VW[:, i, g * HD:(g + 1) * HD] for i in range(n)])

            def place(self, u):
                h, qt = divmod(u, 2)
                return CAT2[half(h), h // 2, qt * P:(qt + 1) * P]

        SPA = SparseAttention()

        def final_vector(v):
            v.stage("final")
            v.wait_ge(*after("rms", "final"))
            v.wait_ge(*v.own)
            for k in range(KT):
                nc.vector.scalar_tensor_tensor(HT[:, X, k, :], XT[:, X, k, :], pr("final_g2", k, 1), RS[:, X, :],
                                               ALU.mult, ALU.mult).then_inc(*v.step("final", k))

        BOTH, ONE = [CTX, X], [X]
        block = ctx.enter_context(nc.Block())

        def queue(eng, name):
            return Steps(eng, semaphore, events, name)

        @block.sync
        def _(eng):
            sp = queue(eng, "sync")
            load_blocks(sp)
            for k in range(KT):
                sp.wait_ge(*after("final", k))
            eng.dma_start(out_t, HT[:, X].rearrange("p a b -> p (a b)")).then_inc(*sp.step(by=16, sem="out_written"))
            sp.wait_ge(*sp.own)

        @block.gpsimd
        def _(eng):
            g = queue(eng, "gpsimd")
            loads_pool(g)
            pool_pool(g)
            ev2_pool(g)
            od_pool(g)

        @block.tensor
        def _(eng):
            pe = queue(eng, "tensor")
            pe.stage("mod")
            side_blocks(pe, 24)
            rms_tensor(pe, "n1_0", BOTH)
            ev_in_tensor(pe)
            att_tensor(pe, LAT)
            att_tensor(pe, CON)
            pool_tensor(pe)
            cat_ready = lambda k: [("pool_done",), ("context_attention", "done")]
            project_tensor(pe, "x01", "ev_out", lambda k: CAT[:, :, k, :], cat_ready, BOTH)
            rms_tensor(pe, "y_x01", BOTH)
            rms_tensor(pe, "n2_0", BOTH)
            mlp_tensor(pe, "x02", 0, BOTH, "n2_0")
            rms_tensor(pe, "y_x02", BOTH)
            rms_tensor(pe, "n1_1", BOTH)
            features_tensor(pe)
            wkv_tensor(pe)
            readout_tensor(pe)
            project_tensor(pe, "x11", "wo", lambda k: MIX[0][:, X, k, :], lambda k: [("read", k)], ONE)
            rms_tensor(pe, "y_x11", ONE)
            rms_tensor(pe, "n2_1", ONE)
            mlp_tensor(pe, "x12", 1, ONE, "n2_1")
            rms_tensor(pe, "y_x12", ONE)
            rms_tensor(pe, "n1_2", ONE)
            ev2_tensor(pe)
            lambda_tensor(pe)
            att_tensor(pe, CAU)
            att_tensor(pe, DIF)
            subln_tensor(pe)
            project_tensor(pe, "x21", "ev2_out", lambda k: CAT2[:, k, :],
                           lambda k: [("causal_attention", "done"), ("head_normed", 3)], ONE)
            rms_tensor(pe, "n2_2", ONE)
            moe_tensor(pe, 0)
            rms_tensor(pe, "n1_3", ONE)
            od_tensor(pe)
            compress_tensor(pe)
            att_tensor(pe, SPA)
            project_tensor(pe, "x31", "od_out", lambda k: CAT2[:, k, :], lambda k: [("sparse_attention", "done")], ONE)
            rms_tensor(pe, "n2_3", ONE)
            moe_tensor(pe, 1)
            rms_tensor(pe, "final", ONE)

        @block.scalar
        def _(eng):
            act = queue(eng, "scalar")

            def before_mlp(key, norm, m, half_, segs, after):
                rms_scalar(act, norm, XT, segs, after)
                modulate_scalar(act, norm, m, half_, segs)

            silu_c(act)
            before_mlp(None, "n1_0", 0, 0, BOTH, [("x0",), ("consts",)])
            ev_out_of(act, 0, act_copy)
            att_scalar(act, LAT)
            att_scalar(act, CON)
            pool_scalar(act)
            take_out(act, "x01", range(0, KT, 2), y_place(BOTH), BOTH, "y_all")
            rms_scalar(act, "y_x01", YT, BOTH, [("y_all2", "x01"), ("y_all", "x01")])
            before_mlp(None, "n2_0", 0, 1, BOTH, [("x", "x01")])
            mlp_scalar(act, "x02", BOTH)
            rms_scalar(act, "y_x02", YT, BOTH, [("y_all2", "x02_down"), ("y_all", "x02_down")])
            before_mlp(None, "n1_1", 1, 0, BOTH, [("x", "x02")])
            features_scalar(act)
            wkv_scalar(act)
            readout_scalar(act)
            take_out(act, "x11", range(0, KT, 2), y_place(ONE), ONE, "y_all")
            rms_scalar(act, "y_x11", YT, ONE, [("y_all2", "x11"), ("y_all", "x11")])
            before_mlp(None, "n2_1", 1, 1, ONE, [("x", "x11")])
            mlp_scalar(act, "x12", ONE)
            rms_scalar(act, "y_x12", YT, ONE, [("y_all2", "x12_down"), ("y_all", "x12_down")])
            before_mlp(None, "n1_2", 2, 0, ONE, [("x", "x12")])
            ev2_scalar(act)
            att_scalar(act, CAU)
            att_scalar(act, DIF)
            subln_scalar(act)
            take_out(act, "x21", range(0, KT, 2), y_place(ONE), ONE, "y_all")
            before_mlp(None, "n2_2", 2, 1, ONE, [("x", "x21")])
            moe_scalar(act, 0)
            before_mlp(None, "n1_3", 3, 0, ONE, [("x", "moe0")])
            od_scalar(act)
            compress_scalar(act)
            att_scalar(act, SPA)
            take_out(act, "x31", range(0, KT, 2), y_place(ONE), ONE, "y_all")
            before_mlp(None, "n2_3", 3, 1, ONE, [("x", "x31")])
            moe_scalar(act, 1)
            rms_scalar(act, "final", XT, ONE, [("x", "moe1")])

        @block.vector
        def _(eng):
            v = queue(eng, "vector")

            def norm(key, m, half_, segs, after, freed=()):
                rms_vector(v, key, XT, segs, after)
                modulate_vector(v, key, m, half_, segs, freed)

            def y_norm(key, segs):
                rms_vector(v, "y_" + key, YT, segs, [("y_all", key), ("y_all2", key)])

            rms_vector(v, "n1_0", XT, BOTH, [("x0",)])
            mod_vectors(v, 0)
            modulate_vector(v, "n1_0", 0, 0, BOTH, [])
            ev_out_of(v, 1, dve_copy)
            att_vector(v, LAT)
            att_vector(v, CON)
            take_out(v, "x01", range(1, KT, 2), y_place(BOTH), BOTH, "y_all2")
            rms_vector(v, "y_x01", YT, BOTH, [("y_all", "x01"), ("y_all2", "x01")])
            residual_vector(v, "x01", 0, 0, BOTH, True)
            norm("n2_0", 0, 1, BOTH, [("x", "x01")])
            mlp_vector(v, "x02", BOTH, 1)
            rms_vector(v, "y_x02", YT, BOTH, [("y_all", "x02_down"), ("y_all2", "x02_down")])
            residual_vector(v, "x02", 0, 1, BOTH, True)
            norm("n1_1", 1, 0, BOTH, [("x", "x02")])
            mixes_vector(v)
            removal_key_vector(v)
            wkv_vector(v)
            readout_vector(v)
            take_out(v, "x11", range(1, KT, 2), y_place(ONE), ONE, "y_all2")
            rms_vector(v, "y_x11", YT, ONE, [("y_all", "x11"), ("y_all2", "x11")])
            residual_vector(v, "x11", 1, 0, ONE, True)
            norm("n2_1", 1, 1, ONE, [("x", "x11")])
            mod_vectors(v, 2)
            mlp_vector(v, "x12", ONE)
            rms_vector(v, "y_x12", YT, ONE, [("y_all", "x12_down"), ("y_all2", "x12_down")])
            residual_vector(v, "x12", 1, 1, ONE, True)
            norm("n1_2", 2, 0, ONE, [("x", "x12")])
            mod_vectors(v, 3)
            ev2_vector(v)
            att_vector(v, CAU)
            att_vector(v, DIF)
            subln_vector(v)
            take_out(v, "x21", range(1, KT, 2), y_place(ONE), ONE, "y_all2")
            residual_vector(v, "x21", 2, 0, ONE, False)
            norm("n2_2", 2, 1, ONE, [("x", "x21")])
            moe_vector(v, 0)
            residual_vector(v, "moe0", 2, 1, ONE, False)
            norm("n1_3", 3, 0, ONE, [("x", "moe0")])
            od_vector(v)
            compress_vector(v)
            att_vector(v, SPA)
            take_out(v, "x31", range(1, KT, 2), y_place(ONE), ONE, "y_all2")
            residual_vector(v, "x31", 3, 0, ONE, False)
            norm("n2_3", 3, 1, ONE, [("x", "x31")])
            moe_vector(v, 1)
            residual_vector(v, "moe1", 3, 1, ONE, False)
            rms_vector(v, "final", XT, ONE, [("x", "moe1")])
            final_vector(v)
    return events


def kernel(**inputs):
    import concourse.bacc as bacc
    from concourse.bass_utils import run_bass_kernel_spmd

    a = {n: np.asarray(x) for n, x in inputs.items()}

    def features_first(x):
        return x.reshape(SEQ, KT, P).transpose(2, 1, 0)

    arrays = {
        "weights": weight_blocks(a),
        "consts": constants(),
        "params": parameters(a),
        "small": small_weights(a),
        "bias": position_bias(a["ev_rpb"]),
        "x_t": np.ascontiguousarray(np.stack([features_first(a["ctx"]), features_first(a["x"])], 1).reshape(P, -1)),
    }
    arrays["pool_inv"] = pool_inverses()

    def build(events):
        nc = bacc.Bacc("TRN2", target_bir_lowering=False, num_devices=1)
        aps = [nc.dram_tensor(n, arrays[n].shape, FP32, kind="ExternalInput").ap()
               for n in ("weights", "consts", "params", "small", "bias", "pool_inv", "x_t")]
        out = nc.dram_tensor("out_t", (P, KT * SEQ), FP32, kind="ExternalOutput").ap()
        return nc, bass_two_blocks(nc, *aps, out, events)

    counted = build(Events())[1]
    nc, _ = build(Events(counted))
    r = run_bass_kernel_spmd(nc, [arrays], core_ids=[0])
    out = np.asarray(r.results[0]["out_t"]).reshape(P, KT, SEQ)
    return np.ascontiguousarray(out.transpose(2, 1, 0).reshape(1, SEQ, D))
```

```python
import numpy as np
import concourse.bass as bass
from concourse import mybir
from contextlib import ExitStack

FP32 = mybir.dt.float32
FP32R = mybir.dt.float32r
ALU = mybir.AluOpType
ACT = mybir.ActivationFunctionType
AX = mybir.AxisListType

P = 128
D = 1024
KT = D // P
SEQ = 256
CTX, X = 0, 1
HD = 64
SLOT = 2048
N_SLOTS = 4
NEG = -1e30
GRID_W, WIN_C, WIN_R = 64, 16, 8
CHUNK = 64
N_CHUNK = SEQ // CHUNK
PAIRS = KT
LEVELS = 6
N_CMP = (SEQ - 32) // 16 + 1
N_EXPERTS = 16
MOD_TILES = 6 * KT
FIRST_MODS = 8
RMS_EPS = 1e-6
GN_EPS = 64e-5

CONST_COLS = {}


def _const(name, width, _at=[0]):
    CONST_COLS[name] = (_at[0], width)
    _at[0] += width


for _n, _w in (("ident", 128), ("ones", 128), ("block_ones", 128), ("swap", 128), ("cos", 256), ("sin", 256),
               ("causal", 128), ("cmp_mask", 2 * N_CMP), ("cmp_live", 2), 
               ("order", 2 * 128), ("first_level", 2 * 64), ("later_levels", 2 * 5 * 64), ("ident64", 64),
               ("scan_keep", 512), ("tie", 4), ("eps", 2)):
    _const(_n, _w)
N_CONST = sum(w for _, w in CONST_COLS.values())


def constants():
    c = {}
    i = np.arange(P)
    c["ident"] = np.eye(P)
    c["ones"] = np.ones((P, P))
    c["block_ones"] = (i[:, None] // HD == i[None, :] // HD).astype(np.float64)
    swap = np.zeros((P, P))
    cos, sin = np.ones((P, SEQ), np.float32), np.zeros((P, SEQ), np.float32)
    inv = np.float32(500000.0) ** (-np.arange(0, 16, 2, dtype=np.float32) / np.float32(16))
    ang = np.arange(SEQ, dtype=np.float32)[:, None] * inv[None, :]
    for p in range(P):
        d = p % HD
        if d < 16:
            swap[p, p + 8 if d < 8 else p - 8] = 1.0
            cos[p] = np.cos(ang[:, d % 8])
            sin[p] = np.sin(ang[:, d % 8]) * (-1 if d < 8 else 1)
    c["swap"], c["cos"], c["sin"] = swap, cos, sin
    c["causal"] = np.where(i[None, :] <= i[:, None], 0.0, NEG)
    q = np.arange(SEQ).reshape(2, P).T
    end = np.arange(N_CMP) * 16 + 31
    c["cmp_mask"] = np.where(end[None, None, :] <= q[:, :, None], 0.0, NEG).reshape(P, -1)
    c["cmp_live"] = (q >= 31).astype(np.float64)
    r, s = (i % 64)[:, None], np.arange(64)[None, :]
    c["order"] = np.concatenate([r < s, r <= s, r > s, r >= s], 1)
    first = lambda a, b: (a // 2 == b // 2) & (a % 2 == 1) & (b % 2 == 0)
    c["first_level"] = np.concatenate([first(r, s), first(s, r)], 1)
    later = []
    for direction in range(2):
        for lv in range(1, LEVELS):
            a, b = (r >> lv, s >> lv) if direction == 0 else (s >> lv, r >> lv)
            later.append((a // 2 == b // 2) & (a % 2 == 1) & (b % 2 == 0))
    c["later_levels"] = np.concatenate(later, 1)
    c["ident64"] = (r == s)
    c["scan_keep"] = np.broadcast_to(np.arange(512) % CHUNK != 0, (P, 512))
    c["tie"] = np.broadcast_to(np.array([4.0, 3.0, 2.0, 1.0]), (P, 4))
    c["eps"] = np.broadcast_to(np.array([RMS_EPS, GN_EPS]), (P, 2))
    out = np.concatenate([np.asarray(c[n], np.float64).reshape(P, w) for n, (_, w) in CONST_COLS.items()], 1)
    return np.ascontiguousarray(out.astype(np.float32))


def pool_inverses():
    t = np.arange(SEQ)
    inverse = [1.0 / (np.clip(t + w // 2, 0, SEQ) - np.clip(t - w // 2, 0, SEQ)) for w in (2, 4, 8, 16)]
    return np.ascontiguousarray(np.broadcast_to(np.concatenate(inverse).astype(np.float32), (P, 4 * SEQ)))


PARAM_COLS = {}


def _param(name, width, _at=[0]):
    PARAM_COLS[name] = (_at[0], width)
    _at[0] += width


for _n, _w in (("c", 16), ("c2", 8), ("ada_b", 4 * MOD_TILES), ("norm_g", 2 * 4 * KT), ("pool_scale", 4),
               ("mu", 6 * KT), ("w0", 2 * KT), ("a0", 2 * KT), ("kk", KT), ("ka", KT), ("rk", KT), ("lng", KT),
               ("lnb", KT), ("norm1_g2", 2 * KT), ("norm2_g2", 2 * KT), ("final_g2", KT), ("lam", 4), ("subln", 1),
               ("cmp_pos", 2 * 16), ("cmp_b1", 4), ("cmp_b2k", 1), ("cmp_b2v", 64), ("cmp_w2", 2 * 2 * 64),
               ("router_b", 2 * 20), ("router_w", 2 * KT * 20), ("gate_w", KT * 48)):
    _param(_n, _w)
N_PARAM = sum(w for _, w in PARAM_COLS.values())


def columns(v):
    v = np.asarray(v)
    return v.reshape(-1, P).T


def parameters(a):
    p = {}
    p["c"] = np.stack([columns(a["c_ctx"]), columns(a["c"])], 2).reshape(P, 16)
    p["c2"] = columns(a["c_2"])
    p["ada_b"] = np.concatenate([columns(a["ada_b"]), columns(a["ada_b_2"])], 1)
    p["norm_g"] = columns(a["norm_g"])
    p["pool_scale"] = columns(a["ev_pool_scale"])
    for n, k in (("mu", "rw_mu"), ("w0", "rw_w0"), ("a0", "rw_a0"), ("kk", "rw_kk"), ("ka", "rw_ka"), ("rk", "rw_rk"),
                 ("lng", "rw_lng"), ("lnb", "rw_lnb"), ("norm1_g2", "norm1_g_2"), ("norm2_g2", "norm2_g_2"),
                 ("final_g2", "final_g_2"), ("subln", "ev_subln_g_2"), ("cmp_b1", "od_cmp_b1_2")):
        p[n] = columns(a[k])
    lam = np.asarray(a["ev_lambda_2"])[0].T
    p["lam"] = np.concatenate([lam, np.zeros_like(lam)], 0)
    p["cmp_pos"] = np.concatenate([columns(np.asarray(a["od_cmp_pos_2"])[0, i].reshape(-1)) for i in range(2)], 1)
    b2 = np.asarray(a["od_cmp_b2_2"])[0]
    p["cmp_b2k"] = np.concatenate([b2[0], b2[0]])[:, None]
    p["cmp_b2v"] = np.broadcast_to(b2[1], (P, 64))
    w2 = np.asarray(a["od_cmp_w2_2"])[0]
    p["cmp_w2"] = w2.reshape(2, 2, P, 64).transpose(2, 0, 1, 3).reshape(P, -1)
    rb = np.concatenate([np.asarray(a["moe_bg_2"]), np.asarray(a["moe_be_2"])], 1)
    p["router_b"] = np.broadcast_to(rb.reshape(1, -1), (P, 40))
    rw = np.concatenate([np.asarray(a["moe_wg_2"]), np.asarray(a["moe_we_2"])], 2)
    p["router_w"] = rw.reshape(2, KT, P, 20).transpose(2, 0, 1, 3).reshape(P, -1)
    gw = np.asarray(a["od_w_in_2"])[0][:, 2560:2608]
    p["gate_w"] = gw.reshape(KT, P, 48).transpose(1, 0, 2).reshape(P, -1)
    return np.ascontiguousarray(np.concatenate([p[n].reshape(P, w) for n, (_, w) in PARAM_COLS.items()], 1))


def weight_blocks(a):
    def cols(w):
        w = np.asarray(w)
        n = w.shape[1] // 256
        return list(w.reshape(KT, P, n, 256).transpose(2, 1, 0, 3).reshape(n, P, SLOT))

    def deep(w):
        w = np.asarray(w)
        return list(w.reshape(2, 16, P, 8, P).transpose(3, 0, 2, 1, 4).reshape(16, P, SLOT))

    def halves(w):
        return list(np.asarray(w).reshape(2, KT, P, 256).transpose(0, 2, 1, 3).reshape(2, P, SLOT))

    def wide(w):
        return [np.asarray(w).reshape(2, P, D).transpose(1, 0, 2).reshape(P, SLOT)]

    mods = [cols(a["ada_w"][0]), cols(a["ada_w"][1]), cols(a["ada_w_2"][0]), cols(a["ada_w_2"][1])]
    g = {
        "mod0": mods[0], "mod1": mods[1], "mod2": mods[2], "mod3": mods[3],
        "ev_in": cols(a["ev_w_in"][0]), "ev_out": cols(a["ev_w_out"][0]),
        "mlp1_0": cols(a["mlp_w1"][0]), "mlp2_0": deep(a["mlp_w2"][0]),
        "mlp1_1": cols(a["mlp_w1"][1]), "mlp2_1": deep(a["mlp_w2"][1]),
        "wr": cols(a["rw_wr"][0]), "wk": cols(a["rw_wk"][0]), "wv": cols(a["rw_wv"][0]), "wo": cols(a["rw_wo"][0]),
        "ev2_in": cols(a["ev_w_in_2"][0]), "ev2_out": cols(a["ev_w_out_2"][0]),
        "od_in": cols(np.asarray(a["od_w_in_2"])[0][:, :2560]), "od_out": cols(a["od_w_out_2"][0]),
        "cmp_k": halves(np.asarray(a["od_cmp_w1_2"])[0, 0]), "cmp_v": halves(np.asarray(a["od_cmp_w1_2"])[0, 1]),
    }
    for layer in range(2):
        up = [cols(a["moe_w_gate_2"][layer, e]) + cols(a["moe_w_up_2"][layer, e]) for e in range(N_EXPERTS)]
        down = [wide(a["moe_w_down_2"][layer, e]) for e in range(N_EXPERTS)]
        g[f"moe{layer}"] = up[0] + [b for e in range(1, N_EXPERTS) for b in up[e] + down[e - 1]] + down[-1]
    taken = dict.fromkeys(g, 0)
    out = []
    for name in block_order():
        out.append(g[name][taken[name]])
        taken[name] += 1
    assert all(taken[n] == len(g[n]) for n in g), taken
    return np.ascontiguousarray(np.stack(out))


def mixed(*runs):
    name, count = runs[0]
    out = []
    done = [0] * len(runs)
    for i in range(count):
        for r, (other, n) in list(enumerate(runs))[1:]:
            while done[r] < n * (i + 1) // count:
                out.append(other)
                done[r] += 1
        out.append(name)
    return out


def block_order():
    order = ["mod0"] * FIRST_MODS + mixed(("ev_in", 8), ("mod0", 24 - FIRST_MODS)) + ["ev_out"] * 4
    order += mixed(("mlp1_0", 16), ("mod1", 24)) + mixed(("mlp2_0", 16), ("mod2", 24))
    order += ["wr"] * 4 + ["wk"] * 4 + ["wv"] * 4 + ["wo"] * 4
    order += mixed(("mlp1_1", 16), ("mod3", 12)) + mixed(("mlp2_1", 16), ("mod3", 12))
    order += ["ev2_in"] * 12 + ["ev2_out"] * 4 + ["moe0"] * 48
    order += ["od_in"] * 10 + ["cmp_k"] * 2 + ["cmp_v"] * 2 + ["od_out"] * 4 + ["moe1"] * 48
    return order


def small_weights(a):
    tall = lambda w: np.asarray(w).reshape(KT, P, P).transpose(1, 0, 2).reshape(P, D)
    pair = lambda w: tall(np.concatenate([np.asarray(w)[0, 0], np.asarray(w)[0, 1]], 1))
    stack = lambda w: np.asarray(w)[0].reshape(P, D)
    pool = np.asarray(a["ev_pool_w"])[0].transpose(1, 0, 2).reshape(P, 512)
    return np.ascontiguousarray(np.concatenate(
        [pair(a["rw_w1"]), pair(a["rw_a1"]), tall(a["rw_g1"]), stack(a["rw_w2"]), stack(a["rw_a2"]),
         np.asarray(a["rw_g2"])[0], pool], 1))


def position_bias(rpb):
    rpb = np.asarray(rpb)[0]
    t = np.arange(SEQ)
    row, col = t // GRID_W, t % GRID_W
    start = np.clip(col - WIN_C // 2, 0, GRID_W - WIN_C)
    ok = (col[None, :] >= start[:, None]) & (col[None, :] < start[:, None] + WIN_C)
    dc = np.clip(col[None, :] - col[:, None], -(WIN_C - 1), WIN_C - 1) + WIN_C - 1
    dr = row[None, :] - row[:, None] + WIN_R - 1
    full = np.where(ok[None], rpb[:, dr, dc], np.float32(NEG))
    return np.ascontiguousarray(full.reshape(8, 2, P, SEQ).transpose(2, 0, 1, 3).reshape(P, -1))


class Events:

    def __init__(self, known=None):
        self.known = known.at if known else {}
        self.where_known = known.where if known else {}
        self.at = {}
        self.where = {}


class Steps:

    def __init__(self, eng, semaphore, events, name):
        self.eng, self.semaphore, self.events, self.name = eng, semaphore, events, name
        self.reached = {}
        self.count = {}
        self.own = (None, 0)
        self.counter = None
        self.at_block = 0
        self.taken = {}
        self.later = []
        self.chains, self.chained = 0, []

    def stage(self, name):
        self.counter = f"{name}_{self.name}"

    def step(self, *event, by=1, sem=None):
        s = sem or self.counter
        self.count[s] = self.count.get(s, 0) + by
        self.own = (s, self.count[s])
        if event:
            self.mark(*event)
        return self.semaphore(s), by

    def mark(self, *event):
        assert event not in self.events.at, event
        self.events.at[event] = self.own

    def wait_ge(self, name, value):
        if name is not None and self.reached.get(name, 0) < value:
            self.reached[name] = value
            self.eng.wait_ge(self.semaphore(name), value)


def bass_two_blocks(nc, weights, consts, params, small, bias, pool_inv, x_t, out_t, events):
    ctx = ExitStack()
    with ctx:
        sems = {}

        def semaphore(name):
            if name not in sems:
                sems[name] = ctx.enter_context(nc.semaphore(name))
            return sems[name]

        def after(*event):
            if not events.known:
                return None, 0
            return events.known[event]

        sb = lambda name, width: ctx.enter_context(nc.sbuf_tensor(name, [P, width], FP32))
        ring = sb("weight_slots", N_SLOTS * SLOT)
        CN = sb("constants", N_CONST)
        PR = sb("parameters", N_PARAM)
        MD = sb("modulations", 4 * 96)
        ARENA = 40100
        arena = sb("arena", ARENA)
        ps = ctx.enter_context(nc.psum_tensor("banks", [P, 8, 512], FP32))

        def cn(name, a=0, w=None, rows=slice(0, P)):
            at, width = CONST_COLS[name]
            return CN[rows, at + a:at + (a + w if w else width)]

        def pr(name, a=0, w=None, rows=slice(0, P)):
            at, width = PARAM_COLS[name]
            return PR[rows, at + a:at + (a + w if w else width)]

        def area(at, *dims):
            n = int(np.prod(dims))
            assert at + n <= ARENA, (at, dims)
            v = arena[:, at:at + n]
            if len(dims) == 1:
                return v
            names = "abcd"[:len(dims)]
            return v.rearrange(f"p ({' '.join(names)}) -> p {' '.join(names)}", **dict(zip(names, dims)))

        def psum(bank, a=0, w=512, rows=slice(0, P)):
            return ps[rows, bank, a:a + w]

        XT = area(0, 2, KT, SEQ)
        HT = area(4096, 2, KT, SEQ)
        YT = area(8192, 2, KT, SEQ)
        SQ = area(12288, 2, KT, SEQ)
        RS = area(16384, 2, SEQ)
        FREE = 16896
        SMALL = ARENA - 6144

        ARENA_AT = nc.sbuf_base - 4 * ARENA

        def rounded(name, at, *dims):
            n = int(np.prod(dims))
            assert at + n <= ARENA, (name, at, dims)
            t = nc.alloc_sbuf_tensor_at(name, [P, n], FP32R, offset=ARENA_AT + 4 * at)
            if len(dims) == 1:
                return t[:, :]
            names = "abcd"[:len(dims)]
            return t[:, :].rearrange(f"p ({' '.join(names)}) -> p {' '.join(names)}", **dict(zip(names, dims)))

        order = block_order()
        N_BLOCKS = len(order)
        block_of = {}
        for j, n in enumerate(order):
            block_of.setdefault(n, []).append(j)


        def load_blocks(sp):
            sp.stage("weights")
            for j in range(N_BLOCKS):
                if j >= N_SLOTS:
                    sp.wait_ge(*after("used", j - N_SLOTS))
                s = j % N_SLOTS
                sp.eng.dma_start(ring[:, s * SLOT:(s + 1) * SLOT], weights[j]).then_inc(*sp.step("block", j, by=16, sem=f"weight_slot{s}"))

        def slot(j, k, width, a=0, w=None, rows=slice(0, P)):
            at = (j % N_SLOTS) * SLOT + k * width + a
            return ring[rows, at:at + (w or width)]

        bank_state = {"next": 0, "holder": [None] * 8, "open": list(range(7))}

        def take_bank(pe, key, banks=None):
            pool = banks or bank_state["open"]
            b = pool[bank_state["next"] % len(pool)]
            bank_state["next"] += 1
            if bank_state["holder"][b] is not None:
                pe.wait_ge(*after("taken", *bank_state["holder"][b]))
            bank_state["holder"][b] = key
            events.where[key] = b
            return b

        def bank_of(key):
            return events.where_known.get(key, 0)

        def mod_of(j):
            m = int(order[j][3])
            return m, block_of[order[j]].index(j)

        SUM_LAG = 4

        def side_blocks(pe, j_next, lag=SUM_LAG):
            while pe.at_block < j_next:
                assert order[pe.at_block].startswith("mod"), (order[pe.at_block], pe.at_block, j_next)
                pe.later.append(pe.at_block)
                pe.at_block += 1
            while pe.later and pe.later[0] < j_next - lag:
                mod_sum(pe, *mod_of(pe.later.pop(0)))

        def next_block(pe, name):
            j = block_of[name][pe.taken.get(name, 0)]
            pe.taken[name] = pe.taken.get(name, 0) + 1
            side_blocks(pe, j)
            pe.wait_ge(*after("block", j))
            assert pe.at_block == j
            pe.at_block += 1
            return j

        XHI = rounded("h_high", 0, KT, SEQ)
        XLO = rounded("h_low", 4096, KT, SEQ)

        class Splits:

            def __init__(self, phase, names, places):
                self.blocks = [j for j, n in enumerate(order) if n in names]
                self.pairs = [(rounded(f"{phase}_w_high{i}", a, SLOT), rounded(f"{phase}_w_low{i}", b, SLOT))
                              for i, (a, b) in enumerate(places)]
                self.ahead = len(places) - 1

            def pair(self, j):
                return self.pairs[self.blocks.index(j) % len(self.pairs)]

            def high(self, act, i):
                if i >= len(self.blocks):
                    return
                j, n = self.blocks[i], len(self.pairs)
                act.wait_ge(*after("block", j))
                if i >= n:
                    act.wait_ge(*after("multiplied", self.blocks[i - n]))
                nc.scalar.activation(self.pair(j)[0], slot(j, 0, SLOT), ACT.Copy).then_inc(*act.step("high", j))

            def low(self, v, i):
                if i >= len(self.blocks):
                    return
                j = self.blocks[i]
                side_chains(v, j)
                v.wait_ge(*after("high", j))
                nc.vector.tensor_tensor(self.pair(j)[1], slot(j, 0, SLOT), self.pair(j)[0], ALU.subtract).then_inc(*v.step("used", j))

            def next(self, pe, name):
                j = block_of[name][pe.taken.get(name, 0)]
                pe.taken[name] = pe.taken.get(name, 0) + 1
                side_blocks(pe, j)
                pe.wait_ge(*after("used", j))
                assert pe.at_block == j
                pe.at_block += 1
                return j

            def columns(self, pe, j, width, a, out, tiles, high, low, start=True, stop=True, check=False, norm=None):
                terms = [(0, high, "h_high"), (1, high, None), (0, low, "h_low")]
                for n, (part, x, ready) in enumerate(terms):
                    for k in range(tiles):
                        if norm and ready:
                            pe.wait_ge(*after(ready, norm, k))
                        at = k * width + a
                        ins = nc.tensor.matmul(out, self.pair(j)[part][:, at:at + P], x(k),
                                               start=start and n == 0 and k == 0,
                                               stop=stop and n == 2 and k == tiles - 1, skip_group_check=check)
                return ins

            def tokens(self, pe, j, key):
                b = take_bank(pe, key)
                for tt_ in range(2):
                    t = slice(tt_ * P, (tt_ + 1) * P)
                    for n, (x, part) in enumerate([(XHI, 0), (XHI, 1), (XLO, 0)]):
                        for k in range(KT):
                            ins = nc.tensor.matmul(psum(b, tt_ * 256, 256), x[:, k, t],
                                                   self.pair(j)[part][:, k * 256:(k + 1) * 256],
                                                   start=(n == 0 and k == 0), stop=(n == 2 and k == KT - 1))
                ins.then_inc(*pe.step(*key))
                pe.mark("multiplied", j)

        def x_high(k):
            return XHI[:, k, :]

        def x_low(k):
            return XLO[:, k, :]

        MOD = [MD[:, 96 * m:96 * m + 96].rearrange("p (t s) -> p t s", s=2) for m in range(4)]
        SC = ctx.enter_context(nc.sbuf_tensor("silu_c", [P, 24], FP32))

        MACC = area(12288, 4, 2, 256)

        def mod_vecs(m, n):
            return (CTX, X) if m == 0 or (m == 1 and n < FIRST_MODS) else (X,)

        def mod_bank(pe, m):
            key = ("mod", m, 0)
            if bank_state["holder"][7] != key:
                if bank_state["holder"][7] is not None:
                    held = bank_state["holder"][7]
                    pe.wait_ge(*after("taken", "mod", held[1], 2 if held[1] == 0 else 0))
                bank_state["holder"][7] = key
                events.where[key] = 7

        def mod_block(pe, j):
            m, n = mod_of(j)
            pe.wait_ge(*after("silu_c"))
            mod_bank(pe, m)
            pe.wait_ge(*after("block", j))
            for i in range(2):
                t = 2 * n + i
                for k in range(KT):
                    ins = nc.tensor.matmul(psum(7, t * 2, 2), slot(j, k, 256, i * P, P), SC[:, 2 * k:2 * k + 2],
                                           start=(k == 0), stop=(k == KT - 1))
            ins.then_inc(*pe.step("mod_summed", m, n))
            pe.mark("used", j)

        def mod_chain(v, j):
            m, n = mod_of(j)
            acc = MACC[:, v.chains % 4]
            v.wait_ge(*after("silu_c"))
            v.wait_ge(*after("block", j))
            if v.chains >= 4:
                v.wait_ge(*after("mod_summed", *v.chained[v.chains - 4]))
            vecs = mod_vecs(m, n)
            for k in range(KT):
                w = slot(j, k, 256)
                if len(vecs) == 1:
                    c = SC[:, 2 * k + 1:2 * k + 2] if m < 2 else SC[:, 16 + k:17 + k]
                    todo = [(acc[:, k % 2], c, k < 2)]
                else:
                    todo = [(acc[:, s], SC[:, 2 * k + s:2 * k + s + 1], k == 0) for s in vecs]
                for a_, c, first in todo:
                    if first:
                        nc.vector.tensor_scalar(a_, w, c, None, ALU.mult).then_inc(*v.step())
                    else:
                        v.wait_ge(v.own[0], v.own[1] - 1)
                        nc.vector.scalar_tensor_tensor(a_, w, c, a_, ALU.mult, ALU.add).then_inc(*v.step())
            v.mark("used", j)
            if len(vecs) == 1:
                v.wait_ge(*v.own)
                nc.vector.tensor_tensor(acc[:, 0], acc[:, 0], acc[:, 1], ALU.add).then_inc(*v.step())
            v.mark("mod_acc", m, n)
            v.chained.append((m, n))
            v.chains += 1

        def mod_sum(pe, m, n):
            mod_bank(pe, m)
            pe.wait_ge(*after("mod_acc", m, n))
            place = chain_place[m, n]
            for i in range(2):
                for a_, s in enumerate(mod_vecs(m, n)):
                    at_ = 2 * (2 * n + i) + s
                    ins = nc.tensor.matmul(psum(7, at_, 1), MACC[:, place, a_, i * P:(i + 1) * P],
                                           cn("ones", 0, 1), start=True, stop=True)
            ins.then_inc(*pe.step("mod_summed", m, n))

        chain_place = {}
        for j in range(FIRST_MODS, N_BLOCKS):
            if order[j].startswith("mod"):
                chain_place[mod_of(j)] = len(chain_place) % 4

        def side_chains(v, j_next):
            while v.at_block < j_next:
                if order[v.at_block].startswith("mod"):
                    mod_chain(v, v.at_block)
                v.at_block += 1

        def silu_c(act):
            act.stage("mod")
            act.wait_ge(*after("params"))
            nc.scalar.activation(SC[:, 0:16], pr("c"), ACT.Silu).then_inc(*act.step())
            nc.scalar.activation(SC[:, 16:24], pr("c2"), ACT.Silu).then_inc(*act.step("silu_c"))

        def mod_vectors(v, m, chunks=range(6)):
            v.stage("mod")
            v.wait_ge(*after("mod_summed", m, 4 * chunks[-1] + 3))
            v.wait_ge(*after("params"))
            M = MOD[m]
            src = psum(7, 0, 2 * MOD_TILES).rearrange("p (t s) -> p t s", s=2)
            bias_at = pr("ada_b", m * MOD_TILES, MOD_TILES)
            gains = {}
            if m < 2:
                for chunk, n, plus in ((1, 0, 1.0), (2, 1, 0.0), (4, 2, 1.0), (5, 3, 0.0)):
                    gains[chunk] = (pr("norm_g", (m * 4 + n) * KT, KT), plus)
            else:
                gains[1] = (pr("norm1_g2", (m - 2) * KT, KT), 1.0)
                gains[4] = (pr("norm2_g2", (m - 2) * KT, KT), 1.0)
            for chunk in chunks:
                vecs = mod_vecs(m, 4 * chunk)
                t, s = slice(chunk * KT, (chunk + 1) * KT), slice(vecs[0], vecs[-1] + 1)
                b = bias_at[:, t].unsqueeze(2).to_broadcast([P, KT, len(vecs)])
                nc.vector.tensor_tensor(M[:, t, s], src[:, t, s], b, ALU.add).then_inc(*v.step())
            v.mark("taken", "mod", m, chunks[0])
            v.wait_ge(*v.own)
            for chunk in chunks:
                if chunk in gains:
                    vecs = mod_vecs(m, 4 * chunk)
                    g, plus = gains[chunk]
                    part = M[:, chunk * KT:(chunk + 1) * KT, vecs[0]:vecs[-1] + 1]
                    nc.vector.scalar_tensor_tensor(part, part, plus, g.unsqueeze(2).to_broadcast([P, KT, len(vecs)]),
                                                   ALU.add, ALU.mult).then_inc(*v.step())
            v.mark("mod_ready", m, chunks[0])

        def mod_part(m, half):
            return 2 if m == 0 and half else 0

        def mod_col(m, chunk, tile, seg):
            s = seg if m < 2 else X
            return MOD[m][:, chunk * KT + tile, s:s + 1]

        def rms_scalar(act, key, src, segs, inputs, meanwhile=None):
            act.stage("norm")
            for e in inputs:
                act.wait_ge(*after(*e))
            for seg in segs:
                nc.scalar.activation(SQ[:, seg, 0:4, :], src[:, seg, 0:4, :], ACT.Square).then_inc(*act.step("squares_low", key, seg))
            if meanwhile is not None:
                meanwhile()
            a, w = segs[0] * SEQ, len(segs) * SEQ
            act.wait_ge(*after("sums", key))
            nc.scalar.activation(RS[:, segs[0]:segs[-1] + 1, :],
                                 psum(bank_of(("sums", key)), 0, w).rearrange("p (s t) -> p s t", t=SEQ),
                                 ACT.Sqrt, bias=cn("eps", 0, 1), scale=1.0 / D).then_inc(*act.step("taken", "sums", key))

        def rms_vector(v, key, src, segs, inputs, meanwhile=None):
            v.stage("norm")
            for e in inputs:
                v.wait_ge(*after(*e))
            for seg in segs:
                nc.vector.tensor_tensor(SQ[:, seg, 4:8, :], src[:, seg, 4:8, :], src[:, seg, 4:8, :], ALU.mult).then_inc(*v.step("squares_high", key, seg))
            if meanwhile is not None:
                meanwhile()
                v.stage("norm")
            v.wait_ge(*after("taken", "sums", key))
            part = RS[:, segs[0]:segs[-1] + 1, :]
            nc.vector.reciprocal(part, part).then_inc(*v.step("rms", key))

        def rms_tensor(pe, key, segs):
            pe.stage("norm")
            b = take_bank(pe, ("sums", key))
            for seg in segs:
                pe.wait_ge(*after("squares_low", key, seg))
                pe.wait_ge(*after("squares_high", key, seg))
            pe.wait_ge(*after("consts"))
            for k in range(KT):
                ins = nc.tensor.matmul(psum(b, 0, len(segs) * SEQ), cn("ones"), SQ[:, segs[0]:segs[-1] + 1, k, :],
                                       start=(k == 0), stop=(k == KT - 1))
            ins.then_inc(*pe.step("sums", key))

        def modulate_vector(v, key, m, half, segs, freed):
            v.wait_ge(*after("mod_ready", m, mod_part(m, half)))
            for e in freed:
                v.wait_ge(*after(*e))
            v.wait_ge(*v.own)
            for k in range(KT):
                for seg in segs:
                    nc.vector.scalar_tensor_tensor(HT[:, seg, k, :], XT[:, seg, k, :],
                                                   mod_col(m, 3 * half + 1, k, seg), RS[:, seg, :],
                                                   ALU.mult, ALU.mult).then_inc(*v.step("scaled", key, k, seg))
            v.mark("scaled_all", key)

        def modulate_scalar(act, key, m, half, segs):
            act.wait_ge(*after("mod_ready", m, mod_part(m, half)))
            for k in range(KT):
                for seg in segs:
                    act.wait_ge(*after("scaled", key, k, seg))
                    nc.scalar.activation(HT[:, seg, k, :], HT[:, seg, k, :], ACT.Identity,
                                         bias=mod_col(m, 3 * half, k, seg)).then_inc(*act.step("h", key, k, seg))
            act.mark("h_all", key)

        def modulate_split_scalar(act, key, m, half):
            act.wait_ge(*after("mod_ready", m, mod_part(m, half)))
            shift = lambda k: mod_col(m, 3 * half, k, X)
            for k in range(KT):
                act.wait_ge(*after("scaled", key, k, X))
                nc.scalar.activation(XHI[:, k], HT[:, X, k, :], ACT.Identity, bias=shift(k)).then_inc(*act.step("h_high", key, k))
                nc.scalar.activation(HT[:, X, k, :], HT[:, X, k, :], ACT.Identity, bias=shift(k)).then_inc(*act.step("h", key, k, X))
            act.mark("h_all", key)

        def low_vector(v, key):
            for k in range(KT):
                v.wait_ge(*after("h", key, k, X))
                nc.vector.tensor_tensor(XLO[:, k], HT[:, X, k, :], XHI[:, k], ALU.subtract).then_inc(*v.step("h_low", key, k))

        def residual_vector(v, key, m, half, segs, normed):
            v.stage("residual")
            v.wait_ge(*after("mod_ready", m, mod_part(m, 1)))
            if normed:
                v.wait_ge(*after("rms", "y_" + key))
                for seg in segs:
                    r = RS[:, seg, :].unsqueeze(1).to_broadcast([P, KT, SEQ])
                    nc.vector.tensor_tensor(YT[:, seg, :, :], YT[:, seg, :, :], r, ALU.mult).then_inc(*v.step())
            else:
                v.wait_ge(*after("y_all", key))
                v.wait_ge(*after("y_all2", key))
            v.wait_ge(*v.own)
            for seg in segs:
                for k in range(KT):
                    nc.vector.scalar_tensor_tensor(XT[:, seg, k, :], YT[:, seg, k, :],
                                                   mod_col(m, 3 * half + 2, k, seg), XT[:, seg, k, :],
                                                   ALU.mult, ALU.add).then_inc(*v.step())
            v.mark("x", key)

        def project_tensor(pe, key, name, moving, ready, segs, stage="project"):
            pe.stage(stage)
            w = len(segs) * SEQ
            n_tiles = 2 * len(block_of[name])
            for g in range(0, n_tiles, 2):
                j = next_block(pe, name)
                for i in range(2):
                    b = take_bank(pe, (key, g + i))
                    for k in range(KT):
                        if ready is not None and g == 0 and i == 0:
                            for e in ready(k):
                                pe.wait_ge(*after(*e))
                        ins = nc.tensor.matmul(psum(b, 0, w), slot(j, k, 256, i * P, P), moving(k),
                                               start=(k == 0), stop=(k == KT - 1))
                    ins.then_inc(*pe.step(key, g + i))
                pe.mark("used", j)

        def take_out(q, key, tiles, place, segs, done, fn=None, then=None):
            for g in tiles:
                q.wait_ge(*after(key, g))
                b = bank_of((key, g))
                src = psum(b, 0, len(segs) * SEQ)
                if len(segs) == 2:
                    src = src.rearrange("p (s t) -> p s t", t=SEQ)
                if fn is not None:
                    ins = fn(g, place(g), src)
                elif q.name == "scalar":
                    ins = nc.scalar.activation(place(g), src, ACT.Copy)
                else:
                    ins = nc.vector.tensor_copy(place(g), src)
                ins.then_inc(*q.step("taken", key, g))
                if g == tiles[-1]:
                    q.mark(done, key)
                if then is not None:
                    then(g)

        def seg_of(segs):
            return slice(segs[0], segs[-1] + 1)

        def h_moving(segs):
            if len(segs) == 2:
                return lambda k: HT[:, :, k, :]
            return lambda k: HT[:, segs[0], k, :]

        def h_ready(key, segs):
            return lambda k: [("h", key, k, seg) for seg in segs]

        def y_place(segs):
            if len(segs) == 2:
                return lambda g: YT[:, :, g, :]
            return lambda g: YT[:, segs[0], g, :]


        S_W, T_W = 528, 640

        def att_places(base):
            return (area(base, 3, S_W), area(base + 3 * S_W, 2, T_W), area(base + 3 * S_W + 2 * T_W, 3, 12))

        def att_tensor(pe, A):
            pe.stage(A.name)

            def scores(u):
                for n, mms in enumerate(A.scores(u)):
                    b = take_bank(pe, (A.name, "scores", u, n))
                    for e in A.ready(u):
                        pe.wait_ge(*after(*e))
                    for (col, w, lhs, rhs) in mms:
                        ins = nc.tensor.matmul(psum(b, col, w), lhs, rhs, start=True, stop=True)
                    ins.then_inc(*pe.step(A.name, "scores", u, n))

            def transposes(u):
                S = att_places(A.base)[0]
                pe.wait_ge(*after(A.name, "weights", u))
                blocks = A.blocks(u)
                for n in range(0, len(blocks), 4):
                    b = take_bank(pe, (A.name, "turned", u, n // 4))
                    for i, (col, w) in enumerate(blocks[n:n + 4]):
                        ins = nc.tensor.transpose(psum(b, i * P, P, slice(0, w)), S[:, u % 3, col:col + w], cn("ident"))
                    ins.then_inc(*pe.step(A.name, "turned", u, n // 4))

            def values(u):
                T = att_places(A.base)[1]
                rows, vs = A.values(u)
                b = take_bank(pe, (A.name, "out", u))
                pe.wait_ge(*after(A.name, "T", u))
                for e in A.values_ready(u):
                    pe.wait_ge(*after(*e))
                for i, (v, (col, w)) in enumerate(zip(vs, A.blocks(u))):
                    ins = nc.tensor.matmul(psum(b, 0, P, rows), v, T[0:w, u % 2, i * P:(i + 1) * P],
                                           start=(i == 0), stop=(i == len(vs) - 1))
                ins.then_inc(*pe.step(A.name, "out", u))

            for i in range(A.n + 2):
                if i < A.n:
                    scores(i)
                if 0 <= i - 1 < A.n:
                    transposes(i - 1)
                if 0 <= i - 2 < A.n:
                    values(i - 2)

        def att_vector(v, A):
            v.stage(A.name)
            S, T, M = att_places(A.base)
            v.wait_ge(*after(*A.place_free))

            def maxima(u):
                s = S[:, u % 3, :]
                if u >= 3:
                    v.wait_ge(*after(A.name, "turned", u - 3, (len(A.blocks(u - 3)) - 1) // 4))
                for i, (n, col, dst, w, mask) in enumerate(A.pieces(u)):
                    v.wait_ge(*after(A.name, "scores", u, n))
                    b = bank_of((A.name, "scores", u, n))
                    if mask is None:
                        ins = nc.vector.tensor_scalar(s[:, dst:dst + w], psum(b, col, w), A.pre, None, ALU.mult)
                    else:
                        ins = nc.vector.scalar_tensor_tensor(s[:, dst:dst + w], psum(b, col, w), A.pre, mask,
                                                             ALU.mult, ALU.add)
                    ins.then_inc(*v.step())
                    if i == A.last_piece(u, n):
                        v.mark("taken", A.name, "scores", u, n)
                v.wait_ge(*v.own)
                maps = A.maps(u)
                for j, (c, w) in enumerate(maps):
                    nc.vector.tensor_reduce(M[:, u % 3, j:j + 1], s[:, c:c + w], AX.X, ALU.max).then_inc(*v.step())
                v.wait_ge(*v.own)
                k = len(maps)
                nc.vector.tensor_scalar(M[:, u % 3, 3:3 + k], M[:, u % 3, 0:k], -A.post, None, ALU.mult).then_inc(*v.step(A.name, "max", u))

            def weights(u):
                s = S[:, u % 3, :]
                maps = A.maps(u)
                k = len(maps)
                v.wait_ge(*after(A.name, "exp", u))
                nc.vector.reciprocal(M[:, u % 3, 9:9 + k], M[:, u % 3, 6:6 + k]).then_inc(*v.step())
                v.wait_ge(*v.own)
                if A.factor is not None:
                    f = A.factor(u)
                    nc.vector.tensor_tensor(M[:, u % 3, 9:9 + k], M[:, u % 3, 9:9 + k], f, ALU.mult).then_inc(*v.step())
                    v.wait_ge(*v.own)
                if A.subtract:
                    (c0, w), (c1, _) = maps
                    nc.vector.tensor_scalar(s[:, c0:c0 + w], s[:, c0:c0 + w], M[:, u % 3, 9:10], None, ALU.mult).then_inc(*v.step())
                    v.wait_ge(*v.own)
                    nc.vector.scalar_tensor_tensor(s[:, c0:c0 + w], s[:, c1:c1 + w], M[:, u % 3, 10:11],
                                                   s[:, c0:c0 + w], ALU.mult, ALU.add).then_inc(*v.step())
                else:
                    for j, (c, w) in enumerate(maps):
                        nc.vector.tensor_scalar(s[:, c:c + w], s[:, c:c + w], M[:, u % 3, 9 + j:10 + j], None,
                                                ALU.mult).then_inc(*v.step())
                v.mark(A.name, "weights", u)

            for i in range(A.n + 1):
                if i < A.n:
                    maxima(i)
                if i >= 1:
                    weights(i - 1)

        def att_scalar(act, A):
            act.stage(A.name)
            S, T, M = att_places(A.base)

            def exps(u):
                act.wait_ge(*after(A.name, "max", u))
                for j, (c, w) in enumerate(A.maps(u)):
                    nc.scalar.activation(S[:, u % 3, c:c + w], S[:, u % 3, c:c + w], ACT.Exp,
                                         bias=M[:, u % 3, 3 + j:4 + j], scale=A.post,
                                         accum_out=M[:, u % 3, 6 + j:7 + j]).then_inc(*act.step())
                act.mark(A.name, "exp", u)

            def turned(u):
                blocks = A.blocks(u)
                if u >= 2:
                    act.wait_ge(*after(A.name, "out", u - 2))
                for n in range(0, len(blocks), 4):
                    act.wait_ge(*after(A.name, "turned", u, n // 4))
                    b = bank_of((A.name, "turned", u, n // 4))
                    part = blocks[n:n + 4]
                    full = [x for x in part if x[1] == P]
                    runs = [(i, 1, w) for i, (_, w) in enumerate(part) if w != P]
                    if full:
                        runs.append((part.index(full[0]), len(full), P))
                    for i, m, w in runs:
                        nc.scalar.activation(T[0:w, u % 2, (n + i) * P:(n + i + m) * P],
                                             psum(b, i * P, m * P, slice(0, w)), ACT.Copy).then_inc(*act.step())
                    act.mark("taken", A.name, "turned", u, n // 4)
                act.mark(A.name, "T", u)

            def out(u):
                act.wait_ge(*after(A.name, "out", u))
                rows, _ = A.values(u)
                nc.scalar.activation(A.place(u), psum(bank_of((A.name, "out", u)), 0, P, rows), ACT.Copy).then_inc(*act.step("taken", A.name, "out", u))

            for i in range(A.n + 3):
                if i < A.n:
                    exps(i)
                if 0 <= i - 1 < A.n:
                    turned(i - 1)
                if 0 <= i - 2 < A.n:
                    out(i - 2)
            act.mark(A.name, "done")

        class Attention:
            factor = None
            subtract = False
            pre, post = 1.0, HD ** -0.5
            place_free = ("consts",)

            def last_piece(self, u, n):
                return max(i for i, p in enumerate(self.pieces(u)) if p[0] == n)

            def ready(self, u):
                return ()

            def values_ready(self, u):
                return ()

        def half(h):
            return slice(HD * (h % 2), HD * (h % 2) + HD)

        QA = area(FREE, 4, 512)
        KA = area(FREE + 2048, 4, 512)
        VA = area(FREE + 4096, 4, 512)
        UP = area(FREE + 6144, 4, 2, 288)
        PW = area(FREE + 8448, 4, P)
        PINV = area(FREE + 8960, 4, SEQ)
        PD = area(FREE + 9984, 4, 2, SEQ)
        PT3 = area(FREE + 12032, 3, 2, 288)
        ATT_A = FREE + 13760
        CAT = SQ
        BIAS = area(8192, 8, 2, SEQ)
        assert ATT_A + 3 * S_W + 2 * T_W + 36 <= SMALL

        def loads_pool(g):
            g.stage("load")
            g.eng.dma_start(PR[:, :], params).then_inc(*g.step("params", by=16, sem="params_loaded"))
            g.eng.dma_start(XT[:, :, :, :].rearrange("p a b c -> p (a b c)"), x_t).then_inc(*g.step("x0", by=16, sem="x_loaded"))
            g.eng.dma_start(CN[:, :], consts).then_inc(*g.step("consts", by=16, sem="consts_loaded"))
            g.eng.dma_start(area(8192, 4096), bias).then_inc(*g.step("bias", by=16, sem="bias_loaded"))
            g.eng.dma_start(PW.rearrange("p a b -> p (a b)"), small[:, 6144:6656]).then_inc(*g.step("pool_w", by=16, sem="pool_w_loaded"))
            g.eng.dma_start(PINV.rearrange("p a b -> p (a b)"), pool_inv).then_inc(*g.step("pool_inv", by=16, sem="pool_inverse_loaded"))
            g.eng.dma_start(area(SMALL, 6144), small[:, 0:6144]).then_inc(*g.step("small", by=16, sem="small_loaded"))

        def pool_pool(g):
            g.stage("pooling")
            nc.gpsimd.memset(UP, 0.0).then_inc(*g.step("pads"))
            g.wait_ge(*after("taken_all", "ev_in"))
            g.wait_ge(*after("taken_all2", "ev_in"))
            g.wait_ge(*after("pool_inv"))
            for gi in range(4):
                u = UP[:, gi]
                src, shifts = u, []
                for lv in range(gi + 1):
                    dst = PT3[:, lv % 2]
                    up, down = (0, 1) if lv == 0 else (1 << (lv - 1), 1 << (lv - 1))
                    lo, hi = 1 << lv, 288 - (1 << lv)
                    g.wait_ge(*g.own)
                    nc.gpsimd.tensor_tensor(dst[:, :, lo:hi], src[:, :, lo + up:hi + up],
                                            src[:, :, lo - down:hi - down], ALU.add).then_inc(*g.step())
                    src = dst
                g.wait_ge(*g.own)
                inv = PINV[:, gi].unsqueeze(1).to_broadcast([P, 2, SEQ])
                nc.gpsimd.tensor_tensor(PD[:, gi], src[:, :, 16:272], inv, ALU.mult).then_inc(*g.step())
                g.wait_ge(*g.own)
                nc.gpsimd.tensor_tensor(PD[:, gi], PD[:, gi], u[:, :, 16:272], ALU.subtract).then_inc(*g.step("pooled", gi))

        def pool_tensor(pe):
            pe.stage("pooling")
            pe.wait_ge(*after("pool_w"))
            for gi in range(4):
                b = take_bank(pe, ("pool", gi))
                pe.wait_ge(*after("pooled", gi))
                ins = nc.tensor.matmul(psum(b), PW[:, gi], PD[:, gi], start=True, stop=True)
                ins.then_inc(*pe.step("pool", gi))

        def pool_scalar(act):
            act.stage("pooling")
            for gi in range(4):
                act.wait_ge(*after("pool", gi))
                b = bank_of(("pool", gi))
                nc.scalar.activation(CAT[:, :, gi, :], psum(b).rearrange("p (s t) -> p s t", t=SEQ), ACT.Copy,
                                     scale=pr("pool_scale", gi, 1)).then_inc(*act.step("taken", "pool", gi))
            act.mark("pool_done")

        def ev_in_tensor(pe):
            project_tensor_n(pe, "ev_in", "ev_in", 6, h_moving([0, 1]), h_ready("n1_0", [0, 1]), [0, 1])
            values_natural(pe, "ev_in", "ev_v", 2, 4, 256)
            side_blocks(pe, block_of["ev_out"][0], 0)

        def project_tensor_n(pe, key, name, blocks, moving, ready, segs):
            pe.stage("project_" + key)
            w = len(segs) * SEQ
            for g in range(0, 2 * blocks, 2):
                j = next_block(pe, name)
                for i in range(2):
                    b = take_bank(pe, (key, g + i))
                    for k in range(KT):
                        if g == 0 and i == 0 and ready:
                            for e in ready(k):
                                pe.wait_ge(*after(*e))
                        ins = nc.tensor.matmul(psum(b, 0, w), slot(j, k, 256, i * P, P), moving(k),
                                               start=(k == 0), stop=(k == KT - 1))
                    ins.then_inc(*pe.step(key, g + i))
                pe.mark("used", j)

        def values_natural(pe, name, key, blocks, n_tok, width, segs=(0, 1)):
            for jj in range(blocks):
                j = next_block(pe, name)
                for seg in range(n_tok // 2):
                    b = take_bank(pe, (key, jj, seg))
                    for half_ in range(2):
                        for k in range(KT):
                            s = segs[seg]
                            ins = nc.tensor.matmul(psum(b, half_ * 256, 256), HT[:, s, k, half_ * P:(half_ + 1) * P],
                                                   slot(j, k, 256), start=(k == 0), stop=(k == KT - 1))
                    ins.then_inc(*pe.step(key, jj, seg))
                pe.mark("used", j)

        def take_values(q, key, blocks, n_tok, place, shares, copy):
            for jj in range(blocks):
                for seg in range(n_tok // 2):
                    if (jj * (n_tok // 2) + seg) % 2 != shares:
                        continue
                    q.wait_ge(*after(key, jj, seg))
                    b = bank_of((key, jj, seg))
                    copy(place(jj, seg), psum(b).rearrange("p (t c) -> p t c", c=256)).then_inc(*q.step("taken", key, jj, seg))
            q.mark(key + "_out", shares)

        act_copy = lambda o, i: nc.scalar.activation(o, i, ACT.Copy)
        dve_copy = lambda o, i: nc.vector.tensor_copy(o, i)

        def ev_place(g):
            if g < 4:
                return UP[:, g, :, 16:272]
            dst = QA[:, g - 4] if g < 8 else KA[:, g - 8]
            return dst.rearrange("p (s t) -> p s t", t=SEQ)

        def ev_out_of(q, share, copy):
            q.stage("project_ev_in")
            q.wait_ge(*after("pads"))
            for g in range(share, 12, 2):
                if share == 1:
                    side_chains(q, block_of["ev_in"][g // 2])
                q.wait_ge(*after("ev_in", g))
                copy(ev_place(g), psum(bank_of(("ev_in", g))).rearrange("p (s t) -> p s t", t=SEQ)).then_inc(*q.step("taken", "ev_in", g))
                if g == 2 + share:
                    q.mark("taken_all" if share == 0 else "taken_all2", "ev_in")
            q.mark("qk_out", share)
            if share == 1:
                side_chains(q, block_of["ev_out"][0])
            take_values(q, "ev_v", 2, 4, lambda jj, seg: VA[:, 2 * seg:2 * seg + 2, jj * 256:(jj + 1) * 256], share, copy)

        class LatentAttention(Attention):
            name, n, base = "latent_attention", 16, ATT_A
            pre, post = HD ** -0.5, 1.0
            place_free = ("bias",)

            def ready(self, u):
                return (("qk_out", 0), ("qk_out", 1))

            def values_ready(self, u):
                return (("ev_v_out", 0), ("ev_v_out", 1))

            def scores(self, u):
                h, qt = divmod(u, 2)
                r = half(h)
                return [[(0, 512, QA[r, h // 2, 256 + qt * P:256 + (qt + 1) * P], KA[r, h // 2, :])]]

            def pieces(self, u):
                h, qt = divmod(u, 2)
                return [(0, 0, 0, 256, None), (0, 256, 256, 256, BIAS[:, h, qt, :])]

            def maps(self, u):
                return [(0, 512)]

            def blocks(self, u):
                return [(i * P, P) for i in range(4)]

            def values(self, u):
                h = u // 2
                return half(h), [VA[:, i, h * HD:(h + 1) * HD] for i in range(4)]

            def place(self, u):
                h, qt = divmod(u, 2)
                return CAT[half(h), X, 4 + h // 2, qt * P:(qt + 1) * P]

        class ContextAttention(LatentAttention):
            name = "context_attention"

            def scores(self, u):
                h, qt = divmod(u, 2)
                r = half(h)
                return [[(0, 256, QA[r, h // 2, qt * P:(qt + 1) * P], KA[r, h // 2, 0:256])]]

            def pieces(self, u):
                return [(0, 0, 0, 256, None)]

            def maps(self, u):
                return [(0, 256)]

            def blocks(self, u):
                return [(i * P, P) for i in range(2)]

            def values(self, u):
                h = u // 2
                return half(h), [VA[:, i, h * HD:(h + 1) * HD] for i in range(2)]

            def place(self, u):
                h, qt = divmod(u, 2)
                return CAT[half(h), CTX, 4 + h // 2, qt * P:(qt + 1) * P]
            place_free = ("latent_attention", "done")

        LAT, CON = LatentAttention(), ContextAttention()

        HID = area(FREE, 2, 32, SEQ)

        def mlp_tensor(pe, key, layer, segs, hkey):
            project_tensor(pe, key + "_up", f"mlp1_{layer}", h_moving(segs), h_ready(hkey, segs), segs, "mlp_up")
            side_blocks(pe, block_of[f"mlp2_{layer}"][0], 0)
            pe.stage("mlp_down")
            w = len(segs) * SEQ
            for g in range(KT):
                b = take_bank(pe, (key + "_down", g))
                for part in range(2):
                    j = next_block(pe, f"mlp2_{layer}")
                    for k in range(16):
                        t = part * 16 + k
                        if g == 0 and t % 8 == 0:
                            for f in range(t, t + 8):
                                pe.wait_ge(*after("hidden", key, f))
                        ins = nc.tensor.matmul(psum(b, 0, w), slot(j, k, P), HID[:, seg_of(segs), t, :],
                                               start=(t == 0), stop=(t == 31))
                    ins.then_inc(*pe.step())
                    pe.mark("used", j)
                pe.mark(key + "_down", g)
            side_blocks(pe, block_of["wr" if layer == 0 else "ev2_in"][0], 0)

        def mlp_scalar(act, key, segs):
            act.stage("mlp_up")
            for f in range(32):
                act.wait_ge(*after(key + "_up", f))
                b = bank_of((key + "_up", f))
                nc.scalar.activation(HID[:, seg_of(segs), f, :],
                                     psum(b, 0, len(segs) * SEQ).rearrange("p (s t) -> p s t", t=SEQ),
                                     ACT.Relu).then_inc(*act.step("taken", key + "_up", f))
            act.stage("mlp_down")
            take_out(act, key + "_down", range(0, KT, 2), y_place(segs), segs, "y_all")

        def mlp_vector(v, key, segs, mods=None):
            v.stage("mlp_up")
            layer = 0 if key == "x02" else 1
            for f in range(32):
                if f % 2 == 0:
                    side_chains(v, block_of[f"mlp1_{layer}"][f // 2])
                v.wait_ge(*after("taken", key + "_up", f))
                part = HID[:, seg_of(segs), f, :]
                nc.vector.tensor_tensor(part, part, part, ALU.mult).then_inc(*v.step("hidden", key, f))
            side_chains(v, block_of[f"mlp2_{layer}"][0])
            if mods is not None:
                mod_vectors(v, mods)
            v.stage("mlp_down")
            for g in range(1, KT, 2):
                side_chains(v, block_of[f"mlp2_{layer}"][2 * g + 1])
                take_out(v, key + "_down", [g], y_place(segs), segs, "y_all2" if g == KT - 1 else f"y_tile{g}")
            side_chains(v, block_of["wr" if layer == 0 else "ev2_in"][0])

        HID_HI = rounded("hidden_high", FREE, 32, SEQ)
        HID_LO = rounded("hidden_low", FREE + 8192, 32, SEQ)
        RELU, RELU2 = area(14336, 3, SEQ), area(14336 + 3 * SEQ, 3, SEQ)
        MLP = Splits("mlp", ["mlp1_1", "mlp2_1"], [(33280, 35328), (37376, 8192)])

        def mlp_split_tensor(pe):
            pe.stage("mlp_up")
            for g in range(0, 32, 2):
                j = MLP.next(pe, "mlp1_1")
                for i in range(2):
                    b = take_bank(pe, ("x12_up", g + i))
                    ins = MLP.columns(pe, j, 256, i * P, psum(b, 0, SEQ), KT, x_high, x_low, norm="n2_1")
                    ins.then_inc(*pe.step("x12_up", g + i))
                pe.mark("multiplied", j)
            pe.stage("mlp_down")
            for g in range(KT):
                b = take_bank(pe, ("x12_down", g))
                for part in range(2):
                    j = MLP.next(pe, "mlp2_1")
                    pe.wait_ge(*after("hidden", "x12", 16 * part + 15))
                    ins = MLP.columns(pe, j, P, 0, psum(b, 0, SEQ), 16, lambda k: HID_HI[:, part * 16 + k],
                                      lambda k: HID_LO[:, part * 16 + k], start=part == 0, stop=part == 1)
                    ins.then_inc(*pe.step())
                    pe.mark("multiplied", j)
                pe.mark("x12_down", g)
            side_blocks(pe, block_of["ev2_in"][0], 0)

        def mlp_split_scalar(act):
            act.stage("mlp_up")
            for i in range(16):
                MLP.high(act, i + MLP.ahead)
                for f in (2 * i, 2 * i + 1):
                    act.wait_ge(*after("x12_up", f))
                    nc.scalar.activation(RELU[:, f % 3], psum(bank_of(("x12_up", f)), 0, SEQ), ACT.Relu).then_inc(*act.step("taken", "x12_up", f))
                for f in (2 * i, 2 * i + 1):
                    act.wait_ge(*after("taken", "x12_up", f))
                    if f >= 3:
                        act.wait_ge(*after("hidden", "x12", f - 3))
                    nc.scalar.activation(RELU2[:, f % 3], RELU[:, f % 3], ACT.Square).then_inc(*act.step("relu2", f))
                for f in (2 * i, 2 * i + 1):
                    act.wait_ge(*after("relu2", f))
                    nc.scalar.activation(HID_HI[:, f], RELU2[:, f % 3], ACT.Copy).then_inc(*act.step("hidden_high", f))
            act.stage("mlp_down")
            for i in range(16):
                MLP.high(act, 16 + i + MLP.ahead)
                if i % 4 == 1:
                    take_out(act, "x12_down", [i // 2], y_place(ONE), ONE, "y_all" if i == 13 else f"y_tile{i // 2}")

        def mlp_split_vector(v):
            v.stage("mlp_up")
            for i in range(16):
                MLP.low(v, i + MLP.ahead)
                for f in (2 * i, 2 * i + 1):
                    v.wait_ge(*after("hidden_high", f))
                    nc.vector.tensor_tensor(HID_LO[:, f], RELU2[:, f % 3], HID_HI[:, f], ALU.subtract).then_inc(*v.step("hidden", "x12", f))
            v.stage("mlp_down")
            for i in range(16):
                MLP.low(v, 16 + i + MLP.ahead)
                if i % 4 == 3:
                    take_out(v, "x12_down", [i // 2], y_place(ONE), ONE, "y_all2" if i == 15 else f"y_tile{i // 2}")
            side_chains(v, block_of["ev2_in"][0])

        RR = area(0, KT, SEQ)
        XX = area(8192, 2, KT, SEQ)
        MIX = [area(12288, 2, KT, SEQ), area(16896, 2, KT, SEQ)]
        KK = area(16896, KT, 512)
        KR = area(20992, KT, 512)
        VP = area(25088, 8, PAIRS, HD)
        HW, HA = area(29184, 512), area(29696, 512)
        GH = area(16384, SEQ)
        LOW = {n: area(SMALL + 1024 * i, D) for i, n in enumerate(("w1", "a1", "g1", "w2", "a2", "g2"))}
        MIX_ORDER = [("r", 0, [X]), ("k", 2, [CTX, X]), ("v", 3, [CTX, X]), ("w", 1, [CTX, X]), ("a", 4, [CTX, X]),
                     ("g", 5, [X])]
        MIX_END = {"r": ("wr", 7), "k": ("wk", 7), "v": ("wv", 3, 1), "w": ("low_w",), "a": ("low_a",)}

        def mixes_vector(v):
            v.stage("mixes")
            v.wait_ge(*after("h_all", "n1_1"))
            H = HT.rearrange("p a b c -> p (a b) c")
            S = XX.rearrange("p a b c -> p (a b) c")
            nc.vector.tensor_tensor(S[:, :, 1:255], H[:, :, 0:254], H[:, :, 2:256], ALU.add).then_inc(*v.step())
            nc.vector.tensor_copy(S[:, :, 0:1], H[:, :, 1:2]).then_inc(*v.step())
            nc.vector.tensor_copy(S[:, :, 255:256], H[:, :, 254:255]).then_inc(*v.step())
            v.wait_ge(*v.own)
            nc.vector.scalar_tensor_tensor(S, S, 0.5, H, ALU.mult, ALU.subtract).then_inc(*v.step())
            v.wait_ge(*v.own)
            for i, (n, mu, segs) in enumerate(MIX_ORDER):
                if i >= 2:
                    v.wait_ge(*after(*MIX_END[MIX_ORDER[i - 2][0]]))
                sg = seg_of(segs)
                for k in range(KT):
                    nc.vector.scalar_tensor_tensor(MIX[i % 2][:, sg, k, :], XX[:, sg, k, :],
                                                   pr("mu", mu * KT + k, 1), HT[:, sg, k, :], ALU.mult, ALU.add).then_inc(*v.step("mix", n, k))
                if n == "k":
                    rw_out(v, "wr", 1, dve_copy)
                if n == "v":
                    rw_out(v, "wk", 1, dve_copy)
                if n == "a":
                    rwv_out(v, 1, dve_copy)

        def rw_out(q, name, share, copy):
            q.stage("project_" + name)
            for g in range(share, KT, 2):
                q.wait_ge(*after(name, g))
                w = SEQ if name == "wr" else 512
                dst = RR[:, g] if name == "wr" else KR[:, g]
                copy(dst, psum(bank_of((name, g)), 0, w)).then_inc(*q.step("taken", name, g))
                q.mark(name + "_out", g)
            q.mark(name + "_out_all", share)

        def rwv_out(q, share, copy):
            q.stage("project_wv")
            for jj in range(4):
                seg = share
                q.wait_ge(*after("wv", jj, seg))
                b = bank_of(("wv", jj, seg))
                copy(VP[:, 4 * seg:4 * seg + 4, 2 * jj:2 * jj + 2, :].rearrange("p c a i -> p c (a i)"),
                     psum(b).rearrange("p (c n) -> p c n", n=P)).then_inc(*q.step("taken", "wv", jj, seg))
            q.mark("wv_out", share)

        def features_tensor(pe):
            mv = lambda i, segs: (lambda k: MIX[i % 2][:, seg_of(segs), k, :])
            project_tensor(pe, "wr", "wr", lambda k: MIX[0][:, X, k, :], lambda k: [("mix", "r", k)], [X], "project_wr")
            project_tensor(pe, "wk", "wk", mv(1, [0, 1]), lambda k: [("mix", "k", k)], [CTX, X], "project_wk")
            pe.stage("project_wv")
            pe.wait_ge(*after("mix", "v", KT - 1))
            for jj in range(4):
                j = next_block(pe, "wv")
                for seg in range(2):
                    b = take_bank(pe, ("wv", jj, seg))
                    for c in range(N_CHUNK):
                        for odd in range(2):
                            for k in range(KT):
                                rhs = slot(j, k, 256).rearrange("p (a o i) -> p a o i", o=2, i=HD)[:, :, odd, :]
                                ins = nc.tensor.matmul(psum(b, c * P, P, half(odd)),
                                                       MIX[0][:, seg, k, c * CHUNK:(c + 1) * CHUNK], rhs,
                                                       start=(k == 0), stop=(k == KT - 1))
                    ins.then_inc(*pe.step("wv", jj, seg))
                pe.mark("used", j)
            pe.stage("low_rank")
            pe.wait_ge(*after("small"))
            for i, (n, w, segs) in enumerate((("w", "w1", [0, 1]), ("a", "a1", [0, 1]), ("g", "g1", [X]))):
                b = take_bank(pe, ("low_" + n,))
                for k in range(KT):
                    pe.wait_ge(*after("mix", n, k))
                    ins = nc.tensor.matmul(psum(b, 0, len(segs) * SEQ), LOW[w][:, k * P:(k + 1) * P],
                                           MIX[(i + 1) % 2][:, seg_of(segs), k, :], start=(k == 0), stop=(k == KT - 1))
                ins.then_inc(*pe.step("low_" + n))
            pe.stage("removal_key")
            for t in range(KT):
                b = take_bank(pe, ("kk_sum", t))
                pe.wait_ge(*after("kk_squares", t))
                nc.tensor.matmul(psum(b), cn("block_ones"), XX_SQ[:, t], start=True, stop=True).then_inc(*pe.step("kk_sum", t))

        XX_SQ = area(8192, KT, 512)

        def features_scalar(act):
            rw_out(act, "wr", 0, act_copy)
            rw_out(act, "wk", 0, act_copy)
            rwv_out(act, 0, act_copy)
            act.stage("low_rank")
            for n, fn, dst, w in (("w", ACT.Tanh, HW, 512), ("a", ACT.Copy, HA, 512), ("g", ACT.Sigmoid, GH, SEQ)):
                act.wait_ge(*after("low_" + n))
                nc.scalar.activation(dst, psum(bank_of(("low_" + n,)), 0, w), fn).then_inc(*act.step("taken", "low_" + n))
            act.stage("removal_key")
            act.wait_ge(*after("mix", "g", KT - 1))
            act.wait_ge(*after("wk_out", KT - 1))
            for t in range(KT):
                nc.scalar.activation(XX_SQ[:, t], KR[:, t], ACT.Square, scale=pr("kk", t, 1)).then_inc(*act.step("kk_squares", t))
            for t in range(KT):
                act.wait_ge(*after("kk_floor", t))
                nc.scalar.activation(XX_SQ[:, t], XX_SQ[:, t], ACT.Sqrt).then_inc(*act.step("kk_root", t))

        def removal_key_vector(v):
            v.stage("removal_key")
            v.wait_ge(*after("wk_out", KT - 2))
            v.wait_ge(*after("low_g"))
            for t in range(KT):
                nc.vector.tensor_scalar(KK[:, t], KR[:, t], pr("kk", t, 1), None, ALU.mult).then_inc(*v.step())
                v.wait_ge(*after("kk_sum", t))
                nc.vector.tensor_scalar(XX_SQ[:, t], psum(bank_of(("kk_sum", t))), 1e-24, None, ALU.max).then_inc(*v.step("taken", "kk_sum", t))
                v.mark("kk_floor", t)
            for t in range(KT):
                v.wait_ge(*after("kk_root", t))
                nc.vector.reciprocal(XX_SQ[:, t], XX_SQ[:, t]).then_inc(*v.step())
                v.wait_ge(*v.own)
                nc.vector.tensor_tensor(KK[:, t], KK[:, t], XX_SQ[:, t], ALU.mult).then_inc(*v.step())
            v.mark("features")

        DECAY = float(np.exp(-0.5))
        at = 4096
        WK = {}
        for n, dims in (("Y", (PAIRS, SEQ)), ("KS", (PAIRS, SEQ)), ("AR", (2, PAIRS, 128)), ("BM", (2, PAIRS, 128)),
                        ("GM", (2, PAIRS, 128)), ("B", (2, PAIRS, 64)), ("G", (2, PAIRS, 64))):
            WK[n] = area(at, *dims)
            at += int(np.prod(dims))
        assert at <= 16384, at
        at = 30208
        for n in ("E", "A", "L", "BN", "C", "S"):
            WK[n] = area(at, 2, PAIRS, 64)
            at += 1024
        assert at <= SMALL + 3072, at
        DEND = ctx.enter_context(nc.sbuf_tensor("decay_end", [P, 16], FP32))[:, :].rearrange("p (d a) -> p d a", d=2)
        WK["X"], WK["XI"], WK["Z"], WK["U"], WK["GN"] = WK["E"], WK["A"], WK["L"], WK["B"], WK["C"]

        def place_of(c, d):
            if d == 0:
                return c
            return 3 - c if c < 4 else 11 - c

        def flat(v):
            return v.rearrange("p a b -> p (a b)")

        def bank3(key, w=64):
            return psum(bank_of(key)).rearrange("p (a b) -> p a b", b=w)

        def pairs_matmul(pe, key, terms, width=64, pairs=range(PAIRS), ready=()):
            b = take_bank(pe, key)
            for e in ready:
                pe.wait_ge(*after(*e))
            for n, p in enumerate(pairs):
                for h in range(2):
                    r = half(h)
                    ts = terms(p, r)
                    for i, (lhs, rhs) in enumerate(ts):
                        ins = nc.tensor.matmul(psum(b, n * width, width, r), lhs, rhs, start=(i == 0),
                                               stop=(i == len(ts) - 1))
            ins.then_inc(*pe.step(*key))

        def pairs_turned(pe, key, src, ready=()):
            for part in range(2):
                b = take_bank(pe, key + (part,))
                for e in ready:
                    pe.wait_ge(*after(*e))
                for n in range(4):
                    ins = nc.tensor.transpose(psum(b, n * P, P, slice(0, 64)), src[:, 4 * part + n, :], cn("ident"))
                ins.then_inc(*pe.step(*key, part))

        def turned_out(act, key, dst):
            for part in range(2):
                act.wait_ge(*after(*key, part))
                src = psum(bank_of(key + (part,)), 0, 512, slice(0, 64)).rearrange("p (a h i) -> p a h i", h=2, i=64)
                for h in range(2):
                    nc.scalar.activation(dst[half(h), 4 * part:4 * part + 4, :], src[:, :, h, :], ACT.Copy).then_inc(
                        *act.step())
                act.mark("taken", *key, part)

        def wkv_tensor(pe):
            pe.stage("recurrence")
            pe.wait_ge(*after("taken", "low_a"))
            pe.wait_ge(*after("taken", "low_w"))
            for c in range(8):
                main = c >= 4
                for n, low, hid in (("w_raw", "w2", HW), ("a_raw", "a2", HA)):
                    banks = [take_bank(pe, (n, c, d)) for d in range(2)]
                    for p in range(PAIRS):
                        for h in range(2):
                            for d in range(2):
                                tok = place_of(c, d) * CHUNK
                                ins = nc.tensor.matmul(psum(banks[d], p * 64, 64, half(h)),
                                                       LOW[low][half(d), p * P + h * 64:p * P + h * 64 + 64],
                                                       hid[half(d), tok:tok + CHUNK], start=True, stop=True)
                    ins.then_inc(*pe.step(n, c))
                for d in range(2):
                    B, G, AR = WK["B"][:, d], WK["G"][:, d], WK["AR"][:, d]
                    w = 128 if main else 64
                    for part in range(2):
                        ps_ = range(4 * part, 4 * part + 4)
                        pairs_matmul(pe, ("bm", c, d, part), lambda p, r: [(B[r, p, :], AR[r, p, 0:w])], w if main else 64,
                                     ps_, [("beta", c, d), ("rho", c, d)])
                    for part in range(2):
                        ps_ = range(4 * part, 4 * part + 4)
                        pairs_matmul(pe, ("gm", c, d, part), lambda p, r: [(G[r, p, :], AR[r, p, 0:w])], w if main else 64,
                                     ps_, [("gamma", c, d)])
                    pairs_turned(pe, ("bn", c, d), B)
                    pairs_turned(pe, ("gn", c, d), G)
                for d in range(2):
                    pairs_turned(pe, ("x", c, d, 0), WK["XI"][:, d], [("inverse_t", c, d, 0)])
                for lv in range(1, LEVELS):
                    for d in range(2):
                        Xm, XI, BM = WK["X"][:, d], WK["XI"][:, d], WK["BM"][:, d]
                        pairs_matmul(pe, ("z", c, d, lv), lambda p, r: [(BM[r, p, 0:64], Xm[r, p, :])],
                                     ready=[("inverse", c, d, lv - 1), ("bm_out", c, d)])
                    for d in range(2):
                        XI, Z = WK["XI"][:, d], WK["Z"][:, d]
                        pairs_matmul(pe, ("dxi", c, d, lv), lambda p, r: [(Z[r, p, :], XI[r, p, :])],
                                     ready=[("z_out", c, d, lv), ("inverse_t", c, d, lv - 1)])
                    for d in range(2):
                        if lv < LEVELS - 1:
                            pairs_turned(pe, ("x", c, d, lv), WK["XI"][:, d], [("inverse_t", c, d, lv)])
                for d in range(2):
                    AR, GM, S, cc = WK["AR"][:, d], WK["GM"][:, d], WK["S"][:, d], place_of(c, d)
                    pairs_matmul(pe, ("w", c, d),
                                 lambda p, r: ([(AR[r, p, 0:64], S[r, p, :])] if c else [])
                                 + [(GM[r, p, 0:64], VP[r, cc, p, :])],
                                 ready=[("gm_out", c, d), ("wv_out", 0), ("wv_out", 1)] + ([("state", c - 1, d)] if c else []))
                for d in range(2):
                    XI, W = WK["XI"][:, d], WK["Z"][:, d]
                    pairs_matmul(pe, ("u", c, d), lambda p, r: [(XI[r, p, :], W[r, p, :])],
                                 ready=[("w_out", c, d), ("inverse_t", c, d, LEVELS - 1)])
                for d in range(2):
                    AR, BM, GM, S, U = (WK[n][:, d] for n in ("AR", "BM", "GM", "S", "U"))
                    BN, GN, cc = WK["BN"][:, d], WK["GN"][:, d], place_of(c, d)
                    pairs_matmul(pe, ("s", c, d), lambda p, r: [(BN[r, p, :], U[r, p, :]), (GN[r, p, :], VP[r, cc, p, :])],
                                 ready=[("u_out", c, d), ("bn_out", c, d), ("gn_out", c, d)])
                    if main:
                        pairs_matmul(pe, ("y", c, d), lambda p, r: [(S[r, p, :], AR[r, p, 64:128]),
                                                                    (U[r, p, :], BM[r, p, 64:128]),
                                                                    (VP[r, cc, p, :], GM[r, p, 64:128])])

        def wkv_scalar(act):
            act.stage("recurrence")
            for c in range(8):
                main = c >= 4
                for d in range(2):
                    E, A, L, C = (WK[n][:, d] for n in ("E", "A", "L", "C"))
                    for n, buf in (("w_in", L), ("a_in", A)):
                        act.wait_ge(*after(n, c, d))
                        nc.scalar.activation(flat(buf), flat(buf), ACT.Sigmoid).then_inc(*act.step(n + "_sig", c, d))
                for d in range(2):
                    E, A, L, C = (WK[n][:, d] for n in ("E", "A", "L", "C"))
                    act.wait_ge(*after("running", c, d))
                    nc.scalar.activation(DEND[:, d], C[:, :, 63] if d == 0 else C[:, :, 0], ACT.Exp,
                                         scale=-DECAY).then_inc(*act.step("decay_end", c, d))
                    nc.scalar.activation(flat(E), flat(E), ACT.Exp, scale=-DECAY).then_inc(*act.step("before", c, d))
                    nc.scalar.activation(flat(L), flat(C), ACT.Exp, scale=DECAY).then_inc(*act.step("inverse_decay", c, d))
                    if main:
                        act.wait_ge(*act.own)
                        nc.scalar.activation(flat(C), flat(C), ACT.Exp, scale=-DECAY).then_inc(*act.step("decay", c, d))
                for d in range(2):
                    for n, dst in (("bn", "BN"), ("gn", "GN")):
                        turned_out(act, (n, c, d), WK[dst][:, d])
                        act.mark(n + "_out", c, d)
                for lv in range(LEVELS - 1):
                    for d in range(2):
                        turned_out(act, ("x", c, d, lv), WK["X"][:, d])
                        act.mark("inverse", c, d, lv)
                for n, dst in (("w", "Z"), ("u", "U")):
                    for d in range(2):
                        act.wait_ge(*after(n, c, d))
                        nc.scalar.activation(WK[dst][:, d], bank3((n, c, d)), ACT.Copy).then_inc(*act.step("taken", n, c, d))
                        act.mark(n + "_out", c, d)

        def wkv_vector(v):
            v.stage("recurrence")
            mul, add, sub = ALU.mult, ALU.add, ALU.subtract
            tt, stt = nc.vector.tensor_tensor, nc.vector.scalar_tensor_tensor

            def over_steps(name, d=0):
                return pr(name, d * KT, KT).unsqueeze(2).to_broadcast([P, PAIRS, 64])
            for c in range(8):
                main = c >= 4
                toks = [slice(place_of(c, d) * CHUNK, place_of(c, d) * CHUNK + CHUNK) for d in range(2)]
                xtoks = [slice(t.start - SEQ, t.stop - SEQ) for t in toks]
                for d in range(2):
                    A, L = WK["A"][:, d], WK["L"][:, d]
                    for n, buf, bias_name in (("w", L, "w0"), ("a", A, "a0")):
                        if c:
                            v.wait_ge(*after("u", c - 1, d))
                        v.wait_ge(*after(n + "_raw", c))
                        tt(buf, bank3((n + "_raw", c, d)), over_steps(bias_name, d), add).then_inc(*v.step("taken", n + "_raw", c, d))
                        v.mark(n + "_in", c, d)
                for d in range(2):
                    E, A, L, C = (WK[n][:, d] for n in ("E", "A", "L", "C"))
                    if c:
                        v.wait_ge(*after("s", c - 1, d))
                    v.wait_ge(*after("w_in_sig", c, d))
                    nc.vector.tensor_tensor_scan(flat(C), cn("scan_keep"), flat(L), 0.0, mul, add).then_inc(*v.step())
                    v.wait_ge(*v.own)
                    if d == 0:
                        tt(E, C, L, sub).then_inc(*v.step())
                    else:
                        tt(E, C[:, :, 63:64].to_broadcast([P, PAIRS, 64]), C, sub).then_inc(*v.step())
                        v.wait_ge(*v.own)
                        tt(C, E, L, add).then_inc(*v.step())
                    v.mark("running", c, d)
                for d in range(2):
                    E, A, L, C, B, G = (WK[n][:, d] for n in ("E", "A", "L", "C", "B", "G"))
                    AR = WK["AR"][:, d]
                    kk, k = KK[:, :, toks[d]], KR[:, :, toks[d]]
                    if c > 4:
                        v.wait_ge(*after("y", c - 1, d))
                    v.wait_ge(*after("before", c, d))
                    tt(AR[:, :, 0:64], kk, E, mul).then_inc(*v.step("alpha", c, d))
                    v.wait_ge(*after("inverse_decay", c, d))
                    v.wait_ge(*after("a_in_sig", c, d))
                    v.wait_ge(*v.own)
                    tt(E, kk, L, mul).then_inc(*v.step())
                    v.wait_ge(*v.own)
                    stt(flat(B), flat(E), -1.0, flat(A), mul, mul).then_inc(*v.step("beta", c, d))
                    if main:
                        v.wait_ge(*after("decay", c, d))
                        tt(AR[:, :, 64:128], RR[:, :, xtoks[d]], C, mul).then_inc(*v.step())
                    v.mark("rho", c, d)
                    v.wait_ge(*v.own)
                    stt(E, A, 1.0, over_steps("ka"), sub, mul).then_inc(*v.step())
                    v.wait_ge(*v.own)
                    stt(E, E, 1.0, k, add, mul).then_inc(*v.step())
                    v.wait_ge(*v.own)
                    if main:
                        ks = WK["KS"][:, :, xtoks[d]]
                        if c < 6:
                            nc.vector.tensor_copy(ks, E).then_inc(*v.step())
                        else:
                            tt(ks, ks, E, add).then_inc(*v.step())
                    tt(G, E, L, mul).then_inc(*v.step("gamma", c, d))
                for d in range(2):
                    X_, XI = WK["X"][:, d], WK["XI"][:, d]
                    I = cn("ident64").unsqueeze(1).to_broadcast([P, PAIRS, 64])
                    w = 128 if main else 64
                    bm, gm = WK["BM"][:, d], WK["GM"][:, d]
                    mask = cn("order", d * 128, w).unsqueeze(1).to_broadcast([P, 4, w])

                    def masked(name, dst):
                        for part in range(2):
                            v.wait_ge(*after(name, c, d, part))
                            src = psum(bank_of((name, c, d, part)), 0, 4 * w).rearrange("p (a b) -> p a b", b=w)
                            tt(dst[:, 4 * part:4 * part + 4, 0:w], src, mask, mul).then_inc(*v.step("taken", name, c, d, part))
                        v.mark(name + "_out", c, d)
                    masked("bm", bm)
                    first = cn("first_level", 64 * (1 - d), 64).unsqueeze(1).to_broadcast([P, PAIRS, 64])
                    v.wait_ge(*v.own)
                    tt(XI, bm[:, :, 0:64], first, mul).then_inc(*v.step())
                    v.wait_ge(*v.own)
                    tt(XI, XI, I, add).then_inc(*v.step("inverse_t", c, d, 0))
                    masked("gm", gm)
                for lv in range(1, LEVELS):
                    for d in range(2):
                        mask = cn("later_levels", (d * 5 + lv - 1) * 64, 64).unsqueeze(1).to_broadcast([P, PAIRS, 64])
                        v.wait_ge(*after("z", c, d, lv))
                        tt(WK["Z"][:, d], bank3(("z", c, d, lv)), mask, mul).then_inc(*v.step("taken", "z", c, d, lv))
                        v.mark("z_out", c, d, lv)
                    for d in range(2):
                        XI = WK["XI"][:, d]
                        v.wait_ge(*after("dxi", c, d, lv))
                        tt(XI, XI, bank3(("dxi", c, d, lv)), add).then_inc(*v.step("taken", "dxi", c, d, lv))
                        v.mark("inverse_t", c, d, lv)
                for d in range(2):
                    S = WK["S"][:, d]
                    end = DEND[:, d].unsqueeze(2).to_broadcast([P, PAIRS, 64])
                    if main:
                        v.wait_ge(*after("y", c, d))
                        ys = WK["Y"][:, :, xtoks[d]]
                        src = bank3(("y", c, d))
                        if c < 6:
                            nc.vector.tensor_copy(ys, src).then_inc(*v.step("taken", "y", c, d))
                        else:
                            tt(ys, ys, src, add).then_inc(*v.step("taken", "y", c, d))
                    v.wait_ge(*after("s", c, d))
                    v.wait_ge(*after("decay_end", c, d))
                    if c:
                        tt(S, S, bank3(("s", c, d)), add).then_inc(*v.step("taken", "s", c, d))
                        v.wait_ge(*v.own)
                        tt(S, S, end, mul).then_inc(*v.step("state", c, d))
                    else:
                        tt(S, bank3(("s", c, d)), end, mul).then_inc(*v.step("taken", "s", c, d))
                        v.mark("state", c, d)
            v.mark("recurrence_done")

        VT = area(16896, KT, SEQ)
        YC = area(18944, KT, SEQ)
        Q1 = area(8192, KT, SEQ)
        Q2 = area(10240, KT, SEQ)
        RD = area(12288, KT, SEQ)

        def readout_tensor(pe):
            pe.stage("readout")
            I = cn("ident64")
            for part in range(4):
                b = take_bank(pe, ("vt", part))
                pe.wait_ge(*after("recurrence_done"))
                for n in range(2):
                    p = 2 * part + n
                    for c in range(4):
                        for h in range(2):
                            ins = nc.tensor.matmul(psum(b, n * SEQ + c * 64, 64, half(h)), VP[half(h), 4 + c, p, :],
                                                   I[half(h), :], start=True, stop=True)
                ins.then_inc(*pe.step("vt", part))
            for t in range(KT):
                b = take_bank(pe, ("y_mean", t))
                nc.tensor.matmul(psum(b, 0, SEQ), cn("block_ones"), WK["Y"][:, t], start=True, stop=True).then_inc(*pe.step("y_mean", t))
            for t in range(KT):
                b = take_bank(pe, ("bonus", t))
                pe.wait_ge(*after("rks", t))
                nc.tensor.matmul(psum(b, 0, SEQ), cn("block_ones"), Q2[:, t], start=True, stop=True).then_inc(*pe.step("bonus", t))
                b = take_bank(pe, ("y_var", t))
                pe.wait_ge(*after("yc_square", t))
                nc.tensor.matmul(psum(b, 0, SEQ), cn("block_ones"), Q1[:, t], start=True, stop=True).then_inc(*pe.step("y_var", t))
                b = take_bank(pe, ("gate", t))
                pe.wait_ge(*after("taken", "low_g"))
                nc.tensor.matmul(psum(b, 0, SEQ), LOW["g2"][:, t * P:(t + 1) * P], GH, start=True, stop=True).then_inc(*pe.step("gate", t))

        def readout_scalar(act):
            act.stage("readout")
            for part in range(4):
                act.wait_ge(*after("vt", part))
                nc.scalar.activation(VT[:, 2 * part:2 * part + 2], psum(bank_of(("vt", part))).rearrange(
            "p (a b) -> p a b", b=SEQ), ACT.Copy).then_inc(*act.step("taken", "vt", part))
            for t in range(KT):
                act.wait_ge(*after("yc", t))
                nc.scalar.activation(Q1[:, t], YC[:, t], ACT.Square).then_inc(*act.step("yc_square", t))
            for t in range(KT):
                act.wait_ge(*after("y_var", t))
                nc.scalar.activation(RD[:, t], psum(bank_of(("y_var", t)), 0, SEQ), ACT.Sqrt,
                                     bias=cn("eps", 1, 1), scale=1.0 / HD).then_inc(*act.step("taken", "y_var", t))

        def readout_vector(v):
            v.stage("readout")
            stt, tt = nc.vector.scalar_tensor_tensor, nc.vector.tensor_tensor
            v.wait_ge(*v.own)
            for t in range(KT):
                v.wait_ge(*after("y_mean", t))
                stt(YC[:, t], psum(bank_of(("y_mean", t)), 0, SEQ), -1.0 / HD, WK["Y"][:, t], ALU.mult, ALU.add).then_inc(*v.step("taken", "y_mean", t))
                v.mark("yc", t)
            v.wait_ge(*after("y_mean", KT - 1))
            for t in range(KT):
                stt(Q2[:, t], RR[:, t], pr("rk", t, 1), WK["KS"][:, t], ALU.mult, ALU.mult).then_inc(*v.step("rks", t))
            v.wait_ge(*after("taken", "vt", 3))
            for t in range(KT):
                v.wait_ge(*after("bonus", t))
                tt(VT[:, t], psum(bank_of(("bonus", t)), 0, SEQ), VT[:, t], ALU.mult).then_inc(*v.step("taken", "bonus", t))
                v.wait_ge(*after("taken", "y_var", t))
                nc.vector.reciprocal(RD[:, t], RD[:, t]).then_inc(*v.step())
                v.wait_ge(*v.own)
                stt(YC[:, t], YC[:, t], pr("lng", t, 1), RD[:, t], ALU.mult, ALU.mult).then_inc(*v.step())
                v.wait_ge(*v.own)
                stt(YC[:, t], YC[:, t], pr("lnb", t, 1), VT[:, t], ALU.add, ALU.add).then_inc(*v.step())
                v.wait_ge(*v.own)
                v.wait_ge(*after("gate", t))
                tt(MIX[0][:, X, t, :], YC[:, t], psum(bank_of(("gate", t)), 0, SEQ), ALU.mult).then_inc(*v.step("taken", "gate", t))
                v.mark("read", t)

        CAT2 = area(12288, KT, SEQ)
        B2 = 31100

        def rope_tensor(pe, key, raw, g, ready):
            b = take_bank(pe, (key + "_rot", g))
            pe.wait_ge(*after(*ready))
            nc.tensor.matmul(psum(b, 0, SEQ), cn("swap"), raw, start=True, stop=True).then_inc(*pe.step(key + "_rot", g))

        def rope_pool(g_, key, g, raw, dst, ready):
            g_.wait_ge(*after(*ready))
            nc.gpsimd.tensor_tensor(dst, raw, cn("cos"), ALU.mult).then_inc(*g_.step(key + "_cos", g))

        def rope_vector(v, key, g, raw, dst):
            v.wait_ge(*after(key + "_rot", g))
            v.wait_ge(*after(key + "_cos", g))
            nc.vector.tensor_tensor(raw, psum(bank_of((key + "_rot", g)), 0, SEQ), cn("sin"), ALU.mult).then_inc(*v.step("taken", key + "_rot", g))
            v.wait_ge(*v.own)
            nc.vector.tensor_tensor(dst, dst, raw, ALU.add).then_inc(*v.step(key + "_roped", g))

        RAW = area(FREE, 16, SEQ)
        QK = area(FREE + 4096, 16, SEQ)
        VV = area(FREE + 8192, 2, D)
        OB = area(FREE + 10240, 4, SEQ)
        ATT_B = FREE + 11264
        LF = area(B2, 16)
        EV2 = Splits("ev2", ["ev2_in"], [(31200, 33248), (35296, 37344), (8192, 12288)])
        E2_BLOCKS = [("t", 0), ("t", 1), ("t", 2), ("t", 3), ("v", 0), ("v", 1), ("t", 4), ("t", 5), ("t", 6), ("t", 7),
                     ("v", 2), ("v", 3)]
        LAMBDA_INIT = 0.8 - 0.6

        def ev2_tensor(pe):
            pe.stage("project_ev2")
            prev = []
            for kind, n in E2_BLOCKS:
                j = EV2.next(pe, "ev2_in")
                if kind == "t":
                    for i in range(2):
                        b = take_bank(pe, ("e2", 2 * n + i))
                        ins = EV2.columns(pe, j, 256, i * P, psum(b, 0, SEQ), KT, x_high, x_low, norm="n1_2")
                        ins.then_inc(*pe.step("e2", 2 * n + i))
                    pe.mark("multiplied", j)
                else:
                    EV2.tokens(pe, j, ("e2v", n))
                for g in prev:
                    rope_tensor(pe, "e2", RAW[:, g], g, ("taken", "e2", g))
                prev = [2 * n, 2 * n + 1] if kind == "t" else []
            assert not prev

        def ev2_scalar(act):
            act.stage("project_ev2")
            for i, (kind, n) in enumerate(E2_BLOCKS):
                EV2.high(act, i + EV2.ahead)
                if kind == "t":
                    for g in (2 * n, 2 * n + 1):
                        act.wait_ge(*after("e2", g))
                        nc.scalar.activation(RAW[:, g], psum(bank_of(("e2", g)), 0, SEQ), ACT.Copy).then_inc(*act.step("taken", "e2", g))
                else:
                    act.wait_ge(*after("e2v", n))
                    nc.scalar.activation(VV[:, :, n * 256:(n + 1) * 256], psum(bank_of(("e2v", n))).rearrange(
                "p (a b) -> p a b", b=256), ACT.Copy).then_inc(*act.step("taken", "e2v", n))
            act.wait_ge(*after("lambda_sums"))
            nc.scalar.activation(LF[:, 4:6], psum(bank_of(("lambda_sums",)), 0, 2), ACT.Exp).then_inc(*act.step("taken", "lambda_sums"))

        def ev2_pool(g_):
            g_.stage("project_ev2")
            for g in range(16):
                rope_pool(g_, "e2", g, RAW[:, g], QK[:, g], ("taken", "e2", g))

        def lambda_tensor(pe):
            b = take_bank(pe, ("lambda_sums",))
            pe.wait_ge(*after("lambda_products"))
            nc.tensor.matmul(psum(b, 0, 2), cn("ones"), LF[:, 0:2], start=True, stop=True).then_inc(*pe.step("lambda_sums"))

        def ev2_vector(v):
            v.stage("project_ev2")
            lp = pr("lam")
            nc.vector.tensor_tensor(LF[:, 0:1], lp[:, 0:1], lp[:, 1:2], ALU.mult).then_inc(*v.step())
            nc.vector.tensor_tensor(LF[:, 1:2], lp[:, 2:3], lp[:, 3:4], ALU.mult).then_inc(*v.step("lambda_products"))
            for i in range(len(E2_BLOCKS)):
                EV2.low(v, i + EV2.ahead)
                if i and E2_BLOCKS[i - 1][0] == "t":
                    n = E2_BLOCKS[i - 1][1]
                    for g in (2 * n, 2 * n + 1):
                        rope_vector(v, "e2", g, RAW[:, g], QK[:, g])
            v.wait_ge(*after("taken", "lambda_sums"))
            nc.vector.memset(LF[:, 8:9], 1.0).then_inc(*v.step())
            nc.vector.tensor_tensor(LF[:, 6:7], LF[:, 5:6], LF[:, 4:5], ALU.subtract).then_inc(*v.step())
            v.wait_ge(*v.own)
            nc.vector.tensor_scalar(LF[:, 9:10], LF[:, 6:7], -LAMBDA_INIT, None, ALU.add).then_inc(*v.step("lambda"))

        def causal_pieces(n, col, dst, qt):
            full = [(n, col, dst, P, None)] if qt else []
            return full + [(n, col + qt * P, dst + qt * P, P, cn("causal"))]

        class CausalAttention(Attention):
            name, n, base = "causal_attention", 16, ATT_B
            place_free = ("e2_roped", 15)

            def ready(self, u):
                return (("e2_roped", 15),)

            def values_ready(self, u):
                return (("taken", "e2v", 3),)

            def scores(self, u):
                h, qt = divmod(u, 2)
                r = half(h)
                return [[(0, P * (qt + 1), QK[r, h // 2, qt * P:(qt + 1) * P], QK[r, 4 + h // 2, 0:P * (qt + 1)])]]

            def pieces(self, u):
                return causal_pieces(0, 0, 0, u % 2)

            def maps(self, u):
                return [(0, P * (u % 2 + 1))]

            def blocks(self, u):
                return [(i * P, P) for i in range(u % 2 + 1)]

            def values(self, u):
                h, qt = divmod(u, 2)
                return half(h), [VV[:, i, h * HD:(h + 1) * HD] for i in range(qt + 1)]

            def place(self, u):
                h, qt = divmod(u, 2)
                return CAT2[half(h), h // 2, qt * P:(qt + 1) * P]

        class DifferentialAttention(CausalAttention):
            name, n = "differential_attention", 8
            subtract = True
            place_free = ("causal_attention", "done")

            def factor(self, u):
                return LF[:, 8:10]

            def scores(self, u):
                h, qt = divmod(u, 2)
                w = P * (qt + 1)
                return [[(0, w, QK[half(m), 8 + h, qt * P:(qt + 1) * P], QK[half(m), 12 + h, 0:w])]
                        for m in range(2)]

            def pieces(self, u):
                return causal_pieces(0, 0, 0, u % 2) + causal_pieces(1, 0, 256, u % 2)

            def maps(self, u):
                w = P * (u % 2 + 1)
                return [(0, w), (256, w)]

            def values(self, u):
                h, qt = divmod(u, 2)
                return slice(0, P), [VV[:, i, 512 + h * P:512 + (h + 1) * P] for i in range(qt + 1)]

            def place(self, u):
                h, qt = divmod(u, 2)
                return OB[:, h, qt * P:(qt + 1) * P]

        CAU, DIF = CausalAttention(), DifferentialAttention()

        def subln_tensor(pe):
            pe.stage("head_norm")
            for h in range(4):
                b = take_bank(pe, ("head_sum", h))
                pe.wait_ge(*after("head_square", h))
                nc.tensor.matmul(psum(b, 0, SEQ), cn("ones"), RAW[:, h], start=True, stop=True).then_inc(*pe.step("head_sum", h))

        def subln_scalar(act):
            act.stage("head_norm")
            act.wait_ge(*act.own)
            for h in range(4):
                nc.scalar.activation(RAW[:, h], OB[:, h], ACT.Square).then_inc(*act.step("head_square", h))
            for h in range(4):
                act.wait_ge(*after("head_sum", h))
                nc.scalar.activation(RAW[:, 4 + h], psum(bank_of(("head_sum", h)), 0, SEQ), ACT.Sqrt,
                                     bias=cn("eps", 0, 1), scale=1.0 / P).then_inc(*act.step("taken", "head_sum", h))

        def subln_vector(v):
            v.stage("head_norm")
            nc.vector.tensor_scalar(LF[:, 10:11], pr("subln"), 1.0 - LAMBDA_INIT, None, ALU.mult).then_inc(*v.step())
            for h in range(4):
                v.wait_ge(*after("taken", "head_sum", h))
                nc.vector.reciprocal(RAW[:, 4 + h], RAW[:, 4 + h]).then_inc(*v.step())
                v.wait_ge(*v.own)
                nc.vector.scalar_tensor_tensor(CAT2[:, 4 + h], OB[:, h], LF[:, 10:11], RAW[:, 4 + h],
                                               ALU.mult, ALU.mult).then_inc(*v.step("head_normed", h))

        CB = area(FREE, N_EXPERTS, SEQ)
        SG = area(FREE + 4096, 3, 512)
        AE = area(FREE + 5632, 3, 512)
        CT = area(FREE + 7168, SEQ)
        RT = FREE + 7424
        LG = area(RT, 2, 20)
        ROUTE_BANKS = [0, 1, 2, 7]
        SUM_BANKS = [3, 4, 5, 6]

        AE_HI = rounded("expert_high", 8192, 3, 512)
        AE_LO = rounded("expert_low", 37304, 3, 512)
        MOE = [Splits(f"moe{l}", [f"moe{l}"], [(25000 + 4096 * i, 27048 + 4096 * i) for i in range(3)]) for l in range(2)]
        EXPERT_ORDER = [("gate", 0), ("up", 0)]
        for e_ in range(1, N_EXPERTS):
            EXPERT_ORDER += [("gate", e_), ("up", e_), ("down", e_ - 1)]
        EXPERT_ORDER.append(("down", N_EXPERTS - 1))

        def moe_tensor(pe, l):
            pe.stage(f"router{l}")
            b = take_bank(pe, ("route", l), ROUTE_BANKS)
            for tt_ in range(2):
                for k in range(KT):
                    if tt_ == 0:
                        pe.wait_ge(*after("h", f"n2_{l + 2}", k, X))
                    ins = nc.tensor.matmul(psum(b, tt_ * 20, 20), HT[:, X, k, tt_ * P:(tt_ + 1) * P],
                                           pr("router_w", (l * KT + k) * 20, 20), start=(k == 0), stop=(k == KT - 1))
            ins.then_inc(*pe.step("route", l))

            def gate_up(e):
                for which in ("gate", "up"):
                    j = MOE[l].next(pe, f"moe{l}")
                    b = take_bank(pe, (which, l, e), ROUTE_BANKS)
                    for i in range(2):
                        ins = MOE[l].columns(pe, j, 256, i * P, psum(b, i * SEQ, SEQ), KT, x_high, x_low,
                                             norm=f"n2_{l + 2}")
                    ins.then_inc(*pe.step(which, l, e))
                    pe.mark("multiplied", j)

            def down(e):
                j = MOE[l].next(pe, f"moe{l}")
                pe.wait_ge(*after("expert", l, e))
                if e == 0:
                    for bk in SUM_BANKS:
                        if bank_state["holder"][bk] is not None:
                            pe.wait_ge(*after("taken", *bank_state["holder"][bk]))
                        bank_state["holder"][bk] = ("moe_y", l, bk)
                        events.where[("moe_y", l, bk)] = bk
                for t in range(KT):
                    ins = MOE[l].columns(pe, j, D, t * P, psum(3 + t // 2, (t % 2) * SEQ, SEQ), 2,
                                                lambda k: AE_HI[:, e % 3, k * SEQ:(k + 1) * SEQ],
                                                lambda k: AE_LO[:, e % 3, k * SEQ:(k + 1) * SEQ],
                                                start=e == 0 and t % 2 == 0, stop=e == N_EXPERTS - 1, check=True)
                ins.then_inc(*pe.step("down", l, e))
                pe.mark("multiplied", j)

            gate_up(0)
            b = take_bank(pe, ("comb_t", l), SUM_BANKS)
            pe.wait_ge(*after("comb", l))
            for tt_ in range(2):
                ins = nc.tensor.transpose(psum(b, tt_ * P, P, slice(0, 16)), COMB[:, tt_, :], cn("ident"))
            ins.then_inc(*pe.step("comb_t", l))
            for n in range(8):
                b = take_bank(pe, ("comb_rows", l, n), SUM_BANKS)
                pe.wait_ge(*after("taken", "comb_t", l))
                for i in range(2):
                    e = 2 * n + i
                    pick = cn("ident", e, 1, slice(0, 16)).to_broadcast([16, P])
                    ins = nc.tensor.matmul(psum(b, i * SEQ, SEQ), pick, CT[0:16, :], start=True, stop=True)
                ins.then_inc(*pe.step("comb_rows", l, n))
            for e in range(1, N_EXPERTS):
                gate_up(e)
                down(e - 1)
            down(N_EXPERTS - 1)

        COMB = area(RT + 200, 2, 16)

        def moe_vector(v, l):
            v.stage(f"router{l}")
            tt, ts = nc.vector.tensor_tensor, nc.vector.tensor_scalar
            at_ = [RT + 400]

            def tmp(*dims):
                r = area(at_[0], *dims)
                at_[0] += int(np.prod(dims))
                return r

            def step(ins):
                ins.then_inc(*v.step())
                v.wait_ge(*v.own)
            low_vector(v, f"n2_{l + 2}")
            v.wait_ge(*after("route", l))
            bias_ = pr("router_b", l * 20, 20).unsqueeze(1).to_broadcast([P, 2, 20])
            tt(LG, psum(bank_of(("route", l)), 0, 40).rearrange("p (a b) -> p a b", b=20), bias_, ALU.add).then_inc(*v.step("taken", "route", l))
            v.wait_ge(*v.own)
            GL = LG[:, :, 0:4]

            def four(x):
                return x.unsqueeze(2).to_broadcast([P, 2, 4])

            def first_max(x):
                m, o, t = tmp(2), tmp(2, 4), tmp(2)
                step(nc.vector.tensor_reduce(m, x, AX.X, ALU.max))
                step(tt(o, x, four(m), ALU.is_equal))
                step(tt(o, o, cn("tie").unsqueeze(1).to_broadcast([P, 2, 4]), ALU.mult))
                step(nc.vector.tensor_reduce(t, o, AX.X, ALU.max))
                step(tt(o, o, four(t), ALU.is_equal))
                return m, o
            gm, goh = first_max(GL)
            z, zs, gw = tmp(2, 4), tmp(2), tmp(2)
            tt(z, GL, four(gm), ALU.subtract).then_inc(*v.step("group_less", l))
            big, elg = tmp(2, 4, 4), tmp(2, 4)
            v.wait_ge(*v.own)
            step(tt(big, LG[:, :, 4:20].rearrange("p t (g e) -> p t g e", e=4),
                    goh.unsqueeze(3).to_broadcast([P, 2, 4, 4]), ALU.mult))
            step(nc.vector.tensor_reduce(elg, big.rearrange("p t g e -> p t e g"), AX.X, ALU.add))
            m1, oh1 = first_max(elg)
            el2 = tmp(2, 4)
            step(nc.vector.scalar_tensor_tensor(el2, oh1, NEG, elg, ALU.mult, ALU.add))
            m2, oh2 = first_max(el2)
            d, w1, w2 = tmp(2), tmp(2), tmp(2)
            tt(d, m2, m1, ALU.subtract).then_inc(*v.step("top_less", l))
            v.wait_ge(*after("route_exp", l))
            step(nc.vector.tensor_reduce(zs, z, AX.X, ALU.add))
            step(nc.vector.reciprocal(gw, zs))
            step(ts(w1, d, 1.0, None, ALU.add))
            step(nc.vector.reciprocal(w1, w1))
            step(tt(w1, w1, gw, ALU.mult))
            step(tt(w2, d, w1, ALU.mult))
            step(tt(oh1, oh1, four(w1), ALU.mult))
            step(tt(oh2, oh2, four(w2), ALU.mult))
            step(tt(oh1, oh1, oh2, ALU.add))
            tt(COMB.rearrange("p t (g e) -> p t g e", e=4), goh.unsqueeze(3).to_broadcast([P, 2, 4, 4]),
               oh1.unsqueeze(2).to_broadcast([P, 2, 4, 4]), ALU.mult).then_inc(*v.step("comb", l))
            v.stage(f"experts{l}")
            for n in range(1, 8, 2):
                v.wait_ge(*after("comb_rows", l, n))
                nc.vector.tensor_copy(CB[:, 2 * n:2 * n + 2], psum(bank_of(("comb_rows", l, n))).rearrange(
              "p (a b) -> p a b", b=SEQ)).then_inc(*v.step("taken", "comb_rows", l, n))
                v.mark("comb_rows_out", l, n)
            for i, (which, e) in enumerate(EXPERT_ORDER):
                MOE[l].low(v, i + MOE[l].ahead)
                if which != "up":
                    continue
                a_ = AE[:, e % 3]
                v.wait_ge(*after("silu", l, e))
                v.wait_ge(*after("up", l, e))
                if e >= 3:
                    v.wait_ge(*after("down", l, e - 3))
                tt(a_, SG[:, e % 3], psum(bank_of(("up", l, e))), ALU.mult).then_inc(*v.step("taken", "up", l, e))
                v.wait_ge(*after("comb_rows_out", l, (e // 2) & ~1))
                v.wait_ge(*v.own)
                a2 = a_.rearrange("p (a b) -> p a b", b=SEQ)
                tt(a2, a2, CB[:, e].unsqueeze(1).to_broadcast([P, 2, SEQ]), ALU.mult).then_inc(*v.step())
                v.wait_ge(*v.own)
                nc.vector.tensor_copy(AE_HI[:, e % 3], a_).then_inc(*v.step())
                v.wait_ge(*v.own)
                tt(AE_LO[:, e % 3], a_, AE_HI[:, e % 3], ALU.subtract).then_inc(*v.step("expert", l, e))
            v.wait_ge(*after("down", l, N_EXPERTS - 1))
            for b in (4, 6):
                t = 2 * (b - 3)
                nc.vector.tensor_copy(YT[:, X, t:t + 2, :], psum(b).rearrange("p (a b) -> p a b", b=SEQ)).then_inc(*v.step("taken", "moe_y", l, b))
            v.mark("y_all2", f"moe{l}")

        Z_AT = RT + 400 + 2 + 8 + 2
        D_AT = Z_AT + 8 + 2 + 2 + 32 + 8 + 12 + 8 + 12

        def moe_scalar(act, l):
            act.stage(f"router{l}")
            z, d = area(Z_AT, 8), area(D_AT, 2)
            act.wait_ge(*after("group_less", l))
            nc.scalar.activation(z, z, ACT.Exp).then_inc(*act.step())
            act.wait_ge(*after("top_less", l))
            nc.scalar.activation(d, d, ACT.Exp).then_inc(*act.step("route_exp", l))
            act.wait_ge(*after("comb_t", l))
            nc.scalar.activation(CT[0:16, :], psum(bank_of(("comb_t", l)), 0, SEQ, slice(0, 16)), ACT.Copy).then_inc(*act.step("taken", "comb_t", l))
            act.stage(f"experts{l}")
            for n in range(0, 8, 2):
                act.wait_ge(*after("comb_rows", l, n))
                nc.scalar.activation(CB[:, 2 * n:2 * n + 2], psum(bank_of(("comb_rows", l, n))).rearrange(
            "p (a b) -> p a b", b=SEQ), ACT.Copy).then_inc(*act.step("taken", "comb_rows", l, n))
                act.mark("comb_rows_out", l, n)
            for i, (which, e) in enumerate(EXPERT_ORDER):
                MOE[l].high(act, i + MOE[l].ahead)
                if which != "gate":
                    continue
                act.wait_ge(*after("gate", l, e))
                if e >= 3:
                    act.wait_ge(*after("taken", "up", l, e - 3))
                nc.scalar.activation(SG[:, e % 3], psum(bank_of(("gate", l, e))), ACT.Silu).then_inc(*act.step("taken", "gate", l, e))
                act.mark("silu", l, e)
            act.wait_ge(*after("down", l, N_EXPERTS - 1))
            for b in (3, 5):
                t = 2 * (b - 3)
                nc.scalar.activation(YT[:, X, t:t + 2, :], psum(b).rearrange("p (a b) -> p a b", b=SEQ),
                                     ACT.Copy).then_inc(*act.step("taken", "moe_y", l, b))
            act.mark("y_all", f"moe{l}")

        RQ = area(FREE, KT, SEQ)
        RK = area(FREE + 2048, 4, 4, SEQ)
        QR = area(FREE + 6144, KT, SEQ)
        KRT = area(FREE + 8192, 3, 4, SEQ)
        ATT_C = FREE + 11264
        VS = area(B2, 2, 256)
        VW = area(B2 + 512, 2, 256)
        BK = area(B2 + 1024, 2, 16, 4, N_CMP)
        HC = area(B2 + 2944, 2, 2, 4 * N_CMP)
        KC = area(B2 + 3184, 4 * N_CMP)
        VC = area(B2 + 3244, 4, HD)
        GT = area(B2 + 3500, 2, 48)
        ROPED = {0: 0, 2: 1, 3: 2}
        OD = Splits("od", ["od_in"], [(34704, 36752), (8192, 12288)])
        OD_BLOCKS = [("q", 0), ("q", 1), ("q", 2), ("q", 3), ("k", 0), ("k", 1), ("k", 2), ("v", 0), ("k", 3), ("v", 1)]

        def od_tensor(pe):
            pe.stage("project_od")
            prev = []
            for kind, n in OD_BLOCKS:
                j = OD.next(pe, "od_in")
                if kind == "v":
                    OD.tokens(pe, j, ("odv", n))
                else:
                    for i in range(2):
                        b = take_bank(pe, ("od" + kind, 2 * n + i))
                        ins = OD.columns(pe, j, 256, i * P, psum(b, 0, SEQ), KT, x_high, x_low, norm="n1_3")
                        ins.then_inc(*pe.step("od" + kind, 2 * n + i))
                    pe.mark("multiplied", j)
                for e in prev:
                    rope_tensor(pe, "od", *e)
                prev = od_ropes(kind, n)
            b = take_bank(pe, ("od_gates",))
            for tt_ in range(2):
                for k in range(KT):
                    ins = nc.tensor.matmul(psum(b, tt_ * 48, 48), HT[:, X, k, tt_ * P:(tt_ + 1) * P],
                                           pr("gate_w", k * 48, 48), start=(k == 0), stop=(k == KT - 1))
            ins.then_inc(*pe.step("od_gates"))

        def od_ropes(kind, n):
            if kind == "q":
                return [(RQ[:, g], g, ("taken", "odq", g)) for g in (2 * n, 2 * n + 1)]
            if kind == "k" and n in ROPED:
                return [(RK[:, n, g], 8 + 4 * ROPED[n] + g, ("taken", "odk", 2 * n + g // 2)) for g in range(4)]
            return []

        def od_dst(g):
            return QR[:, g] if g < 8 else KRT[:, (g - 8) // 4, (g - 8) % 4]

        def od_scalar(act):
            act.stage("project_od")
            for b_, (kind, n) in enumerate(OD_BLOCKS):
                OD.high(act, b_ + OD.ahead)
                if kind == "q":
                    for g in (2 * n, 2 * n + 1):
                        act.wait_ge(*after("odq", g))
                        nc.scalar.activation(RQ[:, g], psum(bank_of(("odq", g)), 0, SEQ), ACT.Copy).then_inc(*act.step("taken", "odq", g))
                elif kind == "k":
                    for i in range(2):
                        act.wait_ge(*after("odk", 2 * n + i))
                        for head, half_ in ((0, 0), (0, 1), (1, 0), (1, 1)):
                            ins = nc.scalar.activation(RK[half(half_), n, 2 * i + head],
                                                       psum(bank_of(("odk", 2 * n + i)), 0, SEQ, half(head)), ACT.Copy)
                            ins.then_inc(*act.step())
                        act.mark("taken", "odk", 2 * n + i)
                else:
                    act.wait_ge(*after("odv", n))
                    nc.scalar.activation(VS if n == 0 else VW, psum(bank_of(("odv", n))).rearrange(
                "p (a b) -> p a b", b=256), ACT.Copy).then_inc(*act.step("taken", "odv", n))
            act.wait_ge(*after("od_gates"))
            nc.scalar.activation(GT, psum(bank_of(("od_gates",)), 0, 96).rearrange("p (a b) -> p a b", b=48),
                                 ACT.Sigmoid).then_inc(*act.step("taken", "od_gates"))

        def od_pool(g_):
            g_.stage("project_od")
            for kind, n in OD_BLOCKS:
                for raw, g, ready in od_ropes(kind, n):
                    rope_pool(g_, "od", g, raw, od_dst(g), ready)

        def od_vector(v):
            v.stage("project_od")
            for i in range(len(OD_BLOCKS)):
                OD.low(v, i + OD.ahead)
                if i == 0:
                    continue
                for raw, g, _ in od_ropes(*OD_BLOCKS[i - 1]):
                    rope_vector(v, "od", g, raw, od_dst(g))
                if OD_BLOCKS[i - 1] == ("k", 1):
                    windows_vector(v)
            v.wait_ge(*after("taken", "od_gates"))
            for qt in range(2):
                c = GT[:, qt, :].rearrange("p (h b) -> p h b", b=3)[:, :, 0:1]
                nc.vector.tensor_scalar(c, c, cn("cmp_live", qt, 1), None, ALU.mult).then_inc(*v.step())
            v.mark("gates")

        def windows_vector(v):
            v.wait_ge(*after("taken", "odk", 3))
            v.wait_ge(*v.own)
            for which, src in ((0, KRT[:, 0]), (1, RK[:, 1])):
                for h in range(2):
                    for g in range(4):
                        rows = half(h)
                        base = src[rows, g, :]
                        lo = base[:, 0:240].rearrange("p (n l o) -> p l n o", l=8, o=2)[:, :, :, h]
                        hi = base[:, 16:256].rearrange("p (n l o) -> p l n o", l=8, o=2)[:, :, :, h]
                        pos = pr("cmp_pos", which * 16, 16, rows)
                        for part, s in ((0, lo), (1, hi)):
                            nc.vector.tensor_tensor(
                          BK[rows, which, 8 * part:8 * part + 8, g, :], s,
                          pos[:, 8 * part:8 * part + 8].unsqueeze(2).to_broadcast([HD, 8, N_CMP]), ALU.add).then_inc(*v.step())
            v.mark("windows")

        def compress_tensor(pe):
            pe.stage("compress")
            pe.wait_ge(*after("windows"))
            for which, name in ((0, "cmp_k"), (1, "cmp_v")):
                banks = [take_bank(pe, ("cmp", which, ft)) for ft in range(2)]
                for part in range(2):
                    j = next_block(pe, name)
                    for ft in range(2):
                        for k in range(KT):
                            t = part * 8 + k
                            ins = nc.tensor.matmul(psum(banks[ft], 0, 4 * N_CMP), slot(j, k, 256, ft * P, P),
                                                   BK[:, which, t].rearrange("p g n -> p (g n)"), start=(t == 0),
                                                   stop=(t == 15))
                        ins.then_inc(*pe.step("cmp", which, ft, part))
                    pe.mark("used", j)
            w2 = lambda which, ft: pr("cmp_w2", (which * 2 + ft) * 64, 64)
            b = take_bank(pe, ("cmp_k2",))
            pe.wait_ge(*after("cmp_hidden", 0, 1))
            for h in range(2):
                for ft in range(2):
                    ins = nc.tensor.matmul(psum(b, 0, 4 * N_CMP, half(h)), w2(0, ft), HC[:, 0, ft], start=(ft == 0),
                                           stop=(ft == 1))
            ins.then_inc(*pe.step("cmp_k2"))
            b = take_bank(pe, ("cmp_v2",))
            pe.wait_ge(*after("cmp_hidden", 1, 1))
            for g in range(4):
                for ft in range(2):
                    ins = nc.tensor.matmul(psum(b, g * HD, HD, slice(0, N_CMP)), HC[:, 1, ft, g * N_CMP:(g + 1) * N_CMP],
                                           w2(1, ft), start=(ft == 0), stop=(ft == 1))
            ins.then_inc(*pe.step("cmp_v2"))

        def compress_scalar(act):
            act.stage("compress")
            for which in range(2):
                for ft in range(2):
                    act.wait_ge(*after("cmp", which, ft, 1))
                    nc.scalar.activation(HC[:, which, ft], psum(bank_of(("cmp", which, ft)), 0, 4 * N_CMP),
                                         ACT.Gelu_apprx_tanh, bias=pr("cmp_b1", which * 2 + ft, 1)).then_inc(*act.step("taken", "cmp", which, ft))
                    act.mark("cmp_hidden", which, ft)
            act.wait_ge(*after("cmp_k2"))
            nc.scalar.activation(KC, psum(bank_of(("cmp_k2",)), 0, 4 * N_CMP), ACT.Identity,
                                 bias=pr("cmp_b2k")).then_inc(*act.step("taken", "cmp_k2"))

        def compress_vector(v):
            v.stage("compress")
            v.wait_ge(*after("cmp_v2"))
            r = slice(0, N_CMP)
            nc.vector.tensor_tensor(VC[r], psum(bank_of(("cmp_v2",)), 0, 256, r).rearrange("p (a b) -> p a b", b=HD),
                                    pr("cmp_b2v", rows=r).unsqueeze(1).to_broadcast([N_CMP, 4, HD]), ALU.add).then_inc(*v.step("taken", "cmp_v2"))

        class SparseAttention(Attention):
            name, n, base = "sparse_attention", 32, ATT_C
            place_free = ("gates",)

            def factor(self, u):
                h, qt = divmod(u, 2)
                return GT[:, qt, 3 * h:3 * h + 3]

            def ready(self, u):
                return (("od_roped", 19), ("taken", "cmp_k2"))

            def values_ready(self, u):
                return (("taken", "cmp_v2"), ("taken", "odv", 1))

            def scores(self, u):
                h, qt = divmod(u, 2)
                g, r, w = h // 4, half(h), P * (qt + 1)
                q = QR[r, h // 2, qt * P:(qt + 1) * P]
                first = [(0, N_CMP, q, KC[r, g * N_CMP:(g + 1) * N_CMP]), (16, w, q, KRT[r, 1, g, 0:w])]
                last = (144 if qt == 0 else 0, w, q, KRT[r, 2, g, 0:w])
                return [first + [last]] if qt == 0 else [first, [last]]

            def pieces(self, u):
                qt = u % 2
                last = (0, 144) if qt == 0 else (1, 0)
                return ([(0, 0, 0, N_CMP, cn("cmp_mask", qt * N_CMP, N_CMP))] + causal_pieces(0, 16, 16, qt)
                        + causal_pieces(*last, 272, qt))

            def maps(self, u):
                w = P * (u % 2 + 1)
                return [(0, N_CMP), (16, w), (272, w)]

            def blocks(self, u):
                n = u % 2 + 1
                return [(0, N_CMP)] + [(16 + i * P, P) for i in range(n)] + [(272 + i * P, P) for i in range(n)]

            def values(self, u):
                h, qt = divmod(u, 2)
                g, n = h // 4, qt + 1
                return half(h), ([VC[0:N_CMP, g]] + [VS[:, i, g * HD:(g + 1) * HD] for i in range(n)]
                                 + [VW[:, i, g * HD:(g + 1) * HD] for i in range(n)])

            def place(self, u):
                h, qt = divmod(u, 2)
                return CAT2[half(h), h // 2, qt * P:(qt + 1) * P]

        SPA = SparseAttention()

        def final_vector(v):
            v.stage("final")
            v.wait_ge(*after("rms", "final"))
            v.wait_ge(*v.own)
            for k in range(KT):
                nc.vector.scalar_tensor_tensor(HT[:, X, k, :], XT[:, X, k, :], pr("final_g2", k, 1), RS[:, X, :],
                                               ALU.mult, ALU.mult).then_inc(*v.step("final", k))

        BOTH, ONE = [CTX, X], [X]
        block = ctx.enter_context(nc.Block())

        def first_blocks(q, split, n=2):
            return lambda g: split(q, (g - 4) // 2) if g >= 4 and (g - 4) // 2 < n else None

        def queue(eng, name):
            return Steps(eng, semaphore, events, name)

        @block.sync
        def _(eng):
            sp = queue(eng, "sync")
            load_blocks(sp)
            for k in range(KT):
                sp.wait_ge(*after("final", k))
            eng.dma_start(out_t, HT[:, X].rearrange("p a b -> p (a b)")).then_inc(*sp.step(by=16, sem="out_written"))
            sp.wait_ge(*sp.own)

        @block.gpsimd
        def _(eng):
            g = queue(eng, "gpsimd")
            loads_pool(g)
            pool_pool(g)
            ev2_pool(g)
            od_pool(g)

        @block.tensor
        def _(eng):
            pe = queue(eng, "tensor")
            pe.stage("mod")
            for j in range(FIRST_MODS):
                mod_block(pe, j)
            pe.at_block = FIRST_MODS
            rms_tensor(pe, "n1_0", BOTH)
            ev_in_tensor(pe)
            att_tensor(pe, LAT)
            att_tensor(pe, CON)
            pool_tensor(pe)
            cat_ready = lambda k: [("pool_done",), ("context_attention", "done")]
            project_tensor(pe, "x01", "ev_out", lambda k: CAT[:, :, k, :], cat_ready, BOTH)
            rms_tensor(pe, "y_x01", BOTH)
            rms_tensor(pe, "n2_0", BOTH)
            mlp_tensor(pe, "x02", 0, BOTH, "n2_0")
            rms_tensor(pe, "y_x02", BOTH)
            rms_tensor(pe, "n1_1", BOTH)
            features_tensor(pe)
            wkv_tensor(pe)
            readout_tensor(pe)
            project_tensor(pe, "x11", "wo", lambda k: MIX[0][:, X, k, :], lambda k: [("read", k)], ONE)
            rms_tensor(pe, "y_x11", ONE)
            rms_tensor(pe, "n2_1", ONE)
            mlp_split_tensor(pe)
            rms_tensor(pe, "y_x12", ONE)
            rms_tensor(pe, "n1_2", ONE)
            ev2_tensor(pe)
            lambda_tensor(pe)
            att_tensor(pe, CAU)
            att_tensor(pe, DIF)
            subln_tensor(pe)
            project_tensor(pe, "x21", "ev2_out", lambda k: CAT2[:, k, :],
                           lambda k: [("causal_attention", "done"), ("head_normed", 3)], ONE)
            rms_tensor(pe, "n2_2", ONE)
            moe_tensor(pe, 0)
            rms_tensor(pe, "n1_3", ONE)
            od_tensor(pe)
            compress_tensor(pe)
            att_tensor(pe, SPA)
            project_tensor(pe, "x31", "od_out", lambda k: CAT2[:, k, :], lambda k: [("sparse_attention", "done")], ONE)
            rms_tensor(pe, "n2_3", ONE)
            moe_tensor(pe, 1)
            rms_tensor(pe, "final", ONE)

        @block.scalar
        def _(eng):
            act = queue(eng, "scalar")

            def norm_split(key, m, half_, inputs, meanwhile=None):
                rms_scalar(act, key, XT, ONE, inputs, meanwhile)
                modulate_split_scalar(act, key, m, half_)

            def before_mlp(key, norm, m, half_, segs, after):
                rms_scalar(act, norm, XT, segs, after)
                modulate_scalar(act, norm, m, half_, segs)

            silu_c(act)
            before_mlp(None, "n1_0", 0, 0, BOTH, [("x0",), ("consts",)])
            ev_out_of(act, 0, act_copy)
            att_scalar(act, LAT)
            att_scalar(act, CON)
            pool_scalar(act)
            take_out(act, "x01", range(0, KT, 2), y_place(BOTH), BOTH, "y_all")
            rms_scalar(act, "y_x01", YT, BOTH, [("y_all2", "x01"), ("y_all", "x01")])
            before_mlp(None, "n2_0", 0, 1, BOTH, [("x", "x01")])
            mlp_scalar(act, "x02", BOTH)
            rms_scalar(act, "y_x02", YT, BOTH, [("mod_summed", 2, 23), ("y_all2", "x02_down"), ("y_all", "x02_down")])
            before_mlp(None, "n1_1", 1, 0, BOTH, [("x", "x02")])
            features_scalar(act)
            wkv_scalar(act)
            readout_scalar(act)
            take_out(act, "x11", range(0, KT, 2), y_place(ONE), ONE, "y_all", then=first_blocks(act, MLP.high, 1))
            rms_scalar(act, "y_x11", YT, ONE, [("y_all2", "x11"), ("y_all", "x11")])
            norm_split("n2_1", 1, 1, [("x", "x11")])
            mlp_split_scalar(act)
            rms_scalar(act, "y_x12", YT, ONE, [("mod_summed", 3, 23), ("y_all2", "x12_down"), ("y_all", "x12_down")],
                       lambda: EV2.high(act, 0))
            norm_split("n1_2", 2, 0, [("x", "x12")], lambda: EV2.high(act, 1))
            ev2_scalar(act)
            att_scalar(act, CAU)
            att_scalar(act, DIF)
            subln_scalar(act)
            take_out(act, "x21", range(0, KT, 2), y_place(ONE), ONE, "y_all", then=first_blocks(act, MOE[0].high))
            norm_split("n2_2", 2, 1, [("x", "x21")])
            moe_scalar(act, 0)
            norm_split("n1_3", 3, 0, [("x", "moe0")], lambda: OD.high(act, 0))
            od_scalar(act)
            compress_scalar(act)
            att_scalar(act, SPA)
            take_out(act, "x31", range(0, KT, 2), y_place(ONE), ONE, "y_all", then=first_blocks(act, MOE[1].high))
            norm_split("n2_3", 3, 1, [("x", "x31")])
            moe_scalar(act, 1)
            rms_scalar(act, "final", XT, ONE, [("x", "moe1")])

        @block.vector
        def _(eng):
            v = queue(eng, "vector")

            def norm(key, m, half_, segs, after, freed=(), meanwhile=None):
                rms_vector(v, key, XT, segs, after, meanwhile)
                modulate_vector(v, key, m, half_, segs, freed)

            def y_norm(key, segs):
                rms_vector(v, "y_" + key, YT, segs, [("y_all", key), ("y_all2", key)])

            rms_vector(v, "n1_0", XT, BOTH, [("x0",)])
            mod_vectors(v, 0, range(2))
            v.at_block = FIRST_MODS
            modulate_vector(v, "n1_0", 0, 0, BOTH, [])
            ev_out_of(v, 1, dve_copy)
            mod_vectors(v, 0, range(2, 6))
            att_vector(v, LAT)
            att_vector(v, CON)
            take_out(v, "x01", range(1, KT, 2), y_place(BOTH), BOTH, "y_all2")
            rms_vector(v, "y_x01", YT, BOTH, [("y_all", "x01"), ("y_all2", "x01")])
            residual_vector(v, "x01", 0, 0, BOTH, True)
            norm("n2_0", 0, 1, BOTH, [("x", "x01")])
            mlp_vector(v, "x02", BOTH, 1)
            rms_vector(v, "y_x02", YT, BOTH, [("mod_summed", 2, 23), ("y_all", "x02_down"), ("y_all2", "x02_down")])
            residual_vector(v, "x02", 0, 1, BOTH, True)
            norm("n1_1", 1, 0, BOTH, [("x", "x02")])
            mixes_vector(v)
            removal_key_vector(v)
            wkv_vector(v)
            readout_vector(v)
            take_out(v, "x11", range(1, KT, 2), y_place(ONE), ONE, "y_all2", then=first_blocks(v, MLP.low, 1))
            rms_vector(v, "y_x11", YT, ONE, [("y_all", "x11"), ("y_all2", "x11")])
            residual_vector(v, "x11", 1, 0, ONE, True)
            norm("n2_1", 1, 1, ONE, [("x", "x11")])
            low_vector(v, "n2_1")
            mod_vectors(v, 2)
            mlp_split_vector(v)
            rms_vector(v, "y_x12", YT, ONE, [("mod_summed", 3, 23), ("y_all", "x12_down"), ("y_all2", "x12_down")],
                       lambda: EV2.low(v, 0))
            residual_vector(v, "x12", 1, 1, ONE, True)
            norm("n1_2", 2, 0, ONE, [("x", "x12")], meanwhile=lambda: EV2.low(v, 1))
            low_vector(v, "n1_2")
            mod_vectors(v, 3)
            ev2_vector(v)
            att_vector(v, CAU)
            att_vector(v, DIF)
            subln_vector(v)
            take_out(v, "x21", range(1, KT, 2), y_place(ONE), ONE, "y_all2", then=first_blocks(v, MOE[0].low))
            residual_vector(v, "x21", 2, 0, ONE, False)
            norm("n2_2", 2, 1, ONE, [("x", "x21")])
            moe_vector(v, 0)
            residual_vector(v, "moe0", 2, 1, ONE, False)
            norm("n1_3", 3, 0, ONE, [("x", "moe0")], meanwhile=lambda: OD.low(v, 0))
            low_vector(v, "n1_3")
            od_vector(v)
            compress_vector(v)
            att_vector(v, SPA)
            take_out(v, "x31", range(1, KT, 2), y_place(ONE), ONE, "y_all2", then=first_blocks(v, MOE[1].low))
            residual_vector(v, "x31", 3, 0, ONE, False)
            norm("n2_3", 3, 1, ONE, [("x", "x31")])
            moe_vector(v, 1)
            residual_vector(v, "moe1", 3, 1, ONE, False)
            rms_vector(v, "final", XT, ONE, [("x", "moe1")])
            final_vector(v)
    return events


def kernel(**inputs):
    import concourse.bacc as bacc
    from concourse.bass_utils import run_bass_kernel_spmd

    a = {n: np.asarray(x) for n, x in inputs.items()}

    def features_first(x):
        return x.reshape(SEQ, KT, P).transpose(2, 1, 0)

    arrays = {
        "weights": weight_blocks(a),
        "consts": constants(),
        "params": parameters(a),
        "small": small_weights(a),
        "bias": position_bias(a["ev_rpb"]),
        "x_t": np.ascontiguousarray(np.stack([features_first(a["ctx"]), features_first(a["x"])], 1).reshape(P, -1)),
    }
    arrays["pool_inv"] = pool_inverses()

    def build(events):
        nc = bacc.Bacc("TRN2", target_bir_lowering=False, num_devices=1)
        aps = [nc.dram_tensor(n, arrays[n].shape, FP32, kind="ExternalInput").ap()
               for n in ("weights", "consts", "params", "small", "bias", "pool_inv", "x_t")]
        out = nc.dram_tensor("out_t", (P, KT * SEQ), FP32, kind="ExternalOutput").ap()
        return nc, bass_two_blocks(nc, *aps, out, events)

    counted = build(Events())[1]
    nc, _ = build(Events(counted))
    r = run_bass_kernel_spmd(nc, [arrays], core_ids=[0])
    out = np.asarray(r.results[0]["out_t"]).reshape(P, KT, SEQ)
    return np.ascontiguousarray(out.transpose(2, 1, 0).reshape(1, SEQ, D))
```

```python
import numpy as np
import concourse.bass as bass
from concourse import mybir
from contextlib import ExitStack

FP32 = mybir.dt.float32
FP32R = mybir.dt.float32r
ALU = mybir.AluOpType
ACT = mybir.ActivationFunctionType
AX = mybir.AxisListType

P = 128
D = 1024
KT = D // P
SEQ = 256
CTX, X = 0, 1
HD = 64
SLOT = 2048
N_SLOTS = 4
NEG = -1e30
GRID_W, WIN_C, WIN_R = 64, 16, 8
CHUNK = 64
N_CHUNK = SEQ // CHUNK
PAIRS = KT
LEVELS = 6
N_CMP = (SEQ - 32) // 16 + 1
N_EXPERTS = 16
MOD_TILES = 6 * KT
FIRST_MODS = 8
RMS_EPS = 1e-6
GN_EPS = 64e-5

CONST_COLS = {}


def _const(name, width, _at=[0]):
    CONST_COLS[name] = (_at[0], width)
    _at[0] += width


for _n, _w in (("ident", 128), ("ones", 128), ("block_ones", 128), ("swap", 128), ("cos", 256), ("sin", 256),
               ("causal", 128), ("cmp_mask", 2 * N_CMP), ("cmp_live", 2), 
               ("order", 2 * 128), ("first_level", 2 * 64), ("later_levels", 2 * 5 * 64), ("ident64", 64),
               ("scan_keep", 512), ("tie", 4), ("eps", 2)):
    _const(_n, _w)
N_CONST = sum(w for _, w in CONST_COLS.values())


def constants():
    c = {}
    i = np.arange(P)
    c["ident"] = np.eye(P)
    c["ones"] = np.ones((P, P))
    c["block_ones"] = (i[:, None] // HD == i[None, :] // HD).astype(np.float64)
    swap = np.zeros((P, P))
    cos, sin = np.ones((P, SEQ), np.float32), np.zeros((P, SEQ), np.float32)
    inv = np.float32(500000.0) ** (-np.arange(0, 16, 2, dtype=np.float32) / np.float32(16))
    ang = np.arange(SEQ, dtype=np.float32)[:, None] * inv[None, :]
    for p in range(P):
        d = p % HD
        if d < 16:
            swap[p, p + 8 if d < 8 else p - 8] = 1.0
            cos[p] = np.cos(ang[:, d % 8])
            sin[p] = np.sin(ang[:, d % 8]) * (-1 if d < 8 else 1)
    c["swap"], c["cos"], c["sin"] = swap, cos, sin
    c["causal"] = np.where(i[None, :] <= i[:, None], 0.0, NEG)
    q = np.arange(SEQ).reshape(2, P).T
    end = np.arange(N_CMP) * 16 + 31
    c["cmp_mask"] = np.where(end[None, None, :] <= q[:, :, None], 0.0, NEG).reshape(P, -1)
    c["cmp_live"] = (q >= 31).astype(np.float64)
    r, s = (i % 64)[:, None], np.arange(64)[None, :]
    c["order"] = np.concatenate([r < s, r <= s, r > s, r >= s], 1)
    first = lambda a, b: (a // 2 == b // 2) & (a % 2 == 1) & (b % 2 == 0)
    c["first_level"] = np.concatenate([first(r, s), first(s, r)], 1)
    later = []
    for direction in range(2):
        for lv in range(1, LEVELS):
            a, b = (r >> lv, s >> lv) if direction == 0 else (s >> lv, r >> lv)
            later.append((a // 2 == b // 2) & (a % 2 == 1) & (b % 2 == 0))
    c["later_levels"] = np.concatenate(later, 1)
    c["ident64"] = (r == s)
    c["scan_keep"] = np.broadcast_to(np.arange(512) % CHUNK != 0, (P, 512))
    c["tie"] = np.broadcast_to(np.array([4.0, 3.0, 2.0, 1.0]), (P, 4))
    c["eps"] = np.broadcast_to(np.array([RMS_EPS, GN_EPS]), (P, 2))
    out = np.concatenate([np.asarray(c[n], np.float64).reshape(P, w) for n, (_, w) in CONST_COLS.items()], 1)
    return np.ascontiguousarray(out.astype(np.float32))


def pool_inverses():
    t = np.arange(SEQ)
    inverse = [1.0 / (np.clip(t + w // 2, 0, SEQ) - np.clip(t - w // 2, 0, SEQ)) for w in (2, 4, 8, 16)]
    return np.ascontiguousarray(np.broadcast_to(np.concatenate(inverse).astype(np.float32), (P, 4 * SEQ)))


PARAM_COLS = {}


def _param(name, width, _at=[0]):
    PARAM_COLS[name] = (_at[0], width)
    _at[0] += width


for _n, _w in (("c", 16), ("c2", 8), ("ada_b", 4 * MOD_TILES), ("norm_g", 2 * 4 * KT), ("pool_scale", 4),
               ("mu", 6 * KT), ("w0", 2 * KT), ("a0", 2 * KT), ("kk", KT), ("ka", KT), ("rk", KT), ("lng", KT),
               ("lnb", KT), ("norm1_g2", 2 * KT), ("norm2_g2", 2 * KT), ("final_g2", KT), ("lam", 4), ("subln", 1),
               ("cmp_pos", 2 * 16), ("cmp_b1", 4), ("cmp_b2k", 1), ("cmp_b2v", 64), ("cmp_w2", 2 * 2 * 64),
               ("router_b", 2 * 20), ("router_w", 2 * KT * 20), ("gate_w", KT * 48)):
    _param(_n, _w)
N_PARAM = sum(w for _, w in PARAM_COLS.values())


def columns(v):
    v = np.asarray(v)
    return v.reshape(-1, P).T


def parameters(a):
    p = {}
    p["c"] = np.stack([columns(a["c_ctx"]), columns(a["c"])], 2).reshape(P, 16)
    p["c2"] = columns(a["c_2"])
    p["ada_b"] = np.concatenate([columns(a["ada_b"]), columns(a["ada_b_2"])], 1)
    p["norm_g"] = columns(a["norm_g"])
    p["pool_scale"] = columns(a["ev_pool_scale"])
    for n, k in (("mu", "rw_mu"), ("w0", "rw_w0"), ("a0", "rw_a0"), ("kk", "rw_kk"), ("ka", "rw_ka"), ("rk", "rw_rk"),
                 ("lng", "rw_lng"), ("lnb", "rw_lnb"), ("norm1_g2", "norm1_g_2"), ("norm2_g2", "norm2_g_2"),
                 ("final_g2", "final_g_2"), ("subln", "ev_subln_g_2"), ("cmp_b1", "od_cmp_b1_2")):
        p[n] = columns(a[k])
    lam = np.asarray(a["ev_lambda_2"])[0].T
    p["lam"] = np.concatenate([lam, np.zeros_like(lam)], 0)
    p["cmp_pos"] = np.concatenate([columns(np.asarray(a["od_cmp_pos_2"])[0, i].reshape(-1)) for i in range(2)], 1)
    b2 = np.asarray(a["od_cmp_b2_2"])[0]
    p["cmp_b2k"] = np.concatenate([b2[0], b2[0]])[:, None]
    p["cmp_b2v"] = np.broadcast_to(b2[1], (P, 64))
    w2 = np.asarray(a["od_cmp_w2_2"])[0]
    p["cmp_w2"] = w2.reshape(2, 2, P, 64).transpose(2, 0, 1, 3).reshape(P, -1)
    rb = np.concatenate([np.asarray(a["moe_bg_2"]), np.asarray(a["moe_be_2"])], 1)
    p["router_b"] = np.broadcast_to(rb.reshape(1, -1), (P, 40))
    rw = np.concatenate([np.asarray(a["moe_wg_2"]), np.asarray(a["moe_we_2"])], 2)
    p["router_w"] = rw.reshape(2, KT, P, 20).transpose(2, 0, 1, 3).reshape(P, -1)
    gw = np.asarray(a["od_w_in_2"])[0][:, 2560:2608]
    p["gate_w"] = gw.reshape(KT, P, 48).transpose(1, 0, 2).reshape(P, -1)
    return np.ascontiguousarray(np.concatenate([p[n].reshape(P, w) for n, (_, w) in PARAM_COLS.items()], 1))


def weight_blocks(a):
    def cols(w):
        w = np.asarray(w)
        n = w.shape[1] // 256
        return list(w.reshape(KT, P, n, 256).transpose(2, 1, 0, 3).reshape(n, P, SLOT))

    def deep(w):
        w = np.asarray(w)
        return list(w.reshape(2, 16, P, 8, P).transpose(3, 0, 2, 1, 4).reshape(16, P, SLOT))

    def quarters(w):
        return [b for q in range(4) for b in cols(np.asarray(w)[q * D:(q + 1) * D])]

    def halves(w):
        return list(np.asarray(w).reshape(2, KT, P, 256).transpose(0, 2, 1, 3).reshape(2, P, SLOT))

    def wide(w):
        return [np.asarray(w).reshape(2, P, D).transpose(1, 0, 2).reshape(P, SLOT)]

    mods = [cols(a["ada_w"][0]), cols(a["ada_w"][1]), cols(a["ada_w_2"][0]), cols(a["ada_w_2"][1])]
    g = {
        "mod0": mods[0], "mod1": mods[1], "mod2": mods[2], "mod3": mods[3],
        "ev_in": cols(a["ev_w_in"][0]), "ev_out": cols(a["ev_w_out"][0]),
        "mlp1_0": cols(a["mlp_w1"][0]), "mlp2_0": quarters(a["mlp_w2"][0]),
        "mlp1_1": cols(a["mlp_w1"][1]), "mlp2_1": deep(a["mlp_w2"][1]),
        "wr": cols(a["rw_wr"][0]), "wk": cols(a["rw_wk"][0]), "wv": cols(a["rw_wv"][0]), "wo": cols(a["rw_wo"][0]),
        "ev2_in": cols(a["ev_w_in_2"][0]), "ev2_out": cols(a["ev_w_out_2"][0]),
        "od_in": cols(np.asarray(a["od_w_in_2"])[0][:, :2560]), "od_out": cols(a["od_w_out_2"][0]),
        "cmp_k": halves(np.asarray(a["od_cmp_w1_2"])[0, 0]), "cmp_v": halves(np.asarray(a["od_cmp_w1_2"])[0, 1]),
    }
    for layer in range(2):
        up = [cols(a["moe_w_gate_2"][layer, e]) + cols(a["moe_w_up_2"][layer, e]) for e in range(N_EXPERTS)]
        down = [wide(a["moe_w_down_2"][layer, e]) for e in range(N_EXPERTS)]
        g[f"moe{layer}"] = up[0] + [b for e in range(1, N_EXPERTS) for b in up[e] + down[e - 1]] + down[-1]
    taken = dict.fromkeys(g, 0)
    out = []
    for name in block_order():
        out.append(g[name][taken[name]])
        taken[name] += 1
    assert all(taken[n] == len(g[n]) for n in g), taken
    return np.ascontiguousarray(np.stack(out))


def mixed(*runs):
    name, count = runs[0]
    out = []
    done = [0] * len(runs)
    for i in range(count):
        for r, (other, n) in list(enumerate(runs))[1:]:
            while done[r] < n * (i + 1) // count:
                out.append(other)
                done[r] += 1
        out.append(name)
    return out


def block_order():
    order = ["mod0"] * FIRST_MODS + mixed(("ev_in", 8), ("mod0", 24 - FIRST_MODS)) + ["ev_out"] * 4
    order += ["mlp1_0"] * 2 + mixed(("mlp1_0", 2), ("mod1", 3)) + mixed(("mlp2_0", 4), ("mod1", 7))
    order += mixed(("mlp1_0", 4), ("mod1", 7)) + mixed(("mlp2_0", 4), ("mod1", 7))
    order += (mixed(("mlp1_0", 4), ("mod2", 6)) + mixed(("mlp2_0", 4), ("mod2", 6))) * 2
    order += ["wr"] * 4 + ["wk"] * 4 + ["wv"] * 4 + ["wo"] * 4
    order += mixed(("mlp1_1", 16), ("mod3", 12)) + mixed(("mlp2_1", 16), ("mod3", 12))
    order += ["ev2_in"] * 12 + ["ev2_out"] * 4 + ["moe0"] * 48
    order += ["od_in"] * 10 + ["cmp_k"] * 2 + ["cmp_v"] * 2 + ["od_out"] * 4 + ["moe1"] * 48
    return order


def small_weights(a):
    tall = lambda w: np.asarray(w).reshape(KT, P, P).transpose(1, 0, 2).reshape(P, D)
    pair = lambda w: tall(np.concatenate([np.asarray(w)[0, 0], np.asarray(w)[0, 1]], 1))
    stack = lambda w: np.asarray(w)[0].reshape(P, D)
    pool = np.asarray(a["ev_pool_w"])[0].transpose(1, 0, 2).reshape(P, 512)
    return np.ascontiguousarray(np.concatenate(
        [pair(a["rw_w1"]), pair(a["rw_a1"]), tall(a["rw_g1"]), stack(a["rw_w2"]), stack(a["rw_a2"]),
         np.asarray(a["rw_g2"])[0], pool], 1))


def position_bias(rpb):
    rpb = np.asarray(rpb)[0]
    t = np.arange(SEQ)
    row, col = t // GRID_W, t % GRID_W
    start = np.clip(col - WIN_C // 2, 0, GRID_W - WIN_C)
    ok = (col[None, :] >= start[:, None]) & (col[None, :] < start[:, None] + WIN_C)
    dc = np.clip(col[None, :] - col[:, None], -(WIN_C - 1), WIN_C - 1) + WIN_C - 1
    dr = row[None, :] - row[:, None] + WIN_R - 1
    full = np.where(ok[None], rpb[:, dr, dc], np.float32(NEG))
    return np.ascontiguousarray(full.reshape(8, 2, P, SEQ).transpose(2, 0, 1, 3).reshape(P, -1))


class Events:

    def __init__(self, known=None):
        self.known = known.at if known else {}
        self.where_known = known.where if known else {}
        self.at = {}
        self.where = {}


class Steps:

    def __init__(self, eng, semaphore, events, name):
        self.eng, self.semaphore, self.events, self.name = eng, semaphore, events, name
        self.reached = {}
        self.count = {}
        self.own = (None, 0)
        self.counter = None
        self.at_block = 0
        self.taken = {}
        self.later = []
        self.chains, self.chained = 0, []

    def stage(self, name):
        self.counter = f"{name}_{self.name}"

    def step(self, *event, by=1, sem=None):
        s = sem or self.counter
        self.count[s] = self.count.get(s, 0) + by
        self.own = (s, self.count[s])
        if event:
            self.mark(*event)
        return self.semaphore(s), by

    def mark(self, *event):
        assert event not in self.events.at, event
        self.events.at[event] = self.own

    def wait_ge(self, name, value):
        if name is not None and self.reached.get(name, 0) < value:
            self.reached[name] = value
            self.eng.wait_ge(self.semaphore(name), value)


def bass_two_blocks(nc, weights, consts, params, small, bias, pool_inv, x_t, out_t, events):
    ctx = ExitStack()
    with ctx:
        sems = {}

        def semaphore(name):
            if name not in sems:
                sems[name] = ctx.enter_context(nc.semaphore(name))
            return sems[name]

        def after(*event):
            if not events.known:
                return None, 0
            return events.known[event]

        sb = lambda name, width: ctx.enter_context(nc.sbuf_tensor(name, [P, width], FP32))
        ring = sb("weight_slots", N_SLOTS * SLOT)
        CN = sb("constants", N_CONST)
        PR = sb("parameters", N_PARAM)
        MD = sb("modulations", 4 * 96)
        ARENA = 40100
        arena = sb("arena", ARENA)
        ps = ctx.enter_context(nc.psum_tensor("banks", [P, 8, 512], FP32))

        def cn(name, a=0, w=None, rows=slice(0, P)):
            at, width = CONST_COLS[name]
            return CN[rows, at + a:at + (a + w if w else width)]

        def pr(name, a=0, w=None, rows=slice(0, P)):
            at, width = PARAM_COLS[name]
            return PR[rows, at + a:at + (a + w if w else width)]

        def area(at, *dims):
            n = int(np.prod(dims))
            assert at + n <= ARENA, (at, dims)
            v = arena[:, at:at + n]
            if len(dims) == 1:
                return v
            names = "abcd"[:len(dims)]
            return v.rearrange(f"p ({' '.join(names)}) -> p {' '.join(names)}", **dict(zip(names, dims)))

        def psum(bank, a=0, w=512, rows=slice(0, P)):
            return ps[rows, bank, a:a + w]

        XT = area(0, 2, KT, SEQ)
        HT = area(4096, 2, KT, SEQ)
        YT = area(8192, 2, KT, SEQ)
        SQ = area(12288, 2, KT, SEQ)
        RS = area(16384, 2, SEQ)
        FREE = 16896
        SMALL = ARENA - 6144

        ARENA_AT = nc.sbuf_base - 4 * ARENA

        def rounded(name, at, *dims):
            n = int(np.prod(dims))
            assert at + n <= ARENA, (name, at, dims)
            t = nc.alloc_sbuf_tensor_at(name, [P, n], FP32R, offset=ARENA_AT + 4 * at)
            if len(dims) == 1:
                return t[:, :]
            names = "abcd"[:len(dims)]
            return t[:, :].rearrange(f"p ({' '.join(names)}) -> p {' '.join(names)}", **dict(zip(names, dims)))

        order = block_order()
        N_BLOCKS = len(order)
        block_of = {}
        for j, n in enumerate(order):
            block_of.setdefault(n, []).append(j)


        def load_blocks(sp):
            sp.stage("weights")
            for j in range(N_BLOCKS):
                if j >= N_SLOTS:
                    sp.wait_ge(*after("used", j - N_SLOTS))
                s = j % N_SLOTS
                sp.eng.dma_start(ring[:, s * SLOT:(s + 1) * SLOT], weights[j]).then_inc(*sp.step("block", j, by=16, sem=f"weight_slot{s}"))

        def slot(j, k, width, a=0, w=None, rows=slice(0, P)):
            at = (j % N_SLOTS) * SLOT + k * width + a
            return ring[rows, at:at + (w or width)]

        bank_state = {"next": 0, "holder": [None] * 8, "open": list(range(7))}

        def take_bank(pe, key, banks=None):
            pool = banks or bank_state["open"]
            b = pool[bank_state["next"] % len(pool)]
            bank_state["next"] += 1
            if bank_state["holder"][b] is not None:
                pe.wait_ge(*after("taken", *bank_state["holder"][b]))
            bank_state["holder"][b] = key
            events.where[key] = b
            return b

        def bank_of(key):
            return events.where_known.get(key, 0)

        def mod_of(j):
            m = int(order[j][3])
            return m, block_of[order[j]].index(j)

        SUM_LAG = 4

        def side_blocks(pe, j_next, lag=SUM_LAG):
            while pe.at_block < j_next:
                assert order[pe.at_block].startswith("mod"), (order[pe.at_block], pe.at_block, j_next)
                pe.later.append(pe.at_block)
                pe.at_block += 1
            while pe.later and pe.later[0] < j_next - lag:
                mod_sum(pe, *mod_of(pe.later.pop(0)))

        def next_block(pe, name):
            j = block_of[name][pe.taken.get(name, 0)]
            pe.taken[name] = pe.taken.get(name, 0) + 1
            side_blocks(pe, j)
            pe.wait_ge(*after("block", j))
            assert pe.at_block == j
            pe.at_block += 1
            return j

        XHI = rounded("h_high", 0, KT, SEQ)
        XLO = rounded("h_low", 4096, KT, SEQ)

        class Splits:

            def __init__(self, phase, names, places):
                self.blocks = [j for j, n in enumerate(order) if n in names]
                self.pairs = [(rounded(f"{phase}_w_high{i}", a, SLOT), rounded(f"{phase}_w_low{i}", b, SLOT))
                              for i, (a, b) in enumerate(places)]
                self.ahead = len(places) - 1

            def pair(self, j):
                return self.pairs[self.blocks.index(j) % len(self.pairs)]

            def high(self, act, i):
                if i >= len(self.blocks):
                    return
                j, n = self.blocks[i], len(self.pairs)
                act.wait_ge(*after("block", j))
                if i >= n:
                    act.wait_ge(*after("multiplied", self.blocks[i - n]))
                nc.scalar.activation(self.pair(j)[0], slot(j, 0, SLOT), ACT.Copy).then_inc(*act.step("high", j))

            def low(self, v, i):
                if i >= len(self.blocks):
                    return
                j = self.blocks[i]
                side_chains(v, j)
                v.wait_ge(*after("high", j))
                nc.vector.tensor_tensor(self.pair(j)[1], slot(j, 0, SLOT), self.pair(j)[0], ALU.subtract).then_inc(*v.step("used", j))

            def next(self, pe, name):
                j = block_of[name][pe.taken.get(name, 0)]
                pe.taken[name] = pe.taken.get(name, 0) + 1
                side_blocks(pe, j, 0)
                pe.wait_ge(*after("used", j))
                assert pe.at_block == j
                pe.at_block += 1
                return j

            def columns(self, pe, j, width, a, out, tiles, high, low, start=True, stop=True, check=False, norm=None):
                terms = [(0, high, "h_high"), (1, high, None), (0, low, "h_low")]
                for n, (part, x, ready) in enumerate(terms):
                    for k in range(tiles):
                        if norm and ready:
                            pe.wait_ge(*after(ready, norm, k))
                        at = k * width + a
                        ins = nc.tensor.matmul(out, self.pair(j)[part][:, at:at + P], x(k),
                                               start=start and n == 0 and k == 0,
                                               stop=stop and n == 2 and k == tiles - 1, skip_group_check=check)
                return ins

            def tokens(self, pe, j, key):
                b = take_bank(pe, key)
                for tt_ in range(2):
                    t = slice(tt_ * P, (tt_ + 1) * P)
                    for n, (x, part) in enumerate([(XHI, 0), (XHI, 1), (XLO, 0)]):
                        for k in range(KT):
                            ins = nc.tensor.matmul(psum(b, tt_ * 256, 256), x[:, k, t],
                                                   self.pair(j)[part][:, k * 256:(k + 1) * 256],
                                                   start=(n == 0 and k == 0), stop=(n == 2 and k == KT - 1))
                ins.then_inc(*pe.step(*key))
                pe.mark("multiplied", j)

        def x_high(k):
            return XHI[:, k, :]

        def x_low(k):
            return XLO[:, k, :]

        MOD = [MD[:, 96 * m:96 * m + 96].rearrange("p (t s) -> p t s", s=2) for m in range(4)]
        SC = ctx.enter_context(nc.sbuf_tensor("silu_c", [P, 24], FP32))

        MACC = area(12288, 4, 2, 256)

        def mod_vecs(m, n):
            return (CTX, X) if m == 0 or (m == 1 and n < FIRST_MODS) else (X,)

        def mod_bank(pe, m):
            key = ("mod", m, 0)
            if bank_state["holder"][7] != key:
                if bank_state["holder"][7] is not None:
                    held = bank_state["holder"][7]
                    pe.wait_ge(*after("taken", "mod", held[1], 2 if held[1] == 0 else 0))
                bank_state["holder"][7] = key
                events.where[key] = 7

        def mod_block(pe, j):
            m, n = mod_of(j)
            pe.wait_ge(*after("silu_c"))
            mod_bank(pe, m)
            pe.wait_ge(*after("block", j))
            for i in range(2):
                t = 2 * n + i
                for k in range(KT):
                    ins = nc.tensor.matmul(psum(7, t * 2, 2), slot(j, k, 256, i * P, P), SC[:, 2 * k:2 * k + 2],
                                           start=(k == 0), stop=(k == KT - 1))
            ins.then_inc(*pe.step("mod_summed", m, n))
            pe.mark("used", j)

        def mod_chain(v, j):
            m, n = mod_of(j)
            acc = chain_sums[m, n]
            v.wait_ge(*after("silu_c"))
            v.wait_ge(*after("block", j))
            if j >= FIRST_MODS and v.chains >= 4:
                v.wait_ge(*after("mod_summed", *v.chained[v.chains - 4]))
            vecs = mod_vecs(m, n)
            for k in range(KT):
                w = slot(j, k, 256)
                if len(vecs) == 1:
                    c = SC[:, 2 * k + 1:2 * k + 2] if m < 2 else SC[:, 16 + k:17 + k]
                    todo = [(acc[:, k % 2], c, k < 2)]
                else:
                    todo = [(acc[:, s], SC[:, 2 * k + s:2 * k + s + 1], k == 0) for s in vecs]
                for a_, c, first in todo:
                    if first:
                        nc.vector.tensor_scalar(a_, w, c, None, ALU.mult).then_inc(*v.step())
                    else:
                        v.wait_ge(v.own[0], v.own[1] - 1)
                        nc.vector.scalar_tensor_tensor(a_, w, c, a_, ALU.mult, ALU.add).then_inc(*v.step())
            v.mark("used", j)
            if len(vecs) == 1:
                v.wait_ge(*v.own)
                nc.vector.tensor_tensor(acc[:, 0], acc[:, 0], acc[:, 1], ALU.add).then_inc(*v.step())
            v.mark("mod_acc", m, n)
            if j >= FIRST_MODS:
                v.chained.append((m, n))
                v.chains += 1

        def mod_sum(pe, m, n):
            mod_bank(pe, m)
            pe.wait_ge(*after("mod_acc", m, n))
            acc = chain_sums[m, n]
            pe.wait_ge(*after("consts"))
            for i in range(2):
                for a_, s in enumerate(mod_vecs(m, n)):
                    at_ = 2 * (2 * n + i) + s
                    ins = nc.tensor.matmul(psum(7, at_, 1), acc[:, a_, i * P:(i + 1) * P],
                                           cn("ones", 0, 1), start=True, stop=True)
            ins.then_inc(*pe.step("mod_summed", m, n))

        FIRST_ACC = area(20992, 4, 2, 256)
        chain_sums = {mod_of(j): FIRST_ACC[:, j // 2] for j in range(1, FIRST_MODS, 2)}
        rest = [j for j in range(FIRST_MODS, N_BLOCKS) if order[j].startswith("mod")]
        chain_sums.update({mod_of(j): MACC[:, i % 4] for i, j in enumerate(rest)})

        def side_chains(v, j_next):
            while v.at_block < j_next:
                if order[v.at_block].startswith("mod"):
                    mod_chain(v, v.at_block)
                v.at_block += 1

        def silu_c(act):
            act.stage("mod")
            act.wait_ge(*after("params"))
            nc.scalar.activation(SC[:, 0:16], pr("c"), ACT.Silu).then_inc(*act.step())
            nc.scalar.activation(SC[:, 16:24], pr("c2"), ACT.Silu).then_inc(*act.step("silu_c"))

        def mod_vectors(v, m, chunks=range(6)):
            v.stage("mod")
            v.wait_ge(*after("mod_summed", m, 4 * chunks[-1] + 3))
            v.wait_ge(*after("params"))
            M = MOD[m]
            src = psum(7, 0, 2 * MOD_TILES).rearrange("p (t s) -> p t s", s=2)
            bias_at = pr("ada_b", m * MOD_TILES, MOD_TILES)
            gains = {}
            if m < 2:
                for chunk, n, plus in ((1, 0, 1.0), (2, 1, 0.0), (4, 2, 1.0), (5, 3, 0.0)):
                    gains[chunk] = (pr("norm_g", (m * 4 + n) * KT, KT), plus)
            else:
                gains[1] = (pr("norm1_g2", (m - 2) * KT, KT), 1.0)
                gains[4] = (pr("norm2_g2", (m - 2) * KT, KT), 1.0)
            for chunk in chunks:
                vecs = mod_vecs(m, 4 * chunk)
                t, s = slice(chunk * KT, (chunk + 1) * KT), slice(vecs[0], vecs[-1] + 1)
                b = bias_at[:, t].unsqueeze(2).to_broadcast([P, KT, len(vecs)])
                nc.vector.tensor_tensor(M[:, t, s], src[:, t, s], b, ALU.add).then_inc(*v.step())
            v.mark("taken", "mod", m, chunks[0])
            v.wait_ge(*v.own)
            for chunk in chunks:
                if chunk in gains:
                    vecs = mod_vecs(m, 4 * chunk)
                    g, plus = gains[chunk]
                    part = M[:, chunk * KT:(chunk + 1) * KT, vecs[0]:vecs[-1] + 1]
                    nc.vector.scalar_tensor_tensor(part, part, plus, g.unsqueeze(2).to_broadcast([P, KT, len(vecs)]),
                                                   ALU.add, ALU.mult).then_inc(*v.step())
            v.mark("mod_ready", m, chunks[0])

        def mod_part(m, half):
            return 2 if m == 0 and half else 0

        def mod_col(m, chunk, tile, seg):
            s = seg if m < 2 else X
            return MOD[m][:, chunk * KT + tile, s:s + 1]

        TOUCH = ctx.enter_context(nc.sbuf_tensor("table_touch", [P, 8], FP32))

        def load_table(act, fn):
            act.wait_ge(*after("consts"))
            act.wait_ge(*act.own)
            nc.scalar.activation(TOUCH[:, 0:1], cn("eps", 0, 1), fn).then_inc(*act.step())

        def rms_scalar(act, key, src, segs, inputs, meanwhile=None):
            act.stage("norm")
            for e in inputs:
                act.wait_ge(*after(*e))
            for seg in segs:
                nc.scalar.activation(SQ[:, seg, 0:4, :], src[:, seg, 0:4, :], ACT.Square).then_inc(*act.step("squares_low", key, seg))
            if meanwhile is not None:
                meanwhile()
            a, w = segs[0] * SEQ, len(segs) * SEQ
            load_table(act, ACT.Sqrt)
            act.wait_ge(*after("sums", key))
            nc.scalar.activation(RS[:, segs[0]:segs[-1] + 1, :],
                                 psum(bank_of(("sums", key)), 0, w).rearrange("p (s t) -> p s t", t=SEQ),
                                 ACT.Sqrt, bias=cn("eps", 0, 1), scale=1.0 / D).then_inc(*act.step("taken", "sums", key))

        def rms_vector(v, key, src, segs, inputs, meanwhile=None):
            v.stage("norm")
            for e in inputs:
                v.wait_ge(*after(*e))
            for seg in segs:
                nc.vector.tensor_tensor(SQ[:, seg, 4:8, :], src[:, seg, 4:8, :], src[:, seg, 4:8, :], ALU.mult).then_inc(*v.step("squares_high", key, seg))
            if meanwhile is not None:
                meanwhile()
                v.stage("norm")
            v.wait_ge(*after("taken", "sums", key))
            part = RS[:, segs[0]:segs[-1] + 1, :]
            nc.vector.reciprocal(part, part).then_inc(*v.step("rms", key))

        def rms_tensor(pe, key, segs):
            pe.stage("norm")
            b = take_bank(pe, ("sums", key))
            for seg in segs:
                pe.wait_ge(*after("squares_low", key, seg))
                pe.wait_ge(*after("squares_high", key, seg))
            pe.wait_ge(*after("consts"))
            for k in range(KT):
                ins = nc.tensor.matmul(psum(b, 0, len(segs) * SEQ), cn("ones"), SQ[:, segs[0]:segs[-1] + 1, k, :],
                                       start=(k == 0), stop=(k == KT - 1))
            ins.then_inc(*pe.step("sums", key))

        def norm_order(key, segs):
            if key == "n1_1":
                return [(k, seg) for seg in reversed(segs) for k in range(KT)]
            return [(k, seg) for k in range(KT) for seg in segs]

        def modulate_vector(v, key, m, half, segs, freed):
            v.wait_ge(*after("mod_ready", m, mod_part(m, half)))
            for e in freed:
                v.wait_ge(*after(*e))
            v.wait_ge(*v.own)
            for k, seg in norm_order(key, segs):
                nc.vector.scalar_tensor_tensor(HT[:, seg, k, :], XT[:, seg, k, :],
                                               mod_col(m, 3 * half + 1, k, seg), RS[:, seg, :],
                                               ALU.mult, ALU.mult).then_inc(*v.step("scaled", key, k, seg))
            v.mark("scaled_all", key)

        def modulate_scalar(act, key, m, half, segs):
            act.wait_ge(*after("mod_ready", m, mod_part(m, half)))
            for k, seg in norm_order(key, segs):
                act.wait_ge(*after("scaled", key, k, seg))
                nc.scalar.activation(HT[:, seg, k, :], HT[:, seg, k, :], ACT.Identity,
                                     bias=mod_col(m, 3 * half, k, seg)).then_inc(*act.step("h", key, k, seg))
            act.mark("h_all", key)

        XHI2 = rounded("both_high", 16896, 2, KT, SEQ)
        XLO2 = rounded("both_low", 4096, 2, KT, SEQ)

        def split_places(segs):
            if len(segs) == 1:
                return lambda k, seg: (XHI[:, k], XLO[:, k])
            return lambda k, seg: (XHI2[:, seg, k], XLO2[:, seg, k])

        def modulate_split_scalar(act, key, m, half, segs):
            act.wait_ge(*after("mod_ready", m, mod_part(m, half)))
            place = split_places(segs)
            for k in range(KT):
                for seg in segs:
                    act.wait_ge(*after("scaled", key, k, seg))
                    shift = mod_col(m, 3 * half, k, seg)
                    nc.scalar.activation(place(k, seg)[0], HT[:, seg, k, :], ACT.Identity, bias=shift).then_inc(*act.step())
                    if seg == segs[-1]:
                        act.mark("h_high", key, k)
                    nc.scalar.activation(HT[:, seg, k, :], HT[:, seg, k, :], ACT.Identity, bias=shift).then_inc(*act.step("h", key, k, seg))
            act.mark("h_all", key)

        def low_vector(v, key, segs):
            place = split_places(segs)
            for k in range(KT):
                for seg in segs:
                    v.wait_ge(*after("h", key, k, seg))
                    hi, lo = place(k, seg)
                    nc.vector.tensor_tensor(lo, HT[:, seg, k, :], hi, ALU.subtract).then_inc(*v.step())
                v.mark("h_low", key, k)

        def residual_vector(v, key, m, half, segs, normed):
            v.stage("residual")
            v.wait_ge(*after("mod_ready", m, mod_part(m, 1)))
            if normed:
                v.wait_ge(*after("rms", "y_" + key))
                for seg in segs:
                    r = RS[:, seg, :].unsqueeze(1).to_broadcast([P, KT, SEQ])
                    nc.vector.tensor_tensor(YT[:, seg, :, :], YT[:, seg, :, :], r, ALU.mult).then_inc(*v.step())
            else:
                v.wait_ge(*after("y_all", key))
                v.wait_ge(*after("y_all2", key))
            v.wait_ge(*v.own)
            for seg in segs:
                for k in range(KT):
                    nc.vector.scalar_tensor_tensor(XT[:, seg, k, :], YT[:, seg, k, :],
                                                   mod_col(m, 3 * half + 2, k, seg), XT[:, seg, k, :],
                                                   ALU.mult, ALU.add).then_inc(*v.step())
            v.mark("x", key)

        def project_tensor(pe, key, name, moving, ready, segs, stage="project"):
            pe.stage(stage)
            w = len(segs) * SEQ
            n_tiles = 2 * len(block_of[name])
            for g in range(0, n_tiles, 2):
                j = next_block(pe, name)
                for i in range(2):
                    b = take_bank(pe, (key, g + i))
                    for k in range(KT):
                        if ready is not None and g == 0 and i == 0:
                            for e in ready(k):
                                pe.wait_ge(*after(*e))
                        ins = nc.tensor.matmul(psum(b, 0, w), slot(j, k, 256, i * P, P), moving(k),
                                               start=(k == 0), stop=(k == KT - 1))
                    ins.then_inc(*pe.step(key, g + i))
                pe.mark("used", j)

        def take_out(q, key, tiles, place, segs, done, fn=None, then=None):
            for g in tiles:
                q.wait_ge(*after(key, g))
                b = bank_of((key, g))
                src = psum(b, 0, len(segs) * SEQ)
                if len(segs) == 2:
                    src = src.rearrange("p (s t) -> p s t", t=SEQ)
                if fn is not None:
                    ins = fn(g, place(g), src)
                elif q.name == "scalar":
                    ins = nc.scalar.activation(place(g), src, ACT.Copy)
                else:
                    ins = nc.vector.tensor_copy(place(g), src)
                ins.then_inc(*q.step("taken", key, g))
                if g == tiles[-1]:
                    q.mark(done, key)
                if then is not None:
                    then(g)

        def seg_of(segs):
            return slice(segs[0], segs[-1] + 1)

        def h_moving(segs):
            if len(segs) == 2:
                return lambda k: HT[:, :, k, :]
            return lambda k: HT[:, segs[0], k, :]

        def h_ready(key, segs):
            return lambda k: [("h", key, k, seg) for seg in segs]

        def y_place(segs):
            if len(segs) == 2:
                return lambda g: YT[:, :, g, :]
            return lambda g: YT[:, segs[0], g, :]


        S_W, T_W = 528, 640

        def att_places(base):
            return (area(base, 3, S_W), area(base + 3 * S_W, 2, T_W), area(base + 3 * S_W + 2 * T_W, 3, 12))

        def att_tensor(pe, A):
            pe.stage(A.name)

            def scores(u):
                for n, mms in enumerate(A.scores(u)):
                    b = take_bank(pe, (A.name, "scores", u, n))
                    for e in A.ready(u):
                        pe.wait_ge(*after(*e))
                    for (col, w, lhs, rhs) in mms:
                        ins = nc.tensor.matmul(psum(b, col, w), lhs, rhs, start=True, stop=True)
                    ins.then_inc(*pe.step(A.name, "scores", u, n))

            def transposes(u):
                S = att_places(A.base)[0]
                pe.wait_ge(*after(A.name, "weights", u))
                blocks = A.blocks(u)
                for n in range(0, len(blocks), 4):
                    b = take_bank(pe, (A.name, "turned", u, n // 4))
                    for i, (col, w) in enumerate(blocks[n:n + 4]):
                        ins = nc.tensor.transpose(psum(b, i * P, P, slice(0, w)), S[:, u % 3, col:col + w], cn("ident"))
                    ins.then_inc(*pe.step(A.name, "turned", u, n // 4))

            def values(u):
                T = att_places(A.base)[1]
                rows, vs = A.values(u)
                b = take_bank(pe, (A.name, "out", u))
                pe.wait_ge(*after(A.name, "T", u))
                for e in A.values_ready(u):
                    pe.wait_ge(*after(*e))
                for i, (v, (col, w)) in enumerate(zip(vs, A.blocks(u))):
                    ins = nc.tensor.matmul(psum(b, 0, P, rows), v, T[0:w, u % 2, i * P:(i + 1) * P],
                                           start=(i == 0), stop=(i == len(vs) - 1))
                ins.then_inc(*pe.step(A.name, "out", u))

            for i in range(A.n + 3):
                if i < A.n:
                    scores(i)
                if 0 <= i - 2 < A.n:
                    transposes(i - 2)
                if 0 <= i - 3 < A.n:
                    values(i - 3)

        def att_vector(v, A, between={}):
            v.stage(A.name)
            S, T, M = att_places(A.base)
            v.wait_ge(*after(*A.place_free))

            def maxima(u):
                s = S[:, u % 3, :]
                if u >= 3:
                    v.wait_ge(*after(A.name, "turned", u - 3, (len(A.blocks(u - 3)) - 1) // 4))
                for i, (n, col, dst, w, mask) in enumerate(A.pieces(u)):
                    v.wait_ge(*after(A.name, "scores", u, n))
                    b = bank_of((A.name, "scores", u, n))
                    if mask is None:
                        ins = nc.vector.tensor_scalar(s[:, dst:dst + w], psum(b, col, w), A.pre, None, ALU.mult)
                    else:
                        ins = nc.vector.scalar_tensor_tensor(s[:, dst:dst + w], psum(b, col, w), A.pre, mask,
                                                             ALU.mult, ALU.add)
                    ins.then_inc(*v.step())
                    if i == A.last_piece(u, n):
                        v.mark("taken", A.name, "scores", u, n)
                v.wait_ge(*v.own)
                maps = A.maps(u)
                for j, (c, w) in enumerate(maps):
                    nc.vector.tensor_reduce(M[:, u % 3, j:j + 1], s[:, c:c + w], AX.X, ALU.max).then_inc(*v.step())
                v.wait_ge(*v.own)
                k = len(maps)
                nc.vector.tensor_scalar(M[:, u % 3, 3:3 + k], M[:, u % 3, 0:k], -A.post, None, ALU.mult).then_inc(*v.step(A.name, "max", u))

            def weights(u):
                s = S[:, u % 3, :]
                maps = A.maps(u)
                k = len(maps)
                v.wait_ge(*after(A.name, "exp", u))
                nc.vector.reciprocal(M[:, u % 3, 9:9 + k], M[:, u % 3, 6:6 + k]).then_inc(*v.step())
                v.wait_ge(*v.own)
                if A.factor is not None:
                    f = A.factor(u)
                    nc.vector.tensor_tensor(M[:, u % 3, 9:9 + k], M[:, u % 3, 9:9 + k], f, ALU.mult).then_inc(*v.step())
                    v.wait_ge(*v.own)
                if A.subtract:
                    (c0, w), (c1, _) = maps
                    nc.vector.tensor_scalar(s[:, c0:c0 + w], s[:, c0:c0 + w], M[:, u % 3, 9:10], None, ALU.mult).then_inc(*v.step())
                    v.wait_ge(*v.own)
                    nc.vector.scalar_tensor_tensor(s[:, c0:c0 + w], s[:, c1:c1 + w], M[:, u % 3, 10:11],
                                                   s[:, c0:c0 + w], ALU.mult, ALU.add).then_inc(*v.step())
                else:
                    for j, (c, w) in enumerate(maps):
                        nc.vector.tensor_scalar(s[:, c:c + w], s[:, c:c + w], M[:, u % 3, 9 + j:10 + j], None,
                                                ALU.mult).then_inc(*v.step())
                v.mark(A.name, "weights", u)

            for i in range(A.n + 1):
                if i < A.n:
                    maxima(i)
                if i >= 1:
                    weights(i - 1)
                if i in between:
                    between[i]()

        def att_scalar(act, A):
            act.stage(A.name)
            load_table(act, ACT.Exp)
            S, T, M = att_places(A.base)

            def exps(u):
                act.wait_ge(*after(A.name, "max", u))
                for j, (c, w) in enumerate(A.maps(u)):
                    nc.scalar.activation(S[:, u % 3, c:c + w], S[:, u % 3, c:c + w], ACT.Exp,
                                         bias=M[:, u % 3, 3 + j:4 + j], scale=A.post,
                                         accum_out=M[:, u % 3, 6 + j:7 + j]).then_inc(*act.step())
                act.mark(A.name, "exp", u)

            def turned(u):
                blocks = A.blocks(u)
                if u >= 2:
                    act.wait_ge(*after(A.name, "out", u - 2))
                for n in range(0, len(blocks), 4):
                    act.wait_ge(*after(A.name, "turned", u, n // 4))
                    b = bank_of((A.name, "turned", u, n // 4))
                    part = blocks[n:n + 4]
                    full = [x for x in part if x[1] == P]
                    runs = [(i, 1, w) for i, (_, w) in enumerate(part) if w != P]
                    if full:
                        runs.append((part.index(full[0]), len(full), P))
                    for i, m, w in runs:
                        nc.scalar.activation(T[0:w, u % 2, (n + i) * P:(n + i + m) * P],
                                             psum(b, i * P, m * P, slice(0, w)), ACT.Copy).then_inc(*act.step())
                    act.mark("taken", A.name, "turned", u, n // 4)
                act.mark(A.name, "T", u)

            def out(u):
                act.wait_ge(*after(A.name, "out", u))
                rows, _ = A.values(u)
                nc.scalar.activation(A.place(u), psum(bank_of((A.name, "out", u)), 0, P, rows), ACT.Copy).then_inc(*act.step("taken", A.name, "out", u))

            for i in range(A.n + 3):
                if i < A.n:
                    exps(i)
                if 0 <= i - 2 < A.n:
                    turned(i - 2)
                if 0 <= i - 3 < A.n:
                    out(i - 3)
            act.mark(A.name, "done")

        class Attention:
            factor = None
            subtract = False
            pre, post = 1.0, HD ** -0.5
            place_free = ("consts",)

            def last_piece(self, u, n):
                return max(i for i, p in enumerate(self.pieces(u)) if p[0] == n)

            def ready(self, u):
                return ()

            def values_ready(self, u):
                return ()

        def half(h):
            return slice(HD * (h % 2), HD * (h % 2) + HD)

        QA = area(FREE, 4, 512)
        KA = area(FREE + 2048, 4, 512)
        VA = area(FREE + 4096, 4, 512)
        UP = area(FREE + 6144, 4, 2, 288)
        PW = area(FREE + 8448, 4, P)
        PINV = area(FREE + 8960, 4, SEQ)
        PD = area(FREE + 9984, 4, 2, SEQ)
        PT3 = area(FREE + 12032, 3, 2, 288)
        ATT_A = FREE + 13760
        CAT = SQ
        BIAS = area(8192, 8, 2, SEQ)
        assert ATT_A + 3 * S_W + 2 * T_W + 36 <= SMALL

        def loads_pool(g):
            g.stage("load")
            g.eng.dma_start(PR[:, :], params).then_inc(*g.step("params", by=16, sem="params_loaded"))
            g.eng.dma_start(XT[:, :, :, :].rearrange("p a b c -> p (a b c)"), x_t).then_inc(*g.step("x0", by=16, sem="x_loaded"))
            g.eng.dma_start(CN[:, :], consts).then_inc(*g.step("consts", by=16, sem="consts_loaded"))
            g.wait_ge(*after("used", FIRST_MODS - 1))
            g.eng.dma_start(area(8192, 4096), bias).then_inc(*g.step("bias", by=16, sem="bias_loaded"))
            g.eng.dma_start(PW.rearrange("p a b -> p (a b)"), small[:, 6144:6656]).then_inc(*g.step("pool_w", by=16, sem="pool_w_loaded"))
            g.eng.dma_start(PINV.rearrange("p a b -> p (a b)"), pool_inv).then_inc(*g.step("pool_inv", by=16, sem="pool_inverse_loaded"))

        def load_low_rank(g):
            g.stage("load")
            g.wait_ge(*after("x02_part", 3, KT - 1))
            g.eng.dma_start(area(SMALL, 5120), small[:, 0:5120]).then_inc(*g.step("small", by=16, sem="small_loaded"))
            nc.gpsimd.memset(HW, 0.0).then_inc(*g.step())
            nc.gpsimd.memset(HA, 0.0).then_inc(*g.step("low_zeros"))
            g.wait_ge(*after("a_raw", 7, 1))
            g.eng.dma_start(LOW["g2"], small[:, 5120:6144]).then_inc(*g.step("gate_w2", by=16, sem="gate_w2_loaded"))

        def pool_pool(g):
            g.stage("pooling")
            nc.gpsimd.memset(UP, 0.0).then_inc(*g.step("pads"))
            g.wait_ge(*after("taken_all", "ev_in"))
            g.wait_ge(*after("taken_all2", "ev_in"))
            g.wait_ge(*after("pool_inv"))
            for gi in range(4):
                u = UP[:, gi]
                src, shifts = u, []
                for lv in range(gi + 1):
                    dst = PT3[:, lv % 2]
                    up, down = (0, 1) if lv == 0 else (1 << (lv - 1), 1 << (lv - 1))
                    lo, hi = 1 << lv, 288 - (1 << lv)
                    g.wait_ge(*g.own)
                    nc.gpsimd.tensor_tensor(dst[:, :, lo:hi], src[:, :, lo + up:hi + up],
                                            src[:, :, lo - down:hi - down], ALU.add).then_inc(*g.step())
                    src = dst
                g.wait_ge(*g.own)
                inv = PINV[:, gi].unsqueeze(1).to_broadcast([P, 2, SEQ])
                nc.gpsimd.tensor_tensor(PD[:, gi], src[:, :, 16:272], inv, ALU.mult).then_inc(*g.step())
                g.wait_ge(*g.own)
                nc.gpsimd.tensor_tensor(PD[:, gi], PD[:, gi], u[:, :, 16:272], ALU.subtract).then_inc(*g.step("pooled", gi))

        def pool_tensor(pe):
            pe.stage("pooling")
            pe.wait_ge(*after("pool_w"))
            for gi in range(4):
                b = take_bank(pe, ("pool", gi))
                pe.wait_ge(*after("pooled", gi))
                ins = nc.tensor.matmul(psum(b), PW[:, gi], PD[:, gi], start=True, stop=True)
                ins.then_inc(*pe.step("pool", gi))

        def pool_scalar(act):
            act.stage("pooling")
            for gi in range(4):
                act.wait_ge(*after("pool", gi))
                b = bank_of(("pool", gi))
                nc.scalar.activation(CAT[:, :, gi, :], psum(b).rearrange("p (s t) -> p s t", t=SEQ), ACT.Copy,
                                     scale=pr("pool_scale", gi, 1)).then_inc(*act.step("taken", "pool", gi))
            act.mark("pool_done")

        def ev_in_tensor(pe):
            project_tensor_n(pe, "ev_in", "ev_in", 6, h_moving([0, 1]), h_ready("n1_0", [0, 1]), [0, 1])
            values_natural(pe, "ev_in", "ev_v", 2, 4, 256)
            side_blocks(pe, block_of["ev_out"][0], 0)

        def project_tensor_n(pe, key, name, blocks, moving, ready, segs):
            pe.stage("project_" + key)
            w = len(segs) * SEQ
            for g in range(0, 2 * blocks, 2):
                j = next_block(pe, name)
                for i in range(2):
                    b = take_bank(pe, (key, g + i))
                    for k in range(KT):
                        if g == 0 and i == 0 and ready:
                            for e in ready(k):
                                pe.wait_ge(*after(*e))
                        ins = nc.tensor.matmul(psum(b, 0, w), slot(j, k, 256, i * P, P), moving(k),
                                               start=(k == 0), stop=(k == KT - 1))
                    ins.then_inc(*pe.step(key, g + i))
                pe.mark("used", j)

        def values_natural(pe, name, key, blocks, n_tok, width, segs=(0, 1)):
            for jj in range(blocks):
                j = next_block(pe, name)
                for seg in range(n_tok // 2):
                    b = take_bank(pe, (key, jj, seg))
                    for half_ in range(2):
                        for k in range(KT):
                            s = segs[seg]
                            ins = nc.tensor.matmul(psum(b, half_ * 256, 256), HT[:, s, k, half_ * P:(half_ + 1) * P],
                                                   slot(j, k, 256), start=(k == 0), stop=(k == KT - 1))
                    ins.then_inc(*pe.step(key, jj, seg))
                pe.mark("used", j)

        def take_values(q, key, blocks, n_tok, place, shares, copy):
            for jj in range(blocks):
                for seg in range(n_tok // 2):
                    if (jj * (n_tok // 2) + seg) % 2 != shares:
                        continue
                    q.wait_ge(*after(key, jj, seg))
                    b = bank_of((key, jj, seg))
                    copy(place(jj, seg), psum(b).rearrange("p (t c) -> p t c", c=256)).then_inc(*q.step("taken", key, jj, seg))
            q.mark(key + "_out", shares)

        act_copy = lambda o, i: nc.scalar.activation(o, i, ACT.Copy)
        dve_copy = lambda o, i: nc.vector.tensor_copy(o, i)

        def ev_place(g):
            if g < 4:
                return UP[:, g, :, 16:272]
            dst = QA[:, g - 4] if g < 8 else KA[:, g - 8]
            return dst.rearrange("p (s t) -> p s t", t=SEQ)

        def ev_out_of(q, share, copy):
            q.stage("project_ev_in")
            q.wait_ge(*after("pads"))
            for g in range(share, 12, 2):
                if share == 1:
                    side_chains(q, block_of["ev_in"][g // 2])
                q.wait_ge(*after("ev_in", g))
                copy(ev_place(g), psum(bank_of(("ev_in", g))).rearrange("p (s t) -> p s t", t=SEQ)).then_inc(*q.step("taken", "ev_in", g))
                if g == 2 + share:
                    q.mark("taken_all" if share == 0 else "taken_all2", "ev_in")
            q.mark("qk_out", share)
            if share == 1:
                side_chains(q, block_of["ev_out"][0])
            take_values(q, "ev_v", 2, 4, lambda jj, seg: VA[:, 2 * seg:2 * seg + 2, jj * 256:(jj + 1) * 256], share, copy)

        class LatentAttention(Attention):
            name, n, base = "latent_attention", 16, ATT_A
            pre, post = HD ** -0.5, 1.0
            place_free = ("bias",)

            def ready(self, u):
                return (("qk_out", 0), ("qk_out", 1))

            def values_ready(self, u):
                return (("ev_v_out", 0), ("ev_v_out", 1))

            def scores(self, u):
                h, qt = divmod(u, 2)
                r = half(h)
                return [[(0, 512, QA[r, h // 2, 256 + qt * P:256 + (qt + 1) * P], KA[r, h // 2, :])]]

            def pieces(self, u):
                h, qt = divmod(u, 2)
                return [(0, 0, 0, 256, None), (0, 256, 256, 256, BIAS[:, h, qt, :])]

            def maps(self, u):
                return [(0, 512)]

            def blocks(self, u):
                return [(i * P, P) for i in range(4)]

            def values(self, u):
                h = u // 2
                return half(h), [VA[:, i, h * HD:(h + 1) * HD] for i in range(4)]

            def place(self, u):
                h, qt = divmod(u, 2)
                return CAT[half(h), X, 4 + h // 2, qt * P:(qt + 1) * P]

        class ContextAttention(LatentAttention):
            name = "context_attention"

            def scores(self, u):
                h, qt = divmod(u, 2)
                r = half(h)
                return [[(0, 256, QA[r, h // 2, qt * P:(qt + 1) * P], KA[r, h // 2, 0:256])]]

            def pieces(self, u):
                return [(0, 0, 0, 256, None)]

            def maps(self, u):
                return [(0, 256)]

            def blocks(self, u):
                return [(i * P, P) for i in range(2)]

            def values(self, u):
                h = u // 2
                return half(h), [VA[:, i, h * HD:(h + 1) * HD] for i in range(2)]

            def place(self, u):
                h, qt = divmod(u, 2)
                return CAT[half(h), CTX, 4 + h // 2, qt * P:(qt + 1) * P]
            place_free = ("latent_attention", "done")

        LAT, CON = LatentAttention(), ContextAttention()

        H8 = area(25088, KT, 2 * SEQ)
        H8_HI = rounded("quarter_high", 20992, KT, 2 * SEQ)
        H8_LO = rounded("quarter_low", 25088, KT, 2 * SEQ)
        MLP0 = Splits("mlp0", ["mlp1_0", "mlp2_0"], [(29184, 31232), (33280, 35328), (14336, 37376)])

        def mlp0_tensor(pe):
            for q in range(4):
                pe.stage(f"mlp_up{q}")
                for c in range(4):
                    j = MLP0.next(pe, "mlp1_0")
                    for i in range(2):
                        f = 8 * q + 2 * c + i
                        b = take_bank(pe, ("x02_up", f))
                        ins = MLP0.columns(pe, j, 256, i * P, psum(b), KT, lambda k: XHI2[:, :, k, :],
                                           lambda k: XLO2[:, :, k, :], norm="n2_0")
                        ins.then_inc(*pe.step("x02_up", f))
                    pe.mark("multiplied", j)
                pe.stage(f"mlp_down{q}")
                for c in range(4):
                    j = MLP0.next(pe, "mlp2_0")
                    pe.wait_ge(*after("hidden", "x02", 8 * q + 7))
                    for i in range(2):
                        g = 2 * c + i
                        b = take_bank(pe, ("x02_part", q, g))
                        ins = MLP0.columns(pe, j, 256, i * P, psum(b), KT, lambda k: H8_HI[:, k], lambda k: H8_LO[:, k])
                        ins.then_inc(*pe.step("x02_part", q, g))
                    pe.mark("multiplied", j)
                if q == 1:
                    side_blocks(pe, block_of["mlp1_0"][8], 0)
            side_blocks(pe, block_of["wr"][0], 0)

        def mlp0_scalar(act):
            act.stage("mlp0")
            for n in range(32):
                q, r = divmod(n, 8)
                MLP0.high(act, n + MLP0.ahead)
                if r < 4:
                    tiles = (8 * q + 2 * r, 8 * q + 2 * r + 1)
                    for f in tiles:
                        act.wait_ge(*after("x02_up", f))
                        if q:
                            act.wait_ge(*after("x02_part", q - 1, KT - 1))
                        nc.scalar.activation(H8[:, f % 8], psum(bank_of(("x02_up", f))), ACT.Relu).then_inc(*act.step("taken", "x02_up", f))
                    for f in tiles:
                        act.wait_ge(*after("taken", "x02_up", f))
                        nc.scalar.activation(H8[:, f % 8], H8[:, f % 8], ACT.Square).then_inc(*act.step("squared", f))
                    for f in tiles:
                        act.wait_ge(*after("squared", f))
                        nc.scalar.activation(H8_HI[:, f % 8], H8[:, f % 8], ACT.Copy).then_inc(*act.step("quarter_high", f))
                elif q == 0:
                    for g in (2 * r - 8, 2 * r - 7):
                        act.wait_ge(*after("x02_part", q, g))
                        nc.scalar.activation(YT[:, :, g, :], two(psum(bank_of(("x02_part", q, g)))), ACT.Copy).then_inc(*act.step("taken", "x02_part", q, g))

        def two(x):
            return x.rearrange("p (s t) -> p s t", t=SEQ)

        def mlp0_vector(v):
            v.stage("mlp0")
            for n in range(32):
                q, r = divmod(n, 8)
                MLP0.low(v, n + MLP0.ahead)
                if r < 4:
                    for f in (8 * q + 2 * r, 8 * q + 2 * r + 1):
                        v.wait_ge(*after("quarter_high", f))
                        nc.vector.tensor_tensor(H8_LO[:, f % 8], H8[:, f % 8], H8_HI[:, f % 8], ALU.subtract).then_inc(*v.step("hidden", "x02", f))
                elif q:
                    for g in (2 * r - 8, 2 * r - 7):
                        v.wait_ge(*after("x02_part", q, g))
                        v.wait_ge(*after("taken", "x02_part", q - 1, g))
                        y = YT[:, :, g, :]
                        nc.vector.tensor_tensor(y, y, two(psum(bank_of(("x02_part", q, g)))), ALU.add).then_inc(*v.step("taken", "x02_part", q, g))
                if n == 15:
                    mod_vectors(v, 1)
                    v.stage("mlp0b")
            v.mark("y_all", "x02_down")
            v.mark("y_all2", "x02_down")
            side_chains(v, block_of["wr"][0])

        HID_HI = rounded("hidden_high", FREE, 32, SEQ)
        HID_LO = rounded("hidden_low", FREE + 8192, 32, SEQ)
        RELU, RELU2 = area(14336, 3, SEQ), area(14336 + 3 * SEQ, 3, SEQ)
        MLP = Splits("mlp", ["mlp1_1", "mlp2_1"], [(33280, 35328), (37376, 8192)])

        def mlp_split_tensor(pe):
            pe.stage("mlp_up")
            for g in range(0, 32, 2):
                j = MLP.next(pe, "mlp1_1")
                for i in range(2):
                    b = take_bank(pe, ("x12_up", g + i))
                    ins = MLP.columns(pe, j, 256, i * P, psum(b, 0, SEQ), KT, x_high, x_low, norm="n2_1")
                    ins.then_inc(*pe.step("x12_up", g + i))
                pe.mark("multiplied", j)
            pe.stage("mlp_down")
            for g in range(KT):
                b = take_bank(pe, ("x12_down", g))
                for part in range(2):
                    j = MLP.next(pe, "mlp2_1")
                    pe.wait_ge(*after("hidden", "x12", 16 * part + 15))
                    ins = MLP.columns(pe, j, P, 0, psum(b, 0, SEQ), 16, lambda k: HID_HI[:, part * 16 + k],
                                      lambda k: HID_LO[:, part * 16 + k], start=part == 0, stop=part == 1)
                    ins.then_inc(*pe.step())
                    pe.mark("multiplied", j)
                pe.mark("x12_down", g)
            side_blocks(pe, block_of["ev2_in"][0], 0)

        def mlp_split_scalar(act):
            act.stage("mlp_up")
            for i in range(16):
                MLP.high(act, i + MLP.ahead)
                for f in (2 * i, 2 * i + 1):
                    act.wait_ge(*after("x12_up", f))
                    nc.scalar.activation(RELU[:, f % 3], psum(bank_of(("x12_up", f)), 0, SEQ), ACT.Relu).then_inc(*act.step("taken", "x12_up", f))
                for f in (2 * i, 2 * i + 1):
                    act.wait_ge(*after("taken", "x12_up", f))
                    if f >= 3:
                        act.wait_ge(*after("hidden", "x12", f - 3))
                    nc.scalar.activation(RELU2[:, f % 3], RELU[:, f % 3], ACT.Square).then_inc(*act.step("relu2", f))
                for f in (2 * i, 2 * i + 1):
                    act.wait_ge(*after("relu2", f))
                    nc.scalar.activation(HID_HI[:, f], RELU2[:, f % 3], ACT.Copy).then_inc(*act.step("hidden_high", f))
            act.stage("mlp_down")
            for i in range(16):
                MLP.high(act, 16 + i + MLP.ahead)
                if i % 4 == 1:
                    take_out(act, "x12_down", [i // 2], y_place(ONE), ONE, "y_all" if i == 13 else f"y_tile{i // 2}")

        def mlp_split_vector(v):
            v.stage("mlp_up")
            for i in range(16):
                MLP.low(v, i + MLP.ahead)
                for f in (2 * i, 2 * i + 1):
                    v.wait_ge(*after("hidden_high", f))
                    nc.vector.tensor_tensor(HID_LO[:, f], RELU2[:, f % 3], HID_HI[:, f], ALU.subtract).then_inc(*v.step("hidden", "x12", f))
            v.stage("mlp_down")
            for i in range(16):
                MLP.low(v, 16 + i + MLP.ahead)
                if i % 4 == 3:
                    take_out(v, "x12_down", [i // 2], y_place(ONE), ONE, "y_all2" if i == 15 else f"y_tile{i // 2}")
            side_chains(v, block_of["ev2_in"][0])

        RR = area(0, KT, SEQ)
        XX = area(8192, 2, KT, SEQ)
        MIX = [area(12288, 2, KT, SEQ), area(16896, 2, KT, SEQ)]
        KK = area(16896, KT, 512)
        KR = area(20992, KT, 512)
        VP = area(25088, 8, PAIRS, HD)
        HW, HA = area(29184, 8, 2, CHUNK), area(SMALL + 5120, 8, 2, CHUNK)
        GH = area(16384, SEQ)
        LOW = {n: area(SMALL + 1024 * i, D) for i, n in enumerate(("w1", "a1", "g1", "w2", "a2", "g2"))}
        MIX_ORDER = [("r", 0, [X]), ("k", 2, [CTX, X]), ("w", 1, [CTX, X]), ("a", 4, [CTX, X]), ("v", 3, [CTX, X]),
                     ("g", 5, [X])]
        MIX_END = {"r": ("wr", 7), "k": ("wk", 7), "v": ("wv", 3, 1), "w": ("low_w",), "a": ("low_a",)}

        def mixes_vector(v):
            v.stage("mixes")

            def shifted(seg):
                v.wait_ge(*after("h", "n1_1", KT - 1, seg))
                H, S = HT[:, seg], XX[:, seg]
                nc.vector.tensor_tensor(S[:, :, 1:255], H[:, :, 0:254], H[:, :, 2:256], ALU.add).then_inc(*v.step())
                nc.vector.tensor_copy(S[:, :, 0:1], H[:, :, 1:2]).then_inc(*v.step())
                nc.vector.tensor_copy(S[:, :, 255:256], H[:, :, 254:255]).then_inc(*v.step())
                v.wait_ge(*v.own)
                nc.vector.scalar_tensor_tensor(S, S, 0.5, H, ALU.mult, ALU.subtract).then_inc(*v.step())
                v.wait_ge(*v.own)

            shifted(X)
            for i, (n, mu, segs) in enumerate(MIX_ORDER):
                if i >= 2:
                    v.wait_ge(*after(*MIX_END[MIX_ORDER[i - 2][0]]))
                sg = seg_of(segs)
                for k in range(KT):
                    nc.vector.scalar_tensor_tensor(MIX[i % 2][:, sg, k, :], XX[:, sg, k, :],
                                                   pr("mu", mu * KT + k, 1), HT[:, sg, k, :], ALU.mult, ALU.add).then_inc(*v.step("mix", n, k))
                if n == "r":
                    shifted(CTX)
                if n == "k":
                    rw_out(v, "wr", 1, dve_copy)
                if n == "w":
                    rw_out(v, "wk", 1, dve_copy)
            rwv_out(v, 1, dve_copy, lambda jj: kk_root_vector(v, kk_tiles(jj)) if jj < 3 else removal_key_vector(v))

        def rw_out(q, name, share, copy):
            q.stage("project_" + name)
            for g in range(share, KT, 2):
                q.wait_ge(*after(name, g))
                w = SEQ if name == "wr" else 512
                dst = RR[:, g] if name == "wr" else KR[:, g]
                copy(dst, psum(bank_of((name, g)), 0, w)).then_inc(*q.step("taken", name, g))
                q.mark(name + "_out", g)
            q.mark(name + "_out_all", share)

        def rwv_out(q, share, copy, then):
            for jj in range(4):
                q.stage("project_wv")
                seg = share
                q.wait_ge(*after("wv", jj, seg))
                b = bank_of(("wv", jj, seg))
                copy(VP[:, 4 * seg:4 * seg + 4, 2 * jj:2 * jj + 2, :].rearrange("p c a i -> p c (a i)"),
                     psum(b).rearrange("p (c n) -> p c n", n=P)).then_inc(*q.step("taken", "wv", jj, seg))
                if jj == 3:
                    q.mark("wv_out", share)
                q.stage("removal_key")
                then(jj)

        def root_of(t):
            return area(30208 + 512 * t, 512) if t < KT - 1 else area(8192, 512)

        def kk_tiles(jj):
            return list(range(3 * jj, min(3 * jj + 3, KT)))

        def features_tensor(pe):
            mv = lambda i, segs: (lambda k: MIX[i % 2][:, seg_of(segs), k, :])
            project_tensor(pe, "wr", "wr", lambda k: MIX[0][:, X, k, :], lambda k: [("mix", "r", k)], [X], "project_wr")
            project_tensor(pe, "wk", "wk", mv(1, [0, 1]), lambda k: [("mix", "k", k)], [CTX, X], "project_wk")
            def low_rank(n, w, mix, segs):
                pe.stage("low_rank")
                pe.wait_ge(*after("small"))
                b = take_bank(pe, ("low_" + n,))
                for k in range(KT):
                    pe.wait_ge(*after("mix", n, k))
                    ins = nc.tensor.matmul(psum(b, 0, len(segs) * SEQ), LOW[w][:, k * P:(k + 1) * P],
                                           MIX[mix][:, seg_of(segs), k, :], start=(k == 0), stop=(k == KT - 1))
                ins.then_inc(*pe.step("low_" + n))

            low_rank("w", "w1", 0, [CTX, X])
            low_rank("a", "a1", 1, [CTX, X])
            pe.stage("project_wv")

            def kk_sum(t):
                b = take_bank(pe, ("kk_sum", t))
                pe.wait_ge(*after("kk_squares", t))
                nc.tensor.matmul(psum(b), cn("block_ones"), root_of(t), start=True, stop=True).then_inc(*pe.step("kk_sum", t))

            pe.wait_ge(*after("mix", "v", KT - 1))
            for jj in range(4):
                j = next_block(pe, "wv")
                for seg in range(2):
                    b = take_bank(pe, ("wv", jj, seg))
                    for c in range(N_CHUNK):
                        for odd in range(2):
                            for k in range(KT):
                                rhs = slot(j, k, 256).rearrange("p (a o i) -> p a o i", o=2, i=HD)[:, :, odd, :]
                                ins = nc.tensor.matmul(psum(b, c * P, P, half(odd)),
                                                       MIX[0][:, seg, k, c * CHUNK:(c + 1) * CHUNK], rhs,
                                                       start=(k == 0), stop=(k == KT - 1))
                    ins.then_inc(*pe.step("wv", jj, seg))
                pe.mark("used", j)
                for t in kk_tiles(jj):
                    kk_sum(t)
                if jj == 0:
                    low_rank("g", "g1", 1, [X])
                    pe.stage("project_wv")

        def features_scalar(act):
            def squares(tiles):
                for t in tiles:
                    act.wait_ge(*after("wk_out", t))
                    nc.scalar.activation(root_of(t), KR[:, t], ACT.Square, scale=pr("kk", t, 1)).then_inc(*act.step("kk_squares", t))

            def roots(tiles):
                for t in tiles:
                    act.wait_ge(*after("taken", "kk_sum", t))
                    nc.scalar.activation(root_of(t), root_of(t), ACT.Sqrt).then_inc(*act.step("kk_root", t))

            rw_out(act, "wr", 0, act_copy)
            rw_out(act, "wk", 0, act_copy)
            act.stage("low_rank")
            act.wait_ge(*after("low_zeros"))
            for n, fn, dst in (("w", ACT.Tanh, HW), ("a", ACT.Copy, HA)):
                act.wait_ge(*after("low_" + n))
                src = psum(bank_of(("low_" + n,))).rearrange("p (a b) -> p a b", b=CHUNK)
                nc.scalar.activation(dst[half(0), :, 0, :], src[half(0)], fn).then_inc(*act.step())
                for c in range(8):
                    nc.scalar.activation(dst[half(1), c, 1, :], src[half(1), place_of(c, 1)], fn).then_inc(*act.step())
                act.mark("taken", "low_" + n)
            act.stage("removal_key")
            squares(range(KT - 1))
            act.wait_ge(*after("mix", "g", KT - 1))
            squares([KT - 1])

            def after_block(jj):
                roots(kk_tiles(jj))
                if jj == 0:
                    act.wait_ge(*after("low_g"))
                    nc.scalar.activation(GH, psum(bank_of(("low_g",)), 0, SEQ), ACT.Sigmoid).then_inc(*act.step("taken", "low_g"))
            rwv_out(act, 0, act_copy, after_block)

        def kk_root_vector(v, tiles):
            for t in tiles:
                v.wait_ge(*after("kk_sum", t))
                nc.vector.tensor_scalar(root_of(t), psum(bank_of(("kk_sum", t))), 1e-24, None, ALU.max).then_inc(*v.step("taken", "kk_sum", t))
            for t in tiles:
                v.wait_ge(*after("kk_root", t))
                nc.vector.reciprocal(root_of(t), root_of(t)).then_inc(*v.step())

        def removal_key_vector(v):
            v.wait_ge(*after("low_g"))
            v.wait_ge(*v.own)
            for t in range(KT):
                nc.vector.scalar_tensor_tensor(KK[:, t], KR[:, t], pr("kk", t, 1), root_of(t),
                                               ALU.mult, ALU.mult).then_inc(*v.step())
            v.mark("features")
            v.wait_ge(*v.own)

        DECAY = float(np.exp(-0.5))
        at = 4096
        WK = {}
        for n, dims in (("Y", (PAIRS, SEQ)), ("KS", (PAIRS, SEQ)), ("AR", (2, PAIRS, 128)), ("BM", (2, PAIRS, 128)),
                        ("GM", (2, PAIRS, 128)), ("B", (2, PAIRS, 64)), ("G", (2, PAIRS, 64))):
            WK[n] = area(at, *dims)
            at += int(np.prod(dims))
        assert at <= 16384, at
        at = 30208
        for n in ("E", "A", "L", "BN", "C", "S"):
            WK[n] = area(at, 2, PAIRS, 64)
            at += 1024
        assert at <= SMALL + 3072, at
        DEND = ctx.enter_context(nc.sbuf_tensor("decay_end", [P, 32], FP32))[:, :].rearrange("p (c d a) -> p c d a", c=2, d=2)
        WK["X"], WK["XI"], WK["Z"], WK["U"], WK["GN"] = WK["E"], WK["A"], WK["L"], WK["B"], WK["C"]

        def place_of(c, d):
            if d == 0:
                return c
            return 3 - c if c < 4 else 11 - c

        def flat(v):
            return v.rearrange("p a b -> p (a b)")

        def bank3(key, w=64):
            return psum(bank_of(key)).rearrange("p (a b) -> p a b", b=w)

        def pairs_matmul(pe, key, terms, width=64, pairs=range(PAIRS), ready=()):
            b = take_bank(pe, key)
            for e in ready:
                pe.wait_ge(*after(*e))
            for n, p in enumerate(pairs):
                for h in range(2):
                    r = half(h)
                    ts = terms(p, r)
                    for i, (lhs, rhs) in enumerate(ts):
                        ins = nc.tensor.matmul(psum(b, n * width, width, r), lhs, rhs, start=(i == 0),
                                               stop=(i == len(ts) - 1))
            ins.then_inc(*pe.step(*key))

        def pairs_turned(pe, key, src, ready=()):
            for part in range(2):
                b = take_bank(pe, key + (part,))
                for e in ready:
                    pe.wait_ge(*after(*e))
                for n in range(4):
                    ins = nc.tensor.transpose(psum(b, n * P, P, slice(0, 64)), src[:, 4 * part + n, :], cn("ident"))
                ins.then_inc(*pe.step(*key, part))

        def turned_out(act, key, dst):
            for part in range(2):
                act.wait_ge(*after(*key, part))
                src = psum(bank_of(key + (part,)), 0, 512, slice(0, 64)).rearrange("p (a h i) -> p a h i", h=2, i=64)
                for h in range(2):
                    nc.scalar.activation(dst[half(h), 4 * part:4 * part + 4, :], src[:, :, h, :], ACT.Copy).then_inc(
                        *act.step())
                act.mark("taken", *key, part)

        TURNS = [("b", 0), ("g", 0), ("b", 1), ("g", 1)]

        def wkv_tensor(pe):
            pe.stage("recurrence")
            pe.wait_ge(*after("taken", "low_a"))
            pe.wait_ge(*after("taken", "low_w"))
            def raws(c):
                for n, low, hid in (("w_raw", "w2", HW), ("a_raw", "a2", HA)):
                    for part in range(2):
                        b = take_bank(pe, (n, c, part))
                        for i in range(4):
                            p = 4 * part + i
                            ins = nc.tensor.matmul(psum(b, i * P, P), LOW[low][:, p * P:(p + 1) * P],
                                                   hid[:, c].rearrange("p a b -> p (a b)"), start=True, stop=True)
                        ins.then_inc(*pe.step(n, c, part))

            raws(0)
            for c in range(8):
                main = c >= 4
                for d in range(2):
                    B, G, AR = WK["B"][:, d], WK["G"][:, d], WK["AR"][:, d]
                    w = 128 if main else 64
                    for part in range(2):
                        ps_ = range(4 * part, 4 * part + 4)
                        pairs_matmul(pe, ("bm", c, d, part), lambda p, r: [(B[r, p, :], AR[r, p, 0:w])], w if main else 64,
                                     ps_, [("beta", c, d), ("rho", c, d)])
                    for part in range(2):
                        ps_ = range(4 * part, 4 * part + 4)
                        pairs_matmul(pe, ("gm", c, d, part), lambda p, r: [(G[r, p, :], AR[r, p, 0:w])], w if main else 64,
                                     ps_, [("gamma", c, d)])
                for d in range(2):
                    pairs_turned(pe, ("x", c, d, 0), WK["XI"][:, d], [("inverse_t", c, d, 0)])
                for lv in range(1, LEVELS):
                    for d in range(2):
                        Xm, XI, BM = WK["X"][:, d], WK["XI"][:, d], WK["BM"][:, d]
                        pairs_matmul(pe, ("z", c, d, lv), lambda p, r: [(BM[r, p, 0:64], Xm[r, p, :])],
                                     ready=[("inverse", c, d, lv - 1), ("bm_out", c, d)])
                    for d in range(2):
                        XI, Z = WK["XI"][:, d], WK["Z"][:, d]
                        pairs_matmul(pe, ("dxi", c, d, lv), lambda p, r: [(Z[r, p, :], XI[r, p, :])],
                                     ready=[("z_out", c, d, lv), ("inverse_t", c, d, lv - 1)])
                    for d in range(2):
                        if lv < LEVELS - 1:
                            pairs_turned(pe, ("x", c, d, lv), WK["XI"][:, d], [("inverse_t", c, d, lv)])
                    if lv < 5 and c < 7:
                        n, d = TURNS[lv - 1]
                        pairs_turned(pe, (n + "n", c, d), WK[n.upper()][:, d])
                for d in range(2):
                    AR, GM, S, cc = WK["AR"][:, d], WK["GM"][:, d], WK["S"][:, d], place_of(c, d)
                    pairs_matmul(pe, ("w", c, d),
                                 lambda p, r: ([(AR[r, p, 0:64], S[r, p, :])] if c else [])
                                 + [(GM[r, p, 0:64], VP[r, cc, p, :])],
                                 ready=[("gm_out", c, d), ("wv_out", 0), ("wv_out", 1)] + ([("state", c - 1, d)] if c else []))
                for d in range(2):
                    XI, W = WK["XI"][:, d], WK["Z"][:, d]
                    pairs_matmul(pe, ("u", c, d), lambda p, r: [(XI[r, p, :], W[r, p, :])],
                                 ready=[("w_out", c, d), ("inverse_t", c, d, LEVELS - 1)])
                if c < 7:
                    raws(c + 1)
                for d in range(2):
                    AR, BM, GM, S, U = (WK[n][:, d] for n in ("AR", "BM", "GM", "S", "U"))
                    BN, GN, cc = WK["BN"][:, d], WK["GN"][:, d], place_of(c, d)
                    if c < 7:
                        pairs_matmul(pe, ("s", c, d),
                                     lambda p, r: [(BN[r, p, :], U[r, p, :]), (GN[r, p, :], VP[r, cc, p, :])],
                                     ready=[("u_out", c, d), ("bn_out", c, d), ("gn_out", c, d)])
                    if main:
                        pairs_matmul(pe, ("y", c, d), lambda p, r: [(S[r, p, :], AR[r, p, 64:128]),
                                                                    (U[r, p, :], BM[r, p, 64:128]),
                                                                    (VP[r, cc, p, :], GM[r, p, 64:128])],
                                     ready=[("u_out", c, d)])

        def wkv_scalar(act):
            act.stage("recurrence")
            for c in range(8):
                main = c >= 4
                load_table(act, ACT.Sigmoid)
                for d in range(2):
                    E, A, L, C = (WK[n][:, d] for n in ("E", "A", "L", "C"))
                    for n, buf in (("w_in", L), ("a_in", A)):
                        act.wait_ge(*after(n, c))
                        nc.scalar.activation(flat(buf), flat(buf), ACT.Sigmoid).then_inc(*act.step(n + "_sig", c, d))
                load_table(act, ACT.Exp)
                for d in range(2):
                    E, A, L, C = (WK[n][:, d] for n in ("E", "A", "L", "C"))
                    act.wait_ge(*after("running", c, d))
                    nc.scalar.activation(DEND[:, c % 2, d], C[:, :, 63] if d == 0 else C[:, :, 0], ACT.Exp,
                                         scale=-DECAY).then_inc(*act.step("decay_end", c, d))
                    nc.scalar.activation(flat(E), flat(E), ACT.Exp, scale=-DECAY).then_inc(*act.step("before", c, d))
                    nc.scalar.activation(flat(L), flat(C), ACT.Exp, scale=DECAY).then_inc(*act.step("inverse_decay", c, d))
                    if main:
                        act.wait_ge(*act.own)
                        nc.scalar.activation(flat(C), flat(C), ACT.Exp, scale=-DECAY).then_inc(*act.step("decay", c, d))
                for lv in range(LEVELS - 1):
                    for d in range(2):
                        turned_out(act, ("x", c, d, lv), WK["X"][:, d])
                        act.mark("inverse", c, d, lv)
                    if lv >= 1 and c < 7:
                        n, d = TURNS[lv - 1]
                        turned_out(act, (n + "n", c, d), WK[n.upper() + "N"][:, d])
                        act.mark(n + "n_out", c, d)
                for n, dst in (("w", "Z"), ("u", "U")):
                    for d in range(2):
                        act.wait_ge(*after(n, c, d))
                        nc.scalar.activation(WK[dst][:, d], bank3((n, c, d)), ACT.Copy).then_inc(*act.step("taken", n, c, d))
                        act.mark(n + "_out", c, d)

        def wkv_vector(v):
            v.stage("recurrence")
            mul, add, sub = ALU.mult, ALU.add, ALU.subtract
            tt, stt = nc.vector.tensor_tensor, nc.vector.scalar_tensor_tensor

            def over_steps(name, d=0):
                return pr(name, d * KT, KT).unsqueeze(2).to_broadcast([P, PAIRS, 64])
            def tokens(c, d):
                return slice(place_of(c, d) * CHUNK, place_of(c, d) * CHUNK + CHUNK)

            def x_tokens(c, d):
                return slice(tokens(c, d).start - SEQ, tokens(c, d).stop - SEQ)

            def raw_in(c):
                if c:
                    for d in range(2):
                        v.wait_ge(*after("u", c - 1, d))
                for n, buf, bias_name in (("w", WK["L"], "w0"), ("a", WK["A"], "a0")):
                    bias_ = pr(bias_name).rearrange("p (d a) -> p a d", d=2)
                    for part in range(2):
                        own = slice(4 * part, 4 * part + 4)
                        v.wait_ge(*after(n + "_raw", c, part))
                        tt(buf[:, :, own, :].rearrange("p d a i -> p a d i"),
                           psum(bank_of((n + "_raw", c, part))).rearrange("p (a d i) -> p a d i", d=2, i=CHUNK),
                           bias_[:, own, :].unsqueeze(3).to_broadcast([P, 4, 2, CHUNK]), add).then_inc(
                               *v.step("taken", n + "_raw", c, part))
                    v.mark(n + "_in", c)

            def running(c, d):
                E, A, L, C = (WK[n][:, d] for n in ("E", "A", "L", "C"))
                if c:
                    v.wait_ge(*after("s", c - 1, d))
                v.wait_ge(*after("w_in_sig", c, d))
                nc.vector.tensor_tensor_scan(flat(C), cn("scan_keep"), flat(L), 0.0, mul, add).then_inc(*v.step())
                v.wait_ge(*v.own)
                if d == 0:
                    tt(E, C, L, sub).then_inc(*v.step())
                else:
                    tt(E, C[:, :, 63:64].to_broadcast([P, PAIRS, 64]), C, sub).then_inc(*v.step())
                    v.wait_ge(*v.own)
                    tt(C, E, L, add).then_inc(*v.step())
                v.mark("running", c, d)

            def operands(c, d):
                main = c >= 4
                E, A, L, C, B, G = (WK[n][:, d] for n in ("E", "A", "L", "C", "B", "G"))
                AR = WK["AR"][:, d]
                kk, k = KK[:, :, tokens(c, d)], KR[:, :, tokens(c, d)]
                if c > 4:
                    v.wait_ge(*after("y", c - 1, d))
                v.wait_ge(*after("before", c, d))
                tt(AR[:, :, 0:64], kk, E, mul).then_inc(*v.step("alpha", c, d))
                v.wait_ge(*after("inverse_decay", c, d))
                v.wait_ge(*after("a_in_sig", c, d))
                v.wait_ge(*v.own)
                tt(E, kk, L, mul).then_inc(*v.step())
                v.wait_ge(*v.own)
                stt(flat(B), flat(E), -1.0, flat(A), mul, mul).then_inc(*v.step("beta", c, d))
                if main:
                    v.wait_ge(*after("decay", c, d))
                    tt(AR[:, :, 64:128], RR[:, :, x_tokens(c, d)], C, mul).then_inc(*v.step())
                v.mark("rho", c, d)
                v.wait_ge(*v.own)
                stt(E, A, 1.0, over_steps("ka"), sub, mul).then_inc(*v.step())
                v.wait_ge(*v.own)
                stt(E, E, 1.0, k, add, mul).then_inc(*v.step())
                v.wait_ge(*v.own)
                if main:
                    ks = WK["KS"][:, :, x_tokens(c, d)]
                    if c < 6:
                        nc.vector.tensor_copy(ks, E).then_inc(*v.step())
                    else:
                        tt(ks, ks, E, add).then_inc(*v.step())
                tt(G, E, L, mul).then_inc(*v.step("gamma", c, d))

            def state(c, d):
                main = c >= 4
                S = WK["S"][:, d]
                end = DEND[:, c % 2, d].unsqueeze(2).to_broadcast([P, PAIRS, 64])
                if main:
                    v.wait_ge(*after("y", c, d))
                    ys = WK["Y"][:, :, x_tokens(c, d)]
                    src = bank3(("y", c, d))
                    if c < 6:
                        nc.vector.tensor_copy(ys, src).then_inc(*v.step("taken", "y", c, d))
                    else:
                        tt(ys, ys, src, add).then_inc(*v.step("taken", "y", c, d))
                if c == 7:
                    return
                v.wait_ge(*after("s", c, d))
                v.wait_ge(*after("decay_end", c, d))
                if c:
                    tt(S, S, bank3(("s", c, d)), add).then_inc(*v.step("taken", "s", c, d))
                    v.wait_ge(*v.own)
                    tt(S, S, end, mul).then_inc(*v.step("state", c, d))
                else:
                    tt(S, bank3(("s", c, d)), end, mul).then_inc(*v.step("taken", "s", c, d))
                    v.mark("state", c, d)

            raw_in(0)
            for c in range(9):
                main = c >= 4
                for d in range(2):
                    if c < 8:
                        running(c, d)
                    if c:
                        state(c - 1, d)
                    if c < 8:
                        operands(c, d)
                if c == 8:
                    break
                for d in range(2):
                    X_, XI = WK["X"][:, d], WK["XI"][:, d]
                    I = cn("ident64").unsqueeze(1).to_broadcast([P, PAIRS, 64])
                    w = 128 if main else 64
                    bm, gm = WK["BM"][:, d], WK["GM"][:, d]
                    mask = cn("order", d * 128, w).unsqueeze(1).to_broadcast([P, 4, w])

                    def masked(name, dst):
                        for part in range(2):
                            v.wait_ge(*after(name, c, d, part))
                            src = psum(bank_of((name, c, d, part)), 0, 4 * w).rearrange("p (a b) -> p a b", b=w)
                            tt(dst[:, 4 * part:4 * part + 4, 0:w], src, mask, mul).then_inc(*v.step("taken", name, c, d, part))
                        v.mark(name + "_out", c, d)
                    masked("bm", bm)
                    first = cn("first_level", 64 * (1 - d), 64).unsqueeze(1).to_broadcast([P, PAIRS, 64])
                    v.wait_ge(*v.own)
                    tt(XI, bm[:, :, 0:64], first, mul).then_inc(*v.step())
                    v.wait_ge(*v.own)
                    tt(XI, XI, I, add).then_inc(*v.step("inverse_t", c, d, 0))
                    masked("gm", gm)
                for lv in range(1, LEVELS):
                    for d in range(2):
                        mask = cn("later_levels", (d * 5 + lv - 1) * 64, 64).unsqueeze(1).to_broadcast([P, PAIRS, 64])
                        v.wait_ge(*after("z", c, d, lv))
                        tt(WK["Z"][:, d], bank3(("z", c, d, lv)), mask, mul).then_inc(*v.step("taken", "z", c, d, lv))
                        v.mark("z_out", c, d, lv)
                    for d in range(2):
                        XI = WK["XI"][:, d]
                        v.wait_ge(*after("dxi", c, d, lv))
                        tt(XI, XI, bank3(("dxi", c, d, lv)), add).then_inc(*v.step("taken", "dxi", c, d, lv))
                        v.mark("inverse_t", c, d, lv)
                if c < 7:
                    raw_in(c + 1)
            v.mark("recurrence_done")

        VT = area(16896, KT, SEQ)
        YC = area(18944, KT, SEQ)
        Q1 = area(8192, KT, SEQ)
        Q2 = area(10240, KT, SEQ)
        RD = area(12288, KT, SEQ)

        def readout_tensor(pe):
            pe.stage("readout")
            I = cn("ident64")
            for part in range(4):
                b = take_bank(pe, ("vt", part))
                pe.wait_ge(*after("recurrence_done"))
                for n in range(2):
                    p = 2 * part + n
                    for c in range(4):
                        for h in range(2):
                            ins = nc.tensor.matmul(psum(b, n * SEQ + c * 64, 64, half(h)), VP[half(h), 4 + c, p, :],
                                                   I[half(h), :], start=True, stop=True)
                ins.then_inc(*pe.step("vt", part))
            for t in range(KT):
                b = take_bank(pe, ("y_mean", t))
                nc.tensor.matmul(psum(b, 0, SEQ), cn("block_ones"), WK["Y"][:, t], start=True, stop=True).then_inc(*pe.step("y_mean", t))
            for t in range(KT):
                b = take_bank(pe, ("bonus", t))
                pe.wait_ge(*after("rks", t))
                nc.tensor.matmul(psum(b, 0, SEQ), cn("block_ones"), Q2[:, t], start=True, stop=True).then_inc(*pe.step("bonus", t))
                b = take_bank(pe, ("y_var", t))
                pe.wait_ge(*after("yc_square", t))
                nc.tensor.matmul(psum(b, 0, SEQ), cn("block_ones"), Q1[:, t], start=True, stop=True).then_inc(*pe.step("y_var", t))
                b = take_bank(pe, ("gate", t))
                pe.wait_ge(*after("taken", "low_g"))
                pe.wait_ge(*after("gate_w2"))
                nc.tensor.matmul(psum(b, 0, SEQ), LOW["g2"][:, t * P:(t + 1) * P], GH, start=True, stop=True).then_inc(*pe.step("gate", t))

        def readout_scalar(act):
            act.stage("readout")
            for part in range(4):
                act.wait_ge(*after("vt", part))
                nc.scalar.activation(VT[:, 2 * part:2 * part + 2], psum(bank_of(("vt", part))).rearrange(
            "p (a b) -> p a b", b=SEQ), ACT.Copy).then_inc(*act.step("taken", "vt", part))
            for t in range(KT):
                act.wait_ge(*after("yc", t))
                nc.scalar.activation(Q1[:, t], YC[:, t], ACT.Square).then_inc(*act.step("yc_square", t))
            for t in range(KT):
                act.wait_ge(*after("y_var", t))
                nc.scalar.activation(RD[:, t], psum(bank_of(("y_var", t)), 0, SEQ), ACT.Sqrt,
                                     bias=cn("eps", 1, 1), scale=1.0 / HD).then_inc(*act.step("taken", "y_var", t))

        def readout_vector(v):
            v.stage("readout")
            stt, tt = nc.vector.scalar_tensor_tensor, nc.vector.tensor_tensor
            v.wait_ge(*v.own)
            for t in range(KT):
                v.wait_ge(*after("y_mean", t))
                stt(YC[:, t], psum(bank_of(("y_mean", t)), 0, SEQ), -1.0 / HD, WK["Y"][:, t], ALU.mult, ALU.add).then_inc(*v.step("taken", "y_mean", t))
                v.mark("yc", t)
            v.wait_ge(*after("y_mean", KT - 1))
            for t in range(KT):
                stt(Q2[:, t], RR[:, t], pr("rk", t, 1), WK["KS"][:, t], ALU.mult, ALU.mult).then_inc(*v.step("rks", t))
            v.wait_ge(*after("taken", "vt", 3))
            for t in range(KT):
                v.wait_ge(*after("bonus", t))
                tt(VT[:, t], psum(bank_of(("bonus", t)), 0, SEQ), VT[:, t], ALU.mult).then_inc(*v.step("taken", "bonus", t))
                v.wait_ge(*after("taken", "y_var", t))
                nc.vector.reciprocal(RD[:, t], RD[:, t]).then_inc(*v.step())
                v.wait_ge(*v.own)
                stt(YC[:, t], YC[:, t], pr("lng", t, 1), RD[:, t], ALU.mult, ALU.mult).then_inc(*v.step())
                v.wait_ge(*v.own)
                stt(YC[:, t], YC[:, t], pr("lnb", t, 1), VT[:, t], ALU.add, ALU.add).then_inc(*v.step())
                v.wait_ge(*v.own)
                v.wait_ge(*after("gate", t))
                tt(MIX[0][:, X, t, :], YC[:, t], psum(bank_of(("gate", t)), 0, SEQ), ALU.mult).then_inc(*v.step("taken", "gate", t))
                v.mark("read", t)

        CAT2 = area(12288, KT, SEQ)
        B2 = 31100

        def rope_tensor(pe, key, raw, g, ready):
            b = take_bank(pe, (key + "_rot", g))
            pe.wait_ge(*after(*ready))
            nc.tensor.matmul(psum(b, 0, SEQ), cn("swap"), raw, start=True, stop=True).then_inc(*pe.step(key + "_rot", g))

        def rope_pool(g_, key, g, raw, dst, ready):
            g_.wait_ge(*after(*ready))
            nc.gpsimd.tensor_tensor(dst, raw, cn("cos"), ALU.mult).then_inc(*g_.step(key + "_cos", g))

        def rope_vector(v, key, g, raw, dst):
            v.wait_ge(*after(key + "_rot", g))
            v.wait_ge(*after(key + "_cos", g))
            nc.vector.tensor_tensor(raw, psum(bank_of((key + "_rot", g)), 0, SEQ), cn("sin"), ALU.mult).then_inc(*v.step("taken", key + "_rot", g))
            v.wait_ge(*v.own)
            nc.vector.tensor_tensor(dst, dst, raw, ALU.add).then_inc(*v.step(key + "_roped", g))

        RAW = area(FREE, 16, SEQ)
        QK = area(FREE + 4096, 16, SEQ)
        VV = area(FREE + 8192, 2, D)
        OB = area(FREE + 10240, 4, SEQ)
        ATT_B = FREE + 11264
        LF = area(B2, 16)
        EV2 = Splits("ev2", ["ev2_in"], [(31200, 33248), (35296, 37344), (8192, 12288)])
        E2_BLOCKS = [("t", 0), ("t", 1), ("t", 2), ("t", 3), ("v", 0), ("v", 1), ("t", 4), ("t", 5), ("t", 6), ("t", 7),
                     ("v", 2), ("v", 3)]
        LAMBDA_INIT = 0.8 - 0.6

        def ev2_tensor(pe):
            pe.stage("project_ev2")
            prev = []
            for kind, n in E2_BLOCKS:
                j = EV2.next(pe, "ev2_in")
                if kind == "t":
                    for i in range(2):
                        b = take_bank(pe, ("e2", 2 * n + i))
                        ins = EV2.columns(pe, j, 256, i * P, psum(b, 0, SEQ), KT, x_high, x_low, norm="n1_2")
                        ins.then_inc(*pe.step("e2", 2 * n + i))
                    pe.mark("multiplied", j)
                else:
                    EV2.tokens(pe, j, ("e2v", n))
                for g in prev:
                    rope_tensor(pe, "e2", RAW[:, g], g, ("taken", "e2", g))
                prev = [2 * n, 2 * n + 1] if kind == "t" else []
            assert not prev

        def ev2_scalar(act):
            act.stage("project_ev2")
            for i, (kind, n) in enumerate(E2_BLOCKS):
                EV2.high(act, i + EV2.ahead)
                if kind == "t":
                    for g in (2 * n, 2 * n + 1):
                        act.wait_ge(*after("e2", g))
                        nc.scalar.activation(RAW[:, g], psum(bank_of(("e2", g)), 0, SEQ), ACT.Copy).then_inc(*act.step("taken", "e2", g))
                else:
                    act.wait_ge(*after("e2v", n))
                    nc.scalar.activation(VV[:, :, n * 256:(n + 1) * 256], psum(bank_of(("e2v", n))).rearrange(
                "p (a b) -> p a b", b=256), ACT.Copy).then_inc(*act.step("taken", "e2v", n))
            act.wait_ge(*after("lambda_sums"))
            nc.scalar.activation(LF[:, 4:6], psum(bank_of(("lambda_sums",)), 0, 2), ACT.Exp).then_inc(*act.step("taken", "lambda_sums"))

        def ev2_pool(g_):
            g_.stage("project_ev2")
            for g in range(16):
                rope_pool(g_, "e2", g, RAW[:, g], QK[:, g], ("taken", "e2", g))

        def lambda_tensor(pe):
            b = take_bank(pe, ("lambda_sums",))
            pe.wait_ge(*after("lambda_products"))
            nc.tensor.matmul(psum(b, 0, 2), cn("ones"), LF[:, 0:2], start=True, stop=True).then_inc(*pe.step("lambda_sums"))

        def ev2_vector(v):
            v.stage("project_ev2")
            lp = pr("lam")
            nc.vector.tensor_tensor(LF[:, 0:1], lp[:, 0:1], lp[:, 1:2], ALU.mult).then_inc(*v.step())
            nc.vector.tensor_tensor(LF[:, 1:2], lp[:, 2:3], lp[:, 3:4], ALU.mult).then_inc(*v.step("lambda_products"))
            for i in range(len(E2_BLOCKS)):
                EV2.low(v, i + EV2.ahead)
                if i and E2_BLOCKS[i - 1][0] == "t":
                    n = E2_BLOCKS[i - 1][1]
                    for g in (2 * n, 2 * n + 1):
                        rope_vector(v, "e2", g, RAW[:, g], QK[:, g])
            v.wait_ge(*after("taken", "lambda_sums"))
            nc.vector.memset(LF[:, 8:9], 1.0).then_inc(*v.step())
            nc.vector.tensor_tensor(LF[:, 6:7], LF[:, 5:6], LF[:, 4:5], ALU.subtract).then_inc(*v.step())
            v.wait_ge(*v.own)
            nc.vector.tensor_scalar(LF[:, 9:10], LF[:, 6:7], -LAMBDA_INIT, None, ALU.add).then_inc(*v.step("lambda"))

        def causal_pieces(n, col, dst, qt):
            full = [(n, col, dst, P, None)] if qt else []
            return full + [(n, col + qt * P, dst + qt * P, P, cn("causal"))]

        class CausalAttention(Attention):
            name, n, base = "causal_attention", 16, ATT_B
            place_free = ("differential_attention", "done")

            def ready(self, u):
                return (("e2_roped", 15),)

            def values_ready(self, u):
                return (("taken", "e2v", 3),)

            def scores(self, u):
                h, qt = divmod(u, 2)
                r = half(h)
                return [[(0, P * (qt + 1), QK[r, h // 2, qt * P:(qt + 1) * P], QK[r, 4 + h // 2, 0:P * (qt + 1)])]]

            def pieces(self, u):
                return causal_pieces(0, 0, 0, u % 2)

            def maps(self, u):
                return [(0, P * (u % 2 + 1))]

            def blocks(self, u):
                return [(i * P, P) for i in range(u % 2 + 1)]

            def values(self, u):
                h, qt = divmod(u, 2)
                return half(h), [VV[:, i, h * HD:(h + 1) * HD] for i in range(qt + 1)]

            def place(self, u):
                h, qt = divmod(u, 2)
                return CAT2[half(h), h // 2, qt * P:(qt + 1) * P]

        class DifferentialAttention(CausalAttention):
            name, n = "differential_attention", 8
            subtract = True
            place_free = ("e2_roped", 15)

            def factor(self, u):
                return LF[:, 8:10]

            def scores(self, u):
                h, qt = divmod(u, 2)
                w = P * (qt + 1)
                return [[(0, w, QK[half(m), 8 + h, qt * P:(qt + 1) * P], QK[half(m), 12 + h, 0:w])]
                        for m in range(2)]

            def pieces(self, u):
                return causal_pieces(0, 0, 0, u % 2) + causal_pieces(1, 0, 256, u % 2)

            def maps(self, u):
                w = P * (u % 2 + 1)
                return [(0, w), (256, w)]

            def values(self, u):
                h, qt = divmod(u, 2)
                return slice(0, P), [VV[:, i, 512 + h * P:512 + (h + 1) * P] for i in range(qt + 1)]

            def place(self, u):
                h, qt = divmod(u, 2)
                return OB[:, h, qt * P:(qt + 1) * P]

        CAU, DIF = CausalAttention(), DifferentialAttention()

        def subln_tensor(pe):
            pe.stage("head_norm")
            for h in range(4):
                b = take_bank(pe, ("head_sum", h))
                pe.wait_ge(*after("head_square", h))
                nc.tensor.matmul(psum(b, 0, SEQ), cn("ones"), RAW[:, h], start=True, stop=True).then_inc(*pe.step("head_sum", h))

        def subln_scalar(act):
            act.stage("head_norm")
            act.wait_ge(*act.own)
            for h in range(4):
                nc.scalar.activation(RAW[:, h], OB[:, h], ACT.Square).then_inc(*act.step("head_square", h))
            load_table(act, ACT.Sqrt)
            for h in range(4):
                act.wait_ge(*after("head_sum", h))
                nc.scalar.activation(RAW[:, 4 + h], psum(bank_of(("head_sum", h)), 0, SEQ), ACT.Sqrt,
                                     bias=cn("eps", 0, 1), scale=1.0 / P).then_inc(*act.step("taken", "head_sum", h))

        def subln_vector(v, h):
            if h == 0:
                nc.vector.tensor_scalar(LF[:, 10:11], pr("subln"), 1.0 - LAMBDA_INIT, None, ALU.mult).then_inc(*v.step())
            v.wait_ge(*after("taken", "head_sum", h))
            nc.vector.reciprocal(RAW[:, 4 + h], RAW[:, 4 + h]).then_inc(*v.step())
            v.wait_ge(*v.own)
            nc.vector.scalar_tensor_tensor(CAT2[:, 4 + h], OB[:, h], LF[:, 10:11], RAW[:, 4 + h],
                                           ALU.mult, ALU.mult).then_inc(*v.step("head_normed", h))

        CB = area(FREE, N_EXPERTS, SEQ)
        SG = area(FREE + 4096, 3, 512)
        AE = area(FREE + 5632, 3, 512)
        CT = area(FREE + 7168, SEQ)
        RT = FREE + 7424
        LG = area(RT, 2, 20)
        ROUTE_BANKS = [0, 1, 2, 7]
        SUM_BANKS = [3, 4, 5, 6]

        AE_HI = rounded("expert_high", 8192, 3, 512)
        AE_LO = rounded("expert_low", 37304, 3, 512)
        MOE = [Splits(f"moe{l}", [f"moe{l}"], [(25000 + 4096 * i, 27048 + 4096 * i) for i in range(3)]) for l in range(2)]
        EXPERT_ORDER = [("gate", 0), ("up", 0)]
        for e_ in range(1, N_EXPERTS):
            EXPERT_ORDER += [("gate", e_), ("up", e_), ("down", e_ - 1)]
        EXPERT_ORDER.append(("down", N_EXPERTS - 1))

        def moe_tensor(pe, l):
            pe.stage(f"router{l}")
            b = take_bank(pe, ("route", l), ROUTE_BANKS)
            for tt_ in range(2):
                for k in range(KT):
                    if tt_ == 0:
                        pe.wait_ge(*after("h", f"n2_{l + 2}", k, X))
                    ins = nc.tensor.matmul(psum(b, tt_ * 20, 20), HT[:, X, k, tt_ * P:(tt_ + 1) * P],
                                           pr("router_w", (l * KT + k) * 20, 20), start=(k == 0), stop=(k == KT - 1))
            ins.then_inc(*pe.step("route", l))

            def gate_up(e):
                for which in ("gate", "up"):
                    j = MOE[l].next(pe, f"moe{l}")
                    b = take_bank(pe, (which, l, e), ROUTE_BANKS)
                    for i in range(2):
                        ins = MOE[l].columns(pe, j, 256, i * P, psum(b, i * SEQ, SEQ), KT, x_high, x_low,
                                             norm=f"n2_{l + 2}")
                    ins.then_inc(*pe.step(which, l, e))
                    pe.mark("multiplied", j)

            def down(e):
                j = MOE[l].next(pe, f"moe{l}")
                pe.wait_ge(*after("expert", l, e))
                if e == 0:
                    for bk in SUM_BANKS:
                        if bank_state["holder"][bk] is not None:
                            pe.wait_ge(*after("taken", *bank_state["holder"][bk]))
                        bank_state["holder"][bk] = ("moe_y", l, bk)
                        events.where[("moe_y", l, bk)] = bk
                for t in range(KT):
                    ins = MOE[l].columns(pe, j, D, t * P, psum(3 + t // 2, (t % 2) * SEQ, SEQ), 2,
                                                lambda k: AE_HI[:, e % 3, k * SEQ:(k + 1) * SEQ],
                                                lambda k: AE_LO[:, e % 3, k * SEQ:(k + 1) * SEQ],
                                                start=e == 0 and t % 2 == 0, stop=e == N_EXPERTS - 1, check=True)
                ins.then_inc(*pe.step("down", l, e))
                pe.mark("multiplied", j)

            gate_up(0)
            b = take_bank(pe, ("comb_t", l), SUM_BANKS)
            pe.wait_ge(*after("comb", l))
            for tt_ in range(2):
                ins = nc.tensor.transpose(psum(b, tt_ * P, P, slice(0, 16)), COMB[:, tt_, :], cn("ident"))
            ins.then_inc(*pe.step("comb_t", l))
            for n in range(8):
                b = take_bank(pe, ("comb_rows", l, n), SUM_BANKS)
                pe.wait_ge(*after("taken", "comb_t", l))
                for i in range(2):
                    e = 2 * n + i
                    pick = cn("ident", e, 1, slice(0, 16)).to_broadcast([16, P])
                    ins = nc.tensor.matmul(psum(b, i * SEQ, SEQ), pick, CT[0:16, :], start=True, stop=True)
                ins.then_inc(*pe.step("comb_rows", l, n))
            for e in range(1, N_EXPERTS):
                gate_up(e)
                down(e - 1)
            down(N_EXPERTS - 1)

        COMB = area(RT + 200, 2, 16)

        def moe_vector(v, l):
            v.stage(f"router{l}")
            tt, ts = nc.vector.tensor_tensor, nc.vector.tensor_scalar
            at_ = [RT + 400]

            def tmp(*dims):
                r = area(at_[0], *dims)
                at_[0] += int(np.prod(dims))
                return r

            def step(ins):
                ins.then_inc(*v.step())
                v.wait_ge(*v.own)
            low_vector(v, f"n2_{l + 2}", [X])
            v.wait_ge(*after("route", l))
            bias_ = pr("router_b", l * 20, 20).unsqueeze(1).to_broadcast([P, 2, 20])
            tt(LG, psum(bank_of(("route", l)), 0, 40).rearrange("p (a b) -> p a b", b=20), bias_, ALU.add).then_inc(*v.step("taken", "route", l))
            v.wait_ge(*v.own)
            GL = LG[:, :, 0:4]

            def four(x):
                return x.unsqueeze(2).to_broadcast([P, 2, 4])

            def first_max(x):
                m, o, t = tmp(2), tmp(2, 4), tmp(2)
                step(nc.vector.tensor_reduce(m, x, AX.X, ALU.max))
                step(tt(o, x, four(m), ALU.is_equal))
                step(tt(o, o, cn("tie").unsqueeze(1).to_broadcast([P, 2, 4]), ALU.mult))
                step(nc.vector.tensor_reduce(t, o, AX.X, ALU.max))
                step(tt(o, o, four(t), ALU.is_equal))
                return m, o
            gm, goh = first_max(GL)
            z, zs, gw = tmp(2, 4), tmp(2), tmp(2)
            tt(z, GL, four(gm), ALU.subtract).then_inc(*v.step("group_less", l))
            big, elg = tmp(2, 4, 4), tmp(2, 4)
            v.wait_ge(*v.own)
            step(tt(big, LG[:, :, 4:20].rearrange("p t (g e) -> p t g e", e=4),
                    goh.unsqueeze(3).to_broadcast([P, 2, 4, 4]), ALU.mult))
            step(nc.vector.tensor_reduce(elg, big.rearrange("p t g e -> p t e g"), AX.X, ALU.add))
            m1, oh1 = first_max(elg)
            el2 = tmp(2, 4)
            step(nc.vector.scalar_tensor_tensor(el2, oh1, NEG, elg, ALU.mult, ALU.add))
            m2, oh2 = first_max(el2)
            d, w1, w2 = tmp(2), tmp(2), tmp(2)
            tt(d, m2, m1, ALU.subtract).then_inc(*v.step("top_less", l))
            v.wait_ge(*after("route_exp", l))
            step(nc.vector.tensor_reduce(zs, z, AX.X, ALU.add))
            step(nc.vector.reciprocal(gw, zs))
            step(ts(w1, d, 1.0, None, ALU.add))
            step(nc.vector.reciprocal(w1, w1))
            step(tt(w1, w1, gw, ALU.mult))
            step(tt(w2, d, w1, ALU.mult))
            step(tt(oh1, oh1, four(w1), ALU.mult))
            step(tt(oh2, oh2, four(w2), ALU.mult))
            step(tt(oh1, oh1, oh2, ALU.add))
            tt(COMB.rearrange("p t (g e) -> p t g e", e=4), goh.unsqueeze(3).to_broadcast([P, 2, 4, 4]),
               oh1.unsqueeze(2).to_broadcast([P, 2, 4, 4]), ALU.mult).then_inc(*v.step("comb", l))
            v.stage(f"experts{l}")
            for n in range(1, 8, 2):
                v.wait_ge(*after("comb_rows", l, n))
                nc.vector.tensor_copy(CB[:, 2 * n:2 * n + 2], psum(bank_of(("comb_rows", l, n))).rearrange(
              "p (a b) -> p a b", b=SEQ)).then_inc(*v.step("taken", "comb_rows", l, n))
                v.mark("comb_rows_out", l, n)
            for i, (which, e) in enumerate(EXPERT_ORDER):
                MOE[l].low(v, i + MOE[l].ahead)
                if which != "up":
                    continue
                a_ = AE[:, e % 3]
                v.wait_ge(*after("silu", l, e))
                v.wait_ge(*after("up", l, e))
                if e >= 3:
                    v.wait_ge(*after("down", l, e - 3))
                tt(a_, SG[:, e % 3], psum(bank_of(("up", l, e))), ALU.mult).then_inc(*v.step("taken", "up", l, e))
                v.wait_ge(*after("comb_rows_out", l, (e // 2) & ~1))
                v.wait_ge(*v.own)
                a2 = a_.rearrange("p (a b) -> p a b", b=SEQ)
                tt(a2, a2, CB[:, e].unsqueeze(1).to_broadcast([P, 2, SEQ]), ALU.mult).then_inc(*v.step())
                v.wait_ge(*v.own)
                nc.vector.tensor_copy(AE_HI[:, e % 3], a_).then_inc(*v.step())
                v.wait_ge(*v.own)
                tt(AE_LO[:, e % 3], a_, AE_HI[:, e % 3], ALU.subtract).then_inc(*v.step("expert", l, e))
            v.wait_ge(*after("down", l, N_EXPERTS - 1))
            for b in (4, 6):
                t = 2 * (b - 3)
                nc.vector.tensor_copy(YT[:, X, t:t + 2, :], psum(b).rearrange("p (a b) -> p a b", b=SEQ)).then_inc(*v.step("taken", "moe_y", l, b))
            v.mark("y_all2", f"moe{l}")

        Z_AT = RT + 400 + 2 + 8 + 2
        D_AT = Z_AT + 8 + 2 + 2 + 32 + 8 + 12 + 8 + 12

        def moe_scalar(act, l):
            act.stage(f"router{l}")
            z, d = area(Z_AT, 8), area(D_AT, 2)
            load_table(act, ACT.Exp)
            act.wait_ge(*after("group_less", l))
            nc.scalar.activation(z, z, ACT.Exp).then_inc(*act.step())
            act.wait_ge(*after("top_less", l))
            nc.scalar.activation(d, d, ACT.Exp).then_inc(*act.step("route_exp", l))
            act.wait_ge(*after("comb_t", l))
            nc.scalar.activation(CT[0:16, :], psum(bank_of(("comb_t", l)), 0, SEQ, slice(0, 16)), ACT.Copy).then_inc(*act.step("taken", "comb_t", l))
            act.stage(f"experts{l}")
            for n in range(0, 8, 2):
                act.wait_ge(*after("comb_rows", l, n))
                nc.scalar.activation(CB[:, 2 * n:2 * n + 2], psum(bank_of(("comb_rows", l, n))).rearrange(
            "p (a b) -> p a b", b=SEQ), ACT.Copy).then_inc(*act.step("taken", "comb_rows", l, n))
                act.mark("comb_rows_out", l, n)
            for i, (which, e) in enumerate(EXPERT_ORDER):
                MOE[l].high(act, i + MOE[l].ahead)
                if which != "gate":
                    continue
                act.wait_ge(*after("gate", l, e))
                if e >= 3:
                    act.wait_ge(*after("taken", "up", l, e - 3))
                nc.scalar.activation(SG[:, e % 3], psum(bank_of(("gate", l, e))), ACT.Silu).then_inc(*act.step("taken", "gate", l, e))
                act.mark("silu", l, e)
            act.wait_ge(*after("down", l, N_EXPERTS - 1))
            for b in (3, 5):
                t = 2 * (b - 3)
                nc.scalar.activation(YT[:, X, t:t + 2, :], psum(b).rearrange("p (a b) -> p a b", b=SEQ),
                                     ACT.Copy).then_inc(*act.step("taken", "moe_y", l, b))
            act.mark("y_all", f"moe{l}")

        RQ = area(FREE, KT, SEQ)
        RK = area(FREE + 2048, 4, 4, SEQ)
        QR = area(FREE + 6144, KT, SEQ)
        KRT = area(FREE + 8192, 3, 4, SEQ)
        ATT_C = FREE + 11264
        VS = area(B2, 2, 256)
        VW = area(B2 + 512, 2, 256)
        BK = area(B2 + 1024, 2, 16, 4, N_CMP)
        HC = area(B2 + 2944, 2, 2, 4 * N_CMP)
        KC = area(B2 + 3184, 4 * N_CMP)
        VC = area(B2 + 3244, 4, HD)
        GT = area(B2 + 3500, 2, 48)
        ROPED = {0: 0, 2: 1, 3: 2}
        OD = Splits("od", ["od_in"], [(34704, 36752), (8192, 12288)])
        OD_BLOCKS = [("q", 0), ("q", 1), ("q", 2), ("q", 3), ("k", 0), ("k", 1), ("k", 2), ("v", 0), ("k", 3), ("v", 1)]

        def od_tensor(pe):
            pe.stage("project_od")
            prev = []
            for kind, n in OD_BLOCKS:
                j = OD.next(pe, "od_in")
                if kind == "v":
                    OD.tokens(pe, j, ("odv", n))
                else:
                    for i in range(2):
                        b = take_bank(pe, ("od" + kind, 2 * n + i))
                        ins = OD.columns(pe, j, 256, i * P, psum(b, 0, SEQ), KT, x_high, x_low, norm="n1_3")
                        ins.then_inc(*pe.step("od" + kind, 2 * n + i))
                    pe.mark("multiplied", j)
                for e in prev:
                    rope_tensor(pe, "od", *e)
                prev = od_ropes(kind, n)
            b = take_bank(pe, ("od_gates",))
            for tt_ in range(2):
                for k in range(KT):
                    ins = nc.tensor.matmul(psum(b, tt_ * 48, 48), HT[:, X, k, tt_ * P:(tt_ + 1) * P],
                                           pr("gate_w", k * 48, 48), start=(k == 0), stop=(k == KT - 1))
            ins.then_inc(*pe.step("od_gates"))

        def od_ropes(kind, n):
            if kind == "q":
                return [(RQ[:, g], g, ("taken", "odq", g)) for g in (2 * n, 2 * n + 1)]
            if kind == "k" and n in ROPED:
                return [(RK[:, n, g], 8 + 4 * ROPED[n] + g, ("taken", "odk", 2 * n + g // 2)) for g in range(4)]
            return []

        def od_dst(g):
            return QR[:, g] if g < 8 else KRT[:, (g - 8) // 4, (g - 8) % 4]

        def od_scalar(act):
            act.stage("project_od")
            for b_, (kind, n) in enumerate(OD_BLOCKS):
                OD.high(act, b_ + OD.ahead)
                if kind == "q":
                    for g in (2 * n, 2 * n + 1):
                        act.wait_ge(*after("odq", g))
                        nc.scalar.activation(RQ[:, g], psum(bank_of(("odq", g)), 0, SEQ), ACT.Copy).then_inc(*act.step("taken", "odq", g))
                elif kind == "k":
                    for i in range(2):
                        act.wait_ge(*after("odk", 2 * n + i))
                        for head, half_ in ((0, 0), (0, 1), (1, 0), (1, 1)):
                            ins = nc.scalar.activation(RK[half(half_), n, 2 * i + head],
                                                       psum(bank_of(("odk", 2 * n + i)), 0, SEQ, half(head)), ACT.Copy)
                            ins.then_inc(*act.step())
                        act.mark("taken", "odk", 2 * n + i)
                else:
                    act.wait_ge(*after("odv", n))
                    nc.scalar.activation(VS if n == 0 else VW, psum(bank_of(("odv", n))).rearrange(
                "p (a b) -> p a b", b=256), ACT.Copy).then_inc(*act.step("taken", "odv", n))
            act.wait_ge(*after("od_gates"))
            nc.scalar.activation(GT, psum(bank_of(("od_gates",)), 0, 96).rearrange("p (a b) -> p a b", b=48),
                                 ACT.Sigmoid).then_inc(*act.step("taken", "od_gates"))

        def od_pool(g_):
            g_.stage("project_od")
            for kind, n in OD_BLOCKS:
                for raw, g, ready in od_ropes(kind, n):
                    rope_pool(g_, "od", g, raw, od_dst(g), ready)

        def od_vector(v):
            v.stage("project_od")
            for i in range(len(OD_BLOCKS)):
                OD.low(v, i + OD.ahead)
                if i == 0:
                    continue
                for raw, g, _ in od_ropes(*OD_BLOCKS[i - 1]):
                    rope_vector(v, "od", g, raw, od_dst(g))
                if OD_BLOCKS[i - 1] == ("k", 1):
                    windows_vector(v)
            v.wait_ge(*after("taken", "od_gates"))
            for qt in range(2):
                c = GT[:, qt, :].rearrange("p (h b) -> p h b", b=3)[:, :, 0:1]
                nc.vector.tensor_scalar(c, c, cn("cmp_live", qt, 1), None, ALU.mult).then_inc(*v.step())
            v.mark("gates")

        def windows_vector(v):
            v.wait_ge(*after("taken", "odk", 3))
            v.wait_ge(*v.own)
            for which, src in ((0, KRT[:, 0]), (1, RK[:, 1])):
                for h in range(2):
                    for g in range(4):
                        rows = half(h)
                        base = src[rows, g, :]
                        lo = base[:, 0:240].rearrange("p (n l o) -> p l n o", l=8, o=2)[:, :, :, h]
                        hi = base[:, 16:256].rearrange("p (n l o) -> p l n o", l=8, o=2)[:, :, :, h]
                        pos = pr("cmp_pos", which * 16, 16, rows)
                        for part, s in ((0, lo), (1, hi)):
                            nc.vector.tensor_tensor(
                          BK[rows, which, 8 * part:8 * part + 8, g, :], s,
                          pos[:, 8 * part:8 * part + 8].unsqueeze(2).to_broadcast([HD, 8, N_CMP]), ALU.add).then_inc(*v.step())
            v.mark("windows")

        def compress_tensor(pe):
            pe.stage("compress")
            pe.wait_ge(*after("windows"))
            for which, name in ((0, "cmp_k"), (1, "cmp_v")):
                banks = [take_bank(pe, ("cmp", which, ft)) for ft in range(2)]
                for part in range(2):
                    j = next_block(pe, name)
                    for ft in range(2):
                        for k in range(KT):
                            t = part * 8 + k
                            ins = nc.tensor.matmul(psum(banks[ft], 0, 4 * N_CMP), slot(j, k, 256, ft * P, P),
                                                   BK[:, which, t].rearrange("p g n -> p (g n)"), start=(t == 0),
                                                   stop=(t == 15))
                        ins.then_inc(*pe.step("cmp", which, ft, part))
                    pe.mark("used", j)
            w2 = lambda which, ft: pr("cmp_w2", (which * 2 + ft) * 64, 64)
            b = take_bank(pe, ("cmp_k2",))
            pe.wait_ge(*after("cmp_hidden", 0, 1))
            for h in range(2):
                for ft in range(2):
                    ins = nc.tensor.matmul(psum(b, 0, 4 * N_CMP, half(h)), w2(0, ft), HC[:, 0, ft], start=(ft == 0),
                                           stop=(ft == 1))
            ins.then_inc(*pe.step("cmp_k2"))
            b = take_bank(pe, ("cmp_v2",))
            pe.wait_ge(*after("cmp_hidden", 1, 1))
            for g in range(4):
                for ft in range(2):
                    ins = nc.tensor.matmul(psum(b, g * HD, HD, slice(0, N_CMP)), HC[:, 1, ft, g * N_CMP:(g + 1) * N_CMP],
                                           w2(1, ft), start=(ft == 0), stop=(ft == 1))
            ins.then_inc(*pe.step("cmp_v2"))

        def compress_scalar(act):
            act.stage("compress")
            for which in range(2):
                for ft in range(2):
                    act.wait_ge(*after("cmp", which, ft, 1))
                    nc.scalar.activation(HC[:, which, ft], psum(bank_of(("cmp", which, ft)), 0, 4 * N_CMP),
                                         ACT.Gelu_apprx_tanh, bias=pr("cmp_b1", which * 2 + ft, 1)).then_inc(*act.step("taken", "cmp", which, ft))
                    act.mark("cmp_hidden", which, ft)
            act.wait_ge(*after("cmp_k2"))
            nc.scalar.activation(KC, psum(bank_of(("cmp_k2",)), 0, 4 * N_CMP), ACT.Identity,
                                 bias=pr("cmp_b2k")).then_inc(*act.step("taken", "cmp_k2"))

        def compress_vector(v):
            v.stage("compress")
            v.wait_ge(*after("cmp_v2"))
            r = slice(0, N_CMP)
            nc.vector.tensor_tensor(VC[r], psum(bank_of(("cmp_v2",)), 0, 256, r).rearrange("p (a b) -> p a b", b=HD),
                                    pr("cmp_b2v", rows=r).unsqueeze(1).to_broadcast([N_CMP, 4, HD]), ALU.add).then_inc(*v.step("taken", "cmp_v2"))

        class SparseAttention(Attention):
            name, n, base = "sparse_attention", 32, ATT_C
            place_free = ("gates",)

            def factor(self, u):
                h, qt = divmod(u, 2)
                return GT[:, qt, 3 * h:3 * h + 3]

            def ready(self, u):
                return (("od_roped", 19), ("taken", "cmp_k2"))

            def values_ready(self, u):
                return (("taken", "cmp_v2"), ("taken", "odv", 1))

            def scores(self, u):
                h, qt = divmod(u, 2)
                g, r, w = h // 4, half(h), P * (qt + 1)
                q = QR[r, h // 2, qt * P:(qt + 1) * P]
                first = [(0, N_CMP, q, KC[r, g * N_CMP:(g + 1) * N_CMP]), (16, w, q, KRT[r, 1, g, 0:w])]
                last = (144 if qt == 0 else 0, w, q, KRT[r, 2, g, 0:w])
                return [first + [last]] if qt == 0 else [first, [last]]

            def pieces(self, u):
                qt = u % 2
                last = (0, 144) if qt == 0 else (1, 0)
                return ([(0, 0, 0, N_CMP, cn("cmp_mask", qt * N_CMP, N_CMP))] + causal_pieces(0, 16, 16, qt)
                        + causal_pieces(*last, 272, qt))

            def maps(self, u):
                w = P * (u % 2 + 1)
                return [(0, N_CMP), (16, w), (272, w)]

            def blocks(self, u):
                n = u % 2 + 1
                return [(0, N_CMP)] + [(16 + i * P, P) for i in range(n)] + [(272 + i * P, P) for i in range(n)]

            def values(self, u):
                h, qt = divmod(u, 2)
                g, n = h // 4, qt + 1
                return half(h), ([VC[0:N_CMP, g]] + [VS[:, i, g * HD:(g + 1) * HD] for i in range(n)]
                                 + [VW[:, i, g * HD:(g + 1) * HD] for i in range(n)])

            def place(self, u):
                h, qt = divmod(u, 2)
                return CAT2[half(h), h // 2, qt * P:(qt + 1) * P]

        SPA = SparseAttention()

        def final_vector(v):
            v.stage("final")
            v.wait_ge(*after("rms", "final"))
            v.wait_ge(*v.own)
            for k in range(KT):
                nc.vector.scalar_tensor_tensor(HT[:, X, k, :], XT[:, X, k, :], pr("final_g2", k, 1), RS[:, X, :],
                                               ALU.mult, ALU.mult).then_inc(*v.step("final", k))

        BOTH, ONE = [CTX, X], [X]
        block = ctx.enter_context(nc.Block())

        def first_blocks(q, split, n=2):
            return lambda g: split(q, (g - 4) // 2) if g >= 4 and (g - 4) // 2 < n else None

        def queue(eng, name):
            return Steps(eng, semaphore, events, name)

        @block.sync
        def _(eng):
            sp = queue(eng, "sync")
            load_blocks(sp)
            for k in range(KT):
                sp.wait_ge(*after("final", k))
            eng.dma_start(out_t, HT[:, X].rearrange("p a b -> p (a b)")).then_inc(*sp.step(by=16, sem="out_written"))
            sp.wait_ge(*sp.own)

        @block.gpsimd
        def _(eng):
            g = queue(eng, "gpsimd")
            loads_pool(g)
            pool_pool(g)
            load_low_rank(g)
            ev2_pool(g)
            od_pool(g)

        @block.tensor
        def _(eng):
            pe = queue(eng, "tensor")
            pe.stage("mod")
            for n in (0, 2, 4, 6):
                mod_block(pe, n)
            mod_sum(pe, 0, 1)
            mod_sum(pe, 0, 3)
            rms_tensor(pe, "n1_0", BOTH)
            pe.stage("mod_b")
            mod_sum(pe, 0, 5)
            mod_sum(pe, 0, 7)
            pe.at_block = FIRST_MODS
            ev_in_tensor(pe)
            att_tensor(pe, LAT)
            att_tensor(pe, CON)
            pool_tensor(pe)
            cat_ready = lambda k: [("pool_done",), ("context_attention", "done")]
            project_tensor(pe, "x01", "ev_out", lambda k: CAT[:, :, k, :], cat_ready, BOTH)
            rms_tensor(pe, "y_x01", BOTH)
            rms_tensor(pe, "n2_0", BOTH)
            mlp0_tensor(pe)
            rms_tensor(pe, "y_x02", BOTH)
            rms_tensor(pe, "n1_1", BOTH)
            features_tensor(pe)
            wkv_tensor(pe)
            readout_tensor(pe)
            project_tensor(pe, "x11", "wo", lambda k: MIX[0][:, X, k, :], lambda k: [("read", k)], ONE)
            rms_tensor(pe, "y_x11", ONE)
            rms_tensor(pe, "n2_1", ONE)
            mlp_split_tensor(pe)
            rms_tensor(pe, "y_x12", ONE)
            rms_tensor(pe, "n1_2", ONE)
            ev2_tensor(pe)
            lambda_tensor(pe)
            att_tensor(pe, DIF)
            subln_tensor(pe)
            att_tensor(pe, CAU)
            project_tensor(pe, "x21", "ev2_out", lambda k: CAT2[:, k, :],
                           lambda k: [("causal_attention", "done"), ("head_normed", 3)], ONE)
            rms_tensor(pe, "n2_2", ONE)
            moe_tensor(pe, 0)
            rms_tensor(pe, "n1_3", ONE)
            od_tensor(pe)
            compress_tensor(pe)
            att_tensor(pe, SPA)
            project_tensor(pe, "x31", "od_out", lambda k: CAT2[:, k, :], lambda k: [("sparse_attention", "done")], ONE)
            rms_tensor(pe, "n2_3", ONE)
            moe_tensor(pe, 1)
            rms_tensor(pe, "final", ONE)

        @block.scalar
        def _(eng):
            act = queue(eng, "scalar")

            def norm_split(key, m, half_, inputs, meanwhile=None, segs=ONE):
                rms_scalar(act, key, XT, segs, inputs, meanwhile)
                modulate_split_scalar(act, key, m, half_, segs)

            def before_mlp(key, norm, m, half_, segs, after):
                rms_scalar(act, norm, XT, segs, after)
                modulate_scalar(act, norm, m, half_, segs)

            silu_c(act)
            before_mlp(None, "n1_0", 0, 0, BOTH, [("x0",), ("consts",)])
            ev_out_of(act, 0, act_copy)
            att_scalar(act, LAT)
            att_scalar(act, CON)
            pool_scalar(act)
            take_out(act, "x01", range(0, KT, 2), y_place(BOTH), BOTH, "y_all")
            rms_scalar(act, "y_x01", YT, BOTH, [("y_all2", "x01"), ("y_all", "x01")], lambda: MLP0.high(act, 0))
            norm_split("n2_0", 0, 1, [("x", "x01")], lambda: MLP0.high(act, 1), BOTH)
            mlp0_scalar(act)
            rms_scalar(act, "y_x02", YT, BOTH, [("mod_summed", 2, 23), ("y_all2", "x02_down"), ("y_all", "x02_down")])
            before_mlp(None, "n1_1", 1, 0, BOTH, [("x", "x02")])
            features_scalar(act)
            wkv_scalar(act)
            readout_scalar(act)
            take_out(act, "x11", range(0, KT, 2), y_place(ONE), ONE, "y_all", then=first_blocks(act, MLP.high, 1))
            rms_scalar(act, "y_x11", YT, ONE, [("y_all2", "x11"), ("y_all", "x11")])
            norm_split("n2_1", 1, 1, [("x", "x11")])
            mlp_split_scalar(act)
            rms_scalar(act, "y_x12", YT, ONE, [("mod_summed", 3, 23), ("y_all2", "x12_down"), ("y_all", "x12_down")],
                       lambda: EV2.high(act, 0))
            norm_split("n1_2", 2, 0, [("x", "x12")], lambda: EV2.high(act, 1))
            ev2_scalar(act)
            att_scalar(act, DIF)
            subln_scalar(act)
            att_scalar(act, CAU)
            take_out(act, "x21", range(0, KT, 2), y_place(ONE), ONE, "y_all", then=first_blocks(act, MOE[0].high))
            norm_split("n2_2", 2, 1, [("x", "x21")])
            moe_scalar(act, 0)
            norm_split("n1_3", 3, 0, [("x", "moe0")], lambda: OD.high(act, 0))
            od_scalar(act)
            compress_scalar(act)
            att_scalar(act, SPA)
            take_out(act, "x31", range(0, KT, 2), y_place(ONE), ONE, "y_all", then=first_blocks(act, MOE[1].high))
            norm_split("n2_3", 3, 1, [("x", "x31")])
            moe_scalar(act, 1)
            rms_scalar(act, "final", XT, ONE, [("x", "moe1")])

        @block.vector
        def _(eng):
            v = queue(eng, "vector")

            def norm(key, m, half_, segs, after, freed=(), meanwhile=None):
                rms_vector(v, key, XT, segs, after, meanwhile)
                modulate_vector(v, key, m, half_, segs, freed)

            def y_norm(key, segs):
                rms_vector(v, "y_" + key, YT, segs, [("y_all", key), ("y_all2", key)])

            v.stage("mod")
            mod_chain(v, 1)
            mod_chain(v, 3)

            def more_chains():
                v.stage("mod")
                mod_chain(v, 5)
                mod_chain(v, 7)

            rms_vector(v, "n1_0", XT, BOTH, [("x0",)], more_chains)
            mod_vectors(v, 0, range(2))
            v.at_block = FIRST_MODS
            modulate_vector(v, "n1_0", 0, 0, BOTH, [])
            ev_out_of(v, 1, dve_copy)
            mod_vectors(v, 0, range(2, 6))
            att_vector(v, LAT)
            att_vector(v, CON)
            take_out(v, "x01", range(1, KT, 2), y_place(BOTH), BOTH, "y_all2")
            rms_vector(v, "y_x01", YT, BOTH, [("y_all", "x01"), ("y_all2", "x01")], lambda: MLP0.low(v, 0))
            residual_vector(v, "x01", 0, 0, BOTH, True)
            norm("n2_0", 0, 1, BOTH, [("x", "x01")], meanwhile=lambda: MLP0.low(v, 1))
            low_vector(v, "n2_0", BOTH)
            mlp0_vector(v)
            rms_vector(v, "y_x02", YT, BOTH, [("mod_summed", 2, 23), ("y_all", "x02_down"), ("y_all2", "x02_down")])
            residual_vector(v, "x02", 0, 1, BOTH, True)
            norm("n1_1", 1, 0, BOTH, [("x", "x02")])
            mixes_vector(v)
            wkv_vector(v)
            readout_vector(v)
            take_out(v, "x11", range(1, KT, 2), y_place(ONE), ONE, "y_all2", then=first_blocks(v, MLP.low, 1))
            rms_vector(v, "y_x11", YT, ONE, [("y_all", "x11"), ("y_all2", "x11")])
            residual_vector(v, "x11", 1, 0, ONE, True)
            norm("n2_1", 1, 1, ONE, [("x", "x11")])
            low_vector(v, "n2_1", ONE)
            mod_vectors(v, 2)
            mlp_split_vector(v)
            rms_vector(v, "y_x12", YT, ONE, [("mod_summed", 3, 23), ("y_all", "x12_down"), ("y_all2", "x12_down")],
                       lambda: EV2.low(v, 0))
            residual_vector(v, "x12", 1, 1, ONE, True)
            norm("n1_2", 2, 0, ONE, [("x", "x12")], meanwhile=lambda: EV2.low(v, 1))
            low_vector(v, "n1_2", ONE)
            mod_vectors(v, 3)
            ev2_vector(v)
            att_vector(v, DIF)
            att_vector(v, CAU, {3: lambda: subln_vector(v, 0), 6: lambda: subln_vector(v, 1),
                                9: lambda: subln_vector(v, 2), 12: lambda: subln_vector(v, 3)})
            take_out(v, "x21", range(1, KT, 2), y_place(ONE), ONE, "y_all2", then=first_blocks(v, MOE[0].low))
            residual_vector(v, "x21", 2, 0, ONE, False)
            norm("n2_2", 2, 1, ONE, [("x", "x21")])
            moe_vector(v, 0)
            residual_vector(v, "moe0", 2, 1, ONE, False)
            norm("n1_3", 3, 0, ONE, [("x", "moe0")], meanwhile=lambda: OD.low(v, 0))
            low_vector(v, "n1_3", ONE)
            od_vector(v)
            compress_vector(v)
            att_vector(v, SPA)
            take_out(v, "x31", range(1, KT, 2), y_place(ONE), ONE, "y_all2", then=first_blocks(v, MOE[1].low))
            residual_vector(v, "x31", 3, 0, ONE, False)
            norm("n2_3", 3, 1, ONE, [("x", "x31")])
            moe_vector(v, 1)
            residual_vector(v, "moe1", 3, 1, ONE, False)
            rms_vector(v, "final", XT, ONE, [("x", "moe1")])
            final_vector(v)
    return events


def kernel(**inputs):
    import concourse.bacc as bacc
    from concourse.bass_utils import run_bass_kernel_spmd

    a = {n: np.asarray(x) for n, x in inputs.items()}

    def features_first(x):
        return x.reshape(SEQ, KT, P).transpose(2, 1, 0)

    arrays = {
        "weights": weight_blocks(a),
        "consts": constants(),
        "params": parameters(a),
        "small": small_weights(a),
        "bias": position_bias(a["ev_rpb"]),
        "x_t": np.ascontiguousarray(np.stack([features_first(a["ctx"]), features_first(a["x"])], 1).reshape(P, -1)),
    }
    arrays["pool_inv"] = pool_inverses()

    def build(events):
        nc = bacc.Bacc("TRN2", target_bir_lowering=False, num_devices=1)
        aps = [nc.dram_tensor(n, arrays[n].shape, FP32, kind="ExternalInput").ap()
               for n in ("weights", "consts", "params", "small", "bias", "pool_inv", "x_t")]
        out = nc.dram_tensor("out_t", (P, KT * SEQ), FP32, kind="ExternalOutput").ap()
        return nc, bass_two_blocks(nc, *aps, out, events)

    counted = build(Events())[1]
    nc, _ = build(Events(counted))
    r = run_bass_kernel_spmd(nc, [arrays], core_ids=[0])
    out = np.asarray(r.results[0]["out_t"]).reshape(P, KT, SEQ)
    return np.ascontiguousarray(out.transpose(2, 1, 0).reshape(1, SEQ, D))
```
